# Optimizing a Trainium2 kernel written in Bass

```python
import jax
import jax.numpy as jnp
from jax import lax
import numpy as np
import math
import jax, jax.numpy as jnp

D_MODEL = 1024
BATCH = 1
SEQ = 256
DEPTH = 1

DN_HEADS = 4
DN_HEAD_DIM = 128
DN_WIDTH = DN_HEADS * DN_HEAD_DIM
DN_CONV = 4
DN_CHUNK = 64
MB_HEADS = 8
MB_HEAD_DIM = 64
MB_WIDTH = MB_HEADS * MB_HEAD_DIM
MB_BLOCK = 256
MB_TOPK = 3
MB_QCHUNK = 32
N_BRANCH = 2
IN_COLS = 4 * DN_WIDTH + 2 * DN_HEADS + 4 * MB_WIDTH + N_BRANCH * D_MODEL
NORM_EPS = 1e-6


def rms_norm(x, gain):
    xf = x.astype(jnp.float32)
    y = xf * lax.rsqrt(jnp.mean(xf * xf, axis=-1, keepdims=True) + NORM_EPS)
    return (y * gain.astype(jnp.float32)).astype(x.dtype)

def l2_normalize(x):
    xf = x.astype(jnp.float32)
    return (xf * lax.rsqrt(jnp.sum(xf * xf, axis=-1, keepdims=True) + NORM_EPS)).astype(x.dtype)

def causal_depthwise_conv(x, w):
    k_width, channels = w.shape
    return lax.conv_general_dilated(
        x, w[:, None, :].astype(x.dtype), window_strides=(1,),
        padding=((k_width - 1, 0),), dimension_numbers=('NWC', 'WIO', 'NWC'),
        feature_group_count=channels)

def to_heads(t, n_heads):
    b, s, _ = t.shape
    return t.reshape(b, s, n_heads, -1).transpose(0, 2, 1, 3)

def gated_delta_rule_chunked(q, k, v, g, beta):
    out_dtype = v.dtype
    f32 = jnp.float32
    b, h, s, dk = k.shape
    dv = v.shape[-1]
    c = DN_CHUNK
    n = s // c
    beta = beta.astype(f32)[..., None]
    qf = (q.astype(f32) * (dk ** -0.5)).reshape(b, h, n, c, dk)
    kf = k.astype(f32)
    vf = v.astype(f32)
    k_beta = (kf * beta).reshape(b, h, n, c, dk)
    v_beta = (vf * beta).reshape(b, h, n, c, dv)
    kf = kf.reshape(b, h, n, c, dk)
    g = jnp.cumsum(g.astype(f32).reshape(b, h, n, c), axis=-1)
    causal = jnp.tril(jnp.ones((c, c), dtype=bool))
    strict = jnp.tril(jnp.ones((c, c), dtype=bool), k=-1)
    decay = jnp.exp(jnp.where(causal, g[..., :, None] - g[..., None, :], -jnp.inf))
    a = jnp.where(strict, jnp.einsum('bhnid,bhnjd->bhnij', k_beta, kf) * decay, 0.0)
    eye = jnp.eye(c, dtype=f32)
    t_inv = lax.linalg.triangular_solve(eye + a, jnp.broadcast_to(eye, a.shape),
                                        left_side=True, lower=True)
    u = t_inv @ v_beta
    w = t_inv @ (k_beta * jnp.exp(g)[..., None])
    qk = jnp.einsum('bhnid,bhnjd->bhnij', qf, kf) * decay

    def chunk_step(state, xs):
        q_i, k_i, u_i, w_i, qk_i, g_i = xs
        v_new = u_i - w_i @ state
        o_i = (q_i * jnp.exp(g_i)[..., None]) @ state + qk_i @ v_new
        g_last = g_i[..., -1:]
        state = state * jnp.exp(g_last)[..., None] + jnp.einsum(
            'bhcd,bhce->bhde', k_i * jnp.exp(g_last - g_i)[..., None], v_new)
        return state, o_i

    xs = tuple(jnp.moveaxis(t_, 2, 0) for t_ in (qf, kf, u, w, qk, g))
    state0 = jnp.zeros((b, h, dk, dv), f32)
    _, o = lax.scan(chunk_step, state0, xs)
    return jnp.moveaxis(o, 0, 2).reshape(b, h, s, dv).astype(out_dtype)

def moba_attention(q, k, v):
    b, h, s, dh = q.shape
    nb = s // MB_BLOCK
    n_sel = min(MB_TOPK, nb)
    scale = dh ** -0.5
    kb = k.reshape(b, h, nb, MB_BLOCK, dh)
    vb = v.reshape(b, h, nb, MB_BLOCK, dh)
    k_mean = jnp.mean(kb.astype(jnp.float32), axis=3).astype(k.dtype)
    bi = jnp.arange(b)[:, None, None, None]
    hi = jnp.arange(h)[None, :, None, None]
    blk_ids = jnp.arange(nb)

    def attend_chunk(ci):
        start = ci * MB_QCHUNK
        own = start // MB_BLOCK
        q_c = lax.dynamic_slice_in_dim(q, start, MB_QCHUNK, axis=2)
        q_pos = start + jnp.arange(MB_QCHUNK)
        gate = jnp.einsum('bhqd,bhnd->bhqn', q_c, k_mean).astype(jnp.float32)
        gate = jnp.where(blk_ids < own, gate, -jnp.inf)
        _, sel = lax.top_k(gate, n_sel)
        sel_ok = sel < own
        k_sel = kb[bi, hi, sel]
        v_sel = vb[bi, hi, sel]
        s_sel = jnp.einsum('bhqd,bhqjtd->bhqjt', q_c, k_sel).astype(jnp.float32) * scale
        s_sel = jnp.where(sel_ok[..., None], s_sel, -jnp.inf).reshape(b, h, MB_QCHUNK, n_sel * MB_BLOCK)
        k_own = lax.dynamic_slice_in_dim(k, own * MB_BLOCK, MB_BLOCK, axis=2)
        v_own = lax.dynamic_slice_in_dim(v, own * MB_BLOCK, MB_BLOCK, axis=2)
        k_pos = own * MB_BLOCK + jnp.arange(MB_BLOCK)
        s_own = jnp.einsum('bhqd,bhtd->bhqt', q_c, k_own).astype(jnp.float32) * scale
        s_own = jnp.where(k_pos[None, :] <= q_pos[:, None], s_own, -jnp.inf)
        p = jax.nn.softmax(jnp.concatenate([s_own, s_sel], axis=-1), axis=-1).astype(v.dtype)
        p_own = p[..., :MB_BLOCK]
        p_sel = p[..., MB_BLOCK:].reshape(b, h, MB_QCHUNK, n_sel, MB_BLOCK)
        return (jnp.einsum('bhqt,bhtd->bhqd', p_own, v_own)
                + jnp.einsum('bhqjt,bhqjtd->bhqd', p_sel, v_sel))

    out = lax.map(attend_chunk, jnp.arange(s // MB_QCHUNK))
    return jnp.moveaxis(out, 0, 2).reshape(b, h, s, dh)

def hybrid_layer(x, c, w_ada, b_ada, g_pre, g_post, w_in, conv_w, a_log, dt_bias,
                 dn_norm_g, w_proj_dn, w_proj_mb, w_out):
    b, s, _ = x.shape
    f32 = jnp.float32
    shift, scale, gate = jnp.split(jax.nn.silu(c) @ w_ada + b_ada, 3, axis=-1)
    h = rms_norm(x, g_pre) * (1 + scale[:, None, :]) + shift[:, None, :]
    sizes = (3 * DN_WIDTH, DN_WIDTH, DN_HEADS, DN_HEADS, 3 * MB_WIDTH, MB_WIDTH, N_BRANCH * D_MODEL)
    cuts = np.cumsum(sizes)[:-1].tolist()
    qkv_dn, z_dn, beta_logit, a_logit, qkv_mb, z_mb, merge_logit = jnp.split(h @ w_in, cuts, axis=-1)

    qkv_dn = jax.nn.silu(causal_depthwise_conv(qkv_dn, conv_w))
    q_dn, k_dn, v_dn = (to_heads(t_, DN_HEADS) for t_ in jnp.split(qkv_dn, 3, axis=-1))
    beta = jax.nn.sigmoid(beta_logit).transpose(0, 2, 1)
    g = (-jnp.exp(a_log.astype(f32))
         * jax.nn.softplus(a_logit.astype(f32) + dt_bias.astype(f32))).transpose(0, 2, 1)
    o_dn = gated_delta_rule_chunked(l2_normalize(q_dn), l2_normalize(k_dn), v_dn, g, beta)
    o_dn = rms_norm(o_dn.transpose(0, 2, 1, 3), dn_norm_g) * jax.nn.silu(
        z_dn.reshape(b, s, DN_HEADS, DN_HEAD_DIM))
    y_dn = o_dn.reshape(b, s, DN_WIDTH) @ w_proj_dn

    pad = (-s) % MB_BLOCK
    q_mb, k_mb, v_mb = (jnp.pad(to_heads(t_, MB_HEADS), ((0, 0), (0, 0), (0, pad), (0, 0)))
                        for t_ in jnp.split(qkv_mb, 3, axis=-1))
    o_mb = moba_attention(q_mb, k_mb, v_mb)[:, :, :s]
    o_mb = o_mb.transpose(0, 2, 1, 3).reshape(b, s, MB_WIDTH) * jax.nn.silu(z_mb)
    y_mb = o_mb @ w_proj_mb

    gate_dn, gate_mb = jnp.split(jax.nn.sigmoid(merge_logit), N_BRANCH, axis=-1)
    mixed = (gate_dn * y_dn + gate_mb * y_mb) @ w_out
    return x + gate[:, None, :] * rms_norm(mixed, g_post)

def first_inputs(seed: int = 0) -> dict:
    key = jax.random.key(seed)
    ks = jax.random.split(key, 16)
    nrm = jax.random.normal
    d = D_MODEL
    dt = jnp.exp(jax.random.uniform(ks[9], (DEPTH, DN_HEADS), minval=np.log(1e-3), maxval=np.log(1e-1)))
    return {
        'x': nrm(ks[0], (BATCH, SEQ, d), jnp.float32),
        'c': nrm(ks[1], (BATCH, d), jnp.float32),
        'w_ada': nrm(ks[2], (DEPTH, d, 3 * d), jnp.float32) * (0.5 * d ** -0.5),
        'b_ada': nrm(ks[3], (DEPTH, 3 * d), jnp.float32) * 0.1,
        'g_pre': 1.0 + 0.02 * nrm(ks[4], (DEPTH, d), jnp.float32),
        'g_post': 1.0 + 0.02 * nrm(ks[5], (DEPTH, d), jnp.float32),
        'w_in': nrm(ks[6], (DEPTH, d, IN_COLS), jnp.float32) * d ** -0.5,
        'conv_w': nrm(ks[7], (DEPTH, DN_CONV, 3 * DN_WIDTH), jnp.float32) * DN_CONV ** -0.5,
        'a_log': jnp.log(jax.random.uniform(ks[8], (DEPTH, DN_HEADS), minval=1.0, maxval=16.0)),
        'dt_bias': dt + jnp.log(-jnp.expm1(-dt)),
        'dn_norm_g': 1.0 + 0.02 * nrm(ks[10], (DEPTH, DN_HEAD_DIM), jnp.float32),
        'w_proj_dn': nrm(ks[11], (DEPTH, DN_WIDTH, d), jnp.float32) * DN_WIDTH ** -0.5,
        'w_proj_mb': nrm(ks[12], (DEPTH, MB_WIDTH, d), jnp.float32) * MB_WIDTH ** -0.5,
        'w_out': nrm(ks[13], (DEPTH, d, d), jnp.float32) * d ** -0.5,
    }

def first_block(x, c, w_ada, b_ada, g_pre, g_post, w_in, conv_w, a_log, dt_bias,
              dn_norm_g, w_proj_dn, w_proj_mb, w_out):
    for l in range(DEPTH):
        x = hybrid_layer(x, c, w_ada[l], b_ada[l], g_pre[l], g_post[l], w_in[l], conv_w[l],
                         a_log[l], dt_bias[l], dn_norm_g[l], w_proj_dn[l], w_proj_mb[l], w_out[l])
    return x


LRU_W = 256
LRU_BLOCKS = 4
LRU_BLOCK_W = LRU_W // LRU_BLOCKS
LRU_C = 8.0
CONV_W = 4
MLSTM_HEADS = 4
MLSTM_HEAD_DIM = 64
MLSTM_W = MLSTM_HEADS * MLSTM_HEAD_DIM
MLSTM_CHUNK = 64
SB_HEADS = 4
SB_HEAD_DIM = 64
SB_W = SB_HEADS * SB_HEAD_DIM
SB_BLOCK = 128
FF = ((8 * D_MODEL // 3 + 255) // 256) * 256
EPS = 1e-6

SPLIT_SIZES = (LRU_W, LRU_W, 2 * MLSTM_W, MLSTM_W, MLSTM_W, MLSTM_HEADS, MLSTM_HEADS,
               SB_W, SB_W, SB_W, D_MODEL, D_MODEL, D_MODEL)
IN_COLS_2 = sum(SPLIT_SIZES)


def rmsnorm(x, g):
    xf = x.astype(jnp.float32)
    y = xf * lax.rsqrt(jnp.mean(xf * xf, axis=-1, keepdims=True) + EPS)
    return (y * g.astype(jnp.float32)).astype(x.dtype)

def causal_dwconv(x, w):
    K, C = w.shape
    return lax.conv_general_dilated(
        x, w.astype(x.dtype)[:, None, :], window_strides=(1,), padding=[(K - 1, 0)],
        dimension_numbers=("NWC", "WIO", "NWC"), feature_group_count=C)

def to_heads_2(t, n_heads):
    B, S, W = t.shape
    return t.reshape(B, S, n_heads, W // n_heads).transpose(0, 2, 1, 3)

def from_heads(t):
    B, H, S, d = t.shape
    return t.transpose(0, 2, 1, 3).reshape(B, S, H * d)

def rg_lru(xb, wa, ba, wx, bx, lam):
    B, S, W = xb.shape
    xf = xb.astype(jnp.float32)
    xh = xf.reshape(B, S, LRU_BLOCKS, LRU_BLOCK_W)
    r = jax.nn.sigmoid(jnp.einsum('bsgi,gij->bsgj', xh, wa.astype(jnp.float32)).reshape(B, S, W)
                       + ba.astype(jnp.float32))
    i = jax.nn.sigmoid(jnp.einsum('bsgi,gij->bsgj', xh, wx.astype(jnp.float32)).reshape(B, S, W)
                       + bx.astype(jnp.float32))
    log_a = -LRU_C * r * jax.nn.softplus(-lam.astype(jnp.float32))
    a = jnp.exp(log_a)
    u = jnp.sqrt(-jnp.expm1(2.0 * log_a)) * (i * xf)

    def combine(left, right):
        a1, b1 = left
        a2, b2 = right
        return a1 * a2, a2 * b1 + b2

    _, h = lax.associative_scan(combine, (a, u), axis=1)
    return h.astype(xb.dtype)

def mlstm_chunkwise(q, k, v, i_pre, f_pre):
    B, H, S, dk = q.shape
    dv = v.shape[-1]
    L = MLSTM_CHUNK
    nc = S // L
    out_dtype = v.dtype
    q = q.astype(jnp.float32)
    k = k.astype(jnp.float32) * (dk ** -0.5)
    v = v.astype(jnp.float32)
    logi = i_pre.astype(jnp.float32)
    logf = jax.nn.log_sigmoid(f_pre.astype(jnp.float32))

    def chunks(t):
        return jnp.moveaxis(t.reshape((B, H, nc, L) + t.shape[3:]), 2, 0)

    tril = jnp.tril(jnp.ones((L, L), dtype=bool))

    def step(carry, inp):
        C, n, m = carry
        qc, kc, vc, ic, fc = inp
        b = jnp.cumsum(fc, axis=-1)
        D = jnp.where(tril, b[..., :, None] - b[..., None, :] + ic[..., None, :], -jnp.inf)
        m_inter = b + m[..., None]
        m_t = jnp.maximum(jnp.max(D, axis=-1), m_inter)
        P = jnp.exp(D - m_t[..., None]) * jnp.einsum('bhtk,bhsk->bhts', qc, kc)
        decay = jnp.exp(m_inter - m_t)
        num = (jnp.einsum('bhts,bhsv->bhtv', P, vc)
               + decay[..., None] * jnp.einsum('bhvk,bhtk->bhtv', C, qc))
        den = jnp.sum(P, axis=-1) + decay * jnp.einsum('bhk,bhtk->bht', n, qc)
        h = num / jnp.maximum(jnp.abs(den), jnp.exp(-m_t))[..., None]
        bL = b[..., -1]
        g = bL[..., None] - b + ic
        m_new = jnp.maximum(bL + m, jnp.max(g, axis=-1))
        wts = jnp.exp(g - m_new[..., None])
        carry_decay = jnp.exp(bL + m - m_new)
        C = carry_decay[..., None, None] * C + jnp.einsum('bhs,bhsv,bhsk->bhvk', wts, vc, kc)
        n = carry_decay[..., None] * n + jnp.einsum('bhs,bhsk->bhk', wts, kc)
        return (C, n, m_new), h

    init = (jnp.zeros((B, H, dv, dk), jnp.float32), jnp.zeros((B, H, dk), jnp.float32),
            jnp.zeros((B, H), jnp.float32))
    _, hs = lax.scan(step, init, (chunks(q), chunks(k), chunks(v), chunks(logi), chunks(logf)))
    return jnp.moveaxis(hs, 0, 2).reshape(B, H, S, dv).astype(out_dtype)

def stick_breaking_attention(q, k, v):
    B, H, S, d = q.shape
    nb = S // SB_BLOCK
    scale = 1.0 / math.sqrt(d)
    loc = jnp.arange(SB_BLOCK)
    diag_mask = loc[None, :] < loc[:, None]
    outs = []
    for bi in range(nb):
        nk = bi + 1
        lk_len = nk * SB_BLOCK
        qblk = q[:, :, bi * SB_BLOCK:(bi + 1) * SB_BLOCK]
        kk = k[:, :, :lk_len]
        vv = v[:, :, :lk_len]
        z = jnp.einsum('bhqd,bhsd->bhqs', qblk, kk).astype(jnp.float32) * scale
        causal = jnp.concatenate(
            [jnp.ones((SB_BLOCK, lk_len - SB_BLOCK), dtype=bool), diag_mask], axis=1)
        log_keep = jnp.where(causal, jax.nn.log_sigmoid(-z), 0.0)
        intra = lax.cumsum(log_keep.reshape(B, H, SB_BLOCK, nk, SB_BLOCK), axis=4, reverse=True)
        bsum = intra[..., 0]
        inter = lax.cumsum(bsum, axis=3, reverse=True) - bsum
        R = (intra + inter[..., None]).reshape(B, H, SB_BLOCK, lk_len)
        A = jnp.where(causal, jnp.exp(z + R), 0.0)
        outs.append(jnp.einsum('bhqs,bhsd->bhqd', A.astype(v.dtype), vv))
    return jnp.concatenate(outs, axis=2)

def second_inputs(seed: int = 0) -> dict:
    key = jax.random.key(seed)
    ks = jax.random.split(key, 24)
    f32 = jnp.float32
    D = D_MODEL

    def nrm(k, shape, fan_in):
        return jax.random.normal(k, shape, f32) * (fan_in ** -0.5)

    a0 = jax.random.uniform(ks[8], (DEPTH, LRU_W), f32, 0.9, 0.999)
    s0 = a0 ** (1.0 / LRU_C)
    lru_lambda = jnp.log(s0) - jnp.log1p(-s0)
    fg_b = (jnp.linspace(3.0, 6.0, MLSTM_HEADS, dtype=f32)[None, :]
            + 0.1 * jax.random.normal(ks[11], (DEPTH, MLSTM_HEADS), f32))
    return {
        "x": jax.random.normal(ks[0], (BATCH, SEQ, D), f32),
        "norm_mix_g": 1.0 + 0.02 * jax.random.normal(ks[1], (DEPTH, D), f32),
        "w_in": nrm(ks[2], (DEPTH, D, IN_COLS_2), D),
        "conv_lru_w": nrm(ks[3], (DEPTH, CONV_W, LRU_W), CONV_W),
        "lru_wa": nrm(ks[4], (DEPTH, LRU_BLOCKS, LRU_BLOCK_W, LRU_BLOCK_W), LRU_BLOCK_W),
        "lru_ba": 0.02 * jax.random.normal(ks[5], (DEPTH, LRU_W), f32),
        "lru_wx": nrm(ks[6], (DEPTH, LRU_BLOCKS, LRU_BLOCK_W, LRU_BLOCK_W), LRU_BLOCK_W),
        "lru_bx": 0.02 * jax.random.normal(ks[7], (DEPTH, LRU_W), f32),
        "lru_lambda": lru_lambda,
        "conv_mlstm_w": nrm(ks[9], (DEPTH, CONV_W, 2 * MLSTM_W), CONV_W),
        "mlstm_ig_b": 0.1 * jax.random.normal(ks[10], (DEPTH, MLSTM_HEADS), f32),
        "mlstm_fg_b": fg_b,
        "w_out_lru": nrm(ks[12], (DEPTH, LRU_W, D), LRU_W),
        "w_out_mlstm": nrm(ks[13], (DEPTH, MLSTM_W, D), MLSTM_W),
        "w_out_sb": nrm(ks[14], (DEPTH, SB_W, D), SB_W),
        "w_o": nrm(ks[15], (DEPTH, D, D), D),
        "norm_ffn_g": 1.0 + 0.02 * jax.random.normal(ks[16], (DEPTH, D), f32),
        "w_ffn_in": nrm(ks[17], (DEPTH, D, 2 * FF), D),
        "w_ffn_out": nrm(ks[18], (DEPTH, FF, D), FF),
        "final_norm_g": 1.0 + 0.02 * jax.random.normal(ks[19], (D,), f32),
    }

def second_block(x, norm_mix_g, w_in, conv_lru_w, lru_wa, lru_ba, lru_wx, lru_bx, lru_lambda,
              conv_mlstm_w, mlstm_ig_b, mlstm_fg_b, w_out_lru, w_out_mlstm, w_out_sb, w_o,
              norm_ffn_g, w_ffn_in, w_ffn_out, final_norm_g):
    split_points = np.cumsum(SPLIT_SIZES)[:-1].tolist()
    for l in range(DEPTH):
        h = rmsnorm(x, norm_mix_g[l])
        proj = h @ w_in[l]
        (lru_x, lru_gate, m_qk, m_v, m_o, m_i, m_f,
         s_q, s_k, s_v, g_a, g_b, g_c) = jnp.split(proj, split_points, axis=-1)

        xa = causal_dwconv(lru_x, conv_lru_w[l])
        ya = rg_lru(xa, lru_wa[l], lru_ba[l], lru_wx[l], lru_bx[l], lru_lambda[l])
        ya = (ya * jax.nn.gelu(lru_gate)) @ w_out_lru[l]

        qk = jax.nn.silu(causal_dwconv(m_qk, conv_mlstm_w[l]))
        mq, mk = jnp.split(qk, 2, axis=-1)
        i_pre = (m_i + mlstm_ig_b[l]).transpose(0, 2, 1)
        f_pre = (m_f + mlstm_fg_b[l]).transpose(0, 2, 1)
        hb = mlstm_chunkwise(to_heads_2(mq, MLSTM_HEADS), to_heads_2(mk, MLSTM_HEADS),
                             to_heads_2(m_v, MLSTM_HEADS), i_pre, f_pre)
        yb = (jax.nn.sigmoid(m_o) * from_heads(hb)) @ w_out_mlstm[l]

        hc = stick_breaking_attention(to_heads_2(s_q, SB_HEADS), to_heads_2(s_k, SB_HEADS),
                                      to_heads_2(s_v, SB_HEADS))
        yc = from_heads(hc) @ w_out_sb[l]

        merged = (jax.nn.sigmoid(g_a) * ya + jax.nn.sigmoid(g_b) * yb
                  + jax.nn.sigmoid(g_c) * yc)
        x = x + merged @ w_o[l]

        hf = rmsnorm(x, norm_ffn_g[l])
        gate, up = jnp.split(hf @ w_ffn_in[l], 2, axis=-1)
        x = x + (jax.nn.silu(gate) * up) @ w_ffn_out[l]
    return rmsnorm(x, final_norm_g)


GRID_W = 64
N_MEM = 256
HEAD_DIM = 64
NA_HEADS = 6
NA_WIDTH = NA_HEADS * HEAD_DIM
NA_WIN_ROWS = 8
NA_WIN_COLS = 16
RW_HEADS = 6
RW_WIDTH = RW_HEADS * HEAD_DIM
DECAY_LORA = 64
AAA_LORA = 64
GATE_LORA = 128
MEM_HEADS = 4
MEM_WIDTH = MEM_HEADS * HEAD_DIM
N_BRANCH_3 = 3
N_EXPERTS = 16
EC_CAPACITY = 2
EXPERT_FF = 2 * D_MODEL
RMS_EPS = 1e-6
GN_EPS = 64e-5
IN_WIDTHS = (NA_WIDTH, NA_WIDTH, NA_WIDTH, RW_WIDTH, RW_WIDTH, RW_WIDTH, DECAY_LORA, AAA_LORA, GATE_LORA, MEM_WIDTH, D_MODEL, D_MODEL, D_MODEL)
D_IN = sum(IN_WIDTHS)


def rms_norm_3(x, g):
    xf = x.astype(jnp.float32)
    y = xf * lax.rsqrt(jnp.mean(xf * xf, axis=-1, keepdims=True) + RMS_EPS)
    return (y * g.astype(jnp.float32)).astype(x.dtype)

def split_columns(p):
    cuts = []
    acc = 0
    for w in IN_WIDTHS[:-1]:
        acc += w
        cuts.append(acc)
    return jnp.split(p, cuts, axis=-1)

def to_heads_3(t, n_heads):
    b, s, c = t.shape
    return t.reshape(b, s, n_heads, c // n_heads)

def neighborhood_attention(q, k, v, rpb):
    b, s, h, dh = q.shape
    rows = s // GRID_W
    kr = min(NA_WIN_ROWS, rows)
    kc = NA_WIN_COLS
    q = (q * (dh ** -0.5)).reshape(b, rows, GRID_W, h, dh).transpose(1, 0, 2, 3, 4)
    k = k.reshape(b, rows, GRID_W, h, dh)
    v = v.reshape(b, rows, GRID_W, h, dh)
    col = jnp.arange(GRID_W)
    col_start = jnp.clip(col - kc // 2, 0, GRID_W - kc)
    col_idx = col_start[:, None] + jnp.arange(kc)[None, :]
    col_off = col_idx - col[:, None] + (NA_WIN_COLS - 1)

    def row_block(args):
        r, q_r = args
        r_start = jnp.clip(r - kr // 2, 0, rows - kr)
        k_win = lax.dynamic_slice_in_dim(k, r_start, kr, axis=1)[:, :, col_idx]
        v_win = lax.dynamic_slice_in_dim(v, r_start, kr, axis=1)[:, :, col_idx]
        row_off = r_start + jnp.arange(kr) - r + (NA_WIN_ROWS - 1)
        bias = rpb[:, row_off[:, None, None], col_off[None, :, :]].transpose(0, 2, 1, 3)
        scores = jnp.einsum('bwhd,biwjhd->bhwij', q_r, k_win).astype(jnp.float32) + bias.astype(jnp.float32)[None]
        probs = jax.nn.softmax(scores.reshape(b, h, GRID_W, kr * kc), axis=-1).reshape(b, h, GRID_W, kr, kc)
        return jnp.einsum('bhwij,biwjhd->bwhd', probs.astype(v.dtype), v_win)

    out = lax.map(row_block, (jnp.arange(rows), q))
    return out.transpose(1, 0, 2, 3, 4).reshape(b, s, h * dh)

def token_shift(t, direction):
    if direction == 0:
        return jnp.pad(t[:, :-1], ((0, 0), (1, 0), (0, 0)))
    return jnp.pad(t[:, 1:], ((0, 0), (0, 1), (0, 0)))

def wkv7_scan(r, w, k, v, a, b, reverse):
    bsz, _, h, n = r.shape

    def step(state, inp):
        r_t, w_t, k_t, v_t, a_t, b_t = inp
        sa = jnp.einsum('bhvk,bhk->bhv', state, a_t)
        state = state * w_t[:, :, None, :] + sa[..., None] * b_t[:, :, None, :] + v_t[..., None] * k_t[:, :, None, :]
        return state, jnp.einsum('bhvk,bhk->bhv', state, r_t)

    xs = tuple(t.transpose(1, 0, 2, 3) for t in (r, w, k, v, a, b))
    _, y = lax.scan(step, jnp.zeros((bsz, h, n, n), jnp.float32), xs, reverse=reverse)
    return y.transpose(1, 0, 2, 3)

def rwkv7_bidirectional(p_r, p_k, p_v, lat_w, lat_a, lat_g, mu_rkv, mu_w, mu_a, w0, w2, a0, a2, k_k, k_a, r_k, g2, ln_g, ln_b):
    out_dtype = p_r.dtype
    f32 = lambda t: t.astype(jnp.float32)
    p_r, p_k, p_v, lat_w, lat_a, lat_g = (f32(t) for t in (p_r, p_k, p_v, lat_w, lat_a, lat_g))
    mu_rkv, mu_w, mu_a, w0, w2, a0, a2 = (f32(t) for t in (mu_rkv, mu_w, mu_a, w0, w2, a0, a2))
    k_k, k_a, r_k, g2, ln_g, ln_b = (f32(t) for t in (k_k, k_a, r_k, g2, ln_g, ln_b))
    bsz, s, c = p_r.shape
    y_sum = jnp.zeros((bsz, s, RW_HEADS, HEAD_DIM), jnp.float32)
    bonus_sum = jnp.zeros((bsz, s, RW_HEADS, HEAD_DIM), jnp.float32)
    for d in range(2):
        def mix(t, mu):
            return t + (token_shift(t, d) - t) * mu
        r = mix(p_r, mu_rkv[d, 0])
        k = mix(p_k, mu_rkv[d, 1])
        v = mix(p_v, mu_rkv[d, 2])
        w_log = -jax.nn.softplus(-(w0[d] + jnp.tanh(mix(lat_w, mu_w[d])) @ w2[d])) - 0.5
        decay = jnp.exp(-jnp.exp(w_log))
        a = jax.nn.sigmoid(a0[d] + mix(lat_a, mu_a[d]) @ a2[d])
        kk = to_heads_3(k * k_k, RW_HEADS)
        kk = kk / jnp.maximum(jnp.sqrt(jnp.sum(kk * kk, axis=-1, keepdims=True)), 1e-12)
        k = k * (1.0 + (a - 1.0) * k_a)
        rh, kh, vh, ah = (to_heads_3(t, RW_HEADS) for t in (r, k, v, a))
        y_sum = y_sum + wkv7_scan(rh, to_heads_3(decay, RW_HEADS), kh, vh, -kk, kk * ah, reverse=(d == 1))
        bonus_sum = bonus_sum + jnp.sum(rh * kh * r_k, axis=-1, keepdims=True) * vh
    mean = jnp.mean(y_sum, axis=-1, keepdims=True)
    var = jnp.mean(jnp.square(y_sum - mean), axis=-1, keepdims=True)
    y = ((y_sum - mean) * lax.rsqrt(var + GN_EPS)).reshape(bsz, s, c) * ln_g + ln_b
    y = y + bonus_sum.reshape(bsz, s, c)
    g = jax.nn.sigmoid(lat_g) @ g2
    return (y * g).astype(out_dtype)

def memory_attention(q, mem_h, w_mem_kv):
    b, s, _ = q.shape
    mk, mv = jnp.split(mem_h @ w_mem_kv, 2, axis=-1)
    qh = to_heads_3(q, MEM_HEADS) * (HEAD_DIM ** -0.5)
    kh = to_heads_3(mk, MEM_HEADS)
    vh = to_heads_3(mv, MEM_HEADS)
    scores = jnp.einsum('bshd,bmhd->bhsm', qh, kh).astype(jnp.float32)
    probs = jax.nn.softmax(scores, axis=-1)
    return jnp.einsum('bhsm,bmhd->bshd', probs.astype(vh.dtype), vh).reshape(b, s, MEM_WIDTH)

def expert_choice_ffn(h, w_router, w_gate, w_up, w_down):
    b, s, d = h.shape
    cap = EC_CAPACITY * s // N_EXPERTS
    affinity = jax.nn.softmax((h @ w_router).astype(jnp.float32), axis=-1)
    top_val, top_idx = lax.top_k(affinity.transpose(0, 2, 1), cap)
    xe = jax.vmap(lambda hb, ib: hb[ib])(h, top_idx)
    act = jax.nn.silu(jnp.einsum('becd,edf->becf', xe, w_gate)) * jnp.einsum('becd,edf->becf', xe, w_up)
    ye = jnp.einsum('becf,efd->becd', act, w_down) * top_val[..., None].astype(h.dtype)
    return jax.vmap(lambda yb, ib: jnp.zeros((s, d), yb.dtype).at[ib.reshape(-1)].add(yb.reshape(-1, d)))(ye, top_idx)

def third_inputs(seed: int = 0) -> dict:
    key = jax.random.key(seed)
    ks = iter(jax.random.split(key, 40))
    L = DEPTH

    def nrm(shape, scale):
        return scale * jax.random.normal(next(ks), shape, jnp.float32)

    def uni(shape):
        return jax.random.uniform(next(ks), shape, jnp.float32, 0.0, 1.0)

    decay_ramp = jnp.linspace(-6.5, -1.5, RW_WIDTH, dtype=jnp.float32)
    return {
        'x': nrm((BATCH, SEQ, D_MODEL), 1.0),
        'mem': nrm((BATCH, N_MEM, D_MODEL), 1.0),
        'norm_mix_g': 1.0 + nrm((L, D_MODEL), 0.02),
        'norm_mem_g': 1.0 + nrm((L, D_MODEL), 0.02),
        'w_in': nrm((L, D_MODEL, D_IN), D_MODEL ** -0.5),
        'na_rpb': nrm((L, NA_HEADS, 2 * NA_WIN_ROWS - 1, 2 * NA_WIN_COLS - 1), 0.05),
        'rw_mu_rkv': uni((L, 2, 3, RW_WIDTH)),
        'rw_mu_w': uni((L, 2, DECAY_LORA)),
        'rw_mu_a': uni((L, 2, AAA_LORA)),
        'rw_w0': decay_ramp + nrm((L, 2, RW_WIDTH), 0.1),
        'rw_w2': nrm((L, 2, DECAY_LORA, RW_WIDTH), 0.1),
        'rw_a0': nrm((L, 2, RW_WIDTH), 0.1),
        'rw_a2': nrm((L, 2, AAA_LORA, RW_WIDTH), 0.1),
        'rw_k_k': 0.85 + nrm((L, RW_WIDTH), 0.02),
        'rw_k_a': 1.0 + nrm((L, RW_WIDTH), 0.02),
        'rw_r_k': nrm((L, RW_HEADS, HEAD_DIM), 0.1),
        'rw_g2': nrm((L, GATE_LORA, RW_WIDTH), GATE_LORA ** -0.5),
        'rw_ln_g': 1.0 + nrm((L, RW_WIDTH), 0.02),
        'rw_ln_b': nrm((L, RW_WIDTH), 0.02),
        'w_mem_kv': nrm((L, D_MODEL, 2 * MEM_WIDTH), D_MODEL ** -0.5),
        'w_branch_na': nrm((L, NA_WIDTH, D_MODEL), NA_WIDTH ** -0.5),
        'w_branch_rw': nrm((L, RW_WIDTH, D_MODEL), RW_WIDTH ** -0.5),
        'w_branch_mem': nrm((L, MEM_WIDTH, D_MODEL), MEM_WIDTH ** -0.5),
        'w_out': nrm((L, D_MODEL, D_MODEL), D_MODEL ** -0.5),
        'norm_ffn_g': 1.0 + nrm((L, D_MODEL), 0.02),
        'w_router': nrm((L, D_MODEL, N_EXPERTS), D_MODEL ** -0.5),
        'w_exp_gate': nrm((L, N_EXPERTS, D_MODEL, EXPERT_FF), D_MODEL ** -0.5),
        'w_exp_up': nrm((L, N_EXPERTS, D_MODEL, EXPERT_FF), D_MODEL ** -0.5),
        'w_exp_down': nrm((L, N_EXPERTS, EXPERT_FF, D_MODEL), EXPERT_FF ** -0.5),
        'norm_final_g': 1.0 + nrm((D_MODEL,), 0.02),
    }

def third_block(x, mem, norm_mix_g, norm_mem_g, w_in, na_rpb, rw_mu_rkv, rw_mu_w, rw_mu_a, rw_w0, rw_w2, rw_a0, rw_a2, rw_k_k, rw_k_a, rw_r_k, rw_g2, rw_ln_g, rw_ln_b, w_mem_kv, w_branch_na, w_branch_rw, w_branch_mem, w_out, norm_ffn_g, w_router, w_exp_gate, w_exp_up, w_exp_down, norm_final_g):
    for l in range(DEPTH):
        h = rms_norm_3(x, norm_mix_g[l])
        (na_q, na_k, na_v, p_r, p_k, p_v, lat_w, lat_a, lat_g, mem_q,
         gate_na, gate_rw, gate_mem) = split_columns(h @ w_in[l])
        y_na = neighborhood_attention(to_heads_3(na_q, NA_HEADS), to_heads_3(na_k, NA_HEADS), to_heads_3(na_v, NA_HEADS), na_rpb[l])
        y_rw = rwkv7_bidirectional(p_r, p_k, p_v, lat_w, lat_a, lat_g, rw_mu_rkv[l], rw_mu_w[l], rw_mu_a[l], rw_w0[l], rw_w2[l], rw_a0[l], rw_a2[l], rw_k_k[l], rw_k_a[l], rw_r_k[l], rw_g2[l], rw_ln_g[l], rw_ln_b[l])
        y_mem = memory_attention(mem_q, rms_norm_3(mem, norm_mem_g[l]), w_mem_kv[l])
        merged = (jax.nn.sigmoid(gate_na) * (y_na @ w_branch_na[l])
                  + jax.nn.sigmoid(gate_rw) * (y_rw @ w_branch_rw[l])
                  + jax.nn.sigmoid(gate_mem) * (y_mem @ w_branch_mem[l]))
        x = x + merged @ w_out[l]
        x = x + expert_choice_ffn(rms_norm_3(x, norm_ffn_g[l]), w_router[l], w_exp_gate[l], w_exp_up[l], w_exp_down[l])
    return rms_norm_3(x, norm_final_g)


def setup_inputs(seed=0):
    out = dict(first_inputs(seed))
    for name, value in second_inputs(seed + 1).items():
        if name != "x":
            out[name + "_2"] = value
    for name, value in third_inputs(seed + 2).items():
        if name != "x":
            out[name + "_3"] = value
    return out


def reference(
    x, c, w_ada, b_ada, g_pre, g_post, w_in, conv_w, a_log, dt_bias, dn_norm_g, w_proj_dn,
    w_proj_mb, w_out, norm_mix_g_2, w_in_2, conv_lru_w_2, lru_wa_2, lru_ba_2, lru_wx_2,
    lru_bx_2, lru_lambda_2, conv_mlstm_w_2, mlstm_ig_b_2, mlstm_fg_b_2, w_out_lru_2,
    w_out_mlstm_2, w_out_sb_2, w_o_2, norm_ffn_g_2, w_ffn_in_2, w_ffn_out_2, final_norm_g_2,
    mem_3, norm_mix_g_3, norm_mem_g_3, w_in_3, na_rpb_3, rw_mu_rkv_3, rw_mu_w_3, rw_mu_a_3,
    rw_w0_3, rw_w2_3, rw_a0_3, rw_a2_3, rw_k_k_3, rw_k_a_3, rw_r_k_3, rw_g2_3, rw_ln_g_3,
    rw_ln_b_3, w_mem_kv_3, w_branch_na_3, w_branch_rw_3, w_branch_mem_3, w_out_3, norm_ffn_g_3,
    w_router_3, w_exp_gate_3, w_exp_up_3, w_exp_down_3, norm_final_g_3,
):
    x = first_block(
        x, c, w_ada, b_ada, g_pre, g_post, w_in, conv_w, a_log, dt_bias, dn_norm_g, w_proj_dn,
        w_proj_mb, w_out,
    )
    x = second_block(
        x, norm_mix_g_2, w_in_2, conv_lru_w_2, lru_wa_2, lru_ba_2, lru_wx_2, lru_bx_2,
        lru_lambda_2, conv_mlstm_w_2, mlstm_ig_b_2, mlstm_fg_b_2, w_out_lru_2, w_out_mlstm_2,
        w_out_sb_2, w_o_2, norm_ffn_g_2, w_ffn_in_2, w_ffn_out_2, final_norm_g_2,
    )
    return third_block(
        x, mem_3, norm_mix_g_3, norm_mem_g_3, w_in_3, na_rpb_3, rw_mu_rkv_3, rw_mu_w_3,
        rw_mu_a_3, rw_w0_3, rw_w2_3, rw_a0_3, rw_a2_3, rw_k_k_3, rw_k_a_3, rw_r_k_3, rw_g2_3,
        rw_ln_g_3, rw_ln_b_3, w_mem_kv_3, w_branch_na_3, w_branch_rw_3, w_branch_mem_3, w_out_3,
        norm_ffn_g_3, w_router_3, w_exp_gate_3, w_exp_up_3, w_exp_down_3, norm_final_g_3,
    )


_drawn_inputs = setup_inputs


def setup_inputs(seed=0):
    import zlib

    import numpy as np

    out = dict(_drawn_inputs(seed))
    spreads = {}
    factors = {'g_pre': 3.109,
     'g_post': 3.6,
     'dn_norm_g': 3.835,
     'norm_mix_g_2': 2.998,
     'lru_ba_2': 8.0,
     'lru_bx_2': 8.0,
     'mlstm_ig_b_2': 31.297,
     'norm_mix_g_3': 3.825,
     'norm_mem_g_3': 26.001,
     'na_rpb_3': 35.48,
     'rw_mu_w_3': 33.098,
     'rw_w2_3': 8.598,
     'rw_a0_3': 3.324,
     'rw_k_k_3': 43.4,
     'rw_k_a_3': 4.801,
     'rw_ln_g_3': 45.096,
     'rw_ln_b_3': 43.984,
     'norm_ffn_g_3': 23.167,
     'norm_final_g_3': 8.112,
     'norm_ffn_g_2': 5.696}
    for name, (base, spread) in spreads.items():
        noise = np.random.default_rng([zlib.crc32(name.encode()), seed]).standard_normal(out[name].shape)
        drawn = base * np.exp(spread * noise) if base else spread * noise
        out[name] = jnp.asarray(drawn.astype(out[name].dtype))
    for name, factor in factors.items():
        out[name] = (out[name] * factor).astype(out[name].dtype)
    return out
```

```python
from contextlib import ExitStack

import concourse.bass as bass
from concourse import mybir
import numpy as np

F32 = mybir.dt.float32
ALU = mybir.AluOpType
ACT = mybir.ActivationFunctionType
AX_X = mybir.AxisListType.X

P = 128
S = 256
TT = S // P
D = 1024
DC = D // P
BANK = 512
TILE = 512
RING = 6
SLOT = DC * TILE
PAD = 4
CHW = PAD + S + PAD
NEG = -1.0e30
EPS = 1e-6

DN_H, DN_D = 4, 128
MB_H, MB_D = 8, 64
LRU_W = 256
ML_H, ML_D = 4, 64
SB_H, SB_D = 4, 64
FF = ((8 * D // 3 + 255) // 256) * 256
FFC = FF // P
NA_H, RW_H, MEM_H, HD = 6, 6, 4, 64
RW_W = RW_H * HD
GRID = 64
NA_ROWS, NA_COLS = 8, 16
EXP, CAP, EFF = 16, 2 * S // 16, 2 * D
BLOCKS = (1, 2, 3)



def constant_tables():
    p = np.arange(P)[:, None]
    f = np.arange(P)[None, :]
    tables = {
        "ident": p == f,
        "anti": p + f == P - 1,
        "ones": np.ones((P, P)),
        "upper": p <= f,
        "lower": p >= f,
        "lower_strict": p > f,
        "upper_strict": p < f,
        "half_ones": p // 64 == f // 64,
        "half_lower_strict": (p > f) & (p // 64 == f // 64),
        "half_upper_strict": (p < f) & (p // 64 == f // 64),
        "half_upper": (p <= f) & (p // 64 == f // 64),
        "half_of": p // 64 == np.arange(2)[None, :],
        "neg_not_lower": np.where(p >= f, 0.0, NEG),
        "neg_not_upper": np.where(p <= f, 0.0, NEG),
        "neg_not_upper_strict": np.where(p < f, 0.0, NEG),
        "causal": np.concatenate([np.where(np.arange(S)[None, :] <= p + t * P, 0.0, NEG) for t in range(TT)], 1),
        "not_chunk_start": np.broadcast_to((np.arange(2 * S) % 64 != 0)[None, :], (P, 2 * S)),
        "slot_number": np.broadcast_to(np.arange(CAP)[None, :], (P, CAP)),
        "four_idents": p % CAP == np.arange(CAP)[None, :],
        "eps": np.full((P, 1), EPS),
        "log_scale": np.full((P, 1), -0.5 * np.log(DN_D)),
        "gn_eps": np.full((P, 1), 64e-5),
        "ln_norm_scale": np.full((P, 1), 0.5 * 17 * np.log(2.0)),
        "tiny": np.full((P, 1), 1e-24),
    }
    for n in range(7):
        b = 1 << n
        m = (p // (2 * b) == f // (2 * b)) & ((p // b) % 2 == 1) & ((f // b) % 2 == 0)
        tables[f"level{n}"] = -1.0 * m
    tables["level0_t"] = tables["level0"].T
    for n in range(4):
        tables[f"four_times{n}"] = p == CAP * n + f % CAP
    w = p % GRID
    start = np.clip(w - NA_COLS // 2, 0, GRID - NA_COLS)
    c = np.arange(GRID)[None, :]
    tables["window"] = np.where((c >= start) & (c < start + NA_COLS), 0.0, NEG)
    return {name: np.asarray(t, np.float32) for name, t in tables.items()}


def constant_places():
    at, places = 0, {}
    for name, t in constant_tables().items():
        places[name] = (at, t.shape[1])
        at += t.shape[1]
    return places, at


PARAM_ROWS = {
    "c": (0, 0, 8, 0, 128), "b_ada": (0, 8, 24, 0, 128), "g_pre": (0, 32, 8, 0, 128),
    "norm_mix_g_2": (0, 40, 8, 0, 128), "norm_ffn_g_2": (0, 48, 8, 0, 128),
    "norm_mix_g_3": (0, 56, 8, 0, 128), "norm_mem_g_3": (0, 64, 8, 0, 128),
    "norm_ffn_g_3": (0, 72, 8, 0, 128), "conv_w": (0, 80, 48, 0, 128),
    "conv_lru_w_2": (1, 0, 8, 0, 128), "conv_mlstm_w_2": (1, 8, 16, 0, 128),
    "lru_ba_2": (1, 24, 2, 0, 128), "lru_bx_2": (1, 26, 2, 0, 128), "lru_lambda_2": (1, 28, 2, 0, 128),
    "rw_mu_rkv_3": (1, 30, 18, 0, 128), "rw_w0_3": (1, 48, 6, 0, 128), "rw_a0_3": (1, 54, 6, 0, 128),
    "rw_k_k_3": (1, 60, 3, 0, 128), "rw_k_a_3": (1, 63, 3, 0, 128), "rw_r_k_3": (1, 66, 3, 0, 128),
    "rw_mu_w_3": (1, 69, 2, 0, 64), "rw_mu_a_3": (1, 69, 2, 64, 64),
}


class Chain:

    def __init__(self, engine, sem):
        self.engine, self.sem, self.n = engine, sem, 0

    def __call__(self, instruction):
        self.n += 1
        instruction.then_inc(self.sem, 1)
        self.engine.wait_ge(self.sem, self.n)


class Chip:

    def __init__(self, nc, ctx, ins):
        self.nc, self.ins = nc, ins

        def sb(name, *shape):
            return ctx.enter_context(nc.sbuf_tensor(name, [P, *shape], F32))

        self.places, width = constant_places()
        self.constants = sb("constants", width)
        self.ring = sb("ring", RING * SLOT)
        self.chan = sb("chan", 20, CHW)
        self.tok = sb("tok", TT, 3840)
        self.small = sb("small", TT, 16)
        self.x = sb("x", TT, D)
        self.xn = sb("xn", TT, D)
        self.hT = sb("hT", DC, S)
        self.param_rows = sb("param_rows", 2, P)
        self.cols = sb("cols", 2, P)
        self.mod = sb("mod", 24)
        self.narrow_w = sb("narrow_w", 2 * 8 * 8 + 8 * 16)
        self.rows_bc = sb("rows_bc", 32)
        self.stat = sb("stat", 128)
        self.ps = ctx.enter_context(nc.psum_tensor("ps", [P, 8, BANK], F32))

        def sem(name):
            return ctx.enter_context(nc.semaphore(name))

        self.sem = sem
        self.params_landed = sem("params_landed")
        self.w_landed = [sem(f"w_landed{u}") for u in range(RING)]
        self.tile_done = [sem(f"tile_done{u}") for u in range(RING)]
        self.psum_free = [sem(f"psum_free{u}") for u in range(2)]
        self.tiles = [0] * RING
        self.copied = [0] * 2
        self.next_slot = 0
        self.products = sem("products")
        self.vectors = sem("vectors")
        self.activations = sem("activations")
        self.pools = sem("pools")
        self.loads = sem("loads")
        self.count = {"products": 0, "vectors": 0, "activations": 0, "pools": 0, "loads": 0}
        self.inverse_products = sem("inverse_products")
        self.inverse_updates = sem("inverse_updates")
        self.inverses = 0
        self.vchain = Chain(nc.vector, sem("vector_chain"))
        self.achain = Chain(nc.scalar, sem("scalar_chain"))

    def const(self, name):
        at, n = self.places[name]
        return self.constants[:, at:at + n]

    def col(self, name, n=0):
        group, row, _, _, _ = PARAM_ROWS[name]
        return self.cols[:, group, row + n:row + n + 1]

    def starts(self):
        return self.count["products"], self.count["vectors"], self.count["activations"]

    def advance(self, **steps):
        for name, n in steps.items():
            self.count[name] += n


class Scratch:

    def __init__(self, k, first_slot=2):
        self.k, self.at, self.end = k, first_slot * SLOT, RING * SLOT

    def take(self, n):
        a = self.k.ring[:, self.at:self.at + n]
        self.at += n
        assert self.at <= self.end
        return a


def over(ap, n):
    return ap.unsqueeze(1).broadcast_to([ap.shape[0], n, ap.shape[1]])


def along(ap, n):
    return ap.unsqueeze(2).broadcast_to([ap.shape[0], ap.shape[1], n])



def load_parameters(k, x):
    nc, ins = k.nc, k.ins
    with nc.Block() as block:
        loads = [(k.constants[:, :], ins["constants"]), (k.x[:, :, :], x.rearrange("b (t p) d -> p (b t) d", p=P))]
        for name, (g, row, n, at, m) in PARAM_ROWS.items():
            flat = ins[name].rearrange({1: "a -> a", 2: "a b -> (a b)", 3: "a b c -> (a b c)", 4: "a b c d -> (a b c d)"}[len(ins[name].shape)])
            loads.append((k.param_rows[row:row + n, g, at:at + m], flat.rearrange("(n m) -> n m", m=m)))
        w1 = ins["w_in"][0, :, 2048:2056].rearrange("(c p) n -> p c n", p=P)
        w2 = ins["w_in_2"][0, :, 1536:1544].rearrange("(c p) n -> p c n", p=P)
        w3 = ins["w_router_3"][0].rearrange("(c p) n -> p c n", p=P)
        loads.append((k.narrow_w[:, 0:64].rearrange("p (c n) -> p c n", n=8), w1))
        loads.append((k.narrow_w[:, 64:128].rearrange("p (c n) -> p c n", n=8), w2))
        loads.append((k.narrow_w[:, 128:256].rearrange("p (c n) -> p c n", n=16), w3))
        for n, name in enumerate(("a_log", "dt_bias", "mlstm_ig_b_2", "mlstm_fg_b_2")):
            loads.append((k.rows_bc[:, 4 * n:4 * n + 4], ins[name].partition_broadcast(P).rearrange("p a n -> p (a n)")))

        @block.gpsimd
        def _(pool):
            nc.gpsimd.memset(k.param_rows[:, :, :], 0.0).then_inc(k.pools, 1)
            nc.gpsimd.memset(k.chan[:, :, :], 0.0)

        @block.sync
        def _(sp):
            sp.dma_start(*loads[1]).then_inc(k.params_landed, 16)
            for u in range(RING):
                dst = k.ring[:, u * SLOT:(u + 1) * SLOT].rearrange("p (c n) -> p c n", n=TILE)
                sp.dma_start(dst, columns(ins["w_ada"], 0, TILE)(u)).then_inc(k.w_landed[u], 16)

        @block.tensor
        def _(pe):
            for u in range(RING):
                pe.sem_inc(k.tile_done[u], 1)
            pe.wait_ge(k.params_landed, 16 * len(loads))
            for g in range(2):
                last = nc.tensor.transpose(k.ps[:, 0, g * P:(g + 1) * P], k.param_rows[:, g, :], k.const("ident"))
            last.then_inc(k.products, 1)

        @block.scalar
        def _(act):
            for u in range(2):
                act.sem_inc(k.psum_free[u], 1)
            act.wait_ge(k.pools, 1)
            for dst, src in loads[0:1] + loads[2:]:
                act.dma_start(dst, src).then_inc(k.params_landed, 16)

        @block.vector
        def _(dve):
            dve.wait_ge(k.products, 1)
            nc.vector.tensor_copy(k.cols[:, :, :].rearrange("p g n -> p (g n)"), k.ps[:, 0, 0:2 * P])
    k.advance(products=1, pools=1)
    k.tiles = [1] * RING


def issue(k, sp, loads):
    for slot, before, dst, src in loads:
        sp.wait_ge(k.tile_done[slot], before + 1)
        sp.dma_start(dst, src).then_inc(k.w_landed[slot], 16)


def turn(k, src, chunks, dst, scale=None, shift=None, norm_of=None, ahead=()):
    nc = k.nc
    p0, v0, a0 = k.starts()
    rstd = k.stat[:, 0:TT]
    sums = k.stat[:, TT:2 * TT]
    with nc.Block() as block:
        @block.sync
        def _(sp):
            issue(k, sp, ahead)

        @block.scalar
        def _(act):
            if norm_of is not None:
                for t in range(TT):
                    last = nc.scalar.activation(src[:, t, 0:D], norm_of[:, t, :], ACT.Square, accum_out=sums[:, t:t + 1])
                k.achain(last)
                k.achain(nc.scalar.activation(rstd, sums, ACT.Ln, bias=k.const("eps"), scale=1.0 / D))
                nc.scalar.activation(rstd, rstd, ACT.Exp, scale=-0.5).then_inc(k.activations, 1)
            for c in [c for c in range(chunks) if c // 2 % 2]:
                act.wait_ge(k.products, p0 + c // 2 + 1)
                view = k.ps[:, c // 2, (c % 2) * S:(c % 2 + 1) * S]
                if scale is not None:
                    nc.scalar.activation(dst[:, c, 0:S], view, ACT.Identity, bias=shift(c) if shift else 0.0, scale=scale(c))
                else:
                    nc.scalar.copy(dst[:, c, 0:S], view)

        @block.vector
        def _(dve):
            if norm_of is not None:
                dve.wait_ge(k.activations, a0 + 1)
                for t in range(TT):
                    nc.vector.tensor_scalar(src[:, t, 0:D], norm_of[:, t, :], rstd[:, t:t + 1], None, ALU.mult).then_inc(k.vectors, 1)
            for c in [c for c in range(chunks) if c // 2 % 2 == 0]:
                dve.wait_ge(k.products, p0 + c // 2 + 1)
                view = k.ps[:, c // 2, (c % 2) * S:(c % 2 + 1) * S]
                if scale is not None and shift is not None:
                    nc.vector.tensor_scalar(dst[:, c, 0:S], view, scale(c), shift(c), ALU.mult, ALU.add)
                elif scale is not None:
                    nc.vector.tensor_scalar(dst[:, c, 0:S], view, scale(c), None, ALU.mult)
                else:
                    nc.vector.tensor_copy(dst[:, c, 0:S], view)

        @block.tensor
        def _(pe):
            if norm_of is not None:
                pe.wait_ge(k.vectors, v0 + TT)
            for b in range((chunks + 1) // 2):
                for c in range(2 * b, min(2 * b + 2, chunks)):
                    for t in range(TT):
                        at = (c % 2) * S + t * P
                        last = nc.tensor.transpose(k.ps[:, b, at:at + P], src[:, t, c * P:(c + 1) * P], k.const("ident"))
                last.then_inc(k.products, 1)
    k.advance(products=(chunks + 1) // 2, vectors=TT if norm_of is not None else 0,
              activations=1 if norm_of is not None else 0)


def each_tile(engine, n, first_slot, body, skip=0):
    if n // 2 > skip // 2:
        with engine.Fori(skip // 2, n // 2) as i:
            for u in range(2):
                body(i, u, (first_slot + u) % 2)
    if n % 2 and skip < n:
        body(n // 2, 0, first_slot)


class Stream:

    def __init__(self, k, parts, chunks=DC):
        self.k, self.parts, self.chunks = k, parts, chunks
        for part in parts:
            n = part["tiles"]
            first = k.next_slot
            part["first_slot"] = first
            part["start"], part["copied"] = list(k.tiles), list(k.copied)
            for slot, m in ((first, (n + 1) // 2), (1 - first, n // 2)):
                k.tiles[slot] += m
                k.copied[slot] += m
            k.next_slot = (first + n) % 2
        self.skip = min(2, parts[0]["tiles"])

    def tile(self, part, n, slot):
        dst = self.k.ring[:, slot * SLOT:(slot + 1) * SLOT].rearrange("p (c n) -> p c n", n=TILE)
        return dst[:, 0:self.chunks, 0:part["width"]], part["w"](n)

    def ahead(self):
        part = self.parts[0]
        slots = [(part["first_slot"] + n) % 2 for n in range(self.skip)]
        return [(slot, part["start"][slot], *self.tile(part, n, slot)) for n, slot in enumerate(slots)]


def project(k, hT, stream, narrow=None, vector=None, scalar=None):
    nc = k.nc
    chunks = stream.chunks
    p0, v0, a0 = k.starts()

    def copies(part):
        if not part["channel_major"]:
            return [(b, part["width"]) for b in range(TT)]
        return [(b, min(2, part["width"] // P - 2 * b) * S) for b in range((part["width"] // P + 1) // 2)]

    with nc.Block() as block:
        @block.sync
        def _(sp):
            for n, part in enumerate(stream.parts):
                def load(i, u, slot):
                    dst, src = stream.tile(part, 2 * i + u, slot)
                    sp.wait_ge(k.tile_done[slot], i + (part["start"][slot] + 1))
                    sp.dma_start(dst, src).then_inc(k.w_landed[slot], 16)
                each_tile(sp, part["tiles"], part["first_slot"], load, skip=0 if n else stream.skip)

        @block.tensor
        def _(pe):
            if narrow:
                w, out, n = narrow
                for t in range(TT):
                    for c in range(chunks):
                        last = nc.tensor.matmul(k.ps[:, 4, t * n:(t + 1) * n], hT[:, c, t * P:(t + 1) * P], w[:, c, :],
                                                start=c == 0, stop=c == chunks - 1)
                last.then_inc(k.products, 1)
            for part in stream.parts:
                width = part["width"]

                def multiply(i, u, slot):
                    wt = k.ring[:, slot * SLOT:(slot + 1) * SLOT].rearrange("p (c n) -> p c n", n=TILE)
                    pe.wait_ge(k.w_landed[slot], i * 16 + 16 * (part["start"][slot] + 1))
                    pe.wait_ge(k.psum_free[slot], i + (part["copied"][slot] + 1))
                    if part["channel_major"]:
                        for n in range(width // P):
                            for c in range(chunks):
                                last = nc.tensor.matmul(k.ps[:, 2 * slot + n // 2, (n % 2) * S:(n % 2 + 1) * S],
                                                        wt[:, c, n * P:(n + 1) * P], hT[:, c, 0:S],
                                                        start=c == 0, stop=c == chunks - 1)
                    else:
                        for t in range(TT):
                            for c in range(chunks):
                                last = nc.tensor.matmul(k.ps[:, 2 * slot + t, 0:width], hT[:, c, t * P:(t + 1) * P],
                                                        wt[:, c, 0:width], start=c == 0, stop=c == chunks - 1)
                    last.then_inc(k.tile_done[slot], 1)
                each_tile(pe, part["tiles"], part["first_slot"], multiply)

        @block.scalar
        def _(act):
            if narrow:
                w, out, n = narrow
                act.wait_ge(k.products, p0 + 1)
                nc.scalar.copy(out, k.ps[:, 4, 0:TT * n].rearrange("p (t n) -> p t n", n=n))
            for part in stream.parts:
                def copy(i, u, slot):
                    act.wait_ge(k.tile_done[slot], i + (part["start"][slot] + 2))
                    for b, n in copies(part):
                        last = nc.scalar.activation(part["out"](2 * i + u, b), shaped(k.ps[:, 2 * slot + b, 0:n], part),
                                                    part.get("func", ACT.Copy))
                    last.then_inc(k.psum_free[slot], 1)
                each_tile(act, part["tiles"], part["first_slot"], copy)
            if scalar:
                scalar(act)

        if vector:
            @block.vector
            def _(dve):
                vector(dve)
    k.advance(products=1 if narrow else 0)


def wait_copied(k, dve, part):
    first, n = part["first_slot"], part["tiles"]
    for slot, m in ((first, (n + 1) // 2), (1 - first, n // 2)):
        if m:
            dve.wait_ge(k.psum_free[slot], part["copied"][slot] + 1 + m)


def shaped(ap, part):
    return ap.rearrange("p (c s) -> p c s", s=S) if part["channel_major"] else ap


def columns(w, first, width):
    def tile(n):
        return w[0, :, bass.ds(n * width + first, width)].rearrange("(c p) n -> p c n", p=P)
    return tile


def to_chan(k, first, width):
    def out(n, b):
        chunks = min(2, width // P - 2 * b)
        return k.chan[:, bass.ds(n * (width // P) + (first + 2 * b), chunks), PAD:PAD + S]
    return out


def to_tok(k, first, width):
    def out(n, b):
        return k.tok[:, b, bass.ds(n * width + first, width)]
    return out


def chan_part(k, w, col, width, tiles, chunk):
    return {"w": columns(w, col, width), "width": width, "tiles": tiles, "channel_major": True,
            "out": to_chan(k, chunk, width)}


def tok_part(k, w, col, width, tiles, at, func=ACT.Copy):
    return {"w": columns(w, col, width), "width": width, "tiles": tiles, "channel_major": False,
            "out": to_tok(k, at, width), "func": func}


class WideStream:

    def __init__(self, k, branches):
        self.branches, self.plan, self.loads = branches, [], []
        for br in branches:
            for at in range(0, br["chunks"], 4):
                n, u = min(4, br["chunks"] - at), k.next_slot
                self.plan.append((br, at, n, u, k.tiles[u]))
                dst = k.ring[:, u * SLOT:u * SLOT + n * D].rearrange("p (c n) -> p c n", n=D)
                self.loads.append((u, k.tiles[u], dst, br["w"][at * P:(at + n) * P, :].rearrange("(c p) n -> p c n", p=P)))
                k.tiles[u] += 1
                k.next_slot = 1 - u

    def ahead(self):
        return self.loads[0:2]


def project_wide(k, stream):
    nc = k.nc
    p0, v0, a0 = k.starts()
    branches, plan = stream.branches, stream.plan
    with nc.Block() as block:
        @block.sync
        def _(sp):
            issue(k, sp, stream.loads[2:])

        @block.tensor
        def _(pe):
            for b, br in enumerate(branches):
                set0 = 4 * (b % 2)
                if b >= 2:
                    pe.wait_ge(k.vectors, v0 + b - 1)
                for at, n, u, before in [x[1:] for x in plan if x[0] is br]:
                    pe.wait_ge(k.w_landed[u], 16 * (before + 1))
                    wt = k.ring[:, u * SLOT:(u + 1) * SLOT].rearrange("p (c n) -> p c n", n=D)
                    for c in range(n):
                        for t in range(TT):
                            for h in range(2):
                                last = nc.tensor.matmul(k.ps[:, set0 + 2 * t + h, :], br["lhs"](at + c)[:, t * P:(t + 1) * P],
                                                        wt[:, c, h * BANK:(h + 1) * BANK],
                                                        start=at + c == 0, stop=at + c == br["chunks"] - 1)
                    last.then_inc(k.tile_done[u], 1)

        @block.vector
        def _(dve):
            for b, br in enumerate(branches):
                _, at, n, u, before = [x for x in plan if x[0] is br][-1]
                dve.wait_ge(k.tile_done[u], before + 2)
                what, dst = br["out"][0:2]
                sums = k.ps[:, 4 * (b % 2):4 * (b % 2) + 4, :].rearrange("p (t h) n -> p t (h n)", t=TT)
                for t in range(TT):
                    if what == "set":
                        last = nc.vector.tensor_copy(dst[:, t, :], sums[:, t, :])
                    elif what == "add":
                        last = nc.vector.tensor_tensor(dst[:, t, :], dst[:, t, :], sums[:, t, :], ALU.add)
                    elif what == "gate_set":
                        last = nc.vector.tensor_tensor(dst[:, t, :], sums[:, t, :], br["out"][2][:, t, :], ALU.mult)
                    else:
                        gate = br["out"][2]
                        last = nc.vector.tensor_tensor(gate[:, t, :], sums[:, t, :], gate[:, t, :], ALU.mult)
                if what == "gate_add":
                    k.vchain(last)
                    for t in range(TT):
                        last = nc.vector.tensor_tensor(dst[:, t, :], dst[:, t, :], gate[:, t, :], ALU.add)
                k.vchain(last)
                dve.sem_inc(k.vectors, 1)
    k.advance(vectors=len(branches))


def half_heads(ap, r):
    return ap[:, r::2, :]


def half_sums(k, heads, r):
    return k.ps[:, 2 * r:2 * r + 2, :].rearrange("p b (h k) -> p (b h) k", k=S)[:, 0:heads // 2, :]


def attention(k, heads, qT, kT, v, scale, mask, out, causal=False, gate=None):
    nc = k.nc
    p0, v0, a0 = k.starts()
    s = Scratch(k)
    score = s.take(heads * S)
    probs_t = s.take(TT * heads * P).rearrange("p (j h q) -> p j h q", j=TT, h=heads)
    top = k.stat[:, 0:heads]
    total = k.stat[:, 16:16 + heads]
    inv = k.stat[:, 32:32 + heads]
    SCORES, TURNED, MIXED = 1, 2, 3
    SHIFTED, DONE = 1, 2
    PROBS, COPIED = 1, 2
    with nc.Block() as block:
        @block.tensor
        def _(pe):
            for t in range(TT):
                keys = (t + 1) * P if causal else S
                if t:
                    pe.wait_ge(k.vectors, v0 + 2 * (t - 1) + DONE)
                for h in range(heads):
                    bank, at = 2 * (h % 2) + h // 4, h // 2 % 2 * S
                    last = nc.tensor.matmul(k.ps[:, bank, at:at + keys], qT(h)[:, t * P:(t + 1) * P],
                                            kT(h)[:, 0:keys], start=True, stop=True)
                last.then_inc(k.products, 1)
                pe.wait_ge(k.activations, a0 + 2 * t + PROBS)
                for j in range(keys // P):
                    for h in range(heads):
                        n = j * heads + h
                        last = nc.tensor.transpose(k.ps[:, 4 + n // 4, (n % 4) * P:(n % 4 + 1) * P],
                                                   score.rearrange("p (h k) -> p h k", h=heads)[:, h, j * P:(j + 1) * P],
                                                   k.const("ident"))
                last.then_inc(k.products, 1)
                pe.wait_ge(k.activations, a0 + 2 * t + COPIED)
                for h in range(heads):
                    for j in range(keys // P):
                        last = nc.tensor.matmul(k.ps[:, 0, h * HD:(h + 1) * HD], probs_t[:, j, h, :], v(j, h),
                                                start=j == 0, stop=j == keys // P - 1)
                last.then_inc(k.products, 1)

        @block.vector
        def _(dve):
            for t in range(TT):
                keys = (t + 1) * P if causal else S
                sc = score.rearrange("p (h k) -> p h k", h=heads)[:, :, 0:keys]
                halves = [(half_heads(sc, r), half_sums(k, heads, r)[:, :, 0:keys], r) for r in range(2)]
                dve.wait_ge(k.products, p0 + 3 * t + SCORES)
                for dst, sums, r in halves:
                    if mask is None:
                        last = nc.vector.tensor_scalar(dst, sums, scale, None, ALU.mult)
                    else:
                        last = nc.vector.scalar_tensor_tensor(out=dst, in0=sums, scalar=scale, in1=half_heads(mask(t), r),
                                                              op0=ALU.mult, op1=ALU.add)
                k.vchain(last)
                k.vchain(nc.vector.tensor_reduce(top, sc, AX_X, ALU.max))
                nc.vector.tensor_tensor(sc, sc, along(top, keys), ALU.subtract).then_inc(k.vectors, 1)
                dve.wait_ge(k.activations, a0 + 2 * t + PROBS)
                k.vchain(nc.vector.tensor_reduce(total, sc, AX_X, ALU.add))
                k.vchain(nc.vector.reciprocal(inv, total))
                dve.wait_ge(k.products, p0 + 3 * t + MIXED)
                nc.vector.tensor_tensor(out[:, t, 0:heads * HD].rearrange("p (h d) -> p h d", h=heads),
                                        k.ps[:, 0, 0:heads * HD].rearrange("p (h d) -> p h d", h=heads),
                                        along(inv, HD), ALU.mult).then_inc(k.vectors, 1)
                if gate is not None:
                    dve.wait_ge(k.vectors, v0 + 2 * t + DONE)
                    nc.vector.tensor_tensor(out[:, t, 0:heads * HD], out[:, t, 0:heads * HD], gate[:, t, :], ALU.mult)

        @block.scalar
        def _(act):
            for t in range(TT):
                keys = (t + 1) * P if causal else S
                sc = score.rearrange("p (h k) -> p h k", h=heads)[:, :, 0:keys]
                act.wait_ge(k.vectors, v0 + 2 * t + SHIFTED)
                nc.scalar.activation(sc, sc, ACT.Exp).then_inc(k.activations, 1)
                act.wait_ge(k.products, p0 + 3 * t + TURNED)
                n = keys // P * heads * P
                nc.scalar.copy(probs_t.rearrange("p j h q -> p (j h q)")[:, 0:n],
                               k.ps[:, 4:8, :].rearrange("p b n -> p (b n)")[:, 0:n]).then_inc(k.activations, 1)
    k.advance(products=3 * TT, vectors=2 * TT, activations=2 * TT)


def convolve(k, dve, first, chunks, weights, dst):
    nc = k.nc
    for tap in range(4):
        for c in range(chunks):
            src = k.chan[:, first + c, PAD - 3 + tap:PAD - 3 + tap + S]
            if tap == 0:
                last = nc.vector.tensor_scalar(dst[:, c, 0:S], src, weights(tap, c), None, ALU.mult)
            else:
                last = nc.vector.scalar_tensor_tensor(out=dst[:, c, 0:S], in0=src, scalar=weights(tap, c),
                                                      in1=dst[:, c, 0:S], op0=ALU.mult, op1=ALU.add)
        k.vchain(last)


def invert_tensor(k, pe, groups, first, levels, A_t, X, Y):
    nc = k.nc
    at = k.inverses
    for n in range(1, levels):
        before = at + 2 * groups * (n - 1)
        for g in range(groups):
            if n > 1:
                pe.wait_ge(k.inverse_updates, before - 2 * groups + groups + g + 1)
            for m in range(4):
                last = nc.tensor.matmul(k.ps[:, first + g, m * P:(m + 1) * P], A_t(4 * g + m), X(4 * g + m), start=True, stop=True)
            last.then_inc(k.inverse_products, 1)
        for g in range(groups):
            pe.wait_ge(k.inverse_updates, before + g + 1)
            for m in range(4):
                nc.tensor.matmul(k.ps[:, first + g, m * P:(m + 1) * P], Y(4 * g + m), k.U(4 * g + m), start=True, stop=True)
            for m in range(4):
                last = nc.tensor.matmul(k.ps[:, first + groups + g, m * P:(m + 1) * P], k.U(4 * g + m), Y(4 * g + m), start=True, stop=True)
            last.then_inc(k.inverse_products, 1)


def invert_vector(k, dve, groups, first, levels, A_t, X, Y):
    nc = k.nc
    at = k.inverses

    def group(f, g):
        base = f(4 * g)
        return f(4 * g, 4)

    for n in range(1, levels):
        before = at + 2 * groups * (n - 1)
        level = over(k.const(f"level{n}"), 4)
        for g in range(groups):
            dve.wait_ge(k.inverse_products, before + g + 1)
            nc.vector.tensor_tensor(group(k.U, g), k.ps[:, first + g, :].rearrange("p (m n) -> p m n", m=4), level, ALU.mult)\
                .then_inc(k.inverse_updates, 1)
        for g in range(groups):
            dve.wait_ge(k.inverse_products, before + groups + g + 1)
            nc.vector.tensor_tensor(group(X, g), group(X, g), k.ps[:, first + g, :].rearrange("p (m n) -> p m n", m=4), ALU.add)
            nc.vector.tensor_tensor(group(Y, g), group(Y, g), k.ps[:, first + groups + g, :].rearrange("p (m n) -> p m n", m=4), ALU.add)\
                .then_inc(k.inverse_updates, 1)


def matrices(ap):
    def f(n, m=None):
        a = ap[:, n * P:(n + (m or 1)) * P]
        return a if m is None else a.rearrange("p (m n) -> p m n", m=m)
    return f



def modulation(k, ahead):
    nc = k.nc
    p0, v0, a0 = k.starts()
    cT = k.stat[:, 64:64 + DC]
    tiles = 3 * D // TILE
    with nc.Block() as block:
        @block.sync
        def _(sp):
            issue(k, sp, ahead)

        @block.scalar
        def _(act):
            group, row, n, _, _ = PARAM_ROWS["c"]
            nc.scalar.activation(cT, k.cols[:, group, row:row + n], ACT.Silu).then_inc(k.activations, 1)

        @block.tensor
        def _(pe):
            pe.wait_ge(k.activations, a0 + 1)
            for u in range(tiles):
                wt = k.ring[:, u * SLOT:(u + 1) * SLOT].rearrange("p (c n) -> p c n", n=TILE)
                pe.wait_ge(k.w_landed[u], 16)
                for n in range(TILE // P):
                    for c in range(DC):
                        last = nc.tensor.matmul(k.ps[:, 0, 4 * u + n:4 * u + n + 1], wt[:, c, n * P:(n + 1) * P],
                                                cT[:, c:c + 1], start=c == 0, stop=c == DC - 1)
                last.then_inc(k.tile_done[u], 1)

        @block.vector
        def _(dve):
            for u in range(tiles):
                dve.wait_ge(k.tile_done[u], 2)
            group, row, n, _, _ = PARAM_ROWS["b_ada"]
            k.vchain(nc.vector.tensor_tensor(k.mod[:, :], k.ps[:, 0, 0:24], k.cols[:, group, row:row + n], ALU.add))
            group, row, n, _, _ = PARAM_ROWS["g_pre"]
            k.vchain(nc.vector.scalar_tensor_tensor(out=k.mod[:, DC:2 * DC], in0=k.mod[:, DC:2 * DC], scalar=1.0,
                                                    in1=k.cols[:, group, row:row + n], op0=ALU.add, op1=ALU.mult))
    k.advance(activations=1)


def delta_rule(k, out):
    nc = k.nc
    s = Scratch(k)
    qkv = s.take(12 * S).rearrange("p (c s) -> p c s", s=S)

    norms = s.take(8 * S)
    k_tok = s.take(TT * 512).rearrange("p (t n) -> p t n", t=TT)
    v_tok = s.take(TT * 512).rearrange("p (t n) -> p t n", t=TT)
    p0, v0, a0 = k.starts()
    with nc.Block() as block:
        @block.scalar
        def _(act):
            nc.scalar.activation(norms, qkv[:, 0:8, :].rearrange("p c s -> p (c s)"), ACT.Square).then_inc(k.activations, 1)
            act.wait_ge(k.products, p0 + 1)
            k.achain(nc.scalar.activation(norms, k.ps[:, 0:4, :].rearrange("p b n -> p (b n)"), ACT.Ln, bias=k.const("eps")))
            nc.scalar.activation(norms[:, 0:4 * S], norms[:, 0:4 * S], ACT.Exp, scale=-0.5, bias=k.const("log_scale"))
            nc.scalar.activation(norms[:, 4 * S:8 * S], norms[:, 4 * S:8 * S], ACT.Exp, scale=-0.5).then_inc(k.activations, 1)

        @block.tensor
        def _(pe):
            pe.wait_ge(k.activations, a0 + 1)
            for b in range(4):
                last = nc.tensor.matmul(k.ps[:, b, :], k.const("ones"), norms[:, b * BANK:(b + 1) * BANK], start=True, stop=True)
            last.then_inc(k.products, 1)
            pe.wait_ge(k.vectors, v0 + 1)
            for t in range(TT):
                for h in range(4):
                    nc.tensor.transpose(k.ps[:, 4 + t, h * P:(h + 1) * P], qkv[:, 4 + h, t * P:(t + 1) * P], k.const("ident"))
                    last = nc.tensor.transpose(k.ps[:, 6 + t, h * P:(h + 1) * P], qkv[:, 8 + h, t * P:(t + 1) * P], k.const("ident"))
            last.then_inc(k.products, 1)

        @block.vector
        def _(dve):
            dve.wait_ge(k.activations, a0 + 2)
            flat = qkv[:, 0:8, :].rearrange("p c s -> p (c s)")
            nc.vector.tensor_tensor(flat, flat, norms, ALU.mult).then_inc(k.vectors, 1)
            dve.wait_ge(k.products, p0 + 2)
            nc.vector.tensor_copy(k_tok.rearrange("p t n -> p (t n)"), k.ps[:, 4:6, :].rearrange("p t n -> p (t n)"))
            nc.vector.tensor_copy(v_tok.rearrange("p t n -> p (t n)"), k.ps[:, 6:8, :].rearrange("p t n -> p (t n)"))
    k.advance(products=2, vectors=1, activations=2)

    beta, g, g_neg, G, eG, eGr, t1, t2 = [k.stat[:, 8 * n:8 * n + 8] for n in range(8)]
    ea = k.stat[:, 64:68]

    def th(a):
        return a.rearrange("p (t h) -> p t h", t=TT)
    p0, v0, a0 = k.starts()
    with nc.Block() as block:
        @block.vector
        def _(dve):
            k.vchain(nc.vector.tensor_tensor(th(t1), k.small[:, :, 4:8], over(k.rows_bc[:, 4:8], TT), ALU.add))
            nc.vector.scalar_tensor_tensor(out=t2, in0=t1, scalar=-1.0, in1=t1, op0=ALU.mult, op1=ALU.max).then_inc(k.vectors, 1)
            dve.wait_ge(k.activations, a0 + 1)
            k.vchain(nc.vector.scalar_tensor_tensor(out=t1, in0=t1, scalar=0.0, in1=t2, op0=ALU.max, op1=ALU.add))
            k.vchain(nc.vector.tensor_tensor(th(g_neg), th(t1), over(ea, TT), ALU.mult))
            nc.vector.tensor_scalar(g, g_neg, -1.0, None, ALU.mult).then_inc(k.vectors, 1)
            dve.wait_ge(k.products, p0 + 1)
            k.vchain(nc.vector.tensor_copy(G, k.ps[:, 0, 0:8]))
            nc.vector.tensor_tensor(t2, k.ps[:, 0, 8:16], G, ALU.subtract).then_inc(k.vectors, 1)

        @block.scalar
        def _(act):
            act.wait_ge(k.vectors, v0 + 1)
            k.achain(nc.scalar.activation(t2, t2, ACT.Exp, scale=-1.0))
            k.achain(nc.scalar.activation(t2, t2, ACT.Ln, bias=k.const("ones")[:, 0:1]))
            nc.scalar.activation(ea, k.rows_bc[:, 0:4], ACT.Exp)
            nc.scalar.activation(th(beta), k.small[:, :, 0:4], ACT.Sigmoid).then_inc(k.activations, 1)
            act.wait_ge(k.vectors, v0 + 3)
            nc.scalar.activation(eG, G, ACT.Exp)
            nc.scalar.activation(eGr, t2, ACT.Exp)

        @block.tensor
        def _(pe):
            pe.wait_ge(k.vectors, v0 + 2)
            nc.tensor.matmul(k.ps[:, 0, 0:8], k.const("upper"), g, start=True, stop=True)
            nc.tensor.matmul(k.ps[:, 0, 8:16], k.const("ones"), g, start=True, stop=True).then_inc(k.products, 1)
    k.advance(products=1, vectors=3, activations=1)

    n8 = 8 * P
    A, A_t, U, X, Y, qk = [matrices(s.take(n8)) for _ in range(6)]
    decay, decay_t = U, X
    k.U = U
    p0, v0, a0 = k.starts()
    start = k.inverses
    with nc.Block() as block:
        @block.tensor
        def _(pe):
            def spread(a, n):
                return a[:, n:n + 1].broadcast_to([P, P])
            for t in range(TT):
                for h in range(4):
                    n = 4 * t + h
                    kT, qT = qkv[:, 4 + h, t * P:(t + 1) * P], qkv[:, h, t * P:(t + 1) * P]
                    c = slice(h * P, (h + 1) * P)
                    nc.tensor.matmul(k.ps[:, t, c], k.const("upper"), spread(g, n), start=True, stop=False)
                    nc.tensor.matmul(k.ps[:, t, c], spread(g_neg, n), k.const("upper"), start=False, stop=True)
                    nc.tensor.matmul(k.ps[:, 2 + t, c], spread(g, n), k.const("upper"), start=True, stop=False)
                    nc.tensor.matmul(k.ps[:, 2 + t, c], k.const("upper"), spread(g_neg, n), start=False, stop=True)
                    nc.tensor.matmul(k.ps[:, 4 + t, c], kT, kT, start=True, stop=True)
                    last = nc.tensor.matmul(k.ps[:, 6 + t, c], kT, qT, start=True, stop=True)
            last.then_inc(k.products, 1)
            pe.wait_ge(k.vectors, v0 + 2)
            for n in range(8):
                last = nc.tensor.transpose(k.ps[:, n // 4, (n % 4) * P:(n % 4 + 1) * P], A(n), k.const("ident"))
            last.then_inc(k.products, 1)
            pe.wait_ge(k.vectors, v0 + 3)
            invert_tensor(k, pe, 2, 2, 7, A_t, X, Y)

        @block.vector
        def _(dve):
            def bank(b):
                return k.ps[:, b:b + 2, :].rearrange("p b (m n) -> p (b m) n", m=4)
            dve.wait_ge(k.products, p0 + 1)
            nc.vector.tensor_tensor(decay(0, 8), bank(0), over(k.const("neg_not_lower"), 8), ALU.add)
            nc.vector.tensor_tensor(decay_t(0, 8), bank(2), over(k.const("neg_not_upper"), 8), ALU.add).then_inc(k.vectors, 1)
            dve.wait_ge(k.activations, a0 + 1)
            k.vchain(nc.vector.tensor_tensor(A(0, 8), bank(4), decay(0, 8), ALU.mult))
            nc.vector.tensor_tensor(qk(0, 8), bank(6), decay_t(0, 8), ALU.mult)
            k.vchain(nc.vector.tensor_tensor(A(0, 8), A(0, 8), over(k.const("lower_strict"), 8), ALU.mult))
            nc.vector.tensor_tensor(A(0, 8), A(0, 8), along(beta, P), ALU.mult).then_inc(k.vectors, 1)
            dve.wait_ge(k.products, p0 + 2)
            k.vchain(nc.vector.tensor_copy(A_t(0, 8), bank(0)))
            nc.vector.tensor_tensor(X(0, 8), A(0, 8), over(k.const("level0"), 8), ALU.mult)
            k.vchain(nc.vector.tensor_tensor(Y(0, 8), A_t(0, 8), over(k.const("level0_t"), 8), ALU.mult))
            nc.vector.tensor_tensor(X(0, 8), X(0, 8), over(k.const("ident"), 8), ALU.add)
            nc.vector.tensor_tensor(Y(0, 8), Y(0, 8), over(k.const("ident"), 8), ALU.add).then_inc(k.vectors, 1)
            invert_vector(k, dve, 2, 2, 7, A_t, X, Y)

        @block.scalar
        def _(act):
            act.wait_ge(k.vectors, v0 + 1)
            nc.scalar.activation(decay(0, 8), decay(0, 8), ACT.Exp)
            nc.scalar.activation(decay_t(0, 8), decay_t(0, 8), ACT.Exp).then_inc(k.activations, 1)
    k.inverses = start + 6 * 2 * 2
    k.advance(products=2, vectors=3, activations=1)

    kb = A(0, 8)
    vb = A_t(0, 8)
    kd = U(0, 4)
    w_t = X(0, 4)
    state = X(4, 4)
    q_state = U(4, 4)
    u_new = s.take(n8).rearrange("p (m n) -> p m n", m=8)
    eighth = "p (m n) -> p m n"
    p0, v0, a0 = k.starts()
    with nc.Block() as block:
        @block.vector
        def _(dve):
            k8 = k_tok.rearrange("p t (m n) -> p (t m) n", m=4)
            v8 = v_tok.rearrange("p t (m n) -> p (t m) n", m=4)
            nc.vector.tensor_tensor(vb, v8, along(beta, P), ALU.mult)
            nc.vector.tensor_tensor(kd, k8[:, 0:4, :], along(eGr[:, 0:4], P), ALU.mult)
            k.vchain(nc.vector.tensor_tensor(kb, k8, along(beta, P), ALU.mult))
            nc.vector.tensor_tensor(kb, kb, along(eG, P), ALU.mult).then_inc(k.vectors, 1)
            dve.wait_ge(k.products, p0 + 1)
            nc.vector.tensor_copy(u_new, k.ps[:, 0:2, :].rearrange("p b (m n) -> p (b m) n", m=4))
            nc.vector.tensor_copy(w_t, k.ps[:, 2, :].rearrange(eighth, m=4)).then_inc(k.vectors, 1)
            dve.wait_ge(k.products, p0 + 2)
            nc.vector.tensor_copy(state, k.ps[:, 3, :].rearrange(eighth, m=4)).then_inc(k.vectors, 1)
            dve.wait_ge(k.products, p0 + 3)
            nc.vector.tensor_tensor(u_new[:, 4:8, :], u_new[:, 4:8, :], k.ps[:, 4, :].rearrange(eighth, m=4), ALU.subtract).then_inc(k.vectors, 1)
            k.vchain(nc.vector.tensor_tensor(q_state, k.ps[:, 5, :].rearrange(eighth, m=4), along(eG[:, 4:8], P), ALU.mult))
            dve.wait_ge(k.products, p0 + 4)
            o = out[:, :, 0:512].rearrange("p t (m n) -> p t m n", m=4)
            nc.vector.tensor_copy(o[:, 0], k.ps[:, 6, :].rearrange(eighth, m=4))
            k.vchain(nc.vector.tensor_tensor(o[:, 1], k.ps[:, 7, :].rearrange(eighth, m=4), q_state, ALU.add))
            for t in range(TT):
                last = nc.vector.tensor_tensor(kb[:, 4 * t:4 * t + 4, :], o[:, t], o[:, t], ALU.mult)
            k.vchain(last)
            nc.vector.tensor_reduce(t1, kb, AX_X, ALU.add).then_inc(k.vectors, 1)
            dve.wait_ge(k.activations, a0 + 1)
            for t in range(TT):
                last = nc.vector.tensor_tensor(o[:, t], o[:, t], along(t1[:, 4 * t:4 * t + 4], P), ALU.mult)
            k.vchain(last)
            for t in range(TT):
                last = nc.vector.tensor_tensor(o[:, t], o[:, t], over(k_tok[:, 0, 0:P], 4), ALU.mult)
            k.vchain(last)
            for t in range(TT):
                last = nc.vector.tensor_tensor(out[:, t, 0:512], out[:, t, 0:512], k.tok[:, t, 0:512], ALU.mult)
            k.vchain(last)

        @block.sync
        def _(sp):
            sp.wait_ge(k.vectors, v0 + 1)
            sp.dma_start(k_tok[:, 0, 0:P], k.ins["dn_norm_g"].partition_broadcast(P).rearrange("p a n -> p (a n)")).then_inc(k.loads, 16)

        @block.scalar
        def _(act):
            act.wait_ge(k.vectors, v0 + 5)
            act.wait_ge(k.loads, 16 * (k.count["loads"] + 1))
            k.achain(nc.scalar.activation(t1, t1, ACT.Ln, bias=k.const("eps"), scale=1.0 / DN_D))
            nc.scalar.activation(t1, t1, ACT.Exp, scale=-0.5).then_inc(k.activations, 1)

        @block.tensor
        def _(pe):
            pe.wait_ge(k.vectors, v0 + 1)
            for n in range(8):
                nc.tensor.matmul(k.ps[:, n // 4, (n % 4) * P:(n % 4 + 1) * P], Y(n), vb[:, n, :], start=True, stop=True)
            for h in range(4):
                last = nc.tensor.matmul(k.ps[:, 2, h * P:(h + 1) * P], kb[:, 4 + h, :], Y(4 + h), start=True, stop=True)
            last.then_inc(k.products, 1)
            pe.wait_ge(k.vectors, v0 + 2)
            for h in range(4):
                last = nc.tensor.matmul(k.ps[:, 3, h * P:(h + 1) * P], kd[:, h, :], u_new[:, h, :], start=True, stop=True)
            last.then_inc(k.products, 1)
            pe.wait_ge(k.vectors, v0 + 3)
            for h in range(4):
                nc.tensor.matmul(k.ps[:, 4, h * P:(h + 1) * P], w_t[:, h, :], state[:, h, :], start=True, stop=True)
                last = nc.tensor.matmul(k.ps[:, 5, h * P:(h + 1) * P], qkv[:, h, P:S], state[:, h, :], start=True, stop=True)
            last.then_inc(k.products, 1)
            pe.wait_ge(k.vectors, v0 + 4)
            for n in range(8):
                last = nc.tensor.matmul(k.ps[:, 6 + n // 4, (n % 4) * P:(n % 4 + 1) * P], qk(n), u_new[:, n, :], start=True, stop=True)
            last.then_inc(k.products, 1)
    k.advance(products=4, vectors=5, activations=1, loads=1)


def first_layer(k):
    nc, w = k.nc, k.ins["w_in"]
    stream = Stream(k, [
        chan_part(k, w, 0, 512, 3, 0),
        chan_part(k, w, 2056, 512, 2, 12),
        tok_part(k, w, 1536, 512, 1, 0, ACT.Silu),
        tok_part(k, w, 3080, 512, 1, 512),
        tok_part(k, w, 3592, 512, 1, 1024, ACT.Silu),
        tok_part(k, w, 4104, 512, 4, 1536, ACT.Sigmoid),
    ])
    modulation(k, stream.ahead())
    turn(k, k.xn, DC, k.hT, scale=lambda c: k.mod[:, DC + c:DC + c + 1], shift=lambda c: k.mod[:, c:c + 1], norm_of=k.x)
    qkv = Scratch(k).take(12 * S).rearrange("p (c s) -> p c s", s=S)

    def convolve_beside(dve):
        wait_copied(k, dve, stream.parts[0])
        convolve(k, dve, 0, 12, lambda tap, c: k.col("conv_w", tap * 12 + c), qkv)
        dve.sem_inc(k.vectors, 1)

    def silu_behind(act):
        act.wait_ge(k.vectors, k.count["vectors"] + 1)
        nc.scalar.activation(qkv, qkv, ACT.Silu)
    project(k, k.hT, stream, narrow=(k.narrow_w[:, 0:64].rearrange("p (c n) -> p c n", n=8), k.small[:, :, 0:8], 8),
            vector=convolve_beside, scalar=silu_behind)
    k.advance(vectors=1)
    delta_rule(k, k.xn)
    turn(k, k.xn, 4, k.hT[:, 0:4, :])
    causal = k.const("causal").rearrange("p (t n) -> p t n", t=TT)
    attention(k, MB_H, lambda h: k.chan[64 * (h % 2):64 * (h % 2) + 64, 12 + h // 2, PAD:PAD + S],
              lambda h: k.chan[64 * (h % 2):64 * (h % 2) + 64, 16 + h // 2, PAD:PAD + S],
              lambda t, h: k.tok[:, t, 512 + h * 64:512 + h * 64 + 64], MB_D ** -0.5,
              lambda t: over(causal[:, t, 0:(t + 1) * P], MB_H), k.xn, causal=True, gate=k.tok[:, :, 1024:1536])
    stream = WideStream(k, [
        {"lhs": lambda c: k.hT[:, c, :], "w": k.ins["w_proj_dn"][0], "chunks": 4, "out": ("gate_set", k.xn, k.tok[:, :, 1536:2560])},
        {"lhs": lambda c: k.hT[:, 4 + c, :], "w": k.ins["w_proj_mb"][0], "chunks": 4, "out": ("gate_add", k.xn, k.tok[:, :, 2560:3584])},
    ])
    turn(k, k.xn, 4, k.hT[:, 4:8, :], ahead=stream.ahead())
    project_wide(k, stream)
    stream = WideStream(k, [{"lhs": lambda c: k.hT[:, c, :], "w": k.ins["w_out"][0], "chunks": DC, "out": ("set", k.xn)}])
    turn(k, k.xn, DC, k.hT, ahead=stream.ahead())
    project_wide(k, stream)

    s = Scratch(k)
    gate_diag = s.take(D)
    gain = s.take(D)
    squares = s.take(TT * D).rearrange("p (t n) -> p t n", t=TT)
    sums, rstd = k.stat[:, 0:2], k.stat[:, 2:4]
    p0, v0, a0 = k.starts()
    with nc.Block() as block:
        @block.sync
        def _(sp):
            sp.dma_start(gain, k.ins["g_post"].partition_broadcast(P).rearrange("p a n -> p (a n)")).then_inc(k.loads, 16)

        @block.vector
        def _(dve):
            for c in range(DC):
                last = nc.vector.tensor_scalar(gate_diag[:, c * P:(c + 1) * P], k.const("ident"), k.mod[:, 2 * DC + c:2 * DC + c + 1], None, ALU.mult)
            last.then_inc(k.vectors, 1)
            dve.wait_ge(k.products, p0 + 1)
            dve.wait_ge(k.loads, 16 * (k.count["loads"] + 1))
            k.vchain(nc.vector.tensor_tensor(gain, gain, k.ps[:, 0:2, :].rearrange("p b n -> p (b n)"), ALU.mult))
            dve.wait_ge(k.activations, a0 + 1)
            for t in range(TT):
                last = nc.vector.scalar_tensor_tensor(out=k.xn[:, t, :], in0=k.xn[:, t, :], scalar=rstd[:, t:t + 1], in1=gain, op0=ALU.mult, op1=ALU.mult)
            k.vchain(last)
            for t in range(TT):
                nc.vector.tensor_tensor(k.x[:, t, :], k.x[:, t, :], k.xn[:, t, :], ALU.add)

        @block.tensor
        def _(pe):
            pe.wait_ge(k.vectors, v0 + 1)
            for b in range(2):
                last = nc.tensor.matmul(k.ps[:, b, :], k.const("ones"), gate_diag[:, b * BANK:(b + 1) * BANK], start=True, stop=True)
            last.then_inc(k.products, 1)

        @block.scalar
        def _(act):
            for t in range(TT):
                last = nc.scalar.activation(squares[:, t, :], k.xn[:, t, :], ACT.Square, accum_out=sums[:, t:t + 1])
            k.achain(last)
            k.achain(nc.scalar.activation(rstd, sums, ACT.Ln, bias=k.const("eps"), scale=1.0 / D))
            nc.scalar.activation(rstd, rstd, ACT.Exp, scale=-0.5).then_inc(k.activations, 1)
    k.advance(products=1, vectors=1, activations=1, loads=1)



def softplus_vector(k, dve, z, magnitude):
    return k.nc.vector.scalar_tensor_tensor(out=magnitude, in0=z, scalar=-1.0, in1=z, op0=ALU.mult, op1=ALU.max)


def softplus_scalar(k, magnitude):
    k.achain(k.nc.scalar.activation(magnitude, magnitude, ACT.Exp, scale=-1.0))
    return k.nc.scalar.activation(magnitude, magnitude, ACT.Ln, bias=k.const("ones")[:, 0:1])


def lru(k, out):
    nc = k.nc
    s = Scratch(k)
    s.take(4 * S)
    xa = s.take(2 * S).rearrange("p (c s) -> p c s", s=S)
    gates_w = s.take(2 * 2 * P).rearrange("p (w c n) -> p w c n", w=2, c=2)
    r, i, a, th, h = [s.take(2 * S).rearrange("p (c s) -> p c s", s=S) for _ in range(5)]
    rate, mag = k.stat[:, 0:2], k.stat[:, 2:4]
    g, row, n, _, _ = PARAM_ROWS["lru_lambda_2"]
    lam = k.cols[:, g, row:row + n]
    p0, v0, a0 = k.starts()
    with nc.Block() as block:
        @block.gpsimd
        def _(pool):
            nc.gpsimd.memset(gates_w, 0.0).then_inc(k.pools, 1)

        @block.sync
        def _(sp):
            sp.wait_ge(k.pools, k.count["pools"] + 1)
            for n, name in enumerate(("lru_wa_2", "lru_wx_2")):
                for half in range(2):
                    q = slice(64 * half, 64 * half + 64)
                    src = k.ins[name][0].rearrange("(c r) i j -> r i c j", r=2)[half]
                    sp.dma_start(gates_w[q, n, :, q], src).then_inc(k.loads, 16)

        @block.tensor
        def _(pe):
            pe.wait_ge(k.loads, 16 * (k.count["loads"] + 4))
            for n in range(2):
                for c in range(2):
                    last = nc.tensor.matmul(k.ps[:, n, c * S:(c + 1) * S], gates_w[:, n, c, :], xa[:, c, :], start=True, stop=True)
            last.then_inc(k.products, 1)

        @block.scalar
        def _(act):
            act.wait_ge(k.vectors, v0 + 1)
            softplus_scalar(k, mag).then_inc(k.activations, 1)
            act.wait_ge(k.products, p0 + 1)
            for c in range(2):
                nc.scalar.activation(r[:, c, :], k.ps[:, 0, c * S:(c + 1) * S], ACT.Sigmoid, bias=k.col("lru_ba_2", c))
                last = nc.scalar.activation(i[:, c, :], k.ps[:, 1, c * S:(c + 1) * S], ACT.Sigmoid, bias=k.col("lru_bx_2", c))
            last.then_inc(k.activations, 1)
            act.wait_ge(k.vectors, v0 + 2)
            nc.scalar.activation(a, r, ACT.Exp)
            nc.scalar.activation(th, r, ACT.Tanh, scale=-1.0).then_inc(k.activations, 1)
            act.wait_ge(k.vectors, v0 + 3)
            nc.scalar.activation(th, th, ACT.Sqrt).then_inc(k.activations, 1)
            nc.scalar.activation(r, k.chan[:, 2:4, PAD:PAD + S], ACT.Gelu_apprx_tanh).then_inc(k.activations, 1)

        @block.vector
        def _(dve):
            softplus_vector(k, dve, lam, mag).then_inc(k.vectors, 1)
            dve.wait_ge(k.activations, a0 + 1)
            k.vchain(nc.vector.tensor_scalar(rate, lam, -1.0, 0.0, ALU.mult, ALU.max))
            k.vchain(nc.vector.tensor_tensor(rate, rate, mag, ALU.add))
            k.vchain(nc.vector.tensor_scalar(rate, rate, -8.0, None, ALU.mult))
            dve.wait_ge(k.activations, a0 + 2)
            for c in range(2):
                last = nc.vector.tensor_scalar(r[:, c, :], r[:, c, :], rate[:, c:c + 1], None, ALU.mult)
            last.then_inc(k.vectors, 1)
            nc.vector.tensor_tensor(i, i, xa, ALU.mult)
            dve.wait_ge(k.activations, a0 + 3)
            k.vchain(nc.vector.tensor_tensor(h, a, a, ALU.mult))
            nc.vector.scalar_tensor_tensor(out=th, in0=h, scalar=1.0, in1=th, op0=ALU.add, op1=ALU.mult).then_inc(k.vectors, 1)
            dve.wait_ge(k.activations, a0 + 4)
            k.vchain(nc.vector.tensor_tensor(i, i, th, ALU.mult))
            for c in range(2):
                last = nc.vector.tensor_tensor_scan(h[:, c, :], a[:, c, :], i[:, c, :], 0.0, ALU.mult, ALU.add)
            k.vchain(last)
            dve.wait_ge(k.activations, a0 + 5)
            nc.vector.tensor_tensor(out, h, r, ALU.mult)
    k.advance(products=1, vectors=3, activations=5, pools=1, loads=4)


def mlstm(k, out):
    nc = k.nc
    s = Scratch(k)
    qk = s.take(4 * S).rearrange("p (c s) -> p c s", s=S)
    s.take(2 * S)
    diag = s.take(8 * P).rearrange("p (m n) -> p m n", n=P)
    w_s = s.take(4 * S).rearrange("p (h n) -> p h n", h=4)
    w_t = s.take(TT * 4 * P).rearrange("p (j h q) -> p j h q", j=TT, h=4)
    f, mag, i, b, rows = [k.stat[:, 8 * n:8 * n + 8] for n in range(5)]
    mu, den, low = [k.stat[:, 40 + 4 * n:44 + 4 * n] for n in range(3)]

    def th(a):
        return a.rearrange("p (t h) -> p t h", t=TT)
    p0, v0, a0 = k.starts()
    with nc.Block() as block:
        @block.vector
        def _(dve):
            nc.vector.tensor_tensor(th(i), k.small[:, :, 0:4], over(k.rows_bc[:, 8:12], TT), ALU.add)
            k.vchain(nc.vector.tensor_tensor(th(f), k.small[:, :, 4:8], over(k.rows_bc[:, 12:16], TT), ALU.add))
            softplus_vector(k, dve, f, mag).then_inc(k.vectors, 1)
            dve.wait_ge(k.activations, a0 + 1)
            nc.vector.scalar_tensor_tensor(out=f, in0=f, scalar=0.0, in1=mag, op0=ALU.min, op1=ALU.subtract).then_inc(k.vectors, 1)
            dve.wait_ge(k.products, p0 + 1)
            k.vchain(nc.vector.tensor_copy(b, k.ps[:, 0, 0:8]))
            k.vchain(nc.vector.tensor_tensor(rows.rearrange("p (h t) -> p t h", t=TT), th(i), th(b), ALU.subtract))
            nc.vector.tensor_tensor(diag, over(k.const("ident"), 8), along(rows, P), ALU.mult).then_inc(k.vectors, 1)

        @block.scalar
        def _(act):
            act.wait_ge(k.vectors, v0 + 1)
            softplus_scalar(k, mag).then_inc(k.activations, 1)

        @block.tensor
        def _(pe):
            pe.wait_ge(k.vectors, v0 + 2)
            nc.tensor.matmul(k.ps[:, 0, 0:4], k.const("upper"), f[:, 0:4], start=True, stop=True)
            nc.tensor.matmul(k.ps[:, 0, 4:8], k.const("upper"), f[:, 4:8], start=True, stop=False)
            nc.tensor.matmul(k.ps[:, 0, 4:8], k.const("ones"), f[:, 0:4], start=False, stop=True).then_inc(k.products, 1)
            pe.wait_ge(k.vectors, v0 + 3)
            for n in range(2):
                nc.tensor.matmul(k.ps[:, 4 + n, :], k.const("ones"), diag[:, 4 * n:4 * n + 4, :].rearrange("p m n -> p (m n)"), start=True, stop=True)
    k.advance(products=1, vectors=3, activations=1)

    causal = k.const("causal").rearrange("p (t n) -> p t n", t=TT)
    SCORES, TURNED, MIXED = 1, 2, 3
    SHIFTED, WEIGHTS, DONE = 1, 2, 3
    EXPS, COPIED = 1, 2
    p0, v0, a0 = k.starts()
    with nc.Block() as block:
        @block.tensor
        def _(pe):
            for t in range(TT):
                keys = (t + 1) * P
                if t:
                    pe.wait_ge(k.vectors, v0 + 3 * (t - 1) + DONE)
                for h in range(4):
                    half = slice(64 * (h % 2), 64 * (h % 2) + 64)
                    last = nc.tensor.matmul(k.ps[:, 2 * (h % 2), h // 2 * S:h // 2 * S + keys], qk[half, h // 2, t * P:(t + 1) * P],
                                            qk[half, 2 + h // 2, 0:keys], start=True, stop=True)
                last.then_inc(k.products, 1)
                pe.wait_ge(k.vectors, v0 + 3 * t + WEIGHTS)
                for j in range(t + 1):
                    for h in range(4):
                        last = nc.tensor.transpose(k.ps[:, 6 + j, h * P:(h + 1) * P], w_s[:, h, j * P:(j + 1) * P], k.const("ident"))
                last.then_inc(k.products, 1)
                pe.wait_ge(k.activations, a0 + 2 * t + COPIED)
                for h in range(4):
                    for j in range(t + 1):
                        last = nc.tensor.matmul(k.ps[:, 1, h * 64:(h + 1) * 64], w_t[:, j, h, :], k.tok[:, j, h * 64:(h + 1) * 64],
                                                start=j == 0, stop=j == t)
                last.then_inc(k.products, 1)

        @block.vector
        def _(dve):
            for t in range(TT):
                keys = (t + 1) * P
                w = w_s[:, :, 0:keys]
                row = k.ps[:, 4:6, :].rearrange("p b (m n) -> p (b m) n", m=2)[:, :, 0:keys]
                k.vchain(nc.vector.tensor_tensor(w, row, over(causal[:, t, 0:keys], 4), ALU.add))
                k.vchain(nc.vector.tensor_reduce(mu, w, AX_X, ALU.max))
                k.vchain(nc.vector.tensor_scalar(mu, mu, 0.0, None, ALU.max))
                nc.vector.tensor_tensor(low, mu, b[:, 4 * t:4 * t + 4], ALU.add)
                nc.vector.tensor_tensor(w, w, along(mu, keys), ALU.subtract).then_inc(k.vectors, 1)
                dve.wait_ge(k.activations, a0 + 2 * t + EXPS)
                dve.wait_ge(k.products, p0 + 3 * t + SCORES)
                for r in range(2):
                    sums = k.ps[:, 2 * r, :].rearrange("p (h n) -> p h n", h=2)[:, :, 0:keys]
                    last = nc.vector.scalar_tensor_tensor(out=half_heads(w, r), in0=sums, scalar=ML_D ** -0.5, in1=half_heads(w, r),
                                                          op0=ALU.mult, op1=ALU.mult)
                last.then_inc(k.vectors, 1)
                dve.wait_ge(k.vectors, v0 + 3 * t + WEIGHTS)
                k.vchain(nc.vector.tensor_reduce(den, w, AX_X, ALU.add))
                k.vchain(nc.vector.scalar_tensor_tensor(out=den, in0=den, scalar=-1.0, in1=den, op0=ALU.mult, op1=ALU.max))
                k.vchain(nc.vector.tensor_tensor(den, den, low, ALU.max))
                k.vchain(nc.vector.reciprocal(den, den))
                dve.wait_ge(k.products, p0 + 3 * t + MIXED)
                o = out[:, t, 0:256]
                k.vchain(nc.vector.tensor_tensor(o.rearrange("p (h d) -> p h d", h=4), k.ps[:, 1, 0:256].rearrange("p (h d) -> p h d", h=4),
                                                 along(den, 64), ALU.mult))
                nc.vector.tensor_tensor(o, o, k.tok[:, t, 256:512], ALU.mult).then_inc(k.vectors, 1)

        @block.scalar
        def _(act):
            for t in range(TT):
                keys = (t + 1) * P
                act.wait_ge(k.vectors, v0 + 3 * t + SHIFTED)
                nc.scalar.activation(low, low, ACT.Exp, scale=-1.0)
                nc.scalar.activation(w_s[:, :, 0:keys], w_s[:, :, 0:keys], ACT.Exp).then_inc(k.activations, 1)
                act.wait_ge(k.products, p0 + 3 * t + TURNED)
                nc.scalar.copy(w_t[:, 0:t + 1, :, :].rearrange("p j h q -> p (j h q)"),
                               k.ps[:, 6:7 + t, :].rearrange("p b n -> p (b n)")).then_inc(k.activations, 1)
    k.advance(products=6, vectors=6, activations=4)


def stick_breaking(k, out):
    nc = k.nc
    s = Scratch(k)
    W = TT * P + P
    z, mag, sp_ = [s.take(4 * W).rearrange("p (h n) -> p h n", h=4) for _ in range(3)]
    sums = k.ps[:, 0:4, 0:W]
    rest = k.ps[:, 4:8, 0:W]
    p0, v0, a0 = k.starts()

    def q(h):
        return k.chan[64 * (h % 2):64 * (h % 2) + 64, 8 + h // 2, PAD:PAD + S]

    def key(h):
        return k.chan[64 * (h % 2):64 * (h % 2) + 64, 10 + h // 2, PAD:PAD + S]

    def v(t, h):
        return k.tok[:, t, 512 + h * 64:512 + (h + 1) * 64]
    with nc.Block() as block:
        @block.tensor
        def _(pe):
            for h in range(4):
                nc.tensor.matmul(k.ps[:, h, 0:S], key(h)[:, 0:P], q(h), start=True, stop=True)
                last = nc.tensor.matmul(k.ps[:, h, S:W], key(h)[:, P:S], q(h)[:, P:S], start=True, stop=True)
            last.then_inc(k.products, 1)
            pe.wait_ge(k.vectors, v0 + 2)
            for h in range(4):
                nc.tensor.matmul(k.ps[:, 4 + h, 0:P], k.const("lower"), sp_[:, h, 0:P], start=True, stop=True)
                nc.tensor.matmul(k.ps[:, 4 + h, P:S], k.const("lower"), sp_[:, h, P:S], start=True, stop=False)
                nc.tensor.matmul(k.ps[:, 4 + h, P:S], k.const("ones"), sp_[:, h, S:W], start=False, stop=True)
                last = nc.tensor.matmul(k.ps[:, 4 + h, S:W], k.const("lower"), sp_[:, h, S:W], start=True, stop=True)
            last.then_inc(k.products, 1)
            pe.wait_ge(k.activations, a0 + 2)
            for h in range(4):
                c = slice(h * 64, (h + 1) * 64)
                nc.tensor.matmul(k.ps[:, 0, c], z[:, h, 0:P], v(0, h), start=True, stop=True)
                nc.tensor.matmul(k.ps[:, 1, c], z[:, h, P:S], v(0, h), start=True, stop=False)
                last = nc.tensor.matmul(k.ps[:, 1, c], z[:, h, S:W], v(1, h), start=False, stop=True)
            last.then_inc(k.products, 1)

        @block.vector
        def _(dve):
            dve.wait_ge(k.products, p0 + 1)
            k.vchain(nc.vector.tensor_scalar(z, sums, SB_D ** -0.5, None, ALU.mult))
            softplus_vector(k, dve, z, mag).then_inc(k.vectors, 1)
            dve.wait_ge(k.activations, a0 + 1)
            k.vchain(nc.vector.scalar_tensor_tensor(out=sp_, in0=z, scalar=0.0, in1=mag, op0=ALU.max, op1=ALU.add))
            nc.vector.tensor_tensor(sp_[:, :, 0:P], sp_[:, :, 0:P], over(k.const("upper_strict"), 4), ALU.mult)
            nc.vector.tensor_tensor(sp_[:, :, S:W], sp_[:, :, S:W], over(k.const("upper_strict"), 4), ALU.mult).then_inc(k.vectors, 1)
            dve.wait_ge(k.products, p0 + 2)
            k.vchain(nc.vector.tensor_tensor(z, z, rest, ALU.subtract))
            nc.vector.tensor_tensor(z[:, :, 0:P], z[:, :, 0:P], over(k.const("neg_not_upper_strict"), 4), ALU.add)
            nc.vector.tensor_tensor(z[:, :, S:W], z[:, :, S:W], over(k.const("neg_not_upper_strict"), 4), ALU.add).then_inc(k.vectors, 1)
            dve.wait_ge(k.products, p0 + 3)
            nc.vector.tensor_copy(out[:, :, 0:256], k.ps[:, 0:2, 0:256])

        @block.scalar
        def _(act):
            act.wait_ge(k.vectors, v0 + 1)
            softplus_scalar(k, mag).then_inc(k.activations, 1)
            act.wait_ge(k.vectors, v0 + 3)
            nc.scalar.activation(z, z, ACT.Exp).then_inc(k.activations, 1)
    k.advance(products=3, vectors=3, activations=2)


def ffn_slot(k, slot):
    return k.ring[:, slot * SLOT:(slot + 1) * SLOT].rearrange("p (g c n) -> p g c n", g=2, n=S)


def ffn_part(k):
    w = k.ins["w_ffn_in_2"][0].rearrange("(c p) (g n) -> p g c n", p=P, g=2)
    return {"w": lambda n: w[:, :, :, bass.ds(n * S, S)], "width": 2 * S, "tiles": FF // S}


class FfnStream(Stream):
    def tile(self, part, n, slot):
        return ffn_slot(self.k, slot), part["w"](n)


def gated_ffn(k, dst, stream, ahead):
    nc = k.nc
    part, = stream.parts
    n_tiles, first, start, free = part["tiles"], part["first_slot"], part["start"], part["copied"]
    s_at = FFC * S
    half = k.ring[:, 2 * SLOT + s_at:2 * SLOT + s_at + 2 * BANK].rearrange("p (u n) -> p u n", u=2)
    silu_done = [k.sem(f"silu_done{u}") for u in range(2)]
    with nc.Block() as block:
        @block.sync
        def _(sp):
            def load(i, u, slot):
                dst, src = stream.tile(part, 2 * i + u, slot)
                sp.wait_ge(k.tile_done[slot], i + (start[slot] + 1))
                sp.dma_start(dst, src).then_inc(k.w_landed[slot], 16)
            each_tile(sp, n_tiles, first, load, skip=stream.skip)
            issue(k, sp, ahead)

        @block.tensor
        def _(pe):
            def multiply(i, u, slot):
                w = ffn_slot(k, slot)
                pe.wait_ge(k.w_landed[slot], i * 16 + 16 * (start[slot] + 1))
                pe.wait_ge(k.psum_free[slot], i + (free[slot] + 1))
                for g in range(2):
                    for n in range(2):
                        for c in range(DC):
                            last = nc.tensor.matmul(k.ps[:, 2 * slot + g, n * S:(n + 1) * S], w[:, g, c, n * P:(n + 1) * P],
                                                    k.hT[:, c, :], start=c == 0, stop=c == DC - 1)
                last.then_inc(k.tile_done[slot], 1)
            each_tile(pe, n_tiles, first, multiply)

        @block.scalar
        def _(act):
            def gate(i, u, slot):
                act.wait_ge(k.tile_done[slot], i + (start[slot] + 2))
                act.wait_ge(k.psum_free[slot], i + (free[slot] + 1))
                nc.scalar.activation(half[:, slot, :], k.ps[:, 2 * slot, :], ACT.Silu).then_inc(silu_done[slot], 1)
            each_tile(act, n_tiles, first, gate)

        @block.vector
        def _(dve):
            def up(i, u, slot):
                dve.wait_ge(silu_done[slot], i + 1)
                nc.vector.tensor_tensor(dst[:, bass.ds(i * (4 * S) + 2 * S * u, 2 * S)], half[:, slot, :], k.ps[:, 2 * slot + 1, :], ALU.mult)\
                    .then_inc(k.psum_free[slot], 1)
            each_tile(dve, n_tiles, first, up)


def second_layer(k):
    nc, w = k.nc, k.ins["w_in_2"]
    stream = Stream(k, [
        chan_part(k, w, 0, 512, 2, 0),
        chan_part(k, w, 1544, 512, 1, 8),
        tok_part(k, w, 1024, 256, 1, 0),
        tok_part(k, w, 1280, 256, 1, 256, ACT.Sigmoid),
        tok_part(k, w, 2056, 256, 1, 512),
        tok_part(k, w, 2312, 512, 6, 768, ACT.Sigmoid),
    ])
    turn(k, k.xn, DC, k.hT, scale=lambda c: k.col("norm_mix_g_2", c), norm_of=k.x, ahead=stream.ahead())
    s = Scratch(k)
    qk = s.take(4 * S).rearrange("p (c s) -> p c s", s=S)
    xa = s.take(2 * S).rearrange("p (c s) -> p c s", s=S)

    def convolve_beside(dve):
        wait_copied(k, dve, stream.parts[0])
        convolve(k, dve, 4, 4, lambda tap, c: k.col("conv_mlstm_w_2", tap * 4 + c), qk)
        dve.sem_inc(k.vectors, 1)
        convolve(k, dve, 0, 2, lambda tap, c: k.col("conv_lru_w_2", tap * 2 + c), xa)

    def silu_behind(act):
        act.wait_ge(k.vectors, k.count["vectors"] + 1)
        nc.scalar.activation(qk, qk, ACT.Silu)
    project(k, k.hT, stream, narrow=(k.narrow_w[:, 64:128].rearrange("p (c n) -> p c n", n=8), k.small[:, :, 0:8], 8),
            vector=convolve_beside, scalar=silu_behind)
    k.advance(vectors=1)
    lru(k, k.hT[:, 0:2, :])
    mlstm(k, k.xn)
    turn(k, k.xn, 2, k.hT[:, 2:4, :])
    stick_breaking(k, k.xn)
    names = ("w_out_lru_2", "w_out_mlstm_2", "w_out_sb_2")
    stream = WideStream(k, [{"lhs": lambda c, n=n: k.hT[:, 2 * n + c, :], "w": k.ins[name][0], "chunks": 2,
                             "out": ("gate_add" if n else "gate_set", k.xn, k.tok[:, :, 768 + n * D:768 + (n + 1) * D])}
                            for n, name in enumerate(names)])
    turn(k, k.xn, 2, k.hT[:, 4:6, :], ahead=stream.ahead())
    project_wide(k, stream)
    stream = WideStream(k, [{"lhs": lambda c: k.hT[:, c, :], "w": k.ins["w_o_2"][0], "chunks": DC, "out": ("add", k.x)}])
    turn(k, k.xn, DC, k.hT, ahead=stream.ahead())
    project_wide(k, stream)

    act = k.ring[:, 2 * SLOT:2 * SLOT + FFC * S]
    stream = FfnStream(k, [ffn_part(k)])
    wide = WideStream(k, [{"lhs": lambda c: act[:, c * S:(c + 1) * S], "w": k.ins["w_ffn_out_2"][0], "chunks": FFC, "out": ("add", k.x)}])
    turn(k, k.xn, DC, k.hT, scale=lambda c: k.col("norm_ffn_g_2", c), norm_of=k.x, ahead=stream.ahead())
    gated_ffn(k, act, stream, wide.ahead())
    project_wide(k, wide)
    norm_rows(k, k.ins["final_norm_g_2"])



def neighbourhood_bias(k, bias):
    nc = k.nc
    rpb = k.ins["na_rpb_3"]
    rows, cols = 2 * NA_ROWS - 1, 2 * NA_COLS - 1
    n_rows = S // GRID
    n = NA_H * S
    mirrored = k.ring[:, 2 * SLOT:2 * SLOT + TT * n]
    v = mirrored.rearrange("p (t h n) -> p t h n", t=TT, h=NA_H)
    p0, v0, a0 = k.starts()
    with nc.Block() as block:
        @block.sync
        def _(sp):
            for r in range(n_rows):
                at = GRID * (1 - r % 2)
                for i in range(n_rows):
                    first = (NA_ROWS - 1 - r + i) * cols + NA_COLS - 1 - (GRID - 1)
                    src = bass.AP(tensor=rpb.tensor, offset=rpb.offset + first, ap=[[1, GRID], [rows * cols, NA_H], [1, GRID]])
                    sp.dma_start(v[at:at + GRID, r // 2, :, i * GRID:(i + 1) * GRID], src).then_inc(k.loads, 16)

        @block.tensor
        def _(pe):
            pe.wait_ge(k.loads, 16 * (k.count["loads"] + n_rows ** 2))
            for b in range(TT * n // BANK):
                last = nc.tensor.matmul(k.ps[:, b, :], k.const("anti"), mirrored[:, b * BANK:(b + 1) * BANK], start=True, stop=True)
            last.then_inc(k.products, 1)

        @block.vector
        def _(dve):
            dve.wait_ge(k.products, p0 + 1)
            nc.vector.tensor_tensor(bias.rearrange("p (m c) -> p m c", c=GRID),
                                    k.ps[:, 0:TT * n // BANK, :].rearrange("p b (m c) -> p (b m) c", c=GRID),
                                    over(k.const("window"), TT * n // GRID), ALU.add)
    k.advance(loads=n_rows ** 2, products=1)


def load_tokens(k, src, dst):
    nc = k.nc
    with nc.Block() as block:
        @block.sync
        def _(sp):
            sp.dma_start(dst, src.rearrange("b (t p) d -> p (b t) d", p=P)).then_inc(k.loads, 16)
            sp.wait_ge(k.loads, 16 * (k.count["loads"] + 1))
    k.advance(loads=1)


def rwkv(k, out):
    nc = k.nc
    N6 = 6 * S

    def chans(at):
        return k.ring[:, at:at + N6].rearrange("p (d s) -> p d s", s=S)
    r, kt, v, b, a = [chans(n * N6) for n in range(5)]
    w_log, L, prod = [chans((5 + n) * N6) for n in range(3)]
    at = 8 * N6
    tmp = k.ring[:, at:at + 10 * S].rearrange("p (c s) -> p c s", s=S)
    at += 10 * S
    lora = k.ring[:, at:at + 2 * RW_W].rearrange("p (d n) -> p d n", d=2)
    at += 2 * RW_W
    lat = k.ring[:, at:at + 2 * S].rearrange("p (d s) -> p d s", d=2)
    at += 2 * S
    g_w = k.ring[:, at:at + RW_W]
    at += RW_W
    lat_g = k.ring[:, at:at + S]
    decay_c = k.stat[:, 0:24].rearrange("p (d j) -> p d j", j=4)
    rk = k.stat[:, 24:48].rearrange("p (t m) -> p t m", t=TT)
    mu_w = PARAM_ROWS["rw_mu_w_3"]
    p0, v0, a0 = k.starts()
    loads0 = k.count["loads"]

    with nc.Block() as block:
        @block.sync
        def _(sp):
            for d in range(2):
                sp.dma_start(lora[0:64, d, :], k.ins["rw_w2_3"][0, d]).then_inc(k.loads, 16)
                sp.dma_start(lora[64:128, d, :], k.ins["rw_a2_3"][0, d]).then_inc(k.loads, 16)
            sp.dma_start(g_w, k.ins["rw_g2_3"][0]).then_inc(k.loads, 16)

        @block.vector
        def _(dve):
            for d in range(2):
                here = k.chan[:, 6:16, PAD:PAD + S]
                there = k.chan[:, 6:16, PAD - 1 + 2 * d:PAD - 1 + 2 * d + S]
                k.vchain(nc.vector.tensor_tensor(tmp, there, here, ALU.subtract))
                for n in range(10):
                    mu = k.col("rw_mu_rkv_3", d * 9 + n) if n < 9 else k.cols[:, 1, mu_w[1] + d:mu_w[1] + d + 1]
                    dst = (r, kt, v)[n // 3][:, 3 * d + n % 3, :] if n < 9 else lat[:, d, :]
                    last = nc.vector.scalar_tensor_tensor(out=dst[:, ::-1] if d else dst, in0=tmp[:, n, :], scalar=mu,
                                                          in1=k.chan[:, 6 + n, PAD:PAD + S], op0=ALU.mult, op1=ALU.add)
                k.vchain(last)
            dve.sem_inc(k.vectors, 1)
            dve.wait_ge(k.activations, a0 + 3)
            k.vchain(nc.vector.tensor_scalar(w_log, w_log, -float(np.exp(-0.5)), None, ALU.mult))
            for n in range(3):
                last = nc.vector.tensor_tensor_scan(L[:, 2 * n:2 * n + 2, :].rearrange("p d s -> p (d s)"), k.const("not_chunk_start"),
                                                    w_log[:, 2 * n:2 * n + 2, :].rearrange("p d s -> p (d s)"), 0.0, ALU.mult, ALU.add)
            k.vchain(last)
            dve.sem_inc(k.vectors, 1)

        @block.scalar
        def _(act):
            nc.scalar.activation(lat_g, k.chan[:, 16, PAD:PAD + S], ACT.Sigmoid).then_inc(k.activations, 1)
            act.wait_ge(k.vectors, v0 + 1)
            nc.scalar.activation(lat[0:64], lat[0:64], ACT.Tanh).then_inc(k.activations, 1)
            act.wait_ge(k.products, p0 + 1)
            for n in range(6):
                c = slice(n % 2 * S, (n % 2 + 1) * S)
                nc.scalar.activation(w_log[:, n, :], k.ps[:, n // 2, c], ACT.Sigmoid, bias=k.col("rw_w0_3", n))
                last = nc.scalar.activation(b[:, n, :], k.ps[:, 4 + n // 2, c], ACT.Sigmoid, bias=k.col("rw_a0_3", n))
            last.then_inc(k.activations, 1)
            for t in range(TT):
                act.wait_ge(k.products, p0 + 2 + t)
                nc.scalar.copy(k.tok[:, t, RW_W:2 * RW_W], k.ps[:, 3 + 4 * t, 0:RW_W])

        @block.tensor
        def _(pe):
            pe.wait_ge(k.loads, 16 * (loads0 + 5))
            pe.wait_ge(k.activations, a0 + 2)
            for d in range(2):
                for c in range(3):
                    n = 3 * d + c
                    cols = slice(n % 2 * S, (n % 2 + 1) * S)
                    nc.tensor.matmul(k.ps[:, n // 2, cols], lora[0:64, d, c * P:(c + 1) * P], lat[0:64, d, :], start=True, stop=True)
                    last = nc.tensor.matmul(k.ps[:, 4 + n // 2, cols], lora[64:128, d, c * P:(c + 1) * P], lat[64:128, d, :], start=True, stop=True)
            last.then_inc(k.products, 1)
            for t in range(TT):
                nc.tensor.matmul(k.ps[:, 3 + 4 * t, 0:RW_W], lat_g[:, t * P:(t + 1) * P], g_w, start=True, stop=True).then_inc(k.products, 1)
    k.advance(products=3, vectors=2, activations=3, loads=5)

    kk = a
    decay = w_log
    tmp6 = tmp[:, 0:6, :]
    p0, v0, a0 = k.starts()
    with nc.Block() as block:
        @block.vector
        def _(dve):
            for n in range(6):
                last = nc.vector.tensor_scalar(kk[:, n, :], kt[:, n, :], k.col("rw_k_k_3", n % 3), None, ALU.mult)
            k.vchain(last)
            nc.vector.tensor_tensor(tmp6, kk, kk, ALU.mult).then_inc(k.vectors, 1)
            for n in range(6):
                last = nc.vector.tensor_scalar(prod[:, n, :], b[:, n, :], -1.0, k.col("rw_k_a_3", n % 3), ALU.add, ALU.mult)
            k.vchain(last)
            k.vchain(nc.vector.scalar_tensor_tensor(out=kt, in0=prod, scalar=1.0, in1=kt, op0=ALU.add, op1=ALU.mult))
            for n in range(6):
                last = nc.vector.scalar_tensor_tensor(out=prod[:, n, :], in0=r[:, n, :], scalar=k.col("rw_r_k_3", n % 3),
                                                      in1=kt[:, n, :], op0=ALU.mult, op1=ALU.mult)
            k.vchain(last)
            dve.sem_inc(k.vectors, 1)
            k.vchain(nc.vector.tensor_tensor(decay, L, w_log, ALU.subtract))
            dve.sem_inc(k.vectors, 1)
            dve.wait_ge(k.products, p0 + 1)
            nc.vector.tensor_scalar(tmp6, k.ps[:, 0:3, :].rearrange("p b (m s) -> p (b m) s", s=S), k.const("tiny"), None, ALU.max).then_inc(k.vectors, 1)
            dve.wait_ge(k.activations, a0 + 1)
            k.vchain(nc.vector.tensor_tensor(kk, kk, tmp6, ALU.mult))
            dve.sem_inc(k.vectors, 1)
            k.vchain(nc.vector.tensor_tensor(b, b, kk, ALU.mult))
            dve.wait_ge(k.activations, a0 + 2)
            nc.vector.scalar_tensor_tensor(out=a, in0=kk, scalar=-1.0, in1=decay, op0=ALU.mult, op1=ALU.mult)
            nc.vector.tensor_tensor(b, b, tmp6, ALU.mult)
            nc.vector.tensor_tensor(kt, kt, tmp6, ALU.mult)
            k.vchain(nc.vector.tensor_tensor(r, r, L, ALU.mult))
            nc.vector.tensor_copy(decay_c.rearrange("p d j -> p (d j)"), L.rearrange("p d (j s) -> p (d j) s", s=64)[:, :, 63])
            dve.wait_ge(k.products, p0 + 2)
            for t in range(TT):
                nc.vector.tensor_copy(rk[:, t, :].rearrange("p (h d) -> p d h", h=2), k.ps[:, 4, 12 * t:12 * t + 12].rearrange("p (d h) -> p d h", h=2))

        @block.tensor
        def _(pe):
            pe.wait_ge(k.vectors, v0 + 1)
            for n in range(3):
                last = nc.tensor.matmul(k.ps[:, n, :], k.const("half_ones"), tmp[:, 2 * n:2 * n + 2, :].rearrange("p c s -> p (c s)"), start=True, stop=True)
            last.then_inc(k.products, 1)
            pe.wait_ge(k.vectors, v0 + 2)
            for t in range(TT):
                for n in range(6):
                    last = nc.tensor.matmul(k.ps[:, 4, 12 * t + 2 * n:12 * t + 2 * n + 2], prod[:, n, t * P:(t + 1) * P], k.const("half_of"), start=True, stop=True)
            last.then_inc(k.products, 1)

        @block.scalar
        def _(act):
            act.wait_ge(k.vectors, v0 + 4)
            k.achain(nc.scalar.activation(tmp6, tmp6, ACT.Ln, scale=float(2.0 ** 17)))
            nc.scalar.activation(tmp6, tmp6, ACT.Exp, scale=-0.5, bias=k.const("ln_norm_scale")).then_inc(k.activations, 1)
            act.wait_ge(k.vectors, v0 + 3)
            nc.scalar.activation(decay, decay, ACT.Exp)
            act.wait_ge(k.vectors, v0 + 5)
            nc.scalar.activation(tmp6, L, ACT.Exp, scale=-1.0)
            k.achain(nc.scalar.activation(L, L, ACT.Exp))
            act.sem_inc(k.activations, 1)
    k.advance(products=2, vectors=5, activations=2)

    base = 5 * N6
    M12 = 12 * P
    A_t, X, Y, U, ak, rb, rkm = [matrices(k.ring[:, base + n * M12:base + (n + 1) * M12]) for n in range(7)]
    base += 7 * M12
    tok4 = [k.ring[:, base + n * 768:base + (n + 1) * 768].rearrange("p (d n) -> p d n", n=P) for n in range(4)]
    a_tok, b_tok, k_tok, v_tok = tok4
    base += 4 * 768
    XA = k.ring[:, base:base + 768].rearrange("p (d n) -> p d n", n=P)
    XW, Z = [k.ring[:, base + (1 + n) * 768:base + (2 + n) * 768].rearrange("p (m n) -> p m n", n=64) for n in range(2)]
    W1 = U(0, 6).rearrange("p m n -> p (m n)").rearrange("p (m n) -> p m n", n=64)
    flat = k.chan[:, 3:20, :].rearrange("p c s -> p (c s)")
    state = [flat[:, n * 384:(n + 1) * 384].rearrange("p (d n) -> p d n", n=64) for n in range(3)]
    y = flat[:, 1152:1152 + 1536].rearrange("p (t m n) -> p t m n", t=TT, n=64)
    bonus = flat[:, 2688:2688 + 1536].rearrange("p (t m n) -> p t m n", t=TT, n=64)
    k.U = U

    def bank_units(first, m, n):
        return k.ps[:, first:first + (m * n + BANK - 1) // BANK, :].rearrange("p b n -> p (b n)")[:, 0:m * n].rearrange("p (m n) -> p m n", n=n)

    with nc.Block() as block:
        @block.vector
        def _(dve):
            nc.vector.memset(state[0], 0.0)

    for t in range(TT):
        cols = slice(t * P, (t + 1) * P)
        p0, v0, a0 = k.starts()
        kinds = [(a, b), (b, a), (kt, a), (b, r), (kt, r)]
        with nc.Block() as block:
            @block.tensor
            def _(pe):
                for n, (lhs, rhs) in enumerate(kinds):
                    if n >= 2:
                        pe.wait_ge(k.vectors, v0 + n - 1)
                    for half in range(2):
                        q = slice(64 * half, 64 * half + 64)
                        for dc in range(6):
                            last = nc.tensor.matmul(k.ps[:, 4 * (n % 2) + 2 * half + dc // 4, dc % 4 * P:(dc % 4 + 1) * P],
                                                    lhs[q, dc, cols], rhs[q, dc, cols], start=True, stop=True)
                    last.then_inc(k.products, 1)
                for n, src in enumerate((a, b, kt, v)):
                    pe.wait_ge(k.vectors, v0 + (4 if n < 2 else 5))
                    for dc in range(6):
                        last = nc.tensor.transpose(k.ps[:, (4, 6, 0, 2)[n] + dc // 4, dc % 4 * P:(dc % 4 + 1) * P],
                                                   src[:, dc, cols], k.const("ident"))
                    last.then_inc(k.products, 1)

            @block.vector
            def _(dve):
                def masked(n, dst, scale, mask):
                    dve.wait_ge(k.products, p0 + n + 1)
                    for half in range(2):
                        last = nc.vector.scalar_tensor_tensor(out=dst(6 * half, 6), in0=bank_units(4 * (n % 2) + 2 * half, 6, P),
                                                              scalar=scale, in1=over(mask, 6), op0=ALU.mult, op1=ALU.mult)
                    last.then_inc(k.vectors, 1)
                masked(0, X, -1.0, k.const("level0"))
                masked(1, A_t, -1.0, k.const("half_upper_strict"))
                masked(2, ak, 1.0, k.const("half_upper_strict"))
                masked(3, rb, 1.0, k.const("half_upper"))
                masked(4, rkm, 1.0, k.const("half_upper"))
                for n, dst in enumerate(tok4):
                    dve.wait_ge(k.products, p0 + 6 + n)
                    nc.vector.tensor_copy(dst, bank_units((4, 6, 0, 2)[n], 6, P)).then_inc(k.vectors, 1)
                k.vchain(nc.vector.tensor_tensor(Y(0, 12), A_t(0, 12), over(k.const("level0_t"), 12), ALU.mult))
                nc.vector.tensor_tensor(X(0, 12), X(0, 12), over(k.const("ident"), 12), ALU.add)
                nc.vector.tensor_tensor(Y(0, 12), Y(0, 12), over(k.const("ident"), 12), ALU.add)
        k.advance(products=9, vectors=9)

        start = k.inverses
        with nc.Block() as block:
            @block.tensor
            def _(pe):
                invert_tensor(k, pe, 3, 0, 6, A_t, X, Y)

            @block.vector
            def _(dve):
                invert_vector(k, dve, 3, 0, 6, A_t, X, Y)
        k.inverses = start + 5 * 2 * 3

        p0, v0, a0 = k.starts()
        with nc.Block() as block:
            @block.tensor
            def _(pe):
                for m in range(12):
                    half, dc = m // 6, m % 6
                    q = slice(64 * half, 64 * half + 64)
                    nc.tensor.matmul(bank_units(0, 12, 64)[:, m, :], ak(m), v_tok[:, dc, q], start=True, stop=True)
                for m in range(12):
                    half, dc = m // 6, m % 6
                    q = slice(64 * half, 64 * half + 64)
                    last = nc.tensor.matmul(k.ps[q, 4 + dc // 4, dc % 4 * P:(dc % 4 + 1) * P], a_tok[:, dc, q], Y(m), start=True, stop=True)
                last.then_inc(k.products, 1)
                pe.wait_ge(k.vectors, v0 + 1)
                for m in range(12):
                    last = nc.tensor.matmul(bank_units(2, 12, 64)[:, m, :], Y(m), W1[:, m, :], start=True, stop=True)
                last.then_inc(k.products, 1)
                for step in range(2):
                    tk = slice(64 * step, 64 * step + 64)
                    pe.wait_ge(k.vectors, v0 + 2 + 2 * step)
                    for m in range(12):
                        half, dc = m // 6, m % 6
                        q = slice(64 * half, 64 * half + 64)
                        last = nc.tensor.matmul(k.ps[tk, 6 + half, dc * 64:(dc + 1) * 64], XA[q, dc, tk], state[step][q, dc, :], start=True, stop=True)
                    last.then_inc(k.products, 1)
                    pe.wait_ge(k.vectors, v0 + 3 + 2 * step)
                    for m in range(12):
                        half, dc = m // 6, m % 6
                        q = slice(64 * half, 64 * half + 64)
                        nc.tensor.matmul(k.ps[q, 0, dc * 64:(dc + 1) * 64], b_tok[tk, dc, q], Z[tk, m, :], start=True, stop=False)
                        last = nc.tensor.matmul(k.ps[q, 0, dc * 64:(dc + 1) * 64], k_tok[tk, dc, q], v_tok[tk, dc, q], start=False, stop=True)
                    last.then_inc(k.products, 1)
                for m in range(12):
                    half, dc = m // 6, m % 6
                    q = slice(64 * half, 64 * half + 64)
                    nc.tensor.matmul(bank_units(4, 12, 64)[:, m, :], rb(m), Z[:, m, :], start=True, stop=False)
                    nc.tensor.matmul(bank_units(4, 12, 64)[:, m, :], rkm(m), v_tok[:, dc, q], start=False, stop=True)
                for m in range(12):
                    half, dc = m // 6, m % 6
                    q = slice(64 * half, 64 * half + 64)
                    for step in range(2):
                        tk = slice(64 * step, 64 * step + 64)
                        last = nc.tensor.matmul(k.ps[tk, 2 + half, dc * 64:(dc + 1) * 64], r[q, dc, t * P + 64 * step:t * P + 64 * step + 64],
                                                state[step][q, dc, :], start=True, stop=True)
                last.then_inc(k.products, 1)

            @block.vector
            def _(dve):
                dve.wait_ge(k.products, p0 + 1)
                nc.vector.tensor_copy(XA, bank_units(4, 6, P))
                nc.vector.tensor_copy(W1, bank_units(0, 12, 64)).then_inc(k.vectors, 1)
                dve.wait_ge(k.products, p0 + 2)
                nc.vector.tensor_copy(XW, bank_units(2, 12, 64)).then_inc(k.vectors, 1)
                dve.wait_ge(k.vectors, v0 + 2)
                for step in range(2):
                    tk = slice(64 * step, 64 * step + 64)
                    dve.wait_ge(k.products, p0 + 3 + 2 * step)
                    for half in range(2):
                        last = nc.vector.tensor_tensor(Z[tk, 6 * half:6 * half + 6, :], XW[tk, 6 * half:6 * half + 6, :],
                                                       k.ps[tk, 6 + half, 0:384].rearrange("p (d n) -> p d n", n=64), ALU.add)
                    last.then_inc(k.vectors, 1)
                    dve.wait_ge(k.products, p0 + 4 + 2 * step)
                    new = state[step + 1]
                    k.vchain(nc.vector.tensor_tensor(new, state[step], k.ps[:, 0, 0:384].rearrange("p (d n) -> p d n", n=64), ALU.add))
                    last = nc.vector.tensor_tensor(new, new, along(decay_c[:, :, 2 * t + step], 64), ALU.mult)
                    last.then_inc(k.vectors, 1)
                for half in range(2):
                    nc.vector.tensor_tensor(bonus[:, t, 6 * half:6 * half + 6, :], v_tok[:, :, 64 * half:64 * half + 64],
                                            along(rk[:, t, 6 * half:6 * half + 6], 64), ALU.mult)
                dve.wait_ge(k.products, p0 + 7)
                k.vchain(nc.vector.tensor_copy(y[:, t], bank_units(4, 12, 64)))
                for half in range(2):
                    last = nc.vector.tensor_tensor(y[:, t, 6 * half:6 * half + 6, :], y[:, t, 6 * half:6 * half + 6, :],
                                                   k.ps[:, 2 + half, 0:384].rearrange("p (d n) -> p d n", n=64), ALU.add)
                k.vchain(last)
                nc.vector.tensor_copy(state[0], state[2])
        k.advance(products=7, vectors=6)

    gain = k.ring[:, 0:RW_W]
    offset = k.ring[:, RW_W:2 * RW_W]
    sq = k.ring[:, 2 * RW_W:4 * RW_W].rearrange("p (t n) -> p t n", t=TT)
    extra = k.ring[:, 4 * RW_W:6 * RW_W].rearrange("p (t n) -> p t n", t=TT)
    mean, rstd = k.stat[:, 48:60], k.stat[:, 60:72]
    yo = out[:, :, 0:RW_W]
    p0, v0, a0 = k.starts()
    loads0 = k.count["loads"]
    with nc.Block() as block:
        @block.sync
        def _(sp):
            sp.dma_start(gain, k.ins["rw_ln_g_3"].partition_broadcast(P).rearrange("p a n -> p (a n)")).then_inc(k.loads, 16)
            sp.dma_start(offset, k.ins["rw_ln_b_3"].partition_broadcast(P).rearrange("p a n -> p (a n)")).then_inc(k.loads, 16)

        @block.tensor
        def _(pe):
            for n, src in enumerate((y, bonus)):
                both = src.rearrange("p t (h d c) n -> p t d c h n", h=2, d=2)
                for t in range(TT):
                    nc.tensor.matmul(k.ps[:, 2 * n + t, 0:RW_W], k.const("ident"), both[:, t, 0], start=True, stop=False)
                    last = nc.tensor.matmul(k.ps[:, 2 * n + t, 0:RW_W], k.const("anti"), both[:, 1 - t, 1], start=False, stop=True)
            last.then_inc(k.products, 1)

        @block.vector
        def _(dve):
            def heads(ap):
                return ap.rearrange("p (h n) -> p h n", n=64)
            dve.wait_ge(k.products, p0 + 1)
            nc.vector.tensor_copy(extra, k.ps[:, 2:4, 0:RW_W])
            k.vchain(nc.vector.tensor_copy(yo, k.ps[:, 0:2, 0:RW_W]))
            for t in range(TT):
                last = nc.vector.tensor_reduce(mean[:, 6 * t:6 * t + 6], heads(yo[:, t]), AX_X, ALU.add)
            k.vchain(last)
            k.vchain(nc.vector.tensor_scalar(mean, mean, 1.0 / 64, None, ALU.mult))
            for t in range(TT):
                last = nc.vector.tensor_tensor(heads(yo[:, t]), heads(yo[:, t]), along(mean[:, 6 * t:6 * t + 6], 64), ALU.subtract)
            k.vchain(last)
            k.vchain(nc.vector.tensor_tensor(sq, yo, yo, ALU.mult))
            nc.vector.tensor_reduce(rstd, sq.rearrange("p t (h n) -> p (t h) n", n=64), AX_X, ALU.add).then_inc(k.vectors, 1)
            dve.wait_ge(k.activations, a0 + 1)
            dve.wait_ge(k.loads, 16 * (loads0 + 2))
            for t in range(TT):
                last = nc.vector.tensor_tensor(heads(yo[:, t]), heads(yo[:, t]), along(rstd[:, 6 * t:6 * t + 6], 64), ALU.mult)
            k.vchain(last)
            k.vchain(nc.vector.tensor_tensor(yo, yo, over(gain, TT), ALU.mult))
            k.vchain(nc.vector.tensor_tensor(yo, yo, over(offset, TT), ALU.add))
            k.vchain(nc.vector.tensor_tensor(yo, yo, extra, ALU.add))
            nc.vector.tensor_tensor(yo, yo, k.tok[:, :, RW_W:2 * RW_W], ALU.mult)

        @block.scalar
        def _(act):
            act.wait_ge(k.vectors, v0 + 1)
            k.achain(nc.scalar.activation(rstd, rstd, ACT.Ln, bias=k.const("gn_eps"), scale=1.0 / 64))
            nc.scalar.activation(rstd, rstd, ACT.Exp, scale=-0.5).then_inc(k.activations, 1)
    k.advance(products=1, vectors=1, activations=1, loads=2)


def expert_tiles(k):
    def w_in(name, n):
        return lambda e: k.ins[name][0, bass.ds(e, 1), :, n * TILE:(n + 1) * TILE].rearrange("a (c p) n -> p (a c) n", p=P)

    def w_down(n):
        return lambda e: k.ins["w_exp_down_3"][0, bass.ds(e, 1), n * TILE:(n + 1) * TILE, :].rearrange("a (c p) n -> p (a c) n", p=P)
    tiles = []
    for n in range(EFF // TILE):
        tiles += [(w_in("w_exp_gate_3", n), TILE), (w_in("w_exp_up_3", n), TILE)]
    return tiles + [(w_down(n), D) for n in range(EFF // TILE)]


def expert_choice(k):
    nc = k.nc
    turn(k, k.xn, DC, k.hT, scale=lambda c: k.col("norm_ffn_g_3", c), norm_of=k.x)
    tok = k.tok[:, :, :].rearrange("p t n -> p (t n)")
    xeT = tok[:, 0:4096].rearrange("p (c n) -> p c n", c=DC)
    one_hot = tok[:, 4096:5120].rearrange("p (t n) -> p t n", t=TT)
    weighted = tok[:, 5120:6144].rearrange("p (t n) -> p t n", t=TT)
    rows = tok[0:EXP, 6144:6144 + 5 * S].rearrange("p (n s) -> p n s", s=S)
    aff_t, work, chosen, number, ones = [rows[:, n, :] for n in range(5)]
    back = k.chan[:, :, :].rearrange("p c s -> p (c s)")[:, 0:EXP * S].rearrange("p (e s) -> p e s", e=EXP)
    aff = k.stat[:, 0:2 * EXP].rearrange("p (t e) -> p t e", t=TT)
    pos = k.stat[:, 32:32 + 2 * EXP].rearrange("p (t e) -> p t e", t=TT)
    top, total = k.stat[:, 64:66], k.stat[:, 66:68]
    best = k.stat[0:EXP, 72:80]
    router = k.narrow_w[:, 128:256].rearrange("p (c n) -> p c n", n=EXP)
    tiles = expert_tiles(k)
    n_tiles = len(tiles)
    base = list(k.tiles)
    first = n_tiles // RING

    refills = k.sem("refills")

    def load(sp, e, q, before):
        src, width = tiles[q]
        u = q % RING
        dst = k.ring[:, u * SLOT:(u + 1) * SLOT].rearrange("p (c n) -> p c n", n=width)
        sp.wait_ge(k.tile_done[u], before)
        sp.sem_inc(refills, 1)
        sp.dma_start(dst, src(e)).then_inc(k.w_landed[u], 16)

    p0, v0, a0 = k.starts()
    with nc.Block() as block:
        @block.sync
        def _(sp):
            for q in range(RING):
                load(sp, 0, q, base[q] + 1)

        @block.tensor
        def _(pe):
            for t in range(TT):
                for c in range(DC):
                    last = nc.tensor.matmul(k.ps[:, 0, t * EXP:(t + 1) * EXP], k.hT[:, c, t * P:(t + 1) * P], router[:, c, :],
                                            start=c == 0, stop=c == DC - 1)
            last.then_inc(k.products, 1)
            pe.wait_ge(k.vectors, v0 + 2)
            for t in range(TT):
                last = nc.tensor.transpose(k.ps[0:EXP, 1, t * P:(t + 1) * P], aff[:, t, :], k.const("ident"))
            last.then_inc(k.products, 1)
            pe.wait_ge(k.vectors, v0 + 3)
            for t in range(TT):
                last = nc.tensor.transpose(k.ps[:, 2, t * EXP:(t + 1) * EXP], number[:, t * P:(t + 1) * P], k.const("ident")[0:EXP, 0:EXP])
            last.then_inc(k.products, 1)

        @block.scalar
        def _(act):
            act.wait_ge(k.vectors, v0 + 1)
            nc.scalar.activation(aff, aff, ACT.Exp).then_inc(k.activations, 1)

        @block.vector
        def _(dve):
            nc.vector.memset(ones, 1.0)
            dve.wait_ge(k.products, p0 + 1)
            k.vchain(nc.vector.tensor_copy(aff, k.ps[:, 0, 0:2 * EXP].rearrange("p (t e) -> p t e", t=TT)))
            k.vchain(nc.vector.tensor_reduce(top, aff, AX_X, ALU.max))
            nc.vector.tensor_tensor(aff, aff, along(top, EXP), ALU.subtract).then_inc(k.vectors, 1)
            dve.wait_ge(k.activations, a0 + 1)
            k.vchain(nc.vector.tensor_reduce(total, aff, AX_X, ALU.add))
            k.vchain(nc.vector.reciprocal(total, total))
            nc.vector.tensor_tensor(aff, aff, along(total, EXP), ALU.mult).then_inc(k.vectors, 1)
            dve.wait_ge(k.products, p0 + 2)
            k.vchain(nc.vector.tensor_copy(aff_t, k.ps[0:EXP, 1, 0:S]))
            for n in range(CAP // 8):
                src = aff_t if n == 0 else work
                k.vchain(nc.vector.max(best, src))
                k.vchain(nc.vector.match_replace(work, best, src, -1.0))
            k.vchain(nc.vector.tensor_scalar(chosen, work, 0.0, None, ALU.is_lt))
            k.vchain(nc.vector.tensor_tensor_scan(number, ones, chosen, 0.0, ALU.mult, ALU.add))
            k.vchain(nc.vector.tensor_tensor(number, number, chosen, ALU.mult))
            nc.vector.tensor_scalar(number, number, -1.0, None, ALU.add).then_inc(k.vectors, 1)
            dve.wait_ge(k.products, p0 + 3)
            k.vchain(nc.vector.tensor_copy(pos, k.ps[:, 2, 0:2 * EXP].rearrange("p (t e) -> p t e", t=TT)))
            for t in range(TT):
                hot = one_hot[:, t, :].rearrange("p (e j) -> p e j", e=EXP)
                last = nc.vector.tensor_tensor(hot, over(k.const("slot_number"), EXP), along(pos[:, t, :], CAP), ALU.is_equal)
            k.vchain(last)
            for t in range(TT):
                hot = one_hot[:, t, :].rearrange("p (e j) -> p e j", e=EXP)
                nc.vector.tensor_tensor(weighted[:, t, :].rearrange("p (e j) -> p e j", e=EXP), hot, along(aff[:, t, :], CAP), ALU.mult)
    k.advance(products=3, vectors=3, activations=1)

    p0, v0, a0 = k.starts()
    order = [2, 3, 4, 5, 6, 7, 0, 1]
    even, odd = order[0::2], order[1::2]
    turned_w = k.hT[:, 0:4, :]
    with nc.Block() as block:
        @block.tensor
        def _(pe):
            for g in range(4):
                for t in range(TT):
                    last = nc.tensor.transpose(k.ps[:, g // 2, g % 2 * S + t * P:g % 2 * S + (t + 1) * P],
                                               weighted[:, t, g * P:(g + 1) * P], k.const("ident"))
            last.then_inc(k.products, 1)
            for c in order:
                if c == 0:
                    pe.wait_ge(k.vectors, v0 + 1)
                for t in range(TT):
                    last = nc.tensor.matmul(k.ps[:, c, :], k.xn[:, t, c * P:(c + 1) * P], one_hot[:, t, :], start=t == 0, stop=t == TT - 1)
                last.then_inc(k.products, 1)
            for n in order:
                if n % 2:
                    pe.wait_ge(k.activations, a0 + odd.index(n) + 1)
                else:
                    pe.wait_ge(k.vectors, v0 + even.index(n) + 2)
                for e in (2 * n, 2 * n + 1):
                    last = nc.tensor.matmul(k.ps[:, n, e % 2 * S:(e % 2 + 1) * S], k.const(f"four_times{e % 4}"), turned_w[:, e // 4, :], start=True, stop=True)
                last.then_inc(k.products, 1)

        @block.vector
        def _(dve):
            dve.wait_ge(k.products, p0 + 1)
            nc.vector.tensor_copy(turned_w.rearrange("p g s -> p (g s)"), k.ps[:, 0:2, :].rearrange("p b n -> p (b n)")).then_inc(k.vectors, 1)
            for c in even:
                dve.wait_ge(k.products, p0 + 2 + order.index(c))
                nc.vector.tensor_scalar(xeT[:, c, :], k.ps[:, c, :], k.col("norm_ffn_g_3", c), None, ALU.mult).then_inc(k.vectors, 1)
            for n in even:
                dve.wait_ge(k.products, p0 + 2 + DC + order.index(n))
                nc.vector.tensor_copy(back[:, 2 * n:2 * n + 2, :].rearrange("p e s -> p (e s)"), k.ps[:, n, :])

        @block.scalar
        def _(act):
            for c in odd:
                act.wait_ge(k.products, p0 + 2 + order.index(c))
                nc.scalar.activation(xeT[:, c, :], k.ps[:, c, :], ACT.Copy, scale=k.col("norm_ffn_g_3", c)).then_inc(k.activations, 1)
            for n in odd:
                act.wait_ge(k.products, p0 + 2 + DC + order.index(n))
                nc.scalar.copy(back[:, 2 * n:2 * n + 2, :].rearrange("p e s -> p (e s)"), k.ps[:, n, :])
    k.advance(products=2 * DC + 1, vectors=DC // 2 + 1, activations=DC // 2)

    hT = k.hT[:, :, :].rearrange("p c s -> p (c s)")
    xn = k.xn[:, :, :].rearrange("p t n -> p (t n)")
    part = [[hT[:, (2 * g + n) * TILE:(2 * g + n + 1) * TILE] for n in range(2)] for g in range(2)]
    y = xn[:, 0:D]
    xe = xn[:, D:D + DC * CAP].rearrange("p (c n) -> p c n", c=DC)
    act_t = xn[:, D + 256:D + 256 + EFF // P * CAP].rearrange("p (f n) -> p f n", n=CAP)
    gated = xn[:, D + 768:D + 768 + 4 * CAP]
    way = tok[:, 4096:4096 + S]
    zeros = tok[:, 4608:4608 + BANK]
    xe_ready = k.sem("expert_tokens_ready")
    last_up = (2 * (EFF // TILE) - 1) % RING
    way_ready, way_used = k.sem("way_back_ready"), k.sem("way_back_used")
    gate_copied, up_copied = k.sem("gate_copied"), k.sem("up_copied")
    turned, silu, hidden = k.sem("turned"), k.sem("silu"), k.sem("hidden")
    y_done, y_copied0, y_copied1 = k.sem("y_done"), k.sem("y_copied0"), k.sem("y_copied1")
    zeroed = k.sem("zeroed")
    NG = EFF // TILE
    with nc.Block() as block:
        @block.sync
        def _(sp):
            with sp.Fori(0, EXP - 1) as e:
                for q in range(RING, n_tiles + RING):
                    u, turn_of_ring = q % RING, q // RING
                    load(sp, e if q < n_tiles else e + 1, q % n_tiles, e * first + (base[u] + 1 + turn_of_ring))
            for q in range(RING, n_tiles):
                load(sp, EXP - 1, q, (EXP - 1) * first + base[q % RING] + 1 + q // RING)

        @block.gpsimd
        def _(pool):
            nc.gpsimd.memset(zeros, 0.0).then_inc(zeroed, 1)
            nc.gpsimd.tensor_copy(xe, xeT[:, :, 0:CAP]).then_inc(xe_ready, 1)
            nc.gpsimd.tensor_copy(way, back[:, 0, :]).then_inc(way_ready, 1)
            with pool.Fori(1, EXP) as e:
                pool.wait_ge(k.tile_done[last_up], e * first + (base[last_up] + 1))
                nc.gpsimd.tensor_copy(xe, xeT[:, :, bass.ds(e * CAP, CAP)]).then_inc(xe_ready, 1)
                pool.wait_ge(way_used, e)
                nc.gpsimd.tensor_copy(way, back[:, bass.ds(e, 1), :].rearrange("p e s -> p (e s)")).then_inc(way_ready, 1)

        @block.tensor
        def _(pe):
            pe.wait_ge(zeroed, 1)
            for b in range(4):
                nc.tensor.matmul(k.ps[:, b, :], zeros[:, 0:P], zeros, start=True, stop=True, skip_group_check=True)
            for sem in (gate_copied, up_copied, y_copied0, y_copied1):
                pe.sem_inc(sem, 1)

            def slot(q, width):
                u = q % RING
                return k.ring[:, u * SLOT:(u + 1) * SLOT].rearrange("p (c n) -> p c n", n=width)

            def landed(e, q):
                u = q % RING
                pe.wait_ge(k.w_landed[u], e * (16 * first) + 16 * (base[u] + 1 + q // RING))

            def gate_up(e, n):
                for g, copied in enumerate((gate_copied, up_copied)):
                    landed(e, 2 * n + g)
                    pe.wait_ge(copied, e * NG + (n + 1))
                    if n == 0:
                        pe.wait_ge((y_copied0, y_copied1)[g], e + 1)
                    for half in range(2):
                        for j in range(4):
                            c = 4 * half + j
                            last = nc.tensor.matmul(k.ps[32 * j:32 * j + 32, 4 + g, :], xe[:, c, :], slot(2 * n + g, TILE)[:, c, :],
                                                    start=half == 0, stop=half == 1)
                    last.then_inc(k.tile_done[(2 * n + g) % RING], 1)

            def turn_part(e, n):
                pe.wait_ge(gate_copied, e * NG + (n + 2))
                pe.wait_ge(up_copied, e * NG + (n + 2))
                if n >= 2:
                    pe.wait_ge(hidden, e * NG + (n - 1))
                for g in range(2):
                    for i in range(4):
                        last = nc.tensor.matmul(k.ps[:, 6 + n % 2, (4 * g + i) * CAP:(4 * g + i + 1) * CAP], part[g][n % 2][:, i * P:(i + 1) * P],
                                                k.const("four_idents"), start=True, stop=True)
                last.then_inc(turned, 1)

            with pe.Fori(0, EXP) as e:
                pe.wait_ge(xe_ready, e + 1)
                gate_up(e, 0)
                for n in range(1, NG):
                    gate_up(e, n)
                    turn_part(e, n - 1)
                turn_part(e, NG - 1)
                for n in range(NG):
                    pe.wait_ge(hidden, e * NG + (n + 1))
                    landed(e, 2 * NG + n)
                    for h in range(2):
                        for j in range(4):
                            last = nc.tensor.matmul(k.ps[32 * j:32 * j + 32, 4 + h, :], act_t[:, 4 * n + j, :],
                                                    slot(2 * NG + n, D)[:, j, h * BANK:(h + 1) * BANK], start=n == 0, stop=n == NG - 1)
                    last.then_inc(k.tile_done[(2 * NG + n) % RING], 1)
                pe.wait_ge(way_ready, e + 1)
                for h in range(2):
                    pe.wait_ge((y_copied0, y_copied1)[h], e + 2)
                    for t in range(TT):
                        last = nc.tensor.matmul(k.ps[:, 2 * t + h, :], way[:, t * P:(t + 1) * P], y[:, h * BANK:(h + 1) * BANK],
                                                start=False, stop=True, skip_group_check=True)
                last.then_inc(way_used, 1)

        @block.scalar
        def _(act):
            with act.Fori(0, EXP) as e:
                def copy(n):
                    u = (2 * n) % RING
                    act.wait_ge(k.tile_done[u], e * first + (base[u] + 2 + 2 * n // RING))
                    if n >= 2:
                        act.wait_ge(turned, e * NG + (n - 1))
                    nc.scalar.copy(part[0][n % 2], k.ps[:, 4, :]).then_inc(gate_copied, 1)

                def gate(n):
                    act.wait_ge(turned, e * NG + (n + 1))
                    if n:
                        act.wait_ge(hidden, e * NG + n)
                    nc.scalar.activation(gated, k.ps[:, 6 + n % 2, 0:4 * CAP], ACT.Silu).then_inc(silu, 1)
                copy(0)
                for n in range(1, NG):
                    copy(n)
                    gate(n - 1)
                gate(NG - 1)
                u = (3 * NG - 1) % RING
                act.wait_ge(k.tile_done[u], e * first + (base[u] + 2 + (3 * NG - 1) // RING))
                nc.scalar.copy(y[:, 0:BANK], k.ps[:, 4, :]).then_inc(y_copied0, 1)

        @block.vector
        def _(dve):
            with dve.Fori(0, EXP) as e:
                def copy(n):
                    u = (2 * n + 1) % RING
                    dve.wait_ge(k.tile_done[u], e * first + (base[u] + 2 + (2 * n + 1) // RING))
                    if n >= 2:
                        dve.wait_ge(turned, e * NG + (n - 1))
                    nc.vector.tensor_copy(part[1][n % 2], k.ps[:, 5, :]).then_inc(up_copied, 1)

                def gate(n):
                    dve.wait_ge(silu, e * NG + (n + 1))
                    nc.vector.tensor_tensor(act_t[:, 4 * n:4 * n + 4, :].rearrange("p f n -> p (f n)"), gated, k.ps[:, 6 + n % 2, 4 * CAP:8 * CAP], ALU.mult)\
                        .then_inc(hidden, 1)
                copy(0)
                for n in range(1, NG):
                    copy(n)
                    gate(n - 1)
                gate(NG - 1)
                u = (3 * NG - 1) % RING
                dve.wait_ge(k.tile_done[u], e * first + (base[u] + 2 + (3 * NG - 1) // RING))
                nc.vector.tensor_copy(y[:, BANK:D], k.ps[:, 5, :]).then_inc(y_copied1, 1)
            dve.wait_ge(way_used, EXP)
            for t in range(TT):
                nc.vector.tensor_tensor(k.x[:, t, :], k.x[:, t, :], k.ps[:, 2 * t:2 * t + 2, :].rearrange("p b n -> p (b n)"), ALU.add)
    for u in range(RING):
        k.tiles[u] += first * EXP


def third_layer(k):
    nc, w = k.nc, k.ins["w_in_3"]
    stream = Stream(k, [
        chan_part(k, w, 0, 384, 2, 0),
        chan_part(k, w, 1152, 384, 3, 6),
        chan_part(k, w, 2304, 512, 1, 15),
        tok_part(k, w, 768, 384, 1, 0),
        tok_part(k, w, 2816, 512, 6, 768, ACT.Sigmoid),
    ])
    turn(k, k.xn, DC, k.hT, scale=lambda c: k.col("norm_mix_g_3", c), norm_of=k.x, ahead=stream.ahead())
    project(k, k.hT, stream)

    def heads(chunk):
        return lambda h: k.chan[64 * (h % 2):64 * (h % 2) + 64, chunk + h // 2, PAD:PAD + S]

    def values(at):
        return lambda t, h: k.tok[:, t, at + h * HD:at + (h + 1) * HD]
    n = TT * NA_H * S
    bias = k.ring[:, RING * SLOT - n:RING * SLOT]
    neighbourhood_bias(k, bias)
    by_tile = bias.rearrange("p (t h n) -> p t h n", t=TT, h=NA_H)
    attention(k, NA_H, heads(0), heads(3), values(0), HD ** -0.5, lambda t: by_tile[:, t], k.xn)
    turn(k, k.xn, 3, k.chan[:, 0:3, PAD:PAD + S])
    mem = k.ring[:, 2 * SLOT:2 * SLOT + TT * D].rearrange("p (t n) -> p t n", t=TT)
    load_tokens(k, k.ins["mem_3"], mem)
    stream = Stream(k, [chan_part(k, k.ins["w_mem_kv_3"], 0, 256, 1, 3), tok_part(k, k.ins["w_mem_kv_3"], 256, 256, 1, 0)])
    turn(k, k.xn, DC, k.hT, scale=lambda c: k.col("norm_mem_g_3", c), norm_of=mem, ahead=stream.ahead())
    project(k, k.hT, stream)
    attention(k, MEM_H, heads(17), heads(3), values(0), HD ** -0.5, None, k.xn)
    turn(k, k.xn, 2, k.hT[:, 6:8, :])
    rwkv(k, k.xn)
    stream = WideStream(k, [
        {"lhs": lambda c: k.chan[:, c, PAD:PAD + S], "w": k.ins["w_branch_na_3"][0], "chunks": 3, "out": ("gate_set", k.xn, k.tok[:, :, 768:1792])},
        {"lhs": lambda c: k.hT[:, 3 + c, :], "w": k.ins["w_branch_rw_3"][0], "chunks": 3, "out": ("gate_add", k.xn, k.tok[:, :, 1792:2816])},
        {"lhs": lambda c: k.hT[:, 6 + c, :], "w": k.ins["w_branch_mem_3"][0], "chunks": 2, "out": ("gate_add", k.xn, k.tok[:, :, 2816:3840])},
    ])
    turn(k, k.xn, 3, k.hT[:, 3:6, :], ahead=stream.ahead())
    project_wide(k, stream)
    stream = WideStream(k, [{"lhs": lambda c: k.hT[:, c, :], "w": k.ins["w_out_3"][0], "chunks": DC, "out": ("add", k.x)}])
    turn(k, k.xn, DC, k.hT, ahead=stream.ahead())
    project_wide(k, stream)
    expert_choice(k)
    norm_rows(k, k.ins["norm_final_g_3"])


def norm_rows(k, gain_row):
    nc = k.nc
    s = Scratch(k)
    gain = s.take(D)
    squares = s.take(TT * D).rearrange("p (t n) -> p t n", t=TT)
    sums, rstd = k.stat[:, 0:2], k.stat[:, 2:4]
    p0, v0, a0 = k.starts()
    with nc.Block() as block:
        @block.sync
        def _(sp):
            sp.dma_start(gain, gain_row.partition_broadcast(P)).then_inc(k.loads, 16)

        @block.scalar
        def _(act):
            for t in range(TT):
                last = nc.scalar.activation(squares[:, t, :], k.x[:, t, :], ACT.Square, accum_out=sums[:, t:t + 1])
            k.achain(last)
            k.achain(nc.scalar.activation(rstd, sums, ACT.Ln, bias=k.const("eps"), scale=1.0 / D))
            nc.scalar.activation(rstd, rstd, ACT.Exp, scale=-0.5).then_inc(k.activations, 1)

        @block.vector
        def _(dve):
            dve.wait_ge(k.activations, a0 + 1)
            dve.wait_ge(k.loads, 16 * (k.count["loads"] + 1))
            for t in range(TT):
                nc.vector.scalar_tensor_tensor(out=k.x[:, t, :], in0=k.x[:, t, :], scalar=rstd[:, t:t + 1], in1=gain, op0=ALU.mult, op1=ALU.mult)
    k.advance(activations=1, loads=1)


def store(k, out):
    nc = k.nc
    stored = k.sem("stored")
    with nc.Block() as block:
        @block.sync
        def _(sp):
            sp.dma_start(out.rearrange("b (t p) d -> p (b t) d", p=P), k.x[:, :, :]).then_inc(stored, 16)
            sp.wait_ge(stored, 16)


def program(nc, x, ins, out):
    with ExitStack() as ctx:
        k = Chip(nc, ctx, ins)
        load_parameters(k, x)
        if 1 in BLOCKS:
            first_layer(k)
        if 2 in BLOCKS:
            second_layer(k)
        if 3 in BLOCKS:
            third_layer(k)
        store(k, out)


def kernel(**inputs):
    import concourse.bacc as bacc
    from concourse.bass_utils import run_bass_kernel_spmd as run

    nc = bacc.Bacc("TRN2", target_bir_lowering=False, num_devices=1)
    arrays = {name: np.ascontiguousarray(a) for name, a in inputs.items()}
    arrays["constants"] = np.concatenate(list(constant_tables().values()), axis=1)
    aps = {name: nc.dram_tensor(f"in_{name}", a.shape, mybir.dt.from_np(a.dtype), kind="ExternalInput").ap()
           for name, a in arrays.items()}
    out = nc.dram_tensor("out", (1, S, D), F32, kind="ExternalOutput").ap()
    program(nc, aps["x"], aps, out)
    r = run(nc, [{f"in_{name}": a for name, a in arrays.items()}], core_ids=[0])
    return r.results[0]["out"]
```

```python
from contextlib import ExitStack

import concourse.bass as bass
from concourse import mybir
import numpy as np

F32 = mybir.dt.float32
ALU = mybir.AluOpType
ACT = mybir.ActivationFunctionType
AX_X = mybir.AxisListType.X

P = 128
S = 256
TT = S // P
D = 1024
DC = D // P
BANK = 512
TILE = 512
RING = 6
SLOT = DC * TILE
PAD = 4
CHW = PAD + S + PAD
NEG = -1.0e30
EPS = 1e-6

DN_H, DN_D = 4, 128
MB_H, MB_D = 8, 64
LRU_W = 256
ML_H, ML_D = 4, 64
SB_H, SB_D = 4, 64
FF = ((8 * D // 3 + 255) // 256) * 256
FFC = FF // P
NA_H, RW_H, MEM_H, HD = 6, 6, 4, 64
RW_W = RW_H * HD
GRID = 64
NA_ROWS, NA_COLS = 8, 16
EXP, CAP, EFF = 16, 2 * S // 16, 2 * D
BLOCKS = (1, 2, 3)



def constant_tables():
    p = np.arange(P)[:, None]
    f = np.arange(P)[None, :]
    tables = {
        "ident": p == f,
        "anti": p + f == P - 1,
        "ones": np.ones((P, P)),
        "upper": p <= f,
        "lower": p >= f,
        "lower_strict": p > f,
        "upper_strict": p < f,
        "half_ones": p // 64 == f // 64,
        "half_upper_strict": (p < f) & (p // 64 == f // 64),
        "half_upper": (p <= f) & (p // 64 == f // 64),
        "half_of": p // 64 == np.arange(2)[None, :],
        "neg_not_lower": np.where(p >= f, 0.0, NEG),
        "neg_not_upper": np.where(p <= f, 0.0, NEG),
        "neg_not_upper_strict": np.where(p < f, 0.0, NEG),
        "causal": np.concatenate([np.where(np.arange(S)[None, :] <= p + t * P, 0.0, NEG) for t in range(TT)], 1),
        "not_chunk_start": np.broadcast_to((np.arange(2 * S) % 64 != 0)[None, :], (P, 2 * S)),
        "slot_number": np.broadcast_to(np.arange(CAP)[None, :], (P, CAP)),
        "four_idents": p % CAP == np.arange(CAP)[None, :],
        "eps": np.full((P, 1), EPS),
        "log_scale": np.full((P, 1), -0.5 * np.log(DN_D)),
        "gn_eps": np.full((P, 1), 64e-5),
        "ln_norm_scale": np.full((P, 1), 0.5 * 17 * np.log(2.0)),
        "tiny": np.full((P, 1), 1e-24),
    }
    for n in range(7):
        b = 1 << n
        m = (p // (2 * b) == f // (2 * b)) & ((p // b) % 2 == 1) & ((f // b) % 2 == 0)
        tables[f"level{n}"] = -1.0 * m
    tables["level0_t"] = tables["level0"].T
    for name in ("ident", "half_upper_strict", "half_upper", "level0_t", *(f"level{n}" for n in range(5))):
        tables["chunk_" + name] = tables[name] * 1.0 @ (p % 64 == np.arange(64)[None, :])
    del tables["half_upper_strict"], tables["half_upper"]
    for n in range(4):
        tables[f"four_times{n}"] = p == CAP * n + f % CAP
    w = p % GRID
    start = np.clip(w - NA_COLS // 2, 0, GRID - NA_COLS)
    c = np.arange(GRID)[None, :]
    tables["window"] = np.where((c >= start) & (c < start + NA_COLS), 0.0, NEG)
    return {name: np.asarray(t, np.float32) for name, t in tables.items()}


def constant_places():
    at, places = 0, {}
    for name, t in constant_tables().items():
        places[name] = (at, t.shape[1])
        at += t.shape[1]
    return places, at


PARAM_ROWS = {
    "c": (0, 0, 8, 0, 128), "b_ada": (0, 8, 24, 0, 128), "g_pre": (0, 32, 8, 0, 128),
    "norm_mix_g_2": (0, 40, 8, 0, 128), "norm_ffn_g_2": (0, 48, 8, 0, 128),
    "norm_mix_g_3": (0, 56, 8, 0, 128), "norm_mem_g_3": (0, 64, 8, 0, 128),
    "norm_ffn_g_3": (0, 72, 8, 0, 128), "conv_w": (0, 80, 48, 0, 128),
    "conv_lru_w_2": (1, 0, 8, 0, 128), "conv_mlstm_w_2": (1, 8, 16, 0, 128),
    "lru_ba_2": (1, 24, 2, 0, 128), "lru_bx_2": (1, 26, 2, 0, 128), "lru_lambda_2": (1, 28, 2, 0, 128),
    "rw_mu_rkv_3": (1, 30, 18, 0, 128), "rw_w0_3": (1, 48, 6, 0, 128), "rw_a0_3": (1, 54, 6, 0, 128),
    "rw_k_k_3": (1, 60, 3, 0, 128), "rw_k_a_3": (1, 63, 3, 0, 128), "rw_r_k_3": (1, 66, 3, 0, 128),
    "rw_mu_w_3": (1, 69, 2, 0, 64), "rw_mu_a_3": (1, 69, 2, 64, 64),
}


class Chain:

    def __init__(self, engine, sem):
        self.engine, self.sem, self.n = engine, sem, 0

    def __call__(self, instruction):
        self.n += 1
        instruction.then_inc(self.sem, 1)
        self.engine.wait_ge(self.sem, self.n)


class Chip:

    def __init__(self, nc, ctx, ins):
        self.nc, self.ins = nc, ins

        def sb(name, *shape):
            return ctx.enter_context(nc.sbuf_tensor(name, [P, *shape], F32))

        self.places, width = constant_places()
        self.constants = sb("constants", width)
        self.ring = sb("ring", RING * SLOT)
        self.chan = sb("chan", 20, CHW)
        self.tok = sb("tok", TT, 3840)
        self.small = sb("small", TT, 16)
        self.x = sb("x", TT, D)
        self.xn = sb("xn", TT, D)
        self.hT = sb("hT", DC, S)
        self.param_rows = sb("param_rows", 2, P)
        self.cols = sb("cols", 2, P)
        self.mod = sb("mod", 24)
        self.narrow_w = sb("narrow_w", 2 * 8 * 8 + 8 * 16)
        self.rows_bc = sb("rows_bc", 32)
        self.stat = sb("stat", 128)
        self.ps = ctx.enter_context(nc.psum_tensor("ps", [P, 8, BANK], F32))

        def sem(name):
            return ctx.enter_context(nc.semaphore(name))

        self.sem = sem
        self.params_landed = sem("params_landed")
        self.x_landed = sem("x_landed")
        self.w_landed = [sem(f"w_landed{u}") for u in range(RING)]
        self.tile_done = [sem(f"tile_done{u}") for u in range(RING)]
        self.psum_free = [sem(f"psum_free{u}") for u in range(2)]
        self.tiles = [0] * RING
        self.copied = [0] * 2
        self.next_slot = 0
        self.products = sem("products")
        self.vectors = sem("vectors")
        self.activations = sem("activations")
        self.pools = sem("pools")
        self.loads = sem("loads")
        self.count = {"products": 0, "vectors": 0, "activations": 0, "pools": 0, "loads": 0}
        self.inverse_products = sem("inverse_products")
        self.inverse_updates = sem("inverse_updates")
        self.inverses = 0
        self.vchain = Chain(nc.vector, sem("vector_chain"))
        self.achain = Chain(nc.scalar, sem("scalar_chain"))

    def const(self, name):
        at, n = self.places[name]
        return self.constants[:, at:at + n]

    def col(self, name, n=0):
        group, row, _, _, _ = PARAM_ROWS[name]
        return self.cols[:, group, row + n:row + n + 1]

    def starts(self):
        return self.count["products"], self.count["vectors"], self.count["activations"]

    def advance(self, **steps):
        for name, n in steps.items():
            self.count[name] += n


class Scratch:

    def __init__(self, k, first_slot=2):
        self.k, self.at, self.end = k, first_slot * SLOT, RING * SLOT

    def take(self, n):
        a = self.k.ring[:, self.at:self.at + n]
        self.at += n
        assert self.at <= self.end
        return a


def over(ap, n):
    return ap.unsqueeze(1).broadcast_to([ap.shape[0], n, ap.shape[1]])


def along(ap, n):
    return ap.unsqueeze(2).broadcast_to([ap.shape[0], ap.shape[1], n])



def load_parameters(k, x):
    nc, ins = k.nc, k.ins
    with nc.Block() as block:
        loads = [(k.constants[:, :], ins["constants"]), (k.x[:, :, :], x.rearrange("b (t p) d -> p (b t) d", p=P))]
        for name, (g, row, n, at, m) in PARAM_ROWS.items():
            flat = ins[name].rearrange({1: "a -> a", 2: "a b -> (a b)", 3: "a b c -> (a b c)", 4: "a b c d -> (a b c d)"}[len(ins[name].shape)])
            loads.append((k.param_rows[row:row + n, g, at:at + m], flat.rearrange("(n m) -> n m", m=m)))
        w1 = ins["w_in"][0, :, 2048:2056].rearrange("(c p) n -> p c n", p=P)
        w2 = ins["w_in_2"][0, :, 1536:1544].rearrange("(c p) n -> p c n", p=P)
        w3 = ins["w_router_3"][0].rearrange("(c p) n -> p c n", p=P)
        loads.append((k.narrow_w[:, 0:64].rearrange("p (c n) -> p c n", n=8), w1))
        loads.append((k.narrow_w[:, 64:128].rearrange("p (c n) -> p c n", n=8), w2))
        loads.append((k.narrow_w[:, 128:256].rearrange("p (c n) -> p c n", n=16), w3))
        for n, name in enumerate(("a_log", "dt_bias", "mlstm_ig_b_2", "mlstm_fg_b_2")):
            loads.append((k.rows_bc[:, 4 * n:4 * n + 4], ins[name].partition_broadcast(P).rearrange("p a n -> p (a n)")))

        small = loads[0:1] + loads[2:]

        @block.gpsimd
        def _(pool):
            nc.gpsimd.memset(k.param_rows[:, :, :], 0.0).then_inc(k.pools, 1)
            nc.gpsimd.memset(k.chan[:, :, :], 0.0)

        @block.sync
        def _(sp):
            def load_w(u):
                if 1 in BLOCKS:
                    dst = k.ring[:, u * SLOT:(u + 1) * SLOT].rearrange("p (c n) -> p c n", n=TILE)
                    sp.dma_start(dst, columns(ins["w_ada"], 0, TILE)(u)).then_inc(k.w_landed[u], 16)
            load_w(0)
            sp.wait_ge(k.pools, 1)
            mine = small[1::2]
            for n, (dst, src) in enumerate(mine):
                if n == len(mine) // 2:
                    load_w(1)
                sp.dma_start(dst, src).then_inc(k.params_landed, 16)
            for u in range(2, RING):
                load_w(u)

        @block.tensor
        def _(pe):
            for u in range(RING):
                pe.sem_inc(k.tile_done[u], 1)
            pe.wait_ge(k.params_landed, 16 * len(small))
            for g in range(2):
                last = nc.tensor.transpose(k.ps[:, 0, g * P:(g + 1) * P], k.param_rows[:, g, :], k.const("ident"))
            last.then_inc(k.products, 1)

        @block.scalar
        def _(act):
            for u in range(2):
                act.sem_inc(k.psum_free[u], 1)
            act.wait_ge(k.pools, 1)
            for dst, src in small[0::2]:
                act.dma_start(dst, src).then_inc(k.params_landed, 16)
            act.dma_start(*loads[1]).then_inc(k.x_landed, 16)
            if 1 not in BLOCKS:
                act.wait_ge(k.x_landed, 16)

        @block.vector
        def _(dve):
            dve.wait_ge(k.products, 1)
            nc.vector.tensor_copy(k.cols[:, :, :].rearrange("p g n -> p (g n)"), k.ps[:, 0, 0:2 * P])
    k.advance(products=1, pools=1)
    if 1 in BLOCKS:
        k.tiles = [1] * RING


def issue(k, sp, loads):
    for slot, before, dst, src in loads:
        sp.wait_ge(k.tile_done[slot], before + 1)
        sp.dma_start(dst, src).then_inc(k.w_landed[slot], 16)


def turn(k, src, chunks, dst, scale=None, shift=None, norm_of=None, ahead=()):
    nc = k.nc
    p0, v0, a0 = k.starts()
    rstd = k.stat[:, 0:TT]
    sums = k.stat[:, TT:2 * TT]
    with nc.Block() as block:
        @block.sync
        def _(sp):
            issue(k, sp, ahead)

        @block.scalar
        def _(act):
            if norm_of is not None:
                for t in range(TT):
                    last = nc.scalar.activation(src[:, t, 0:D], norm_of[:, t, :], ACT.Square, accum_out=sums[:, t:t + 1])
                k.achain(last)
                k.achain(nc.scalar.activation(rstd, sums, ACT.Ln, bias=k.const("eps"), scale=1.0 / D))
                nc.scalar.activation(rstd, rstd, ACT.Exp, scale=-0.5).then_inc(k.activations, 1)
            for c in [c for c in range(chunks) if c // 2 % 2]:
                act.wait_ge(k.products, p0 + c // 2 + 1)
                view = k.ps[:, c // 2, (c % 2) * S:(c % 2 + 1) * S]
                if scale is not None:
                    nc.scalar.activation(dst[:, c, 0:S], view, ACT.Identity, bias=shift(c) if shift else 0.0, scale=scale(c))
                else:
                    nc.scalar.copy(dst[:, c, 0:S], view)

        @block.vector
        def _(dve):
            if norm_of is not None:
                dve.wait_ge(k.activations, a0 + 1)
                for t in range(TT):
                    nc.vector.tensor_scalar(src[:, t, 0:D], norm_of[:, t, :], rstd[:, t:t + 1], None, ALU.mult).then_inc(k.vectors, 1)
            for c in [c for c in range(chunks) if c // 2 % 2 == 0]:
                dve.wait_ge(k.products, p0 + c // 2 + 1)
                view = k.ps[:, c // 2, (c % 2) * S:(c % 2 + 1) * S]
                if scale is not None and shift is not None:
                    nc.vector.tensor_scalar(dst[:, c, 0:S], view, scale(c), shift(c), ALU.mult, ALU.add)
                elif scale is not None:
                    nc.vector.tensor_scalar(dst[:, c, 0:S], view, scale(c), None, ALU.mult)
                else:
                    nc.vector.tensor_copy(dst[:, c, 0:S], view)

        @block.tensor
        def _(pe):
            if norm_of is not None:
                pe.wait_ge(k.vectors, v0 + TT)
            for b in range((chunks + 1) // 2):
                for c in range(2 * b, min(2 * b + 2, chunks)):
                    for t in range(TT):
                        at = (c % 2) * S + t * P
                        last = nc.tensor.transpose(k.ps[:, b, at:at + P], src[:, t, c * P:(c + 1) * P], k.const("ident"))
                last.then_inc(k.products, 1)
    k.advance(products=(chunks + 1) // 2, vectors=TT if norm_of is not None else 0,
              activations=1 if norm_of is not None else 0)


def each_tile(engine, n, first_slot, body, skip=0):
    if n // 2 > skip // 2:
        with engine.Fori(skip // 2, n // 2) as i:
            for u in range(2):
                body(i, u, (first_slot + u) % 2)
    if n % 2 and skip < n:
        body(n // 2, 0, first_slot)


class Stream:

    def __init__(self, k, parts, chunks=DC):
        self.k, self.parts, self.chunks = k, parts, chunks
        for part in parts:
            n = part["tiles"]
            first = k.next_slot
            part["first_slot"] = first
            part["start"], part["copied"] = list(k.tiles), list(k.copied)
            for slot, m in ((first, (n + 1) // 2), (1 - first, n // 2)):
                k.tiles[slot] += m
                k.copied[slot] += m
            k.next_slot = (first + n) % 2
        self.skip = min(2, parts[0]["tiles"])

    def tile(self, part, n, slot):
        dst = self.k.ring[:, slot * SLOT:(slot + 1) * SLOT].rearrange("p (c n) -> p c n", n=TILE)
        return dst[:, 0:self.chunks, 0:part["width"]], part["w"](n)

    def ahead(self):
        part = self.parts[0]
        slots = [(part["first_slot"] + n) % 2 for n in range(self.skip)]
        return [(slot, part["start"][slot], *self.tile(part, n, slot)) for n, slot in enumerate(slots)]


def project(k, hT, stream, narrow=None, vector=None, scalar=None):
    nc = k.nc
    chunks = stream.chunks
    p0, v0, a0 = k.starts()

    def copies(part):
        if not part["channel_major"]:
            return [(b, part["width"]) for b in range(TT)]
        return [(b, min(2, part["width"] // P - 2 * b) * S) for b in range((part["width"] // P + 1) // 2)]

    with nc.Block() as block:
        @block.sync
        def _(sp):
            for n, part in enumerate(stream.parts):
                def load(i, u, slot):
                    dst, src = stream.tile(part, 2 * i + u, slot)
                    sp.wait_ge(k.tile_done[slot], i + (part["start"][slot] + 1))
                    sp.dma_start(dst, src).then_inc(k.w_landed[slot], 16)
                each_tile(sp, part["tiles"], part["first_slot"], load, skip=0 if n else stream.skip)

        @block.tensor
        def _(pe):
            if narrow:
                w, out, n = narrow
                for t in range(TT):
                    for c in range(chunks):
                        last = nc.tensor.matmul(k.ps[:, 4, t * n:(t + 1) * n], hT[:, c, t * P:(t + 1) * P], w[:, c, :],
                                                start=c == 0, stop=c == chunks - 1)
                last.then_inc(k.products, 1)
            for part in stream.parts:
                width = part["width"]

                def multiply(i, u, slot):
                    wt = k.ring[:, slot * SLOT:(slot + 1) * SLOT].rearrange("p (c n) -> p c n", n=TILE)
                    pe.wait_ge(k.w_landed[slot], i * 16 + 16 * (part["start"][slot] + 1))
                    pe.wait_ge(k.psum_free[slot], i + (part["copied"][slot] + 1))
                    if part["channel_major"]:
                        for n in range(width // P):
                            for c in range(chunks):
                                last = nc.tensor.matmul(k.ps[:, 2 * slot + n // 2, (n % 2) * S:(n % 2 + 1) * S],
                                                        wt[:, c, n * P:(n + 1) * P], hT[:, c, 0:S],
                                                        start=c == 0, stop=c == chunks - 1)
                    else:
                        for t in range(TT):
                            for c in range(chunks):
                                last = nc.tensor.matmul(k.ps[:, 2 * slot + t, 0:width], hT[:, c, t * P:(t + 1) * P],
                                                        wt[:, c, 0:width], start=c == 0, stop=c == chunks - 1)
                    last.then_inc(k.tile_done[slot], 1)
                each_tile(pe, part["tiles"], part["first_slot"], multiply)

        @block.scalar
        def _(act):
            if narrow:
                w, out, n = narrow
                act.wait_ge(k.products, p0 + 1)
                nc.scalar.copy(out, k.ps[:, 4, 0:TT * n].rearrange("p (t n) -> p t n", n=n))
            for part in stream.parts:
                def copy(i, u, slot):
                    act.wait_ge(k.tile_done[slot], i + (part["start"][slot] + 2))
                    for b, n in copies(part):
                        last = nc.scalar.activation(part["out"](2 * i + u, b), shaped(k.ps[:, 2 * slot + b, 0:n], part),
                                                    part.get("func", ACT.Copy))
                    last.then_inc(k.psum_free[slot], 1)
                each_tile(act, part["tiles"], part["first_slot"], copy)
            if scalar:
                scalar(act)

        if vector:
            @block.vector
            def _(dve):
                vector(dve)
    k.advance(products=1 if narrow else 0)


def wait_copied(k, dve, part):
    first, n = part["first_slot"], part["tiles"]
    for slot, m in ((first, (n + 1) // 2), (1 - first, n // 2)):
        if m:
            dve.wait_ge(k.psum_free[slot], part["copied"][slot] + 1 + m)


def shaped(ap, part):
    return ap.rearrange("p (c s) -> p c s", s=S) if part["channel_major"] else ap


def columns(w, first, width):
    def tile(n):
        return w[0, :, bass.ds(n * width + first, width)].rearrange("(c p) n -> p c n", p=P)
    return tile


def to_chan(k, first, width):
    def out(n, b):
        chunks = min(2, width // P - 2 * b)
        return k.chan[:, bass.ds(n * (width // P) + (first + 2 * b), chunks), PAD:PAD + S]
    return out


def to_tok(k, first, width):
    def out(n, b):
        return k.tok[:, b, bass.ds(n * width + first, width)]
    return out


def chan_part(k, w, col, width, tiles, chunk):
    return {"w": columns(w, col, width), "width": width, "tiles": tiles, "channel_major": True,
            "out": to_chan(k, chunk, width)}


def tok_part(k, w, col, width, tiles, at, func=ACT.Copy):
    return {"w": columns(w, col, width), "width": width, "tiles": tiles, "channel_major": False,
            "out": to_tok(k, at, width), "func": func}


class WideStream:

    def __init__(self, k, branches):
        self.branches, self.plan, self.loads = branches, [], []
        for br in branches:
            for at in range(0, br["chunks"], 4):
                n, u = min(4, br["chunks"] - at), k.next_slot
                self.plan.append((br, at, n, u, k.tiles[u]))
                dst = k.ring[:, u * SLOT:u * SLOT + n * D].rearrange("p (c n) -> p c n", n=D)
                self.loads.append((u, k.tiles[u], dst, br["w"][at * P:(at + n) * P, :].rearrange("(c p) n -> p c n", p=P)))
                k.tiles[u] += 1
                k.next_slot = 1 - u

    def ahead(self):
        return self.loads[0:2]


def project_wide(k, stream):
    nc = k.nc
    p0, v0, a0 = k.starts()
    branches, plan = stream.branches, stream.plan
    with nc.Block() as block:
        @block.sync
        def _(sp):
            issue(k, sp, stream.loads[2:])

        @block.tensor
        def _(pe):
            for b, br in enumerate(branches):
                set0 = 4 * (b % 2)
                if b >= 2:
                    pe.wait_ge(k.vectors, v0 + b - 1)
                for at, n, u, before in [x[1:] for x in plan if x[0] is br]:
                    pe.wait_ge(k.w_landed[u], 16 * (before + 1))
                    wt = k.ring[:, u * SLOT:(u + 1) * SLOT].rearrange("p (c n) -> p c n", n=D)
                    for c in range(n):
                        for t in range(TT):
                            for h in range(2):
                                last = nc.tensor.matmul(k.ps[:, set0 + 2 * t + h, :], br["lhs"](at + c)[:, t * P:(t + 1) * P],
                                                        wt[:, c, h * BANK:(h + 1) * BANK],
                                                        start=at + c == 0, stop=at + c == br["chunks"] - 1)
                    last.then_inc(k.tile_done[u], 1)

        @block.vector
        def _(dve):
            for b, br in enumerate(branches):
                _, at, n, u, before = [x for x in plan if x[0] is br][-1]
                dve.wait_ge(k.tile_done[u], before + 2)
                what, dst = br["out"][0:2]
                sums = k.ps[:, 4 * (b % 2):4 * (b % 2) + 4, :].rearrange("p (t h) n -> p t (h n)", t=TT)
                for t in range(TT):
                    if what == "set":
                        last = nc.vector.tensor_copy(dst[:, t, :], sums[:, t, :])
                    elif what == "add":
                        last = nc.vector.tensor_tensor(dst[:, t, :], dst[:, t, :], sums[:, t, :], ALU.add)
                    elif what == "gate_set":
                        last = nc.vector.tensor_tensor(dst[:, t, :], sums[:, t, :], br["out"][2][:, t, :], ALU.mult)
                    else:
                        gate = br["out"][2]
                        last = nc.vector.tensor_tensor(gate[:, t, :], sums[:, t, :], gate[:, t, :], ALU.mult)
                if what == "gate_add":
                    k.vchain(last)
                    for t in range(TT):
                        last = nc.vector.tensor_tensor(dst[:, t, :], dst[:, t, :], gate[:, t, :], ALU.add)
                k.vchain(last)
                dve.sem_inc(k.vectors, 1)
    k.advance(vectors=len(branches))


def attention(k, heads, qT, kT, v, scale, mask, out, causal=False, gate=None):
    nc = k.nc
    p0, v0, a0 = k.starts()
    s = Scratch(k)
    half = heads // 2
    scores = [s.take(half * S).rearrange("p (h k) -> p h k", h=half) for u in range(4)]
    probs_t = [s.take(TT * half * P) for u in range(4)]

    def stat(n, u):
        return k.stat[:, 16 * n + 4 * u:16 * n + 4 * u + half]

    def keys(u):
        return (u // 2 + 1) * P if causal else S

    def sums(u):
        r = u % 2
        return k.ps[:, 2 * r:2 * r + 2, :].rearrange("p b (h k) -> p (b h) k", k=S)[:, 0:half, 0:keys(u)]

    def by_parity(ap, u):
        return ap[:, u // 2, 0:heads * HD].rearrange("p (h r d) -> p h r d", r=2, d=HD)[:, :, u % 2, :]
    scored = [1, 2, 3, 4]
    turned = [5, 6, 9, 10]
    mixed = [7, 8, 11, 12]
    read = [1, 3, 5, 8]
    shifted = [2, 4, 6, 9]
    done = [7, 10, 11, 12]
    probs = [1, 2, 4, 6]
    copied = [3, 5, 7, 8]
    with nc.Block() as block:
        @block.tensor
        def _(pe):
            def score(u):
                if u >= 2:
                    pe.wait_ge(k.vectors, v0 + read[u - 2])
                t, r = u // 2, u % 2
                for i in range(half):
                    last = nc.tensor.matmul(k.ps[:, 2 * r + i // 2, i % 2 * S:i % 2 * S + keys(u)],
                                            qT(2 * i + r)[:, t * P:(t + 1) * P], kT(2 * i + r)[:, 0:keys(u)], start=True, stop=True)
                last.then_inc(k.products, 1)

            def turn_probs(u):
                pe.wait_ge(k.activations, a0 + probs[u])
                if u >= 2:
                    pe.wait_ge(k.vectors, v0 + done[u - 2])
                for j in range(keys(u) // P):
                    for i in range(half):
                        n = j * half + i
                        last = nc.tensor.transpose(k.ps[:, 4 + 2 * (u % 2) + n // 4, (n % 4) * P:(n % 4 + 1) * P],
                                                   scores[u][:, i, j * P:(j + 1) * P], k.const("ident"))
                last.then_inc(k.products, 1)

            def mix(u):
                pe.wait_ge(k.activations, a0 + copied[u])
                for i in range(half):
                    for j in range(keys(u) // P):
                        n = j * half + i
                        last = nc.tensor.matmul(k.ps[:, 4 + 2 * (u % 2), i * HD:(i + 1) * HD], probs_t[u][:, n * P:(n + 1) * P],
                                                v(j, 2 * i + u % 2), start=j == 0, stop=j == keys(u) // P - 1)
                last.then_inc(k.products, 1)
            for u in range(4):
                score(u)
            for t in range(TT):
                turn_probs(2 * t)
                turn_probs(2 * t + 1)
                mix(2 * t)
                mix(2 * t + 1)

        @block.vector
        def _(dve):
            def shift(u):
                sc = scores[u][:, :, 0:keys(u)]
                dve.wait_ge(k.products, p0 + scored[u])
                if mask is None:
                    k.vchain(nc.vector.tensor_reduce(stat(0, u), sums(u), AX_X, ALU.max))
                    nc.vector.tensor_tensor(sc, sums(u), along(stat(0, u), keys(u)), ALU.subtract).then_inc(k.vectors, 2)
                else:
                    nc.vector.scalar_tensor_tensor(out=sc, in0=sums(u), scalar=scale, in1=mask(u // 2)[:, u % 2::2, :],
                                                   op0=ALU.mult, op1=ALU.add).then_inc(k.vectors, 1)
                    dve.wait_ge(k.vectors, v0 + read[u])
                    k.vchain(nc.vector.tensor_reduce(stat(0, u), sc, AX_X, ALU.max))
                    nc.vector.tensor_tensor(sc, sc, along(stat(0, u), keys(u)), ALU.subtract).then_inc(k.vectors, 1)

            def invert_totals(u):
                dve.wait_ge(k.activations, a0 + probs[u])
                k.vchain(nc.vector.tensor_reduce(stat(1, u), scores[u][:, :, 0:keys(u)], AX_X, ALU.add))
                k.vchain(nc.vector.reciprocal(stat(2, u), stat(1, u)))

            def finish(u):
                dve.wait_ge(k.products, p0 + mixed[u])
                sums_u = k.ps[:, 4 + 2 * (u % 2), 0:half * HD].rearrange("p (h d) -> p h d", h=half)
                nc.vector.tensor_tensor(by_parity(out, u), sums_u, along(stat(2, u), HD), ALU.mult).then_inc(k.vectors, 1)
                if gate is not None:
                    dve.wait_ge(k.vectors, v0 + done[u])
                    nc.vector.tensor_tensor(by_parity(out, u), by_parity(out, u), by_parity(gate, u), ALU.mult)
            shift(0)
            shift(1)
            invert_totals(0)
            shift(2)
            finish(0)
            invert_totals(1)
            shift(3)
            finish(1)
            invert_totals(2)
            invert_totals(3)
            finish(2)
            finish(3)

        @block.scalar
        def _(act):
            def exponential(u):
                sc = scores[u][:, :, 0:keys(u)]
                act.wait_ge(k.vectors, v0 + shifted[u])
                nc.scalar.activation(sc, sc, ACT.Exp, scale=scale if mask is None else 1.0).then_inc(k.activations, 1)

            def copy(u):
                act.wait_ge(k.products, p0 + turned[u])
                n = keys(u) // P * half * P
                b = 4 + 2 * (u % 2)
                nc.scalar.copy(probs_t[u][:, 0:n], k.ps[:, b:b + 2, :].rearrange("p b n -> p (b n)")[:, 0:n]).then_inc(k.activations, 1)
            exponential(0)
            exponential(1)
            copy(0)
            exponential(2)
            copy(1)
            exponential(3)
            copy(2)
            copy(3)
    k.advance(products=12, vectors=12, activations=8)


def convolve(k, dve, first, chunks, weights, dst):
    nc = k.nc
    for tap in range(4):
        for c in range(chunks):
            src = k.chan[:, first + c, PAD - 3 + tap:PAD - 3 + tap + S]
            if tap == 0:
                last = nc.vector.tensor_scalar(dst[:, c, 0:S], src, weights(tap, c), None, ALU.mult)
            else:
                last = nc.vector.scalar_tensor_tensor(out=dst[:, c, 0:S], in0=src, scalar=weights(tap, c),
                                                      in1=dst[:, c, 0:S], op0=ALU.mult, op1=ALU.add)
        k.vchain(last)


def invert_tensor(k, pe, groups, first, levels, A_t, X, Y):
    nc = k.nc
    at = k.inverses
    for n in range(1, levels):
        before = at + 2 * groups * (n - 1)
        for g in range(groups):
            if n > 1:
                pe.wait_ge(k.inverse_updates, before - 2 * groups + groups + g + 1)
            for m in range(4):
                last = nc.tensor.matmul(k.ps[:, first + g, m * P:(m + 1) * P], A_t(4 * g + m), X(4 * g + m), start=True, stop=True)
            last.then_inc(k.inverse_products, 1)
        for g in range(groups):
            pe.wait_ge(k.inverse_updates, before + g + 1)
            for m in range(4):
                nc.tensor.matmul(k.ps[:, first + g, m * P:(m + 1) * P], Y(4 * g + m), k.U(4 * g + m), start=True, stop=True)
            for m in range(4):
                last = nc.tensor.matmul(k.ps[:, first + groups + g, m * P:(m + 1) * P], k.U(4 * g + m), Y(4 * g + m), start=True, stop=True)
            last.then_inc(k.inverse_products, 1)


def invert_vector(k, dve, groups, first, levels, A_t, X, Y):
    nc = k.nc
    at = k.inverses

    def group(f, g):
        base = f(4 * g)
        return f(4 * g, 4)

    for n in range(1, levels):
        before = at + 2 * groups * (n - 1)
        level = over(k.const(f"level{n}"), 4)
        for g in range(groups):
            dve.wait_ge(k.inverse_products, before + g + 1)
            nc.vector.tensor_tensor(group(k.U, g), k.ps[:, first + g, :].rearrange("p (m n) -> p m n", m=4), level, ALU.mult)\
                .then_inc(k.inverse_updates, 1)
        for g in range(groups):
            dve.wait_ge(k.inverse_products, before + groups + g + 1)
            nc.vector.tensor_tensor(group(X, g), group(X, g), k.ps[:, first + g, :].rearrange("p (m n) -> p m n", m=4), ALU.add)
            nc.vector.tensor_tensor(group(Y, g), group(Y, g), k.ps[:, first + groups + g, :].rearrange("p (m n) -> p m n", m=4), ALU.add)\
                .then_inc(k.inverse_updates, 1)


def matrices(ap):
    def f(n, m=None):
        a = ap[:, n * P:(n + (m or 1)) * P]
        return a if m is None else a.rearrange("p (m n) -> p m n", m=m)
    return f



def modulation(k, ahead):
    nc = k.nc
    p0, v0, a0 = k.starts()
    cw = k.hT[:, 0, 0:DC * 32].rearrange("p (c n) -> p c n", n=32)
    rstd, sums = k.stat[:, 0:TT], k.stat[:, TT:2 * TT]
    rows = k.tok[:, 0, 0:3 * D]
    tiles = 3 * D // TILE
    with nc.Block() as block:
        @block.sync
        def _(sp):
            issue(k, sp, ahead)

        @block.tensor
        def _(pe):
            pe.wait_ge(k.activations, a0 + 1)

            def turn_rows(u):
                if u % 2:
                    pe.wait_ge(k.vectors, v0 + u // 2 + 1)
                else:
                    pe.wait_ge(k.activations, a0 + u // 2 + 3)
                for n in range(TILE // P):
                    at = u * TILE + n * P
                    last = nc.tensor.matmul(k.ps[:, 6, at // P:at // P + 1], rows[:, at:at + P], k.const("four_idents")[:, 0:1], start=True, stop=True)
                return last
            for u in range(tiles):
                wt = k.ring[:, u * SLOT:(u + 1) * SLOT].rearrange("p (c n) -> p c n", n=TILE)
                pe.wait_ge(k.w_landed[u], 16)
                for half in range(2):
                    for j in range(4):
                        c = 4 * half + j
                        last = nc.tensor.matmul(k.ps[32 * j:32 * j + 32, u, :], cw[:, c, :], wt[:, c, :], start=half == 0, stop=half == 1)
                last.then_inc(k.tile_done[u], 1)
                if u:
                    turn_rows(u - 1)
            turn_rows(tiles - 1).then_inc(k.products, 1)

        @block.scalar
        def _(act):
            group, row, n, _, _ = PARAM_ROWS["c"]
            nc.scalar.activation(cw, along(k.cols[:, group, row:row + n], 32), ACT.Silu).then_inc(k.activations, 1)
            act.wait_ge(k.x_landed, 16)
            for t in range(TT):
                last = nc.scalar.activation(k.xn[:, t, :], k.x[:, t, :], ACT.Square, accum_out=sums[:, t:t + 1])
            k.achain(last)
            k.achain(nc.scalar.activation(rstd, sums, ACT.Ln, bias=k.const("eps"), scale=1.0 / D))
            nc.scalar.activation(rstd, rstd, ACT.Exp, scale=-0.5).then_inc(k.activations, 1)
            for u in range(0, tiles, 2):
                act.wait_ge(k.tile_done[u], 2)
                nc.scalar.copy(rows[:, u * TILE:(u + 1) * TILE], k.ps[:, u, :]).then_inc(k.activations, 1)

        @block.vector
        def _(dve):
            dve.wait_ge(k.activations, a0 + 2)
            for t in range(TT):
                nc.vector.tensor_scalar(k.xn[:, t, :], k.x[:, t, :], rstd[:, t:t + 1], None, ALU.mult)
            for u in range(1, tiles, 2):
                dve.wait_ge(k.tile_done[u], 2)
                nc.vector.tensor_copy(rows[:, u * TILE:(u + 1) * TILE], k.ps[:, u, :]).then_inc(k.vectors, 1)
            dve.wait_ge(k.products, p0 + 1)
            group, row, n, _, _ = PARAM_ROWS["b_ada"]
            k.vchain(nc.vector.tensor_tensor(k.mod[:, :], k.ps[:, 6, 0:24], k.cols[:, group, row:row + n], ALU.add))
            group, row, n, _, _ = PARAM_ROWS["g_pre"]
            k.vchain(nc.vector.scalar_tensor_tensor(out=k.mod[:, DC:2 * DC], in0=k.mod[:, DC:2 * DC], scalar=1.0,
                                                    in1=k.cols[:, group, row:row + n], op0=ALU.add, op1=ALU.mult))
    k.advance(products=1, vectors=tiles // 2, activations=2 + tiles // 2)


def delta_rule(k, out):
    nc = k.nc
    s = Scratch(k)
    qkv = s.take(12 * S).rearrange("p (c s) -> p c s", s=S)

    norms = s.take(8 * S)
    k_tok = s.take(TT * 512).rearrange("p (t n) -> p t n", t=TT)
    v_tok = s.take(TT * 512).rearrange("p (t n) -> p t n", t=TT)
    p0, v0, a0 = k.starts()
    with nc.Block() as block:
        @block.scalar
        def _(act):
            nc.scalar.activation(norms, qkv[:, 0:8, :].rearrange("p c s -> p (c s)"), ACT.Square).then_inc(k.activations, 1)
            act.wait_ge(k.products, p0 + 1)
            k.achain(nc.scalar.activation(norms, k.ps[:, 0:4, :].rearrange("p b n -> p (b n)"), ACT.Ln, bias=k.const("eps")))
            nc.scalar.activation(norms[:, 0:4 * S], norms[:, 0:4 * S], ACT.Exp, scale=-0.5, bias=k.const("log_scale"))
            nc.scalar.activation(norms[:, 4 * S:8 * S], norms[:, 4 * S:8 * S], ACT.Exp, scale=-0.5).then_inc(k.activations, 1)

        @block.tensor
        def _(pe):
            pe.wait_ge(k.activations, a0 + 1)
            for b in range(4):
                last = nc.tensor.matmul(k.ps[:, b, :], k.const("ones"), norms[:, b * BANK:(b + 1) * BANK], start=True, stop=True)
            last.then_inc(k.products, 1)
            pe.wait_ge(k.vectors, v0 + 1)
            for t in range(TT):
                for h in range(4):
                    nc.tensor.transpose(k.ps[:, 4 + t, h * P:(h + 1) * P], qkv[:, 4 + h, t * P:(t + 1) * P], k.const("ident"))
                    last = nc.tensor.transpose(k.ps[:, 6 + t, h * P:(h + 1) * P], qkv[:, 8 + h, t * P:(t + 1) * P], k.const("ident"))
            last.then_inc(k.products, 1)

        @block.vector
        def _(dve):
            dve.wait_ge(k.activations, a0 + 2)
            flat = qkv[:, 0:8, :].rearrange("p c s -> p (c s)")
            nc.vector.tensor_tensor(flat, flat, norms, ALU.mult).then_inc(k.vectors, 1)
            dve.wait_ge(k.products, p0 + 2)
            nc.vector.tensor_copy(k_tok.rearrange("p t n -> p (t n)"), k.ps[:, 4:6, :].rearrange("p t n -> p (t n)"))
            nc.vector.tensor_copy(v_tok.rearrange("p t n -> p (t n)"), k.ps[:, 6:8, :].rearrange("p t n -> p (t n)"))
    k.advance(products=2, vectors=1, activations=2)

    beta, g, g_neg, G, eG, eGr, t1, t2 = [k.stat[:, 8 * n:8 * n + 8] for n in range(8)]
    ea = k.stat[:, 64:68]

    def th(a):
        return a.rearrange("p (t h) -> p t h", t=TT)
    p0, v0, a0 = k.starts()
    with nc.Block() as block:
        @block.vector
        def _(dve):
            k.vchain(nc.vector.tensor_tensor(th(t1), k.small[:, :, 4:8], over(k.rows_bc[:, 4:8], TT), ALU.add))
            nc.vector.scalar_tensor_tensor(out=t2, in0=t1, scalar=-1.0, in1=t1, op0=ALU.mult, op1=ALU.max).then_inc(k.vectors, 1)
            dve.wait_ge(k.activations, a0 + 1)
            k.vchain(nc.vector.scalar_tensor_tensor(out=t1, in0=t1, scalar=0.0, in1=t2, op0=ALU.max, op1=ALU.add))
            k.vchain(nc.vector.tensor_tensor(th(g_neg), th(t1), over(ea, TT), ALU.mult))
            nc.vector.tensor_scalar(g, g_neg, -1.0, None, ALU.mult).then_inc(k.vectors, 1)
            dve.wait_ge(k.products, p0 + 1)
            k.vchain(nc.vector.tensor_copy(G, k.ps[:, 0, 0:8]))
            nc.vector.tensor_tensor(t2, k.ps[:, 0, 8:16], G, ALU.subtract).then_inc(k.vectors, 1)

        @block.scalar
        def _(act):
            act.wait_ge(k.vectors, v0 + 1)
            k.achain(nc.scalar.activation(t2, t2, ACT.Exp, scale=-1.0))
            k.achain(nc.scalar.activation(t2, t2, ACT.Ln, bias=k.const("ones")[:, 0:1]))
            nc.scalar.activation(ea, k.rows_bc[:, 0:4], ACT.Exp)
            nc.scalar.activation(th(beta), k.small[:, :, 0:4], ACT.Sigmoid).then_inc(k.activations, 1)
            act.wait_ge(k.vectors, v0 + 3)
            nc.scalar.activation(eG, G, ACT.Exp)
            nc.scalar.activation(eGr, t2, ACT.Exp)

        @block.tensor
        def _(pe):
            pe.wait_ge(k.vectors, v0 + 2)
            nc.tensor.matmul(k.ps[:, 0, 0:8], k.const("upper"), g, start=True, stop=True)
            nc.tensor.matmul(k.ps[:, 0, 8:16], k.const("ones"), g, start=True, stop=True).then_inc(k.products, 1)
    k.advance(products=1, vectors=3, activations=1)

    n8 = 8 * P
    A, A_t, U, X, Y, qk = [matrices(s.take(n8)) for _ in range(6)]
    decay, decay_t = U, X
    k.U = U
    p0, v0, a0 = k.starts()
    start = k.inverses
    with nc.Block() as block:
        @block.tensor
        def _(pe):
            def spread(a, n):
                return a[:, n:n + 1].broadcast_to([P, P])
            for t in range(TT):
                for h in range(4):
                    n = 4 * t + h
                    kT, qT = qkv[:, 4 + h, t * P:(t + 1) * P], qkv[:, h, t * P:(t + 1) * P]
                    c = slice(h * P, (h + 1) * P)
                    nc.tensor.matmul(k.ps[:, t, c], k.const("upper"), spread(g, n), start=True, stop=False)
                    nc.tensor.matmul(k.ps[:, t, c], spread(g_neg, n), k.const("upper"), start=False, stop=True)
                    nc.tensor.matmul(k.ps[:, 2 + t, c], spread(g, n), k.const("upper"), start=True, stop=False)
                    nc.tensor.matmul(k.ps[:, 2 + t, c], k.const("upper"), spread(g_neg, n), start=False, stop=True)
                    nc.tensor.matmul(k.ps[:, 4 + t, c], kT, kT, start=True, stop=True)
                    last = nc.tensor.matmul(k.ps[:, 6 + t, c], kT, qT, start=True, stop=True)
            last.then_inc(k.products, 1)
            pe.wait_ge(k.vectors, v0 + 2)
            for n in range(8):
                last = nc.tensor.transpose(k.ps[:, n // 4, (n % 4) * P:(n % 4 + 1) * P], A(n), k.const("ident"))
            last.then_inc(k.products, 1)
            pe.wait_ge(k.vectors, v0 + 3)
            invert_tensor(k, pe, 2, 2, 7, A_t, X, Y)

        @block.vector
        def _(dve):
            def bank(b):
                return k.ps[:, b:b + 2, :].rearrange("p b (m n) -> p (b m) n", m=4)
            dve.wait_ge(k.products, p0 + 1)
            nc.vector.tensor_tensor(decay(0, 8), bank(0), over(k.const("neg_not_lower"), 8), ALU.add)
            nc.vector.tensor_tensor(decay_t(0, 8), bank(2), over(k.const("neg_not_upper"), 8), ALU.add).then_inc(k.vectors, 1)
            dve.wait_ge(k.activations, a0 + 1)
            k.vchain(nc.vector.tensor_tensor(A(0, 8), bank(4), decay(0, 8), ALU.mult))
            nc.vector.tensor_tensor(qk(0, 8), bank(6), decay_t(0, 8), ALU.mult)
            k.vchain(nc.vector.tensor_tensor(A(0, 8), A(0, 8), over(k.const("lower_strict"), 8), ALU.mult))
            nc.vector.tensor_tensor(A(0, 8), A(0, 8), along(beta, P), ALU.mult).then_inc(k.vectors, 1)
            dve.wait_ge(k.products, p0 + 2)
            k.vchain(nc.vector.tensor_copy(A_t(0, 8), bank(0)))
            nc.vector.tensor_tensor(X(0, 8), A(0, 8), over(k.const("level0"), 8), ALU.mult)
            k.vchain(nc.vector.tensor_tensor(Y(0, 8), A_t(0, 8), over(k.const("level0_t"), 8), ALU.mult))
            nc.vector.tensor_tensor(X(0, 8), X(0, 8), over(k.const("ident"), 8), ALU.add)
            nc.vector.tensor_tensor(Y(0, 8), Y(0, 8), over(k.const("ident"), 8), ALU.add).then_inc(k.vectors, 1)
            invert_vector(k, dve, 2, 2, 7, A_t, X, Y)

        @block.scalar
        def _(act):
            act.wait_ge(k.vectors, v0 + 1)
            nc.scalar.activation(decay(0, 8), decay(0, 8), ACT.Exp)
            nc.scalar.activation(decay_t(0, 8), decay_t(0, 8), ACT.Exp).then_inc(k.activations, 1)
    k.inverses = start + 6 * 2 * 2
    k.advance(products=2, vectors=3, activations=1)

    kb = A(0, 8)
    vb = A_t(0, 8)
    kd = U(0, 4)
    w_t = X(0, 4)
    state = X(4, 4)
    q_state = U(4, 4)
    u_new = s.take(n8).rearrange("p (m n) -> p m n", m=8)
    eighth = "p (m n) -> p m n"
    p0, v0, a0 = k.starts()
    with nc.Block() as block:
        @block.vector
        def _(dve):
            k8 = k_tok.rearrange("p t (m n) -> p (t m) n", m=4)
            v8 = v_tok.rearrange("p t (m n) -> p (t m) n", m=4)
            nc.vector.tensor_tensor(vb, v8, along(beta, P), ALU.mult)
            nc.vector.tensor_tensor(kd, k8[:, 0:4, :], along(eGr[:, 0:4], P), ALU.mult)
            k.vchain(nc.vector.tensor_tensor(kb, k8, along(beta, P), ALU.mult))
            nc.vector.tensor_tensor(kb, kb, along(eG, P), ALU.mult).then_inc(k.vectors, 1)
            dve.wait_ge(k.products, p0 + 1)
            nc.vector.tensor_copy(u_new, k.ps[:, 0:2, :].rearrange("p b (m n) -> p (b m) n", m=4))
            nc.vector.tensor_copy(w_t, k.ps[:, 2, :].rearrange(eighth, m=4)).then_inc(k.vectors, 1)
            dve.wait_ge(k.products, p0 + 2)
            nc.vector.tensor_copy(state, k.ps[:, 3, :].rearrange(eighth, m=4)).then_inc(k.vectors, 1)
            dve.wait_ge(k.products, p0 + 3)
            nc.vector.tensor_tensor(u_new[:, 4:8, :], u_new[:, 4:8, :], k.ps[:, 4, :].rearrange(eighth, m=4), ALU.subtract).then_inc(k.vectors, 1)
            k.vchain(nc.vector.tensor_tensor(q_state, k.ps[:, 5, :].rearrange(eighth, m=4), along(eG[:, 4:8], P), ALU.mult))
            dve.wait_ge(k.products, p0 + 4)
            o = out[:, :, 0:512].rearrange("p t (m n) -> p t m n", m=4)
            nc.vector.tensor_copy(o[:, 0], k.ps[:, 6, :].rearrange(eighth, m=4))
            k.vchain(nc.vector.tensor_tensor(o[:, 1], k.ps[:, 7, :].rearrange(eighth, m=4), q_state, ALU.add))
            for t in range(TT):
                last = nc.vector.tensor_tensor(kb[:, 4 * t:4 * t + 4, :], o[:, t], o[:, t], ALU.mult)
            k.vchain(last)
            nc.vector.tensor_reduce(t1, kb, AX_X, ALU.add).then_inc(k.vectors, 1)
            dve.wait_ge(k.activations, a0 + 1)
            for t in range(TT):
                last = nc.vector.tensor_tensor(o[:, t], o[:, t], along(t1[:, 4 * t:4 * t + 4], P), ALU.mult)
            k.vchain(last)
            for t in range(TT):
                last = nc.vector.tensor_tensor(o[:, t], o[:, t], over(k_tok[:, 0, 0:P], 4), ALU.mult)
            k.vchain(last)
            for t in range(TT):
                last = nc.vector.tensor_tensor(out[:, t, 0:512], out[:, t, 0:512], k.tok[:, t, 0:512], ALU.mult)
            k.vchain(last)

        @block.sync
        def _(sp):
            sp.wait_ge(k.vectors, v0 + 1)
            sp.dma_start(k_tok[:, 0, 0:P], k.ins["dn_norm_g"].partition_broadcast(P).rearrange("p a n -> p (a n)")).then_inc(k.loads, 16)

        @block.scalar
        def _(act):
            act.wait_ge(k.vectors, v0 + 5)
            act.wait_ge(k.loads, 16 * (k.count["loads"] + 1))
            k.achain(nc.scalar.activation(t1, t1, ACT.Ln, bias=k.const("eps"), scale=1.0 / DN_D))
            nc.scalar.activation(t1, t1, ACT.Exp, scale=-0.5).then_inc(k.activations, 1)

        @block.tensor
        def _(pe):
            pe.wait_ge(k.vectors, v0 + 1)
            for n in range(8):
                nc.tensor.matmul(k.ps[:, n // 4, (n % 4) * P:(n % 4 + 1) * P], Y(n), vb[:, n, :], start=True, stop=True)
            for h in range(4):
                last = nc.tensor.matmul(k.ps[:, 2, h * P:(h + 1) * P], kb[:, 4 + h, :], Y(4 + h), start=True, stop=True)
            last.then_inc(k.products, 1)
            pe.wait_ge(k.vectors, v0 + 2)
            for h in range(4):
                last = nc.tensor.matmul(k.ps[:, 3, h * P:(h + 1) * P], kd[:, h, :], u_new[:, h, :], start=True, stop=True)
            last.then_inc(k.products, 1)
            pe.wait_ge(k.vectors, v0 + 3)
            for h in range(4):
                nc.tensor.matmul(k.ps[:, 4, h * P:(h + 1) * P], w_t[:, h, :], state[:, h, :], start=True, stop=True)
                last = nc.tensor.matmul(k.ps[:, 5, h * P:(h + 1) * P], qkv[:, h, P:S], state[:, h, :], start=True, stop=True)
            last.then_inc(k.products, 1)
            pe.wait_ge(k.vectors, v0 + 4)
            for n in range(8):
                last = nc.tensor.matmul(k.ps[:, 6 + n // 4, (n % 4) * P:(n % 4 + 1) * P], qk(n), u_new[:, n, :], start=True, stop=True)
            last.then_inc(k.products, 1)
    k.advance(products=4, vectors=5, activations=1, loads=1)


def first_layer(k):
    nc, w = k.nc, k.ins["w_in"]
    stream = Stream(k, [
        chan_part(k, w, 0, 512, 3, 0),
        chan_part(k, w, 2056, 512, 2, 12),
        tok_part(k, w, 1536, 512, 1, 0, ACT.Silu),
        tok_part(k, w, 3080, 512, 1, 512),
        tok_part(k, w, 3592, 512, 1, 1024, ACT.Silu),
        tok_part(k, w, 4104, 512, 4, 1536, ACT.Sigmoid),
    ])
    modulation(k, stream.ahead())
    turn(k, k.xn, DC, k.hT, scale=lambda c: k.mod[:, DC + c:DC + c + 1], shift=lambda c: k.mod[:, c:c + 1])
    qkv = Scratch(k).take(12 * S).rearrange("p (c s) -> p c s", s=S)

    def convolve_beside(dve):
        wait_copied(k, dve, stream.parts[0])
        convolve(k, dve, 0, 12, lambda tap, c: k.col("conv_w", tap * 12 + c), qkv)
        dve.sem_inc(k.vectors, 1)

    def silu_behind(act):
        act.wait_ge(k.vectors, k.count["vectors"] + 1)
        nc.scalar.activation(qkv, qkv, ACT.Silu)
    project(k, k.hT, stream, narrow=(k.narrow_w[:, 0:64].rearrange("p (c n) -> p c n", n=8), k.small[:, :, 0:8], 8),
            vector=convolve_beside, scalar=silu_behind)
    k.advance(vectors=1)
    delta_rule(k, k.xn)
    turn(k, k.xn, 4, k.hT[:, 0:4, :])
    causal = k.const("causal").rearrange("p (t n) -> p t n", t=TT)
    attention(k, MB_H, lambda h: k.chan[64 * (h % 2):64 * (h % 2) + 64, 12 + h // 2, PAD:PAD + S],
              lambda h: k.chan[64 * (h % 2):64 * (h % 2) + 64, 16 + h // 2, PAD:PAD + S],
              lambda t, h: k.tok[:, t, 512 + h * 64:512 + h * 64 + 64], MB_D ** -0.5,
              lambda t: over(causal[:, t, 0:(t + 1) * P], MB_H), k.xn, causal=True, gate=k.tok[:, :, 1024:1536])
    stream = WideStream(k, [
        {"lhs": lambda c: k.hT[:, c, :], "w": k.ins["w_proj_dn"][0], "chunks": 4, "out": ("gate_set", k.xn, k.tok[:, :, 1536:2560])},
        {"lhs": lambda c: k.hT[:, 4 + c, :], "w": k.ins["w_proj_mb"][0], "chunks": 4, "out": ("gate_add", k.xn, k.tok[:, :, 2560:3584])},
    ])
    turn(k, k.xn, 4, k.hT[:, 4:8, :], ahead=stream.ahead())
    project_wide(k, stream)
    stream = WideStream(k, [{"lhs": lambda c: k.hT[:, c, :], "w": k.ins["w_out"][0], "chunks": DC, "out": ("set", k.xn)}])
    turn(k, k.xn, DC, k.hT, ahead=stream.ahead())
    project_wide(k, stream)

    s = Scratch(k)
    gate_diag = s.take(D)
    gain = s.take(D)
    squares = s.take(TT * D).rearrange("p (t n) -> p t n", t=TT)
    sums, rstd = k.stat[:, 0:2], k.stat[:, 2:4]
    p0, v0, a0 = k.starts()
    with nc.Block() as block:
        @block.sync
        def _(sp):
            sp.dma_start(gain, k.ins["g_post"].partition_broadcast(P).rearrange("p a n -> p (a n)")).then_inc(k.loads, 16)

        @block.vector
        def _(dve):
            for c in range(DC):
                last = nc.vector.tensor_scalar(gate_diag[:, c * P:(c + 1) * P], k.const("ident"), k.mod[:, 2 * DC + c:2 * DC + c + 1], None, ALU.mult)
            last.then_inc(k.vectors, 1)
            dve.wait_ge(k.products, p0 + 1)
            dve.wait_ge(k.loads, 16 * (k.count["loads"] + 1))
            k.vchain(nc.vector.tensor_tensor(gain, gain, k.ps[:, 0:2, :].rearrange("p b n -> p (b n)"), ALU.mult))
            dve.wait_ge(k.activations, a0 + 1)
            for t in range(TT):
                last = nc.vector.scalar_tensor_tensor(out=k.xn[:, t, :], in0=k.xn[:, t, :], scalar=rstd[:, t:t + 1], in1=gain, op0=ALU.mult, op1=ALU.mult)
            k.vchain(last)
            for t in range(TT):
                nc.vector.tensor_tensor(k.x[:, t, :], k.x[:, t, :], k.xn[:, t, :], ALU.add)

        @block.tensor
        def _(pe):
            pe.wait_ge(k.vectors, v0 + 1)
            for b in range(2):
                last = nc.tensor.matmul(k.ps[:, b, :], k.const("ones"), gate_diag[:, b * BANK:(b + 1) * BANK], start=True, stop=True)
            last.then_inc(k.products, 1)

        @block.scalar
        def _(act):
            for t in range(TT):
                last = nc.scalar.activation(squares[:, t, :], k.xn[:, t, :], ACT.Square, accum_out=sums[:, t:t + 1])
            k.achain(last)
            k.achain(nc.scalar.activation(rstd, sums, ACT.Ln, bias=k.const("eps"), scale=1.0 / D))
            nc.scalar.activation(rstd, rstd, ACT.Exp, scale=-0.5).then_inc(k.activations, 1)
    k.advance(products=1, vectors=1, activations=1, loads=1)



def softplus_vector(k, dve, z, magnitude):
    return k.nc.vector.scalar_tensor_tensor(out=magnitude, in0=z, scalar=-1.0, in1=z, op0=ALU.mult, op1=ALU.max)


def softplus_scalar(k, magnitude):
    k.achain(k.nc.scalar.activation(magnitude, magnitude, ACT.Exp, scale=-1.0))
    return k.nc.scalar.activation(magnitude, magnitude, ACT.Ln, bias=k.const("ones")[:, 0:1])


def lru(k, out):
    nc = k.nc
    s = Scratch(k)
    s.take(4 * S)
    xa = s.take(2 * S).rearrange("p (c s) -> p c s", s=S)
    gates_w = s.take(2 * 2 * P).rearrange("p (w c n) -> p w c n", w=2, c=2)
    r, i, a, th, h = [s.take(2 * S).rearrange("p (c s) -> p c s", s=S) for _ in range(5)]
    rate, mag = k.stat[:, 0:2], k.stat[:, 2:4]
    g, row, n, _, _ = PARAM_ROWS["lru_lambda_2"]
    lam = k.cols[:, g, row:row + n]
    p0, v0, a0 = k.starts()
    with nc.Block() as block:
        @block.gpsimd
        def _(pool):
            nc.gpsimd.memset(gates_w, 0.0).then_inc(k.pools, 1)

        @block.sync
        def _(sp):
            sp.wait_ge(k.pools, k.count["pools"] + 1)
            for n, name in enumerate(("lru_wa_2", "lru_wx_2")):
                for half in range(2):
                    q = slice(64 * half, 64 * half + 64)
                    src = k.ins[name][0].rearrange("(c r) i j -> r i c j", r=2)[half]
                    sp.dma_start(gates_w[q, n, :, q], src).then_inc(k.loads, 16)

        @block.tensor
        def _(pe):
            pe.wait_ge(k.loads, 16 * (k.count["loads"] + 4))
            for n in range(2):
                for c in range(2):
                    last = nc.tensor.matmul(k.ps[:, n, c * S:(c + 1) * S], gates_w[:, n, c, :], xa[:, c, :], start=True, stop=True)
            last.then_inc(k.products, 1)

        @block.scalar
        def _(act):
            act.wait_ge(k.vectors, v0 + 1)
            softplus_scalar(k, mag).then_inc(k.activations, 1)
            act.wait_ge(k.products, p0 + 1)
            for c in range(2):
                nc.scalar.activation(r[:, c, :], k.ps[:, 0, c * S:(c + 1) * S], ACT.Sigmoid, bias=k.col("lru_ba_2", c))
                last = nc.scalar.activation(i[:, c, :], k.ps[:, 1, c * S:(c + 1) * S], ACT.Sigmoid, bias=k.col("lru_bx_2", c))
            last.then_inc(k.activations, 1)
            act.wait_ge(k.vectors, v0 + 2)
            nc.scalar.activation(a, r, ACT.Exp)
            nc.scalar.activation(th, r, ACT.Tanh, scale=-1.0).then_inc(k.activations, 1)
            act.wait_ge(k.vectors, v0 + 3)
            nc.scalar.activation(th, th, ACT.Sqrt).then_inc(k.activations, 1)
            nc.scalar.activation(r, k.chan[:, 2:4, PAD:PAD + S], ACT.Gelu_apprx_tanh).then_inc(k.activations, 1)

        @block.vector
        def _(dve):
            softplus_vector(k, dve, lam, mag).then_inc(k.vectors, 1)
            dve.wait_ge(k.activations, a0 + 1)
            k.vchain(nc.vector.tensor_scalar(rate, lam, -1.0, 0.0, ALU.mult, ALU.max))
            k.vchain(nc.vector.tensor_tensor(rate, rate, mag, ALU.add))
            k.vchain(nc.vector.tensor_scalar(rate, rate, -8.0, None, ALU.mult))
            dve.wait_ge(k.activations, a0 + 2)
            for c in range(2):
                last = nc.vector.tensor_scalar(r[:, c, :], r[:, c, :], rate[:, c:c + 1], None, ALU.mult)
            last.then_inc(k.vectors, 1)
            nc.vector.tensor_tensor(i, i, xa, ALU.mult)
            dve.wait_ge(k.activations, a0 + 3)
            k.vchain(nc.vector.tensor_tensor(h, a, a, ALU.mult))
            nc.vector.scalar_tensor_tensor(out=th, in0=h, scalar=1.0, in1=th, op0=ALU.add, op1=ALU.mult).then_inc(k.vectors, 1)
            dve.wait_ge(k.activations, a0 + 4)
            k.vchain(nc.vector.tensor_tensor(i, i, th, ALU.mult))
            for c in range(2):
                last = nc.vector.tensor_tensor_scan(h[:, c, :], a[:, c, :], i[:, c, :], 0.0, ALU.mult, ALU.add)
            k.vchain(last)
            dve.wait_ge(k.activations, a0 + 5)
            nc.vector.tensor_tensor(out, h, r, ALU.mult)
    k.advance(products=1, vectors=3, activations=5, pools=1, loads=4)


def mlstm(k, out):
    nc = k.nc
    s = Scratch(k)
    qk = s.take(4 * S).rearrange("p (c s) -> p c s", s=S)
    s.take(2 * S)
    diag = s.take(8 * P).rearrange("p (m n) -> p m n", n=P)
    w_s = s.take(4 * S).rearrange("p (h n) -> p h n", h=4)
    w_t = s.take(TT * 4 * P).rearrange("p (j h q) -> p j h q", j=TT, h=4)
    f, mag, i, b, rows = [k.stat[:, 8 * n:8 * n + 8] for n in range(5)]
    mu, den, low = [k.stat[:, 40 + 4 * n:44 + 4 * n] for n in range(3)]

    def th(a):
        return a.rearrange("p (t h) -> p t h", t=TT)
    p0, v0, a0 = k.starts()
    with nc.Block() as block:
        @block.vector
        def _(dve):
            nc.vector.tensor_tensor(th(i), k.small[:, :, 0:4], over(k.rows_bc[:, 8:12], TT), ALU.add)
            k.vchain(nc.vector.tensor_tensor(th(f), k.small[:, :, 4:8], over(k.rows_bc[:, 12:16], TT), ALU.add))
            softplus_vector(k, dve, f, mag).then_inc(k.vectors, 1)
            dve.wait_ge(k.activations, a0 + 1)
            nc.vector.scalar_tensor_tensor(out=f, in0=f, scalar=0.0, in1=mag, op0=ALU.min, op1=ALU.subtract).then_inc(k.vectors, 1)
            dve.wait_ge(k.products, p0 + 1)
            k.vchain(nc.vector.tensor_copy(b, k.ps[:, 0, 0:8]))
            k.vchain(nc.vector.tensor_tensor(rows.rearrange("p (h t) -> p t h", t=TT), th(i), th(b), ALU.subtract))
            nc.vector.tensor_tensor(diag, over(k.const("ident"), 8), along(rows, P), ALU.mult).then_inc(k.vectors, 1)

        @block.scalar
        def _(act):
            act.wait_ge(k.vectors, v0 + 1)
            softplus_scalar(k, mag).then_inc(k.activations, 1)

        @block.tensor
        def _(pe):
            pe.wait_ge(k.vectors, v0 + 2)
            nc.tensor.matmul(k.ps[:, 0, 0:4], k.const("upper"), f[:, 0:4], start=True, stop=True)
            nc.tensor.matmul(k.ps[:, 0, 4:8], k.const("upper"), f[:, 4:8], start=True, stop=False)
            nc.tensor.matmul(k.ps[:, 0, 4:8], k.const("ones"), f[:, 0:4], start=False, stop=True).then_inc(k.products, 1)
            pe.wait_ge(k.vectors, v0 + 3)
            for n in range(2):
                nc.tensor.matmul(k.ps[:, 4 + n, :], k.const("ones"), diag[:, 4 * n:4 * n + 4, :].rearrange("p m n -> p (m n)"), start=True, stop=True)
    k.advance(products=1, vectors=3, activations=1)

    causal = k.const("causal").rearrange("p (t n) -> p t n", t=TT)
    SCORES, TURNED, MIXED = 1, 2, 3
    SHIFTED, WEIGHTS, DONE = 1, 2, 3
    EXPS, COPIED = 1, 2
    p0, v0, a0 = k.starts()
    with nc.Block() as block:
        @block.tensor
        def _(pe):
            for t in range(TT):
                keys = (t + 1) * P
                if t:
                    pe.wait_ge(k.vectors, v0 + 3 * (t - 1) + DONE)
                for h in range(4):
                    half = slice(64 * (h % 2), 64 * (h % 2) + 64)
                    last = nc.tensor.matmul(k.ps[:, 2 * (h % 2), h // 2 * S:h // 2 * S + keys], qk[half, h // 2, t * P:(t + 1) * P],
                                            qk[half, 2 + h // 2, 0:keys], start=True, stop=True)
                last.then_inc(k.products, 1)
                pe.wait_ge(k.vectors, v0 + 3 * t + WEIGHTS)
                for j in range(t + 1):
                    for h in range(4):
                        last = nc.tensor.transpose(k.ps[:, 6 + j, h * P:(h + 1) * P], w_s[:, h, j * P:(j + 1) * P], k.const("ident"))
                last.then_inc(k.products, 1)
                pe.wait_ge(k.activations, a0 + 2 * t + COPIED)
                for h in range(4):
                    for j in range(t + 1):
                        last = nc.tensor.matmul(k.ps[:, 1, h * 64:(h + 1) * 64], w_t[:, j, h, :], k.tok[:, j, h * 64:(h + 1) * 64],
                                                start=j == 0, stop=j == t)
                last.then_inc(k.products, 1)

        @block.vector
        def _(dve):
            for t in range(TT):
                keys = (t + 1) * P
                w = w_s[:, :, 0:keys]
                row = k.ps[:, 4:6, :].rearrange("p b (m n) -> p (b m) n", m=2)[:, :, 0:keys]
                k.vchain(nc.vector.tensor_tensor(w, row, over(causal[:, t, 0:keys], 4), ALU.add))
                k.vchain(nc.vector.tensor_reduce(mu, w, AX_X, ALU.max))
                k.vchain(nc.vector.tensor_scalar(mu, mu, 0.0, None, ALU.max))
                nc.vector.tensor_tensor(low, mu, b[:, 4 * t:4 * t + 4], ALU.add)
                nc.vector.tensor_tensor(w, w, along(mu, keys), ALU.subtract).then_inc(k.vectors, 1)
                dve.wait_ge(k.activations, a0 + 2 * t + EXPS)
                dve.wait_ge(k.products, p0 + 3 * t + SCORES)
                for r in range(2):
                    sums = k.ps[:, 2 * r, :].rearrange("p (h n) -> p h n", h=2)[:, :, 0:keys]
                    last = nc.vector.scalar_tensor_tensor(out=w[:, r::2, :], in0=sums, scalar=ML_D ** -0.5, in1=w[:, r::2, :],
                                                          op0=ALU.mult, op1=ALU.mult)
                last.then_inc(k.vectors, 1)
                dve.wait_ge(k.vectors, v0 + 3 * t + WEIGHTS)
                k.vchain(nc.vector.tensor_reduce(den, w, AX_X, ALU.add))
                k.vchain(nc.vector.scalar_tensor_tensor(out=den, in0=den, scalar=-1.0, in1=den, op0=ALU.mult, op1=ALU.max))
                k.vchain(nc.vector.tensor_tensor(den, den, low, ALU.max))
                k.vchain(nc.vector.reciprocal(den, den))
                dve.wait_ge(k.products, p0 + 3 * t + MIXED)
                o = out[:, t, 0:256]
                k.vchain(nc.vector.tensor_tensor(o.rearrange("p (h d) -> p h d", h=4), k.ps[:, 1, 0:256].rearrange("p (h d) -> p h d", h=4),
                                                 along(den, 64), ALU.mult))
                nc.vector.tensor_tensor(o, o, k.tok[:, t, 256:512], ALU.mult).then_inc(k.vectors, 1)

        @block.scalar
        def _(act):
            for t in range(TT):
                keys = (t + 1) * P
                act.wait_ge(k.vectors, v0 + 3 * t + SHIFTED)
                nc.scalar.activation(low, low, ACT.Exp, scale=-1.0)
                nc.scalar.activation(w_s[:, :, 0:keys], w_s[:, :, 0:keys], ACT.Exp).then_inc(k.activations, 1)
                act.wait_ge(k.products, p0 + 3 * t + TURNED)
                nc.scalar.copy(w_t[:, 0:t + 1, :, :].rearrange("p j h q -> p (j h q)"),
                               k.ps[:, 6:7 + t, :].rearrange("p b n -> p (b n)")).then_inc(k.activations, 1)
    k.advance(products=6, vectors=6, activations=4)


def stick_breaking(k, out):
    nc = k.nc
    s = Scratch(k)
    W = TT * P + P
    z, mag, sp_ = [s.take(4 * W).rearrange("p (h n) -> p h n", h=4) for _ in range(3)]
    p0, v0, a0 = k.starts()

    def q(h):
        return k.chan[64 * (h % 2):64 * (h % 2) + 64, 8 + h // 2, PAD:PAD + S]

    def key(h):
        return k.chan[64 * (h % 2):64 * (h % 2) + 64, 10 + h // 2, PAD:PAD + S]

    def v(t, h):
        return k.tok[:, t, 512 + h * 64:512 + (h + 1) * 64]
    pairs = [(g, slice(2 * g, 2 * g + 2)) for g in range(2)]
    with nc.Block() as block:
        @block.tensor
        def _(pe):
            for g, pair in pairs:
                for h in (2 * g, 2 * g + 1):
                    nc.tensor.matmul(k.ps[:, h, 0:S], key(h)[:, 0:P], q(h), start=True, stop=True)
                    last = nc.tensor.matmul(k.ps[:, h, S:W], key(h)[:, P:S], q(h)[:, P:S], start=True, stop=True)
                last.then_inc(k.products, 1)
            for g, pair in pairs:
                pe.wait_ge(k.vectors, v0 + 3 + g)
                for h in (2 * g, 2 * g + 1):
                    nc.tensor.matmul(k.ps[:, 4 + h, 0:P], k.const("lower"), sp_[:, h, 0:P], start=True, stop=True)
                    nc.tensor.matmul(k.ps[:, 4 + h, P:S], k.const("lower"), sp_[:, h, P:S], start=True, stop=False)
                    nc.tensor.matmul(k.ps[:, 4 + h, P:S], k.const("ones"), sp_[:, h, S:W], start=False, stop=True)
                    last = nc.tensor.matmul(k.ps[:, 4 + h, S:W], k.const("lower"), sp_[:, h, S:W], start=True, stop=True)
                last.then_inc(k.products, 1)
            for g, pair in pairs:
                pe.wait_ge(k.activations, a0 + 3 + g)
                for h in (2 * g, 2 * g + 1):
                    c = slice(h % 2 * 64, (h % 2 + 1) * 64)
                    nc.tensor.matmul(k.ps[:, 2 * g, c], z[:, h, 0:P], v(0, h), start=True, stop=True)
                    nc.tensor.matmul(k.ps[:, 2 * g + 1, c], z[:, h, P:S], v(0, h), start=True, stop=False)
                    last = nc.tensor.matmul(k.ps[:, 2 * g + 1, c], z[:, h, S:W], v(1, h), start=False, stop=True)
                last.then_inc(k.products, 1)

        @block.vector
        def _(dve):
            for g, pair in pairs:
                dve.wait_ge(k.products, p0 + 1 + g)
                k.vchain(nc.vector.tensor_scalar(z[:, pair], k.ps[:, pair, 0:W], SB_D ** -0.5, None, ALU.mult))
                softplus_vector(k, dve, z[:, pair], mag[:, pair]).then_inc(k.vectors, 1)
            for g, pair in pairs:
                dve.wait_ge(k.activations, a0 + 1 + g)
                k.vchain(nc.vector.scalar_tensor_tensor(out=sp_[:, pair], in0=z[:, pair], scalar=0.0, in1=mag[:, pair], op0=ALU.max, op1=ALU.add))
                nc.vector.tensor_tensor(sp_[:, pair, 0:P], sp_[:, pair, 0:P], over(k.const("upper_strict"), 2), ALU.mult)
                nc.vector.tensor_tensor(sp_[:, pair, S:W], sp_[:, pair, S:W], over(k.const("upper_strict"), 2), ALU.mult).then_inc(k.vectors, 1)
            for g, pair in pairs:
                dve.wait_ge(k.products, p0 + 3 + g)
                k.vchain(nc.vector.tensor_tensor(z[:, pair], z[:, pair], k.ps[:, 4 + 2 * g:6 + 2 * g, 0:W], ALU.subtract))
                nc.vector.tensor_tensor(z[:, pair, 0:P], z[:, pair, 0:P], over(k.const("neg_not_upper_strict"), 2), ALU.add)
                nc.vector.tensor_tensor(z[:, pair, S:W], z[:, pair, S:W], over(k.const("neg_not_upper_strict"), 2), ALU.add).then_inc(k.vectors, 1)
            for g, pair in pairs:
                dve.wait_ge(k.products, p0 + 5 + g)
                nc.vector.tensor_copy(out[:, :, g * P:(g + 1) * P], k.ps[:, pair, 0:P])

        @block.scalar
        def _(act):
            for g, pair in pairs:
                act.wait_ge(k.vectors, v0 + 1 + g)
                softplus_scalar(k, mag[:, pair]).then_inc(k.activations, 1)
            for g, pair in pairs:
                act.wait_ge(k.vectors, v0 + 5 + g)
                nc.scalar.activation(z[:, pair], z[:, pair], ACT.Exp).then_inc(k.activations, 1)
    k.advance(products=6, vectors=6, activations=4)


def ffn_slot(k, slot):
    return k.ring[:, slot * SLOT:(slot + 1) * SLOT].rearrange("p (g c n) -> p g c n", g=2, n=S)


def ffn_part(k):
    w = k.ins["w_ffn_in_2"][0].rearrange("(c p) (g n) -> p g c n", p=P, g=2)
    return {"w": lambda n: w[:, :, :, bass.ds(n * S, S)], "width": 2 * S, "tiles": FF // S}


class FfnStream(Stream):
    def tile(self, part, n, slot):
        return ffn_slot(self.k, slot), part["w"](n)


def gated_ffn(k, dst, stream, ahead):
    nc = k.nc
    part, = stream.parts
    n_tiles, first, start, free = part["tiles"], part["first_slot"], part["start"], part["copied"]
    s_at = FFC * S
    half = k.ring[:, 2 * SLOT + s_at:2 * SLOT + s_at + 2 * BANK].rearrange("p (u n) -> p u n", u=2)
    silu_done = [k.sem(f"silu_done{u}") for u in range(2)]
    with nc.Block() as block:
        @block.sync
        def _(sp):
            def load(i, u, slot):
                dst, src = stream.tile(part, 2 * i + u, slot)
                sp.wait_ge(k.tile_done[slot], i + (start[slot] + 1))
                sp.dma_start(dst, src).then_inc(k.w_landed[slot], 16)
            each_tile(sp, n_tiles, first, load, skip=stream.skip)
            issue(k, sp, ahead)

        @block.tensor
        def _(pe):
            def multiply(i, u, slot):
                w = ffn_slot(k, slot)
                pe.wait_ge(k.w_landed[slot], i * 16 + 16 * (start[slot] + 1))
                pe.wait_ge(k.psum_free[slot], i + (free[slot] + 1))
                for g in range(2):
                    for n in range(2):
                        for c in range(DC):
                            last = nc.tensor.matmul(k.ps[:, 2 * slot + g, n * S:(n + 1) * S], w[:, g, c, n * P:(n + 1) * P],
                                                    k.hT[:, c, :], start=c == 0, stop=c == DC - 1)
                last.then_inc(k.tile_done[slot], 1)
            each_tile(pe, n_tiles, first, multiply)

        @block.scalar
        def _(act):
            def gate(i, u, slot):
                act.wait_ge(k.tile_done[slot], i + (start[slot] + 2))
                act.wait_ge(k.psum_free[slot], i + (free[slot] + 1))
                nc.scalar.activation(half[:, slot, :], k.ps[:, 2 * slot, :], ACT.Silu).then_inc(silu_done[slot], 1)
            each_tile(act, n_tiles, first, gate)

        @block.vector
        def _(dve):
            def up(i, u, slot):
                dve.wait_ge(silu_done[slot], i + 1)
                nc.vector.tensor_tensor(dst[:, bass.ds(i * (4 * S) + 2 * S * u, 2 * S)], half[:, slot, :], k.ps[:, 2 * slot + 1, :], ALU.mult)\
                    .then_inc(k.psum_free[slot], 1)
            each_tile(dve, n_tiles, first, up)


def second_layer(k):
    nc, w = k.nc, k.ins["w_in_2"]
    stream = Stream(k, [
        chan_part(k, w, 0, 512, 2, 0),
        chan_part(k, w, 1544, 512, 1, 8),
        tok_part(k, w, 1024, 256, 1, 0),
        tok_part(k, w, 1280, 256, 1, 256, ACT.Sigmoid),
        tok_part(k, w, 2056, 256, 1, 512),
        tok_part(k, w, 2312, 512, 6, 768, ACT.Sigmoid),
    ])
    turn(k, k.xn, DC, k.hT, scale=lambda c: k.col("norm_mix_g_2", c), norm_of=k.x, ahead=stream.ahead())
    s = Scratch(k)
    qk = s.take(4 * S).rearrange("p (c s) -> p c s", s=S)
    xa = s.take(2 * S).rearrange("p (c s) -> p c s", s=S)

    def convolve_beside(dve):
        wait_copied(k, dve, stream.parts[0])
        convolve(k, dve, 4, 4, lambda tap, c: k.col("conv_mlstm_w_2", tap * 4 + c), qk)
        dve.sem_inc(k.vectors, 1)
        convolve(k, dve, 0, 2, lambda tap, c: k.col("conv_lru_w_2", tap * 2 + c), xa)

    def silu_behind(act):
        act.wait_ge(k.vectors, k.count["vectors"] + 1)
        nc.scalar.activation(qk, qk, ACT.Silu)
    project(k, k.hT, stream, narrow=(k.narrow_w[:, 64:128].rearrange("p (c n) -> p c n", n=8), k.small[:, :, 0:8], 8),
            vector=convolve_beside, scalar=silu_behind)
    k.advance(vectors=1)
    lru(k, k.hT[:, 0:2, :])
    mlstm(k, k.xn)
    turn(k, k.xn, 2, k.hT[:, 2:4, :])
    stick_breaking(k, k.xn)
    names = ("w_out_lru_2", "w_out_mlstm_2", "w_out_sb_2")
    stream = WideStream(k, [{"lhs": lambda c, n=n: k.hT[:, 2 * n + c, :], "w": k.ins[name][0], "chunks": 2,
                             "out": ("gate_add" if n else "gate_set", k.xn, k.tok[:, :, 768 + n * D:768 + (n + 1) * D])}
                            for n, name in enumerate(names)])
    turn(k, k.xn, 2, k.hT[:, 4:6, :], ahead=stream.ahead())
    project_wide(k, stream)
    stream = WideStream(k, [{"lhs": lambda c: k.hT[:, c, :], "w": k.ins["w_o_2"][0], "chunks": DC, "out": ("add", k.x)}])
    turn(k, k.xn, DC, k.hT, ahead=stream.ahead())
    project_wide(k, stream)

    act = k.ring[:, 2 * SLOT:2 * SLOT + FFC * S]
    stream = FfnStream(k, [ffn_part(k)])
    wide = WideStream(k, [{"lhs": lambda c: act[:, c * S:(c + 1) * S], "w": k.ins["w_ffn_out_2"][0], "chunks": FFC, "out": ("add", k.x)}])
    turn(k, k.xn, DC, k.hT, scale=lambda c: k.col("norm_ffn_g_2", c), norm_of=k.x, ahead=stream.ahead())
    gated_ffn(k, act, stream, wide.ahead())
    project_wide(k, wide)
    norm_rows(k, k.ins["final_norm_g_2"])



def neighbourhood_bias(k, bias):
    nc = k.nc
    rpb = k.ins["na_rpb_3"]
    rows, cols = 2 * NA_ROWS - 1, 2 * NA_COLS - 1
    n_rows = S // GRID
    n = NA_H * S
    mirrored = k.ring[:, 2 * SLOT:2 * SLOT + TT * n]
    v = mirrored.rearrange("p (t h n) -> p t h n", t=TT, h=NA_H)
    p0, v0, a0 = k.starts()
    with nc.Block() as block:
        @block.sync
        def _(sp):
            for r in range(n_rows):
                at = GRID * (1 - r % 2)
                for i in range(n_rows):
                    first = (NA_ROWS - 1 - r + i) * cols + NA_COLS - 1 - (GRID - 1)
                    src = bass.AP(tensor=rpb.tensor, offset=rpb.offset + first, ap=[[1, GRID], [rows * cols, NA_H], [1, GRID]])
                    sp.dma_start(v[at:at + GRID, r // 2, :, i * GRID:(i + 1) * GRID], src).then_inc(k.loads, 16)

        @block.tensor
        def _(pe):
            pe.wait_ge(k.loads, 16 * (k.count["loads"] + n_rows ** 2))
            for b in range(TT * n // BANK):
                last = nc.tensor.matmul(k.ps[:, b, :], k.const("anti"), mirrored[:, b * BANK:(b + 1) * BANK], start=True, stop=True)
            last.then_inc(k.products, 1)

        @block.vector
        def _(dve):
            dve.wait_ge(k.products, p0 + 1)
            nc.vector.tensor_tensor(bias.rearrange("p (m c) -> p m c", c=GRID),
                                    k.ps[:, 0:TT * n // BANK, :].rearrange("p b (m c) -> p (b m) c", c=GRID),
                                    over(k.const("window"), TT * n // GRID), ALU.add)
    k.advance(loads=n_rows ** 2, products=1)


def load_tokens(k, src, dst):
    nc = k.nc
    with nc.Block() as block:
        @block.sync
        def _(sp):
            sp.dma_start(dst, src.rearrange("b (t p) d -> p (b t) d", p=P)).then_inc(k.loads, 16)
            sp.wait_ge(k.loads, 16 * (k.count["loads"] + 1))
    k.advance(loads=1)


def rwkv(k, out):
    nc = k.nc
    N6 = 6 * S

    def chans(at):
        return k.ring[:, at:at + N6].rearrange("p (d s) -> p d s", s=S)
    r, kt, v, b, a = [chans(n * N6) for n in range(5)]
    w_log, L, prod = [chans((5 + n) * N6) for n in range(3)]
    at = 8 * N6
    tmp = k.ring[:, at:at + 10 * S].rearrange("p (c s) -> p c s", s=S)
    at += 10 * S
    lora = k.ring[:, at:at + 2 * RW_W].rearrange("p (d n) -> p d n", d=2)
    at += 2 * RW_W
    lat = k.ring[:, at:at + 2 * S].rearrange("p (d s) -> p d s", d=2)
    at += 2 * S
    g_w = k.ring[:, at:at + RW_W]
    at += RW_W
    lat_g = k.ring[:, at:at + S]
    decay_c = k.stat[:, 0:24].rearrange("p (d j) -> p d j", j=4)
    rk = k.stat[:, 24:48]
    mu_w = PARAM_ROWS["rw_mu_w_3"]
    p0, v0, a0 = k.starts()
    loads0 = k.count["loads"]

    with nc.Block() as block:
        @block.sync
        def _(sp):
            for d in range(2):
                sp.dma_start(lora[0:64, d, :], k.ins["rw_w2_3"][0, d]).then_inc(k.loads, 16)
                sp.dma_start(lora[64:128, d, :], k.ins["rw_a2_3"][0, d]).then_inc(k.loads, 16)
            sp.dma_start(g_w, k.ins["rw_g2_3"][0]).then_inc(k.loads, 16)

        @block.vector
        def _(dve):
            for d in range(2):
                here = k.chan[:, 6:16, PAD:PAD + S]
                there = k.chan[:, 6:16, PAD - 1 + 2 * d:PAD - 1 + 2 * d + S]
                k.vchain(nc.vector.tensor_tensor(tmp, there, here, ALU.subtract))
                for n in range(10):
                    mu = k.col("rw_mu_rkv_3", d * 9 + n) if n < 9 else k.cols[:, 1, mu_w[1] + d:mu_w[1] + d + 1]
                    dst = (r, kt, v)[n // 3][:, 3 * d + n % 3, :] if n < 9 else lat[:, d, :]
                    last = nc.vector.scalar_tensor_tensor(out=dst[:, ::-1] if d else dst, in0=tmp[:, n, :], scalar=mu,
                                                          in1=k.chan[:, 6 + n, PAD:PAD + S], op0=ALU.mult, op1=ALU.add)
                k.vchain(last)
            dve.sem_inc(k.vectors, 1)
            dve.wait_ge(k.activations, a0 + 3)
            k.vchain(nc.vector.tensor_scalar(w_log, w_log, -float(np.exp(-0.5)), None, ALU.mult))
            for n in range(3):
                last = nc.vector.tensor_tensor_scan(L[:, 2 * n:2 * n + 2, :].rearrange("p d s -> p (d s)"), k.const("not_chunk_start"),
                                                    w_log[:, 2 * n:2 * n + 2, :].rearrange("p d s -> p (d s)"), 0.0, ALU.mult, ALU.add)
            k.vchain(last)
            dve.sem_inc(k.vectors, 1)

        @block.scalar
        def _(act):
            nc.scalar.activation(lat_g, k.chan[:, 16, PAD:PAD + S], ACT.Sigmoid).then_inc(k.activations, 1)
            act.wait_ge(k.vectors, v0 + 1)
            nc.scalar.activation(lat[0:64], lat[0:64], ACT.Tanh).then_inc(k.activations, 1)
            act.wait_ge(k.products, p0 + 1)
            for n in range(6):
                c = slice(n % 2 * S, (n % 2 + 1) * S)
                nc.scalar.activation(w_log[:, n, :], k.ps[:, n // 2, c], ACT.Sigmoid, bias=k.col("rw_w0_3", n))
                last = nc.scalar.activation(b[:, n, :], k.ps[:, 4 + n // 2, c], ACT.Sigmoid, bias=k.col("rw_a0_3", n))
            last.then_inc(k.activations, 1)
            for t in range(TT):
                act.wait_ge(k.products, p0 + 2 + t)
                nc.scalar.copy(k.tok[:, t, RW_W:2 * RW_W], k.ps[:, 3 + 4 * t, 0:RW_W])

        @block.tensor
        def _(pe):
            pe.wait_ge(k.loads, 16 * (loads0 + 5))
            pe.wait_ge(k.activations, a0 + 2)
            for d in range(2):
                for c in range(3):
                    n = 3 * d + c
                    cols = slice(n % 2 * S, (n % 2 + 1) * S)
                    nc.tensor.matmul(k.ps[:, n // 2, cols], lora[0:64, d, c * P:(c + 1) * P], lat[0:64, d, :], start=True, stop=True)
                    last = nc.tensor.matmul(k.ps[:, 4 + n // 2, cols], lora[64:128, d, c * P:(c + 1) * P], lat[64:128, d, :], start=True, stop=True)
            last.then_inc(k.products, 1)
            for t in range(TT):
                nc.tensor.matmul(k.ps[:, 3 + 4 * t, 0:RW_W], lat_g[:, t * P:(t + 1) * P], g_w, start=True, stop=True).then_inc(k.products, 1)
    k.advance(products=3, vectors=2, activations=3, loads=5)

    kk = a
    decay = w_log
    tmp6 = tmp[:, 0:6, :]
    p0, v0, a0 = k.starts()
    with nc.Block() as block:
        @block.vector
        def _(dve):
            for n in range(6):
                last = nc.vector.tensor_scalar(kk[:, n, :], kt[:, n, :], k.col("rw_k_k_3", n % 3), None, ALU.mult)
            k.vchain(last)
            nc.vector.tensor_tensor(tmp6, kk, kk, ALU.mult).then_inc(k.vectors, 1)
            for n in range(6):
                last = nc.vector.tensor_scalar(prod[:, n, :], b[:, n, :], -1.0, k.col("rw_k_a_3", n % 3), ALU.add, ALU.mult)
            k.vchain(last)
            k.vchain(nc.vector.scalar_tensor_tensor(out=kt, in0=prod, scalar=1.0, in1=kt, op0=ALU.add, op1=ALU.mult))
            for n in range(6):
                last = nc.vector.scalar_tensor_tensor(out=prod[:, n, :], in0=r[:, n, :], scalar=k.col("rw_r_k_3", n % 3),
                                                      in1=kt[:, n, :], op0=ALU.mult, op1=ALU.mult)
            k.vchain(last)
            dve.sem_inc(k.vectors, 1)
            k.vchain(nc.vector.tensor_tensor(decay, L, w_log, ALU.subtract))
            dve.sem_inc(k.vectors, 1)
            dve.wait_ge(k.products, p0 + 1)
            nc.vector.tensor_scalar(tmp6, k.ps[:, 0:3, :].rearrange("p b (m s) -> p (b m) s", s=S), k.const("tiny"), None, ALU.max).then_inc(k.vectors, 1)
            dve.wait_ge(k.activations, a0 + 1)
            k.vchain(nc.vector.tensor_tensor(kk, kk, tmp6, ALU.mult))
            dve.sem_inc(k.vectors, 1)
            k.vchain(nc.vector.tensor_tensor(b, b, kk, ALU.mult))
            dve.wait_ge(k.activations, a0 + 2)
            nc.vector.scalar_tensor_tensor(out=a, in0=kk, scalar=-1.0, in1=decay, op0=ALU.mult, op1=ALU.mult)
            nc.vector.tensor_tensor(b, b, tmp6, ALU.mult)
            nc.vector.tensor_tensor(kt, kt, tmp6, ALU.mult)
            k.vchain(nc.vector.tensor_tensor(r, r, L, ALU.mult))
            nc.vector.tensor_copy(decay_c.rearrange("p d j -> p (d j)"), L.rearrange("p d (j s) -> p (d j) s", s=64)[:, :, 63])
            dve.wait_ge(k.products, p0 + 2)
            nc.vector.tensor_copy(rk.rearrange("p (h t d) -> p t d h", h=2, t=TT), k.ps[:, 4, 0:24].rearrange("p (t d h) -> p t d h", t=TT, h=2))

        @block.tensor
        def _(pe):
            pe.wait_ge(k.vectors, v0 + 1)
            for n in range(3):
                last = nc.tensor.matmul(k.ps[:, n, :], k.const("half_ones"), tmp[:, 2 * n:2 * n + 2, :].rearrange("p c s -> p (c s)"), start=True, stop=True)
            last.then_inc(k.products, 1)
            pe.wait_ge(k.vectors, v0 + 2)
            for t in range(TT):
                for n in range(6):
                    last = nc.tensor.matmul(k.ps[:, 4, 12 * t + 2 * n:12 * t + 2 * n + 2], prod[:, n, t * P:(t + 1) * P], k.const("half_of"), start=True, stop=True)
            last.then_inc(k.products, 1)

        @block.scalar
        def _(act):
            act.wait_ge(k.vectors, v0 + 4)
            k.achain(nc.scalar.activation(tmp6, tmp6, ACT.Ln, scale=float(2.0 ** 17)))
            nc.scalar.activation(tmp6, tmp6, ACT.Exp, scale=-0.5, bias=k.const("ln_norm_scale")).then_inc(k.activations, 1)
            act.wait_ge(k.vectors, v0 + 3)
            nc.scalar.activation(decay, decay, ACT.Exp)
            act.wait_ge(k.vectors, v0 + 5)
            nc.scalar.activation(tmp6, L, ACT.Exp, scale=-1.0)
            k.achain(nc.scalar.activation(L, L, ACT.Exp))
            act.sem_inc(k.activations, 1)
    k.advance(products=2, vectors=5, activations=2)

    M = 2 * TT * 6
    W = M * 64
    base = 5 * N6
    A_t, X, Y, U, ak, rb, rkm = [k.ring[:, base + n * W:base + (n + 1) * W].rearrange("p (m n) -> p m n", n=64) for n in range(7)]
    base += 7 * W
    a_tok, b_tok, k_tok, v_tok = [k.ring[:, base + n * TT * 768:base + (n + 1) * TT * 768].rearrange("p (d n) -> p d n", n=P) for n in range(4)]
    base += 4 * TT * 768
    assert base <= RING * SLOT
    XA = k.ring[:, N6:2 * N6].rearrange("p (d n) -> p d n", n=P)
    XW, Z, W1 = [k.ring[:, (2 + n) * N6:(3 + n) * N6].rearrange("p (m n) -> p m n", n=64) for n in range(3)]
    flat = k.chan[:, 3:20, :].rearrange("p c s -> p (c s)")
    y = flat[:, 0:W].rearrange("p (m n) -> p m n", n=64)
    bonus = flat[:, W:2 * W].rearrange("p (m n) -> p m n", n=64)
    xn = out.rearrange("p t n -> p (t n)")
    state = [xn[:, n * 384:(n + 1) * 384].rearrange("p (d n) -> p d n", n=64) for n in range(4)]

    def bank_units(first, m, n):
        return k.ps[:, first:first + (m * n + BANK - 1) // BANK, :].rearrange("p b n -> p (b n)")[:, 0:m * n].rearrange("p (m n) -> p m n", n=n)

    def rows64(j):
        return slice(64 * j, 64 * j + 64)

    kinds = [(a, b), (b, a), (kt, a), (b, r), (kt, r)]
    turned_at = (4, 0, 4, 0)
    p0, v0, a0 = k.starts()
    with nc.Block() as block:
        @block.tensor
        def _(pe):
            for n, (lhs, rhs) in enumerate(kinds):
                if n >= 2:
                    pe.wait_ge(k.vectors, v0 + n - 1)
                for half in range(2):
                    for j in range(2):
                        q = rows64(half)
                        for t in range(TT):
                            for dc in range(6):
                                at = 6 * t + dc
                                tk = slice(t * P + 64 * j, t * P + 64 * j + 64)
                                last = nc.tensor.matmul(k.ps[rows64(j), 4 * (n % 2) + 2 * half + at // 8, at % 8 * 64:(at % 8 + 1) * 64],
                                                        lhs[q, dc, tk], rhs[q, dc, tk], start=True, stop=True)
                last.then_inc(k.products, 1)
            for n, src in enumerate((a, b, kt, v)):
                if n < 2:
                    pe.wait_ge(k.vectors, v0 + 4 + n)
                else:
                    pe.wait_ge(k.activations, a0 + n - 1)
                for at in range(TT * 6):
                    last = nc.tensor.transpose(k.ps[:, turned_at[n] + at // 4, at % 4 * P:(at % 4 + 1) * P],
                                               src[:, at % 6, at // 6 * P:(at // 6 + 1) * P], k.const("ident"))
                last.then_inc(k.products, 1)

        @block.vector
        def _(dve):
            def masked(n, dst, scale, mask):
                dve.wait_ge(k.products, p0 + n + 1)
                for half in range(2):
                    last = nc.vector.scalar_tensor_tensor(out=dst[:, 12 * half:12 * half + 12, :], in0=bank_units(4 * (n % 2) + 2 * half, 12, 64),
                                                          scalar=scale, in1=over(mask, 12), op0=ALU.mult, op1=ALU.mult)
                last.then_inc(k.vectors, 1)
            masked(0, X, -1.0, k.const("chunk_level0"))
            masked(1, A_t, -1.0, k.const("chunk_half_upper_strict"))
            masked(2, ak, 1.0, k.const("chunk_half_upper_strict"))
            masked(3, rb, 1.0, k.const("chunk_half_upper"))
            masked(4, rkm, 1.0, k.const("chunk_half_upper"))
            nc.vector.memset(state[0], 0.0)
            dve.wait_ge(k.vectors, v0 + 2)
            k.vchain(nc.vector.tensor_tensor(Y, A_t, over(k.const("chunk_level0_t"), M), ALU.mult))
            nc.vector.tensor_tensor(X, X, over(k.const("chunk_ident"), M), ALU.add)
            nc.vector.tensor_tensor(Y, Y, over(k.const("chunk_ident"), M), ALU.add)

        @block.scalar
        def _(act):
            for n, dst in enumerate((a_tok, b_tok, k_tok, v_tok)):
                act.wait_ge(k.products, p0 + 6 + n)
                nc.scalar.copy(dst, bank_units(turned_at[n], TT * 6, P)).then_inc(k.activations, 1)
    k.advance(products=9, vectors=5, activations=4)

    GROUPS = M // 8
    low, high = slice(0, 32), slice(32, 64)
    p0, v0, a0 = k.starts()
    with nc.Block() as block:
        @block.tensor
        def _(pe):
            def products(bank, lhs, rhs, g):
                for j in range(2):
                    q = rows64(j)
                    for m in range(8):
                        last = nc.tensor.matmul(k.ps[q, bank, m * 64:(m + 1) * 64], lhs[q, 8 * g + m, :], rhs[q, 8 * g + m, :], start=True, stop=True)
                return last
            for n in range(4):
                before = v0 + 2 * GROUPS * n
                for g in range(GROUPS):
                    if n:
                        pe.wait_ge(k.vectors, before - GROUPS + g + 1)
                    products(g, A_t, X, g).then_inc(k.products, 1)
                for g in range(GROUPS):
                    pe.wait_ge(k.vectors, before + g + 1)
                    products(g, Y, U, g)
                    products(GROUPS + g, U, Y, g).then_inc(k.products, 1)

            def block_products(bank, lhs, rhs, g, lhs_cols, rhs_cols, rows, to):
                for j in range(2):
                    q, dst = slice(64 * j + rows, 64 * j + rows + 32), slice(64 * j + to, 64 * j + to + 32)
                    for m in range(8):
                        last = nc.tensor.matmul(k.ps[dst, bank, m * 32:(m + 1) * 32], lhs[q, 8 * g + m, lhs_cols], rhs[q, 8 * g + m, rhs_cols],
                                                start=True, stop=True)
                return last
            before = v0 + 2 * GROUPS * 4
            for g in range(GROUPS):
                pe.wait_ge(k.vectors, before - GROUPS + g + 1)
                block_products(g, A_t, X, g, high, low, 0, 32).then_inc(k.products, 1)
            for g in range(GROUPS):
                pe.wait_ge(k.vectors, before + g + 1)
                block_products(GROUPS + g, U, Y, g, low, high, 32, 0).then_inc(k.products, 1)

        @block.vector
        def _(dve):
            for n in range(4):
                before = p0 + 2 * GROUPS * n
                for g in range(GROUPS):
                    dve.wait_ge(k.products, before + g + 1)
                    nc.vector.tensor_tensor(U[:, 8 * g:8 * g + 8, :], bank_units(g, 8, 64), over(k.const(f"chunk_level{n + 1}"), 8), ALU.mult).then_inc(k.vectors, 1)
                for g in range(GROUPS):
                    dve.wait_ge(k.products, before + GROUPS + g + 1)
                    nc.vector.tensor_tensor(X[:, 8 * g:8 * g + 8, :], X[:, 8 * g:8 * g + 8, :], bank_units(g, 8, 64), ALU.add)
                    nc.vector.tensor_tensor(Y[:, 8 * g:8 * g + 8, :], Y[:, 8 * g:8 * g + 8, :], bank_units(GROUPS + g, 8, 64), ALU.add).then_inc(k.vectors, 1)
            before = p0 + 2 * GROUPS * 4
            for g in range(GROUPS):
                dve.wait_ge(k.products, before + g + 1)
                for j in range(2):
                    q = slice(64 * j + 32, 64 * j + 64)
                    last = nc.vector.tensor_scalar(U[q, 8 * g:8 * g + 8, low], bank_units(g, 8, 32)[q], -1.0, None, ALU.mult)
                last.then_inc(k.vectors, 1)
            for g in range(GROUPS):
                dve.wait_ge(k.products, before + GROUPS + g + 1)
                for j in range(2):
                    q = slice(64 * j, 64 * j + 32)
                    last = nc.vector.tensor_tensor(Y[q, 8 * g:8 * g + 8, high], Y[q, 8 * g:8 * g + 8, high], bank_units(GROUPS + g, 8, 32)[q], ALU.add)
                last.then_inc(k.vectors, 1)
    k.advance(products=2 * GROUPS * 5, vectors=2 * GROUPS * 5)

    p0, v0, a0 = k.starts()
    units = [(half, t, dc) for half in range(2) for t in range(TT) for dc in range(6)]
    STEPS = 2 * TT
    with nc.Block() as block:
        @block.tensor
        def _(pe):
            for j in range(2):
                q = rows64(j)
                for m, (half, t, dc) in enumerate(units):
                    last = nc.tensor.matmul(bank_units(0, M, 64)[q, m, :], ak[q, m, :], v_tok[q, 6 * t + dc, rows64(half)], start=True, stop=True)
            last.then_inc(k.products, 1)
            for j in range(2):
                q = rows64(j)
                for m, (half, t, dc) in enumerate(units):
                    at = 6 * t + dc
                    last = nc.tensor.matmul(k.ps[rows64(half), 4 + 2 * j + at // 8, at % 8 * 64:(at % 8 + 1) * 64],
                                            a_tok[q, at, rows64(half)], Y[q, m, :], start=True, stop=True)
            last.then_inc(k.products, 1)
            pe.wait_ge(k.vectors, v0 + 1)
            for j in range(2):
                q = rows64(j)
                for m in range(M):
                    last = nc.tensor.matmul(bank_units(0, M, 64)[q, m, :], Y[q, m, :], W1[q, m, :], start=True, stop=True)
            last.then_inc(k.products, 1)
            for step in range(STEPS):
                t, j = step // 2, step % 2
                tk = rows64(j)
                pe.wait_ge(k.vectors, v0 + 2 + 2 * step)
                pe.wait_ge(k.activations, a0 + 1 + step)
                for bank, lhs in ((4, XA), (6, r)):
                    for half in range(2):
                        q = rows64(half)
                        for dc in range(6):
                            rows = lhs[q, 6 * t + dc, tk] if bank == 4 else lhs[q, dc, t * P + 64 * j:t * P + 64 * j + 64]
                            last = nc.tensor.matmul(k.ps[tk, bank + half, dc * 64:(dc + 1) * 64], rows, state[step][q, dc, :], start=True, stop=True)
                    last.then_inc(k.products, 1)
                pe.wait_ge(k.vectors, v0 + 3 + 2 * step)
                if step < STEPS - 1:
                    for half in range(2):
                        q = rows64(half)
                        for dc in range(6):
                            nc.tensor.matmul(k.ps[q, 3, dc * 64:(dc + 1) * 64], b_tok[tk, 6 * t + dc, q], Z[tk, 12 * half + 6 * t + dc, :], start=True, stop=False)
                            last = nc.tensor.matmul(k.ps[q, 3, dc * 64:(dc + 1) * 64], k_tok[tk, 6 * t + dc, q], v_tok[tk, 6 * t + dc, q], start=False, stop=True)
                    last.then_inc(k.products, 1)
                for m, (half, t_m, dc) in enumerate(units):
                    if t_m == t:
                        nc.tensor.matmul(bank_units(0, M, 64)[tk, m, :], rb[tk, m, :], Z[tk, m, :], start=True, stop=False)
                        last = nc.tensor.matmul(bank_units(0, M, 64)[tk, m, :], rkm[tk, m, :], v_tok[tk, 6 * t + dc, rows64(half)], start=False, stop=True)
            last.then_inc(k.products, 1)

        @block.vector
        def _(dve):
            dve.wait_ge(k.products, p0 + 1)
            nc.vector.tensor_copy(W1, bank_units(0, M, 64)).then_inc(k.vectors, 1)
            dve.wait_ge(k.products, p0 + 3)
            nc.vector.tensor_copy(XW, bank_units(0, M, 64)).then_inc(k.vectors, 1)
            dve.wait_ge(k.vectors, v0 + 2)
            for step in range(STEPS):
                t, tk = step // 2, rows64(step % 2)
                dve.wait_ge(k.products, p0 + 4 + 3 * step)
                for half in range(2):
                    m = slice(12 * half + 6 * t, 12 * half + 6 * t + 6)
                    last = nc.vector.tensor_tensor(Z[tk, m, :], XW[tk, m, :], k.ps[tk, 4 + half, 0:384].rearrange("p (d n) -> p d n", n=64), ALU.add)
                last.then_inc(k.vectors, 1)
                if step < STEPS - 1:
                    dve.wait_ge(k.products, p0 + 6 + 3 * step)
                    new = state[step + 1]
                    k.vchain(nc.vector.tensor_tensor(new, state[step], k.ps[:, 3, 0:384].rearrange("p (d n) -> p d n", n=64), ALU.add))
                    nc.vector.tensor_tensor(new, new, along(decay_c[:, :, step], 64), ALU.mult).then_inc(k.vectors, 1)
            for half in range(2):
                m = slice(12 * half, 12 * half + 12)
                nc.vector.tensor_tensor(bonus[:, m, :], v_tok[:, :, rows64(half)], along(rk[:, m], 64), ALU.mult)
            dve.wait_ge(k.products, p0 + 3 * STEPS + 3)
            dve.wait_ge(k.activations, a0 + 1 + STEPS)
            nc.vector.tensor_tensor(y, y, bank_units(0, M, 64), ALU.add)

        @block.scalar
        def _(act):
            act.wait_ge(k.products, p0 + 2)
            for j in range(2):
                last = nc.scalar.copy(XA[:, :, rows64(j)], bank_units(4 + 2 * j, 12, 64))
            last.then_inc(k.activations, 1)
            for step in range(STEPS):
                t, tk = step // 2, rows64(step % 2)
                act.wait_ge(k.products, p0 + 5 + 3 * step)
                for half in range(2):
                    last = nc.scalar.copy(y[tk, 12 * half + 6 * t:12 * half + 6 * t + 6, :], k.ps[tk, 6 + half, 0:384].rearrange("p (d n) -> p d n", n=64))
                last.then_inc(k.activations, 1)
    k.advance(products=3 + 3 * STEPS, vectors=1 + 2 * STEPS, activations=1 + STEPS)

    gain = k.ring[:, 0:RW_W]
    offset = k.ring[:, RW_W:2 * RW_W]
    sq = k.ring[:, 2 * RW_W:4 * RW_W].rearrange("p (t n) -> p t n", t=TT)
    extra = k.ring[:, 4 * RW_W:6 * RW_W].rearrange("p (t n) -> p t n", t=TT)
    mean, rstd = k.stat[:, 48:60], k.stat[:, 60:72]
    yo = out[:, :, 0:RW_W]
    p0, v0, a0 = k.starts()
    loads0 = k.count["loads"]
    with nc.Block() as block:
        @block.sync
        def _(sp):
            sp.dma_start(gain, k.ins["rw_ln_g_3"].partition_broadcast(P).rearrange("p a n -> p (a n)")).then_inc(k.loads, 16)
            sp.dma_start(offset, k.ins["rw_ln_b_3"].partition_broadcast(P).rearrange("p a n -> p (a n)")).then_inc(k.loads, 16)

        @block.tensor
        def _(pe):
            for n, src in enumerate((y, bonus)):
                both = src.rearrange("p (h t d c) n -> p t d c h n", h=2, t=TT, d=2)
                for t in range(TT):
                    nc.tensor.matmul(k.ps[:, 2 * n + t, 0:RW_W], k.const("ident"), both[:, t, 0], start=True, stop=False)
                    last = nc.tensor.matmul(k.ps[:, 2 * n + t, 0:RW_W], k.const("anti"), both[:, 1 - t, 1], start=False, stop=True)
            last.then_inc(k.products, 1)

        @block.vector
        def _(dve):
            def heads(ap):
                return ap.rearrange("p (h n) -> p h n", n=64)
            dve.wait_ge(k.products, p0 + 1)
            nc.vector.tensor_copy(extra, k.ps[:, 2:4, 0:RW_W])
            k.vchain(nc.vector.tensor_copy(yo, k.ps[:, 0:2, 0:RW_W]))
            for t in range(TT):
                last = nc.vector.tensor_reduce(mean[:, 6 * t:6 * t + 6], heads(yo[:, t]), AX_X, ALU.add)
            k.vchain(last)
            k.vchain(nc.vector.tensor_scalar(mean, mean, 1.0 / 64, None, ALU.mult))
            for t in range(TT):
                last = nc.vector.tensor_tensor(heads(yo[:, t]), heads(yo[:, t]), along(mean[:, 6 * t:6 * t + 6], 64), ALU.subtract)
            k.vchain(last)
            k.vchain(nc.vector.tensor_tensor(sq, yo, yo, ALU.mult))
            nc.vector.tensor_reduce(rstd, sq.rearrange("p t (h n) -> p (t h) n", n=64), AX_X, ALU.add).then_inc(k.vectors, 1)
            dve.wait_ge(k.activations, a0 + 1)
            dve.wait_ge(k.loads, 16 * (loads0 + 2))
            for t in range(TT):
                last = nc.vector.tensor_tensor(heads(yo[:, t]), heads(yo[:, t]), along(rstd[:, 6 * t:6 * t + 6], 64), ALU.mult)
            k.vchain(last)
            k.vchain(nc.vector.tensor_tensor(yo, yo, over(gain, TT), ALU.mult))
            k.vchain(nc.vector.tensor_tensor(yo, yo, over(offset, TT), ALU.add))
            k.vchain(nc.vector.tensor_tensor(yo, yo, extra, ALU.add))
            nc.vector.tensor_tensor(yo, yo, k.tok[:, :, RW_W:2 * RW_W], ALU.mult)

        @block.scalar
        def _(act):
            act.wait_ge(k.vectors, v0 + 1)
            k.achain(nc.scalar.activation(rstd, rstd, ACT.Ln, bias=k.const("gn_eps"), scale=1.0 / 64))
            nc.scalar.activation(rstd, rstd, ACT.Exp, scale=-0.5).then_inc(k.activations, 1)
    k.advance(products=1, vectors=1, activations=1, loads=2)


def expert_tiles(k):
    def w_in(name, n):
        return lambda e: k.ins[name][0, bass.ds(e, 1), :, n * TILE:(n + 1) * TILE].rearrange("a (c p) n -> p (a c) n", p=P)

    def w_down(n):
        return lambda e: k.ins["w_exp_down_3"][0, bass.ds(e, 1), n * TILE:(n + 1) * TILE, :].rearrange("a (c p) n -> p (a c) n", p=P)
    tiles = []
    for n in range(EFF // TILE):
        tiles += [(w_in("w_exp_gate_3", n), TILE), (w_in("w_exp_up_3", n), TILE)]
    return tiles + [(w_down(n), D) for n in range(EFF // TILE)]


def expert_choice(k):
    nc = k.nc
    turn(k, k.xn, DC, k.hT, scale=lambda c: k.col("norm_ffn_g_3", c), norm_of=k.x)
    tok = k.tok[:, :, :].rearrange("p t n -> p (t n)")
    xeT = tok[:, 0:4096].rearrange("p (c n) -> p c n", c=DC)
    one_hot = tok[:, 4096:5120].rearrange("p (t n) -> p t n", t=TT)
    weighted = tok[:, 5120:6144].rearrange("p (t n) -> p t n", t=TT)
    rows = tok[0:EXP, 6144:6144 + 5 * S].rearrange("p (n s) -> p n s", s=S)
    aff_t, work, chosen, number, ones = [rows[:, n, :] for n in range(5)]
    back = k.chan[:, :, :].rearrange("p c s -> p (c s)")[:, 0:EXP * S].rearrange("p (e s) -> p e s", e=EXP)
    aff = k.stat[:, 0:2 * EXP].rearrange("p (t e) -> p t e", t=TT)
    pos = k.stat[:, 32:32 + 2 * EXP].rearrange("p (t e) -> p t e", t=TT)
    top, total = k.stat[:, 64:66], k.stat[:, 66:68]
    best = k.stat[0:EXP, 72:80]
    router = k.narrow_w[:, 128:256].rearrange("p (c n) -> p c n", n=EXP)
    tiles = expert_tiles(k)
    n_tiles = len(tiles)
    base = list(k.tiles)
    first = n_tiles // RING

    refills = k.sem("refills")

    def load(sp, e, q, before):
        src, width = tiles[q]
        u = q % RING
        dst = k.ring[:, u * SLOT:(u + 1) * SLOT].rearrange("p (c n) -> p c n", n=width)
        sp.wait_ge(k.tile_done[u], before)
        sp.sem_inc(refills, 1)
        sp.dma_start(dst, src(e)).then_inc(k.w_landed[u], 16)

    p0, v0, a0 = k.starts()
    with nc.Block() as block:
        @block.sync
        def _(sp):
            for q in range(RING):
                load(sp, 0, q, base[q] + 1)

        @block.tensor
        def _(pe):
            for t in range(TT):
                for c in range(DC):
                    last = nc.tensor.matmul(k.ps[:, 0, t * EXP:(t + 1) * EXP], k.hT[:, c, t * P:(t + 1) * P], router[:, c, :],
                                            start=c == 0, stop=c == DC - 1)
            last.then_inc(k.products, 1)
            pe.wait_ge(k.vectors, v0 + 2)
            for t in range(TT):
                last = nc.tensor.transpose(k.ps[0:EXP, 1, t * P:(t + 1) * P], aff[:, t, :], k.const("ident"))
            last.then_inc(k.products, 1)
            pe.wait_ge(k.vectors, v0 + 3)
            for t in range(TT):
                last = nc.tensor.transpose(k.ps[:, 2, t * EXP:(t + 1) * EXP], number[:, t * P:(t + 1) * P], k.const("ident")[0:EXP, 0:EXP])
            last.then_inc(k.products, 1)

        @block.scalar
        def _(act):
            act.wait_ge(k.vectors, v0 + 1)
            nc.scalar.activation(aff, aff, ACT.Exp).then_inc(k.activations, 1)

        @block.vector
        def _(dve):
            nc.vector.memset(ones, 1.0)
            dve.wait_ge(k.products, p0 + 1)
            k.vchain(nc.vector.tensor_copy(aff, k.ps[:, 0, 0:2 * EXP].rearrange("p (t e) -> p t e", t=TT)))
            k.vchain(nc.vector.tensor_reduce(top, aff, AX_X, ALU.max))
            nc.vector.tensor_tensor(aff, aff, along(top, EXP), ALU.subtract).then_inc(k.vectors, 1)
            dve.wait_ge(k.activations, a0 + 1)
            k.vchain(nc.vector.tensor_reduce(total, aff, AX_X, ALU.add))
            k.vchain(nc.vector.reciprocal(total, total))
            nc.vector.tensor_tensor(aff, aff, along(total, EXP), ALU.mult).then_inc(k.vectors, 1)
            dve.wait_ge(k.products, p0 + 2)
            k.vchain(nc.vector.tensor_copy(aff_t, k.ps[0:EXP, 1, 0:S]))
            for n in range(CAP // 8):
                src = aff_t if n == 0 else work
                k.vchain(nc.vector.max(best, src))
                k.vchain(nc.vector.match_replace(work, best, src, -1.0))
            k.vchain(nc.vector.tensor_scalar(chosen, work, 0.0, None, ALU.is_lt))
            k.vchain(nc.vector.tensor_tensor_scan(number, ones, chosen, 0.0, ALU.mult, ALU.add))
            k.vchain(nc.vector.tensor_tensor(number, number, chosen, ALU.mult))
            nc.vector.tensor_scalar(number, number, -1.0, None, ALU.add).then_inc(k.vectors, 1)
            dve.wait_ge(k.products, p0 + 3)
            k.vchain(nc.vector.tensor_copy(pos, k.ps[:, 2, 0:2 * EXP].rearrange("p (t e) -> p t e", t=TT)))
            for t in range(TT):
                hot = one_hot[:, t, :].rearrange("p (e j) -> p e j", e=EXP)
                last = nc.vector.tensor_tensor(hot, over(k.const("slot_number"), EXP), along(pos[:, t, :], CAP), ALU.is_equal)
            k.vchain(last)
            for t in range(TT):
                hot = one_hot[:, t, :].rearrange("p (e j) -> p e j", e=EXP)
                nc.vector.tensor_tensor(weighted[:, t, :].rearrange("p (e j) -> p e j", e=EXP), hot, along(aff[:, t, :], CAP), ALU.mult)
    k.advance(products=3, vectors=3, activations=1)

    p0, v0, a0 = k.starts()
    order = [2, 3, 4, 5, 6, 7, 0, 1]
    even, odd = order[0::2], order[1::2]
    turned_w = k.hT[:, 0:4, :]
    with nc.Block() as block:
        @block.tensor
        def _(pe):
            for g in range(4):
                for t in range(TT):
                    last = nc.tensor.transpose(k.ps[:, g // 2, g % 2 * S + t * P:g % 2 * S + (t + 1) * P],
                                               weighted[:, t, g * P:(g + 1) * P], k.const("ident"))
            last.then_inc(k.products, 1)
            for c in order:
                if c == 0:
                    pe.wait_ge(k.vectors, v0 + 1)
                for t in range(TT):
                    last = nc.tensor.matmul(k.ps[:, c, :], k.xn[:, t, c * P:(c + 1) * P], one_hot[:, t, :], start=t == 0, stop=t == TT - 1)
                last.then_inc(k.products, 1)
            for n in order:
                if n % 2:
                    pe.wait_ge(k.activations, a0 + odd.index(n) + 1)
                else:
                    pe.wait_ge(k.vectors, v0 + even.index(n) + 2)
                for e in (2 * n, 2 * n + 1):
                    last = nc.tensor.matmul(k.ps[:, n, e % 2 * S:(e % 2 + 1) * S], k.const(f"four_times{e % 4}"), turned_w[:, e // 4, :], start=True, stop=True)
                last.then_inc(k.products, 1)

        @block.vector
        def _(dve):
            dve.wait_ge(k.products, p0 + 1)
            nc.vector.tensor_copy(turned_w.rearrange("p g s -> p (g s)"), k.ps[:, 0:2, :].rearrange("p b n -> p (b n)")).then_inc(k.vectors, 1)
            for c in even:
                dve.wait_ge(k.products, p0 + 2 + order.index(c))
                nc.vector.tensor_scalar(xeT[:, c, :], k.ps[:, c, :], k.col("norm_ffn_g_3", c), None, ALU.mult).then_inc(k.vectors, 1)
            for n in even:
                dve.wait_ge(k.products, p0 + 2 + DC + order.index(n))
                nc.vector.tensor_copy(back[:, 2 * n:2 * n + 2, :].rearrange("p e s -> p (e s)"), k.ps[:, n, :])

        @block.scalar
        def _(act):
            for c in odd:
                act.wait_ge(k.products, p0 + 2 + order.index(c))
                nc.scalar.activation(xeT[:, c, :], k.ps[:, c, :], ACT.Copy, scale=k.col("norm_ffn_g_3", c)).then_inc(k.activations, 1)
            for n in odd:
                act.wait_ge(k.products, p0 + 2 + DC + order.index(n))
                nc.scalar.copy(back[:, 2 * n:2 * n + 2, :].rearrange("p e s -> p (e s)"), k.ps[:, n, :])
    k.advance(products=2 * DC + 1, vectors=DC // 2 + 1, activations=DC // 2)

    hT = k.hT[:, :, :].rearrange("p c s -> p (c s)")
    xn = k.xn[:, :, :].rearrange("p t n -> p (t n)")
    part = [[hT[:, (2 * g + n) * TILE:(2 * g + n + 1) * TILE] for n in range(2)] for g in range(2)]
    y = xn[:, 0:D]
    xe = xn[:, D:D + DC * CAP].rearrange("p (c n) -> p c n", c=DC)
    act_t = xn[:, D + 256:D + 256 + EFF // P * CAP].rearrange("p (f n) -> p f n", n=CAP)
    gated = xn[:, D + 768:D + 768 + 4 * CAP]
    way = tok[:, 4096:4096 + S]
    zeros = tok[:, 4608:4608 + BANK]
    xe_ready = k.sem("expert_tokens_ready")
    last_up = (2 * (EFF // TILE) - 1) % RING
    way_ready, way_used = k.sem("way_back_ready"), k.sem("way_back_used")
    gate_copied, up_copied = k.sem("gate_copied"), k.sem("up_copied")
    turned, silu, hidden = k.sem("turned"), k.sem("silu"), k.sem("hidden")
    y_done, y_copied0, y_copied1 = k.sem("y_done"), k.sem("y_copied0"), k.sem("y_copied1")
    zeroed = k.sem("zeroed")
    NG = EFF // TILE
    with nc.Block() as block:
        @block.sync
        def _(sp):
            with sp.Fori(0, EXP - 1) as e:
                for q in range(RING, n_tiles + RING):
                    u, turn_of_ring = q % RING, q // RING
                    load(sp, e if q < n_tiles else e + 1, q % n_tiles, e * first + (base[u] + 1 + turn_of_ring))
            for q in range(RING, n_tiles):
                load(sp, EXP - 1, q, (EXP - 1) * first + base[q % RING] + 1 + q // RING)

        @block.gpsimd
        def _(pool):
            nc.gpsimd.memset(zeros, 0.0).then_inc(zeroed, 1)
            nc.gpsimd.tensor_copy(xe, xeT[:, :, 0:CAP]).then_inc(xe_ready, 1)
            nc.gpsimd.tensor_copy(way, back[:, 0, :]).then_inc(way_ready, 1)
            with pool.Fori(1, EXP) as e:
                pool.wait_ge(k.tile_done[last_up], e * first + (base[last_up] + 1))
                nc.gpsimd.tensor_copy(xe, xeT[:, :, bass.ds(e * CAP, CAP)]).then_inc(xe_ready, 1)
                pool.wait_ge(way_used, e)
                nc.gpsimd.tensor_copy(way, back[:, bass.ds(e, 1), :].rearrange("p e s -> p (e s)")).then_inc(way_ready, 1)

        @block.tensor
        def _(pe):
            pe.wait_ge(zeroed, 1)
            for b in range(4):
                nc.tensor.matmul(k.ps[:, b, :], zeros[:, 0:P], zeros, start=True, stop=True, skip_group_check=True)
            for sem in (gate_copied, up_copied, y_copied0, y_copied1):
                pe.sem_inc(sem, 1)

            def slot(q, width):
                u = q % RING
                return k.ring[:, u * SLOT:(u + 1) * SLOT].rearrange("p (c n) -> p c n", n=width)

            def landed(e, q):
                u = q % RING
                pe.wait_ge(k.w_landed[u], e * (16 * first) + 16 * (base[u] + 1 + q // RING))

            def gate_up(e, n):
                for g, copied in enumerate((gate_copied, up_copied)):
                    landed(e, 2 * n + g)
                    pe.wait_ge(copied, e * NG + (n + 1))
                    if n == 0:
                        pe.wait_ge((y_copied0, y_copied1)[g], e + 1)
                    for half in range(2):
                        for j in range(4):
                            c = 4 * half + j
                            last = nc.tensor.matmul(k.ps[32 * j:32 * j + 32, 4 + g, :], xe[:, c, :], slot(2 * n + g, TILE)[:, c, :],
                                                    start=half == 0, stop=half == 1)
                    last.then_inc(k.tile_done[(2 * n + g) % RING], 1)

            def turn_part(e, n):
                pe.wait_ge(gate_copied, e * NG + (n + 2))
                pe.wait_ge(up_copied, e * NG + (n + 2))
                if n >= 2:
                    pe.wait_ge(hidden, e * NG + (n - 1))
                for g in range(2):
                    for i in range(4):
                        last = nc.tensor.matmul(k.ps[:, 6 + n % 2, (4 * g + i) * CAP:(4 * g + i + 1) * CAP], part[g][n % 2][:, i * P:(i + 1) * P],
                                                k.const("four_idents"), start=True, stop=True)
                last.then_inc(turned, 1)

            with pe.Fori(0, EXP) as e:
                pe.wait_ge(xe_ready, e + 1)
                gate_up(e, 0)
                for n in range(1, NG):
                    gate_up(e, n)
                    turn_part(e, n - 1)
                turn_part(e, NG - 1)
                for n in range(NG):
                    pe.wait_ge(hidden, e * NG + (n + 1))
                    landed(e, 2 * NG + n)
                    for h in range(2):
                        for j in range(4):
                            last = nc.tensor.matmul(k.ps[32 * j:32 * j + 32, 4 + h, :], act_t[:, 4 * n + j, :],
                                                    slot(2 * NG + n, D)[:, j, h * BANK:(h + 1) * BANK], start=n == 0, stop=n == NG - 1)
                    last.then_inc(k.tile_done[(2 * NG + n) % RING], 1)
                pe.wait_ge(way_ready, e + 1)
                for h in range(2):
                    pe.wait_ge((y_copied0, y_copied1)[h], e + 2)
                    for t in range(TT):
                        last = nc.tensor.matmul(k.ps[:, 2 * t + h, :], way[:, t * P:(t + 1) * P], y[:, h * BANK:(h + 1) * BANK],
                                                start=False, stop=True, skip_group_check=True)
                last.then_inc(way_used, 1)

        @block.scalar
        def _(act):
            with act.Fori(0, EXP) as e:
                def copy(n):
                    u = (2 * n) % RING
                    act.wait_ge(k.tile_done[u], e * first + (base[u] + 2 + 2 * n // RING))
                    if n >= 2:
                        act.wait_ge(turned, e * NG + (n - 1))
                    nc.scalar.copy(part[0][n % 2], k.ps[:, 4, :]).then_inc(gate_copied, 1)

                def gate(n):
                    act.wait_ge(turned, e * NG + (n + 1))
                    if n:
                        act.wait_ge(hidden, e * NG + n)
                    nc.scalar.activation(gated, k.ps[:, 6 + n % 2, 0:4 * CAP], ACT.Silu).then_inc(silu, 1)
                copy(0)
                for n in range(1, NG):
                    copy(n)
                    gate(n - 1)
                gate(NG - 1)
                u = (3 * NG - 1) % RING
                act.wait_ge(k.tile_done[u], e * first + (base[u] + 2 + (3 * NG - 1) // RING))
                nc.scalar.copy(y[:, 0:BANK], k.ps[:, 4, :]).then_inc(y_copied0, 1)

        @block.vector
        def _(dve):
            with dve.Fori(0, EXP) as e:
                def copy(n):
                    u = (2 * n + 1) % RING
                    dve.wait_ge(k.tile_done[u], e * first + (base[u] + 2 + (2 * n + 1) // RING))
                    if n >= 2:
                        dve.wait_ge(turned, e * NG + (n - 1))
                    nc.vector.tensor_copy(part[1][n % 2], k.ps[:, 5, :]).then_inc(up_copied, 1)

                def gate(n):
                    dve.wait_ge(silu, e * NG + (n + 1))
                    nc.vector.tensor_tensor(act_t[:, 4 * n:4 * n + 4, :].rearrange("p f n -> p (f n)"), gated, k.ps[:, 6 + n % 2, 4 * CAP:8 * CAP], ALU.mult)\
                        .then_inc(hidden, 1)
                copy(0)
                for n in range(1, NG):
                    copy(n)
                    gate(n - 1)
                gate(NG - 1)
                u = (3 * NG - 1) % RING
                dve.wait_ge(k.tile_done[u], e * first + (base[u] + 2 + (3 * NG - 1) // RING))
                nc.vector.tensor_copy(y[:, BANK:D], k.ps[:, 5, :]).then_inc(y_copied1, 1)
            dve.wait_ge(way_used, EXP)
            for t in range(TT):
                nc.vector.tensor_tensor(k.x[:, t, :], k.x[:, t, :], k.ps[:, 2 * t:2 * t + 2, :].rearrange("p b n -> p (b n)"), ALU.add)
    for u in range(RING):
        k.tiles[u] += first * EXP


def third_layer(k):
    nc, w = k.nc, k.ins["w_in_3"]
    stream = Stream(k, [
        chan_part(k, w, 0, 384, 2, 0),
        chan_part(k, w, 1152, 384, 3, 6),
        chan_part(k, w, 2304, 512, 1, 15),
        tok_part(k, w, 768, 384, 1, 0),
        tok_part(k, w, 2816, 512, 6, 768, ACT.Sigmoid),
    ])
    turn(k, k.xn, DC, k.hT, scale=lambda c: k.col("norm_mix_g_3", c), norm_of=k.x, ahead=stream.ahead())
    project(k, k.hT, stream)

    def heads(chunk):
        return lambda h: k.chan[64 * (h % 2):64 * (h % 2) + 64, chunk + h // 2, PAD:PAD + S]

    def values(at):
        return lambda t, h: k.tok[:, t, at + h * HD:at + (h + 1) * HD]
    n = TT * NA_H * S
    bias = k.ring[:, RING * SLOT - n:RING * SLOT]
    neighbourhood_bias(k, bias)
    by_tile = bias.rearrange("p (t h n) -> p t h n", t=TT, h=NA_H)
    attention(k, NA_H, heads(0), heads(3), values(0), HD ** -0.5, lambda t: by_tile[:, t], k.xn)
    turn(k, k.xn, 3, k.chan[:, 0:3, PAD:PAD + S])
    mem = k.ring[:, 2 * SLOT:2 * SLOT + TT * D].rearrange("p (t n) -> p t n", t=TT)
    load_tokens(k, k.ins["mem_3"], mem)
    stream = Stream(k, [chan_part(k, k.ins["w_mem_kv_3"], 0, 256, 1, 3), tok_part(k, k.ins["w_mem_kv_3"], 256, 256, 1, 0)])
    turn(k, k.xn, DC, k.hT, scale=lambda c: k.col("norm_mem_g_3", c), norm_of=mem, ahead=stream.ahead())
    project(k, k.hT, stream)
    attention(k, MEM_H, heads(17), heads(3), values(0), HD ** -0.5, None, k.xn)
    turn(k, k.xn, 2, k.hT[:, 6:8, :])
    rwkv(k, k.xn)
    stream = WideStream(k, [
        {"lhs": lambda c: k.chan[:, c, PAD:PAD + S], "w": k.ins["w_branch_na_3"][0], "chunks": 3, "out": ("gate_set", k.xn, k.tok[:, :, 768:1792])},
        {"lhs": lambda c: k.hT[:, 3 + c, :], "w": k.ins["w_branch_rw_3"][0], "chunks": 3, "out": ("gate_add", k.xn, k.tok[:, :, 1792:2816])},
        {"lhs": lambda c: k.hT[:, 6 + c, :], "w": k.ins["w_branch_mem_3"][0], "chunks": 2, "out": ("gate_add", k.xn, k.tok[:, :, 2816:3840])},
    ])
    turn(k, k.xn, 3, k.hT[:, 3:6, :], ahead=stream.ahead())
    project_wide(k, stream)
    stream = WideStream(k, [{"lhs": lambda c: k.hT[:, c, :], "w": k.ins["w_out_3"][0], "chunks": DC, "out": ("add", k.x)}])
    turn(k, k.xn, DC, k.hT, ahead=stream.ahead())
    project_wide(k, stream)
    expert_choice(k)
    norm_rows(k, k.ins["norm_final_g_3"])


def norm_rows(k, gain_row):
    nc = k.nc
    s = Scratch(k)
    gain = s.take(D)
    squares = s.take(TT * D).rearrange("p (t n) -> p t n", t=TT)
    sums, rstd = k.stat[:, 0:2], k.stat[:, 2:4]
    p0, v0, a0 = k.starts()
    with nc.Block() as block:
        @block.sync
        def _(sp):
            sp.dma_start(gain, gain_row.partition_broadcast(P)).then_inc(k.loads, 16)

        @block.scalar
        def _(act):
            for t in range(TT):
                last = nc.scalar.activation(squares[:, t, :], k.x[:, t, :], ACT.Square, accum_out=sums[:, t:t + 1])
            k.achain(last)
            k.achain(nc.scalar.activation(rstd, sums, ACT.Ln, bias=k.const("eps"), scale=1.0 / D))
            nc.scalar.activation(rstd, rstd, ACT.Exp, scale=-0.5).then_inc(k.activations, 1)

        @block.vector
        def _(dve):
            dve.wait_ge(k.activations, a0 + 1)
            dve.wait_ge(k.loads, 16 * (k.count["loads"] + 1))
            for t in range(TT):
                nc.vector.scalar_tensor_tensor(out=k.x[:, t, :], in0=k.x[:, t, :], scalar=rstd[:, t:t + 1], in1=gain, op0=ALU.mult, op1=ALU.mult)
    k.advance(activations=1, loads=1)


def store(k, out):
    nc = k.nc
    stored = k.sem("stored")
    with nc.Block() as block:
        @block.sync
        def _(sp):
            sp.dma_start(out.rearrange("b (t p) d -> p (b t) d", p=P), k.x[:, :, :]).then_inc(stored, 16)
            sp.wait_ge(stored, 16)


def program(nc, x, ins, out):
    with ExitStack() as ctx:
        k = Chip(nc, ctx, ins)
        load_parameters(k, x)
        if 1 in BLOCKS:
            first_layer(k)
        if 2 in BLOCKS:
            second_layer(k)
        if 3 in BLOCKS:
            third_layer(k)
        store(k, out)


def kernel(**inputs):
    import concourse.bacc as bacc
    from concourse.bass_utils import run_bass_kernel_spmd as run

    nc = bacc.Bacc("TRN2", target_bir_lowering=False, num_devices=1)
    arrays = {name: np.ascontiguousarray(a) for name, a in inputs.items()}
    arrays["constants"] = np.concatenate(list(constant_tables().values()), axis=1)
    aps = {name: nc.dram_tensor(f"in_{name}", a.shape, mybir.dt.from_np(a.dtype), kind="ExternalInput").ap()
           for name, a in arrays.items()}
    out = nc.dram_tensor("out", (1, S, D), F32, kind="ExternalOutput").ap()
    program(nc, aps["x"], aps, out)
    r = run(nc, [{f"in_{name}": a for name, a in arrays.items()}], core_ids=[0])
    return r.results[0]["out"]
```

```python
from contextlib import ExitStack

import concourse.bass as bass
from concourse import mybir
import numpy as np

F32 = mybir.dt.float32
ALU = mybir.AluOpType
ACT = mybir.ActivationFunctionType
AX_X = mybir.AxisListType.X

P = 128
S = 256
TT = S // P
D = 1024
DC = D // P
BANK = 512
TILE = 512
RING = 6
SLOT = DC * TILE
PAD = 4
CHW = PAD + S + PAD
NEG = -1.0e30
EPS = 1e-6

DN_H, DN_D = 4, 128
MB_H, MB_D = 8, 64
LRU_W = 256
ML_H, ML_D = 4, 64
SB_H, SB_D = 4, 64
FF = ((8 * D // 3 + 255) // 256) * 256
FFC = FF // P
NA_H, RW_H, MEM_H, HD = 6, 6, 4, 64
RW_W = RW_H * HD
RW_M = RW_H * 2 * TT
GRID = 64
NA_ROWS, NA_COLS = 8, 16
EXP, CAP, EFF = 16, 2 * S // 16, 2 * D



def constant_tables():
    p = np.arange(P)[:, None]
    f = np.arange(P)[None, :]
    tables = {
        "ident": p == f,
        "anti": p + f == P - 1,
        "ones": np.ones((P, P)),
        "upper": p <= f,
        "lower": p >= f,
        "lower_strict": p > f,
        "upper_strict": p < f,
        "half_ones": p // 64 == f // 64,
        "half_upper_strict": (p < f) & (p // 64 == f // 64),
        "half_upper": (p <= f) & (p // 64 == f // 64),
        "half_of": p // 64 == np.arange(2)[None, :],
        "neg_not_lower": np.where(p >= f, 0.0, NEG),
        "neg_not_upper": np.where(p <= f, 0.0, NEG),
        "neg_not_upper_strict": np.where(p < f, 0.0, NEG),
        "causal": np.concatenate([np.where(np.arange(S)[None, :] <= p + t * P, 0.0, NEG) for t in range(TT)], 1),
        "not_chunk_start": np.broadcast_to((np.arange(2 * S) % 64 != 0)[None, :], (P, 2 * S)),
        "slot_number": np.broadcast_to(np.arange(CAP)[None, :], (P, CAP)),
        "four_idents": p % CAP == np.arange(CAP)[None, :],
        "eps": np.full((P, 1), EPS),
        "log_scale": np.full((P, 1), -0.5 * np.log(DN_D)),
        "gn_eps": np.full((P, 1), 64e-5),
        "ln_norm_scale": np.full((P, 1), 0.5 * 17 * np.log(2.0)),
        "tiny": np.full((P, 1), 1e-24),
    }
    for n in range(7):
        b = 1 << n
        m = (p // (2 * b) == f // (2 * b)) & ((p // b) % 2 == 1) & ((f // b) % 2 == 0)
        tables[f"level{n}"] = -1.0 * m
    tables["level0_t"] = tables["level0"].T
    for name in ("ident", "half_upper_strict", "half_upper", "level0_t", *(f"level{n}" for n in range(5))):
        tables["chunk_" + name] = tables[name] * 1.0 @ (p % 64 == np.arange(64)[None, :])
    del tables["half_upper_strict"], tables["half_upper"]
    for n in range(4):
        tables[f"four_times{n}"] = p == CAP * n + f % CAP
    w = p % GRID
    start = np.clip(w - NA_COLS // 2, 0, GRID - NA_COLS)
    c = np.arange(GRID)[None, :]
    tables["window"] = np.where((c >= start) & (c < start + NA_COLS), 0.0, NEG)
    return {name: np.asarray(t, np.float32) for name, t in tables.items()}


def constant_places():
    at, places = 0, {}
    for name, t in constant_tables().items():
        places[name] = (at, t.shape[1])
        at += t.shape[1]
    return places, at


PARAM_ROWS = {
    "c": (0, 0, 8, 0, 128), "b_ada": (0, 8, 24, 0, 128), "g_pre": (0, 32, 8, 0, 128),
    "norm_mix_g_2": (0, 40, 8, 0, 128), "norm_ffn_g_2": (0, 48, 8, 0, 128),
    "norm_mix_g_3": (0, 56, 8, 0, 128), "norm_mem_g_3": (0, 64, 8, 0, 128),
    "norm_ffn_g_3": (0, 72, 8, 0, 128), "conv_w": (0, 80, 48, 0, 128),
    "conv_lru_w_2": (1, 0, 8, 0, 128), "conv_mlstm_w_2": (1, 8, 16, 0, 128),
    "lru_ba_2": (1, 24, 2, 0, 128), "lru_bx_2": (1, 26, 2, 0, 128), "lru_lambda_2": (1, 28, 2, 0, 128),
    "rw_mu_rkv_3": (1, 30, 18, 0, 128), "rw_w0_3": (1, 48, 6, 0, 128), "rw_a0_3": (1, 54, 6, 0, 128),
    "rw_k_k_3": (1, 60, 3, 0, 128), "rw_k_a_3": (1, 63, 3, 0, 128), "rw_r_k_3": (1, 66, 3, 0, 128),
    "rw_mu_w_3": (1, 69, 2, 0, 64), "rw_mu_a_3": (1, 69, 2, 64, 64),
}


class Chain:

    def __init__(self, engine, sem):
        self.engine, self.sem, self.n = engine, sem, 0

    def __call__(self, instruction):
        self.n += 1
        instruction.then_inc(self.sem, 1)
        self.engine.wait_ge(self.sem, self.n)


class Chip:

    def __init__(self, nc, ctx, ins):
        self.nc, self.ins = nc, ins

        def sb(name, *shape):
            return ctx.enter_context(nc.sbuf_tensor(name, [P, *shape], F32))

        self.places, width = constant_places()
        self.constants = sb("constants", width)
        self.ring = sb("ring", RING * SLOT)
        self.chan = sb("chan", 20, CHW)
        self.tok = sb("tok", TT, 3840)
        self.small = sb("small", TT, 16)
        self.x = sb("x", TT, D)
        self.xn = sb("xn", TT, D)
        self.hT = sb("hT", DC, S)
        self.param_rows = sb("param_rows", 2, P)
        self.cols = sb("cols", 2, P)
        self.mod = sb("mod", 24)
        self.narrow_w = sb("narrow_w", 2 * 8 * 8 + 8 * 16)
        self.rows_bc = sb("rows_bc", 32)
        self.stat = sb("stat", 128)
        self.ps = ctx.enter_context(nc.psum_tensor("ps", [P, 8, BANK], F32))

        def sem(name):
            return ctx.enter_context(nc.semaphore(name))

        self.sem = sem
        self.params_landed = sem("params_landed")
        self.x_landed = sem("x_landed")
        self.w_landed = [sem(f"w_landed{u}") for u in range(RING)]
        self.tile_done = [sem(f"tile_done{u}") for u in range(RING)]
        self.psum_free = [sem(f"psum_free{u}") for u in range(2)]
        self.tiles = [0] * RING
        self.copied = [0] * 2
        self.next_slot = 0
        self.products = sem("products")
        self.vectors = sem("vectors")
        self.activations = sem("activations")
        self.pools = sem("pools")
        self.loads = sem("loads")
        self.count = {"products": 0, "vectors": 0, "activations": 0, "pools": 0, "loads": 0}
        self.inverse_products = sem("inverse_products")
        self.inverse_updates = sem("inverse_updates")
        self.inverses = 0
        self.vchain = Chain(nc.vector, sem("vector_chain"))
        self.achain = Chain(nc.scalar, sem("scalar_chain"))

    def const(self, name):
        at, n = self.places[name]
        return self.constants[:, at:at + n]

    def col(self, name, n=0):
        group, row, _, _, _ = PARAM_ROWS[name]
        return self.cols[:, group, row + n:row + n + 1]

    def starts(self):
        return self.count["products"], self.count["vectors"], self.count["activations"]

    def advance(self, **steps):
        for name, n in steps.items():
            self.count[name] += n


class Scratch:

    def __init__(self, k, first_slot=2):
        self.k, self.at, self.end = k, first_slot * SLOT, RING * SLOT

    def take(self, n):
        a = self.k.ring[:, self.at:self.at + n]
        self.at += n
        assert self.at <= self.end
        return a


def over(ap, n):
    return ap.unsqueeze(1).broadcast_to([ap.shape[0], n, ap.shape[1]])


def along(ap, n):
    return ap.unsqueeze(2).broadcast_to([ap.shape[0], ap.shape[1], n])



def load_parameters(k, x):
    nc, ins = k.nc, k.ins
    with nc.Block() as block:
        loads = [(k.constants[:, :], ins["constants"]), (k.x[:, :, :], x.rearrange("b (t p) d -> p (b t) d", p=P))]
        for name, (g, row, n, at, m) in PARAM_ROWS.items():
            flat = ins[name].rearrange({1: "a -> a", 2: "a b -> (a b)", 3: "a b c -> (a b c)", 4: "a b c d -> (a b c d)"}[len(ins[name].shape)])
            loads.append((k.param_rows[row:row + n, g, at:at + m], flat.rearrange("(n m) -> n m", m=m)))
        w1 = ins["w_in"][0, :, 2048:2056].rearrange("(c p) n -> p c n", p=P)
        w2 = ins["w_in_2"][0, :, 1536:1544].rearrange("(c p) n -> p c n", p=P)
        w3 = ins["w_router_3"][0].rearrange("(c p) n -> p c n", p=P)
        loads.append((k.narrow_w[:, 0:64].rearrange("p (c n) -> p c n", n=8), w1))
        loads.append((k.narrow_w[:, 64:128].rearrange("p (c n) -> p c n", n=8), w2))
        loads.append((k.narrow_w[:, 128:256].rearrange("p (c n) -> p c n", n=16), w3))
        for n, name in enumerate(("a_log", "dt_bias", "mlstm_ig_b_2", "mlstm_fg_b_2")):
            loads.append((k.rows_bc[:, 4 * n:4 * n + 4], ins[name].partition_broadcast(P).rearrange("p a n -> p (a n)")))

        small = loads[0:1] + loads[2:]

        @block.gpsimd
        def _(pool):
            nc.gpsimd.memset(k.param_rows[:, :, :], 0.0).then_inc(k.pools, 1)
            nc.gpsimd.memset(k.chan[:, :, :], 0.0)

        @block.sync
        def _(sp):
            def load_w(u):
                dst = k.ring[:, u * SLOT:(u + 1) * SLOT].rearrange("p (c n) -> p c n", n=TILE)
                sp.dma_start(dst, columns(ins["w_ada"], 0, TILE)(u)).then_inc(k.w_landed[u], 16)
            load_w(0)
            sp.wait_ge(k.pools, 1)
            mine = small[1::2]
            for n, (dst, src) in enumerate(mine):
                if n == len(mine) // 2:
                    load_w(1)
                sp.dma_start(dst, src).then_inc(k.params_landed, 16)
            for u in range(2, RING):
                load_w(u)

        @block.tensor
        def _(pe):
            for u in range(RING):
                pe.sem_inc(k.tile_done[u], 1)
            pe.wait_ge(k.params_landed, 16 * len(small))
            for g in range(2):
                last = nc.tensor.transpose(k.ps[:, 0, g * P:(g + 1) * P], k.param_rows[:, g, :], k.const("ident"))
            last.then_inc(k.products, 1)

        @block.scalar
        def _(act):
            for u in range(2):
                act.sem_inc(k.psum_free[u], 1)
            act.wait_ge(k.pools, 1)
            for dst, src in small[0::2]:
                act.dma_start(dst, src).then_inc(k.params_landed, 16)
            act.dma_start(*loads[1]).then_inc(k.x_landed, 16)

        @block.vector
        def _(dve):
            dve.wait_ge(k.products, 1)
            nc.vector.tensor_copy(k.cols[:, :, :].rearrange("p g n -> p (g n)"), k.ps[:, 0, 0:2 * P])
    k.advance(products=1, pools=1)
    k.tiles = [1] * RING


def issue(k, sp, loads):
    for slot, before, dst, src in loads:
        sp.wait_ge(k.tile_done[slot], before + 1)
        sp.dma_start(dst, src).then_inc(k.w_landed[slot], 16)


def turn(k, src, chunks, dst, scale=None, shift=None, norm_of=None, ahead=()):
    nc = k.nc
    p0, v0, a0 = k.starts()
    rstd = k.stat[:, 0:TT]
    sums = k.stat[:, TT:2 * TT]
    with nc.Block() as block:
        @block.sync
        def _(sp):
            issue(k, sp, ahead)

        @block.scalar
        def _(act):
            if norm_of is not None:
                for t in range(TT):
                    last = nc.scalar.activation(src[:, t, 0:D], norm_of[:, t, :], ACT.Square, accum_out=sums[:, t:t + 1])
                k.achain(last)
                k.achain(nc.scalar.activation(rstd, sums, ACT.Ln, bias=k.const("eps"), scale=1.0 / D))
                nc.scalar.activation(rstd, rstd, ACT.Exp, scale=-0.5).then_inc(k.activations, 1)
            for c in [c for c in range(chunks) if c // 2 % 2]:
                act.wait_ge(k.products, p0 + c // 2 + 1)
                view = k.ps[:, c // 2, (c % 2) * S:(c % 2 + 1) * S]
                if scale is not None:
                    nc.scalar.activation(dst[:, c, 0:S], view, ACT.Identity, bias=shift(c) if shift else 0.0, scale=scale(c))
                else:
                    nc.scalar.copy(dst[:, c, 0:S], view)

        @block.vector
        def _(dve):
            if norm_of is not None:
                dve.wait_ge(k.activations, a0 + 1)
                for t in range(TT):
                    nc.vector.tensor_scalar(src[:, t, 0:D], norm_of[:, t, :], rstd[:, t:t + 1], None, ALU.mult).then_inc(k.vectors, 1)
            for c in [c for c in range(chunks) if c // 2 % 2 == 0]:
                dve.wait_ge(k.products, p0 + c // 2 + 1)
                view = k.ps[:, c // 2, (c % 2) * S:(c % 2 + 1) * S]
                if scale is not None and shift is not None:
                    nc.vector.tensor_scalar(dst[:, c, 0:S], view, scale(c), shift(c), ALU.mult, ALU.add)
                elif scale is not None:
                    nc.vector.tensor_scalar(dst[:, c, 0:S], view, scale(c), None, ALU.mult)
                else:
                    nc.vector.tensor_copy(dst[:, c, 0:S], view)

        @block.tensor
        def _(pe):
            if norm_of is not None:
                pe.wait_ge(k.vectors, v0 + TT)
            for b in range((chunks + 1) // 2):
                for c in range(2 * b, min(2 * b + 2, chunks)):
                    for t in range(TT):
                        at = (c % 2) * S + t * P
                        last = nc.tensor.transpose(k.ps[:, b, at:at + P], src[:, t, c * P:(c + 1) * P], k.const("ident"))
                last.then_inc(k.products, 1)
    k.advance(products=(chunks + 1) // 2, vectors=TT if norm_of is not None else 0,
              activations=1 if norm_of is not None else 0)


def each_tile(engine, n, first_slot, body, skip=0):
    if n // 2 > skip // 2:
        with engine.Fori(skip // 2, n // 2) as i:
            for u in range(2):
                body(i, u, (first_slot + u) % 2)
    if n % 2 and skip < n:
        body(n // 2, 0, first_slot)


class Stream:

    def __init__(self, k, parts, chunks=DC):
        self.k, self.parts, self.chunks = k, parts, chunks
        for part in parts:
            n = part["tiles"]
            first = k.next_slot
            part["first_slot"] = first
            part["start"], part["copied"] = list(k.tiles), list(k.copied)
            for slot, m in ((first, (n + 1) // 2), (1 - first, n // 2)):
                k.tiles[slot] += m
                k.copied[slot] += m
            k.next_slot = (first + n) % 2
        self.skip = min(2, parts[0]["tiles"])

    def tile(self, part, n, slot):
        dst = self.k.ring[:, slot * SLOT:(slot + 1) * SLOT].rearrange("p (c n) -> p c n", n=TILE)
        return dst[:, 0:self.chunks, 0:part["width"]], part["w"](n)

    def ahead(self):
        part = self.parts[0]
        slots = [(part["first_slot"] + n) % 2 for n in range(self.skip)]
        return [(slot, part["start"][slot], *self.tile(part, n, slot)) for n, slot in enumerate(slots)]


def project(k, hT, stream, narrow=None, vector=None, between=None, sync=None, gpsimd=None):
    nc = k.nc
    chunks = stream.chunks
    p0, v0, a0 = k.starts()
    between = between or {}

    def beside(n, name, engine):
        if name in between.get(n, {}):
            between[n][name](engine)

    def copies(part):
        if not part["channel_major"]:
            return [(b, part["width"]) for b in range(TT)]
        return [(b, min(2, part["width"] // P - 2 * b) * S) for b in range((part["width"] // P + 1) // 2)]

    with nc.Block() as block:
        @block.sync
        def _(sp):
            if sync:
                sync(sp)
            for n, part in enumerate(stream.parts):
                def load(i, u, slot):
                    dst, src = stream.tile(part, 2 * i + u, slot)
                    sp.wait_ge(k.tile_done[slot], i + (part["start"][slot] + 1))
                    sp.dma_start(dst, src).then_inc(k.w_landed[slot], 16)
                each_tile(sp, part["tiles"], part["first_slot"], load, skip=0 if n else stream.skip)

        @block.tensor
        def _(pe):
            if narrow:
                w, out, n = narrow
                for t in range(TT):
                    for c in range(chunks):
                        last = nc.tensor.matmul(k.ps[:, 4, t * n:(t + 1) * n], hT[:, c, t * P:(t + 1) * P], w[:, c, :],
                                                start=c == 0, stop=c == chunks - 1)
                last.then_inc(k.products, 1)
            for index, part in enumerate(stream.parts):
                beside(index, "tensor", pe)
                width = part["width"]

                def multiply(i, u, slot):
                    wt = k.ring[:, slot * SLOT:(slot + 1) * SLOT].rearrange("p (c n) -> p c n", n=TILE)
                    pe.wait_ge(k.w_landed[slot], i * 16 + 16 * (part["start"][slot] + 1))
                    pe.wait_ge(k.psum_free[slot], i + (part["copied"][slot] + 1))
                    if part["channel_major"]:
                        for n in range(width // P):
                            for c in range(chunks):
                                last = nc.tensor.matmul(k.ps[:, 2 * slot + n // 2, (n % 2) * S:(n % 2 + 1) * S],
                                                        wt[:, c, n * P:(n + 1) * P], hT[:, c, 0:S],
                                                        start=c == 0, stop=c == chunks - 1)
                    else:
                        for t in range(TT):
                            for c in range(chunks):
                                last = nc.tensor.matmul(k.ps[:, 2 * slot + t, 0:width], hT[:, c, t * P:(t + 1) * P],
                                                        wt[:, c, 0:width], start=c == 0, stop=c == chunks - 1)
                    last.then_inc(k.tile_done[slot], 1)
                each_tile(pe, part["tiles"], part["first_slot"], multiply)

        @block.scalar
        def _(act):
            if narrow:
                w, out, n = narrow
                act.wait_ge(k.products, p0 + 1)
                nc.scalar.copy(out, k.ps[:, 4, 0:TT * n].rearrange("p (t n) -> p t n", n=n))
            for index, part in enumerate(stream.parts):
                beside(index, "scalar", act)

                def copy(i, u, slot):
                    act.wait_ge(k.tile_done[slot], i + (part["start"][slot] + 2))
                    for b, n in copies(part):
                        last = nc.scalar.activation(part["out"](2 * i + u, b), shaped(k.ps[:, 2 * slot + b, 0:n], part),
                                                    part.get("func", ACT.Copy))
                    last.then_inc(k.psum_free[slot], 1)
                each_tile(act, part["tiles"], part["first_slot"], copy)
            beside(len(stream.parts), "scalar", act)

        if vector:
            @block.vector
            def _(dve):
                vector(dve)

        if gpsimd:
            @block.gpsimd
            def _(pool):
                gpsimd(pool)
    k.advance(products=1 if narrow else 0)


def wait_copied(k, dve, part):
    first, n = part["first_slot"], part["tiles"]
    for slot, m in ((first, (n + 1) // 2), (1 - first, n // 2)):
        if m:
            dve.wait_ge(k.psum_free[slot], part["copied"][slot] + 1 + m)


def shaped(ap, part):
    return ap.rearrange("p (c s) -> p c s", s=S) if part["channel_major"] else ap


def columns(w, first, width):
    def tile(n):
        return w[0, :, bass.ds(n * width + first, width)].rearrange("(c p) n -> p c n", p=P)
    return tile


def to_chan(k, first, width):
    def out(n, b):
        chunks = min(2, width // P - 2 * b)
        return k.chan[:, bass.ds(n * (width // P) + (first + 2 * b), chunks), PAD:PAD + S]
    return out


def to_tok(k, first, width):
    def out(n, b):
        return k.tok[:, b, bass.ds(n * width + first, width)]
    return out


def chan_part(k, w, col, width, tiles, chunk):
    return {"w": columns(w, col, width), "width": width, "tiles": tiles, "channel_major": True,
            "out": to_chan(k, chunk, width)}


def tok_part(k, w, col, width, tiles, at, func=ACT.Copy):
    return {"w": columns(w, col, width), "width": width, "tiles": tiles, "channel_major": False,
            "out": to_tok(k, at, width), "func": func}


class WideStream:

    def __init__(self, k, branches):
        self.branches, self.plan, self.loads = branches, [], []
        for br in branches:
            for at in range(0, br["chunks"], 4):
                n, u = min(4, br["chunks"] - at), k.next_slot
                self.plan.append((br, at, n, u, k.tiles[u]))
                dst = k.ring[:, u * SLOT:u * SLOT + n * D].rearrange("p (c n) -> p c n", n=D)
                self.loads.append((u, k.tiles[u], dst, br["w"][at * P:(at + n) * P, :].rearrange("(c p) n -> p c n", p=P)))
                k.tiles[u] += 1
                k.next_slot = 1 - u

    def ahead(self):
        return self.loads[0:2]


def project_wide(k, stream):
    nc = k.nc
    p0, v0, a0 = k.starts()
    branches, plan = stream.branches, stream.plan
    halves = [(t, h) for t in range(TT) for h in range(2)]
    with nc.Block() as block:
        @block.sync
        def _(sp):
            issue(k, sp, stream.loads[2:])

        @block.tensor
        def _(pe):
            for b, br in enumerate(branches):
                set0 = 4 * (b % 2)
                if b >= 2:
                    pe.wait_ge(k.vectors, v0 + b - 1)
                for at, n, u, before in [x[1:] for x in plan if x[0] is br]:
                    pe.wait_ge(k.w_landed[u], 16 * (before + 1))
                    wt = k.ring[:, u * SLOT:(u + 1) * SLOT].rearrange("p (c n) -> p c n", n=D)
                    for t, h in halves:
                        for c in range(n):
                            last = nc.tensor.matmul(k.ps[:, set0 + 2 * t + h, :], br["lhs"](at + c)[:, t * P:(t + 1) * P],
                                                    wt[:, c, h * BANK:(h + 1) * BANK],
                                                    start=at + c == 0, stop=at + c == br["chunks"] - 1)
                        if at + n == br["chunks"] and (t, h) != halves[-1]:
                            last.then_inc(k.products, 1)
                    last.then_inc(k.tile_done[u], 1)

        @block.vector
        def _(dve):
            for b, br in enumerate(branches):
                _, at, n, u, before = [x for x in plan if x[0] is br][-1]
                what, dst = br["out"][0:2]
                for n, (t, h) in enumerate(halves):
                    if (t, h) != halves[-1]:
                        dve.wait_ge(k.products, p0 + 3 * b + n + 1)
                    else:
                        dve.wait_ge(k.tile_done[u], before + 2)
                    sums = k.ps[:, 4 * (b % 2) + n, :]
                    cols = slice(h * BANK, (h + 1) * BANK)
                    if what == "set":
                        last = nc.vector.tensor_copy(dst[:, t, cols], sums)
                    elif what == "add":
                        last = nc.vector.tensor_tensor(dst[:, t, cols], dst[:, t, cols], sums, ALU.add)
                    elif what == "gate_set":
                        last = nc.vector.tensor_tensor(dst[:, t, cols], sums, br["out"][2][:, t, cols], ALU.mult)
                    else:
                        gate = br["out"][2]
                        k.vchain(nc.vector.tensor_tensor(gate[:, t, cols], sums, gate[:, t, cols], ALU.mult))
                        last = nc.vector.tensor_tensor(dst[:, t, cols], dst[:, t, cols], gate[:, t, cols], ALU.add)
                k.vchain(last)
                dve.sem_inc(k.vectors, 1)
    k.advance(products=3 * len(branches), vectors=len(branches))


def attention(k, heads, qT, kT, v, scale, mask, out, causal=False, gate=None):
    nc = k.nc
    p0, v0, a0 = k.starts()
    s = Scratch(k)
    half = heads // 2
    scores = [s.take(half * S).rearrange("p (h k) -> p h k", h=half) for u in range(4)]
    probs_t = [s.take(TT * half * P) for u in range(4)]

    def stat(n, u):
        return k.stat[:, 16 * n + 4 * u:16 * n + 4 * u + half]

    def keys(u):
        return (u // 2 + 1) * P if causal else S

    def sums(u):
        r = u % 2
        return k.ps[:, 2 * r:2 * r + 2, :].rearrange("p b (h k) -> p (b h) k", k=S)[:, 0:half, 0:keys(u)]

    def by_parity(ap, u):
        return ap[:, u // 2, 0:heads * HD].rearrange("p (h r d) -> p h r d", r=2, d=HD)[:, :, u % 2, :]
    scored = [1, 2, 3, 4]
    turned = [5, 6, 9, 10]
    mixed = [7, 8, 11, 12]
    read = [1, 3, 5, 8]
    shifted = [2, 4, 6, 9]
    done = [7, 10, 11, 12]
    probs = [1, 2, 4, 6]
    copied = [3, 5, 7, 8]
    with nc.Block() as block:
        @block.tensor
        def _(pe):
            def score(u):
                if u >= 2:
                    pe.wait_ge(k.vectors, v0 + read[u - 2])
                t, r = u // 2, u % 2
                for i in range(half):
                    last = nc.tensor.matmul(k.ps[:, 2 * r + i // 2, i % 2 * S:i % 2 * S + keys(u)],
                                            qT(2 * i + r)[:, t * P:(t + 1) * P], kT(2 * i + r)[:, 0:keys(u)], start=True, stop=True)
                last.then_inc(k.products, 1)

            def turn_probs(u):
                pe.wait_ge(k.activations, a0 + probs[u])
                if u >= 2:
                    pe.wait_ge(k.vectors, v0 + done[u - 2])
                for j in range(keys(u) // P):
                    for i in range(half):
                        n = j * half + i
                        last = nc.tensor.transpose(k.ps[:, 4 + 2 * (u % 2) + n // 4, (n % 4) * P:(n % 4 + 1) * P],
                                                   scores[u][:, i, j * P:(j + 1) * P], k.const("ident"))
                last.then_inc(k.products, 1)

            def mix(u):
                pe.wait_ge(k.activations, a0 + copied[u])
                for i in range(half):
                    for j in range(keys(u) // P):
                        n = j * half + i
                        last = nc.tensor.matmul(k.ps[:, 4 + 2 * (u % 2), i * HD:(i + 1) * HD], probs_t[u][:, n * P:(n + 1) * P],
                                                v(j, 2 * i + u % 2), start=j == 0, stop=j == keys(u) // P - 1)
                last.then_inc(k.products, 1)
            for u in range(4):
                score(u)
            for t in range(TT):
                turn_probs(2 * t)
                turn_probs(2 * t + 1)
                mix(2 * t)
                mix(2 * t + 1)

        @block.vector
        def _(dve):
            def shift(u):
                sc = scores[u][:, :, 0:keys(u)]
                dve.wait_ge(k.products, p0 + scored[u])
                if mask is None:
                    k.vchain(nc.vector.tensor_reduce(stat(0, u), sums(u), AX_X, ALU.max))
                    nc.vector.tensor_tensor(sc, sums(u), along(stat(0, u), keys(u)), ALU.subtract).then_inc(k.vectors, 2)
                else:
                    nc.vector.scalar_tensor_tensor(out=sc, in0=sums(u), scalar=scale, in1=mask(u // 2)[:, u % 2::2, :],
                                                   op0=ALU.mult, op1=ALU.add).then_inc(k.vectors, 1)
                    dve.wait_ge(k.vectors, v0 + read[u])
                    k.vchain(nc.vector.tensor_reduce(stat(0, u), sc, AX_X, ALU.max))
                    nc.vector.tensor_tensor(sc, sc, along(stat(0, u), keys(u)), ALU.subtract).then_inc(k.vectors, 1)

            def invert_totals(u):
                dve.wait_ge(k.activations, a0 + probs[u])
                k.vchain(nc.vector.tensor_reduce(stat(1, u), scores[u][:, :, 0:keys(u)], AX_X, ALU.add))
                k.vchain(nc.vector.reciprocal(stat(2, u), stat(1, u)))

            def finish(u):
                dve.wait_ge(k.products, p0 + mixed[u])
                sums_u = k.ps[:, 4 + 2 * (u % 2), 0:half * HD].rearrange("p (h d) -> p h d", h=half)
                nc.vector.tensor_tensor(by_parity(out, u), sums_u, along(stat(2, u), HD), ALU.mult).then_inc(k.vectors, 1)
                if gate is not None:
                    dve.wait_ge(k.vectors, v0 + done[u])
                    nc.vector.tensor_tensor(by_parity(out, u), by_parity(out, u), by_parity(gate, u), ALU.mult)
            shift(0)
            shift(1)
            invert_totals(0)
            shift(2)
            finish(0)
            invert_totals(1)
            shift(3)
            finish(1)
            invert_totals(2)
            invert_totals(3)
            finish(2)
            finish(3)

        @block.scalar
        def _(act):
            def exponential(u):
                sc = scores[u][:, :, 0:keys(u)]
                act.wait_ge(k.vectors, v0 + shifted[u])
                nc.scalar.activation(sc, sc, ACT.Exp, scale=scale if mask is None else 1.0).then_inc(k.activations, 1)

            def copy(u):
                act.wait_ge(k.products, p0 + turned[u])
                n = keys(u) // P * half * P
                b = 4 + 2 * (u % 2)
                nc.scalar.copy(probs_t[u][:, 0:n], k.ps[:, b:b + 2, :].rearrange("p b n -> p (b n)")[:, 0:n]).then_inc(k.activations, 1)
            exponential(0)
            exponential(1)
            copy(0)
            exponential(2)
            copy(1)
            exponential(3)
            copy(2)
            copy(3)
    k.advance(products=12, vectors=12, activations=8)


def convolve(k, dve, first, chunks, weights, dst):
    nc = k.nc
    for tap in range(4):
        for c in range(chunks):
            src = k.chan[:, first + c, PAD - 3 + tap:PAD - 3 + tap + S]
            if tap == 0:
                last = nc.vector.tensor_scalar(dst[:, c, 0:S], src, weights(tap, c), None, ALU.mult)
            else:
                last = nc.vector.scalar_tensor_tensor(out=dst[:, c, 0:S], in0=src, scalar=weights(tap, c),
                                                      in1=dst[:, c, 0:S], op0=ALU.mult, op1=ALU.add)
        k.vchain(last)


def invert_tensor(k, pe, groups, first, levels, A_t, X, Y):
    nc = k.nc
    at = k.inverses
    for n in range(1, levels):
        before = at + 2 * groups * (n - 1)
        for g in range(groups):
            if n > 1:
                pe.wait_ge(k.inverse_updates, before - 2 * groups + groups + g + 1)
            for m in range(4):
                last = nc.tensor.matmul(k.ps[:, first + g, m * P:(m + 1) * P], A_t(4 * g + m), X(4 * g + m), start=True, stop=True)
            last.then_inc(k.inverse_products, 1)
        for g in range(groups):
            pe.wait_ge(k.inverse_updates, before + g + 1)
            for m in range(4 if n < levels - 1 else 0):
                nc.tensor.matmul(k.ps[:, first + g, m * P:(m + 1) * P], Y(4 * g + m), k.U(4 * g + m), start=True, stop=True)
            for m in range(4):
                last = nc.tensor.matmul(k.ps[:, first + groups + g, m * P:(m + 1) * P], k.U(4 * g + m), Y(4 * g + m), start=True, stop=True)
            last.then_inc(k.inverse_products, 1)


def invert_vector(k, dve, groups, first, levels, A_t, X, Y):
    nc = k.nc
    at = k.inverses

    def group(f, g):
        base = f(4 * g)
        return f(4 * g, 4)

    for n in range(1, levels):
        before = at + 2 * groups * (n - 1)
        level = over(k.const(f"level{n}"), 4)
        for g in range(groups):
            dve.wait_ge(k.inverse_products, before + g + 1)
            nc.vector.tensor_tensor(group(k.U, g), k.ps[:, first + g, :].rearrange("p (m n) -> p m n", m=4), level, ALU.mult)\
                .then_inc(k.inverse_updates, 1)
        for g in range(groups):
            dve.wait_ge(k.inverse_products, before + groups + g + 1)
            if n < levels - 1:
                nc.vector.tensor_tensor(group(X, g), group(X, g), k.ps[:, first + g, :].rearrange("p (m n) -> p m n", m=4), ALU.add)
            nc.vector.tensor_tensor(group(Y, g), group(Y, g), k.ps[:, first + groups + g, :].rearrange("p (m n) -> p m n", m=4), ALU.add)\
                .then_inc(k.inverse_updates, 1)


def matrices(ap):
    def f(n, m=None):
        a = ap[:, n * P:(n + (m or 1)) * P]
        return a if m is None else a.rearrange("p (m n) -> p m n", m=m)
    return f



def modulation(k, ahead):
    nc = k.nc
    p0, v0, a0 = k.starts()
    cw = k.hT[:, 0, 0:DC * 32].rearrange("p (c n) -> p c n", n=32)
    rstd, sums = k.stat[:, 0:TT], k.stat[:, TT:2 * TT]
    rows = k.tok[:, 0, 0:3 * D]
    tiles = 3 * D // TILE
    with nc.Block() as block:
        @block.sync
        def _(sp):
            issue(k, sp, ahead)

        @block.tensor
        def _(pe):
            pe.wait_ge(k.activations, a0 + 1)

            def turn_rows(u):
                if u % 2:
                    pe.wait_ge(k.vectors, v0 + u // 2 + 1)
                else:
                    pe.wait_ge(k.activations, a0 + u // 2 + 3)
                for n in range(TILE // P):
                    at = u * TILE + n * P
                    last = nc.tensor.matmul(k.ps[:, 6, at // P:at // P + 1], rows[:, at:at + P], k.const("four_idents")[:, 0:1], start=True, stop=True)
                return last
            for u in range(tiles):
                wt = k.ring[:, u * SLOT:(u + 1) * SLOT].rearrange("p (c n) -> p c n", n=TILE)
                pe.wait_ge(k.w_landed[u], 16)
                for half in range(2):
                    for j in range(4):
                        c = 4 * half + j
                        last = nc.tensor.matmul(k.ps[32 * j:32 * j + 32, u, :], cw[:, c, :], wt[:, c, :], start=half == 0, stop=half == 1)
                last.then_inc(k.tile_done[u], 1)
                if u:
                    turn_rows(u - 1)
            turn_rows(tiles - 1).then_inc(k.products, 1)

        @block.scalar
        def _(act):
            group, row, n, _, _ = PARAM_ROWS["c"]
            nc.scalar.activation(cw, along(k.cols[:, group, row:row + n], 32), ACT.Silu).then_inc(k.activations, 1)
            act.wait_ge(k.x_landed, 16)
            for t in range(TT):
                last = nc.scalar.activation(k.xn[:, t, :], k.x[:, t, :], ACT.Square, accum_out=sums[:, t:t + 1])
            k.achain(last)
            k.achain(nc.scalar.activation(rstd, sums, ACT.Ln, bias=k.const("eps"), scale=1.0 / D))
            nc.scalar.activation(rstd, rstd, ACT.Exp, scale=-0.5).then_inc(k.activations, 1)
            for u in range(0, tiles, 2):
                act.wait_ge(k.tile_done[u], 2)
                nc.scalar.copy(rows[:, u * TILE:(u + 1) * TILE], k.ps[:, u, :]).then_inc(k.activations, 1)

        @block.vector
        def _(dve):
            dve.wait_ge(k.activations, a0 + 2)
            for t in range(TT):
                nc.vector.tensor_scalar(k.xn[:, t, :], k.x[:, t, :], rstd[:, t:t + 1], None, ALU.mult)
            for u in range(1, tiles, 2):
                dve.wait_ge(k.tile_done[u], 2)
                nc.vector.tensor_copy(rows[:, u * TILE:(u + 1) * TILE], k.ps[:, u, :]).then_inc(k.vectors, 1)
            dve.wait_ge(k.products, p0 + 1)
            group, row, n, _, _ = PARAM_ROWS["b_ada"]
            k.vchain(nc.vector.tensor_tensor(k.mod[:, :], k.ps[:, 6, 0:24], k.cols[:, group, row:row + n], ALU.add))
            group, row, n, _, _ = PARAM_ROWS["g_pre"]
            k.vchain(nc.vector.scalar_tensor_tensor(out=k.mod[:, DC:2 * DC], in0=k.mod[:, DC:2 * DC], scalar=1.0,
                                                    in1=k.cols[:, group, row:row + n], op0=ALU.add, op1=ALU.mult))
    k.advance(products=1, vectors=tiles // 2, activations=2 + tiles // 2)


class FirstScratch(Scratch):

    def __init__(self, k):
        super().__init__(k)
        self.qkv = self.take(12 * S).rearrange("p (c s) -> p c s", s=S)
        self.norms = self.take(8 * S)
        self.k_tok = self.take(TT * 512).rearrange("p (t n) -> p t n", t=TT)
        self.v_tok = self.take(TT * 512).rearrange("p (t n) -> p t n", t=TT)
        self.beta, self.g, self.g_neg, self.G, self.eG, self.eGr, self.t1, self.t2 = [k.stat[:, 8 * n:8 * n + 8] for n in range(8)]
        self.ea = k.stat[:, 64:68]


def delta_inputs(k, s, part0):
    nc = k.nc
    qkv, norms = s.qkv, s.norms
    flat = qkv[:, 0:8, :].rearrange("p c s -> p (c s)")
    p0, v0, a0 = k.starts()
    p0 += 1
    MAGNITUDE, ROWS, DECAYS, NORMALISED, REST = [v0 + n for n in (1, 2, 3, 5, 4)]
    SOFTPLUS, SQUARES, NORMS = [a0 + n for n in (1, 2, 3)]
    RUNNING, NORM_SUMS, TURNED = [p0 + n for n in (1, 2, 3)]

    def th(a):
        return a.rearrange("p (t h) -> p t h", t=TT)

    def vector(dve):
        wait_copied(k, dve, part0)
        k.vchain(nc.vector.tensor_tensor(th(s.t1), k.small[:, :, 4:8], over(k.rows_bc[:, 4:8], TT), ALU.add))
        nc.vector.scalar_tensor_tensor(out=s.t2, in0=s.t1, scalar=-1.0, in1=s.t1, op0=ALU.mult, op1=ALU.max).then_inc(k.vectors, 1)
        convolve(k, dve, 0, 12, lambda tap, c: k.col("conv_w", tap * 12 + c), qkv)
        dve.sem_inc(k.vectors, 1)
        dve.wait_ge(k.activations, SOFTPLUS)
        k.vchain(nc.vector.scalar_tensor_tensor(out=s.t1, in0=s.t1, scalar=0.0, in1=s.t2, op0=ALU.max, op1=ALU.add))
        k.vchain(nc.vector.tensor_tensor(th(s.g_neg), th(s.t1), over(s.ea, TT), ALU.mult))
        nc.vector.tensor_scalar(s.g, s.g_neg, -1.0, None, ALU.mult).then_inc(k.vectors, 1)
        dve.wait_ge(k.products, RUNNING)
        k.vchain(nc.vector.tensor_copy(s.G, k.ps[:, 4, 0:8]))
        nc.vector.tensor_tensor(s.t2, k.ps[:, 4, 8:16], s.G, ALU.subtract).then_inc(k.vectors, 1)
        dve.wait_ge(k.activations, NORMS)
        nc.vector.tensor_tensor(flat, flat, norms, ALU.mult).then_inc(k.vectors, 1)
        dve.wait_ge(k.products, TURNED)
        nc.vector.tensor_copy(s.k_tok.rearrange("p t n -> p (t n)"), k.ps[:, 4:6, :].rearrange("p t n -> p (t n)"))
        nc.vector.tensor_copy(s.v_tok.rearrange("p t n -> p (t n)"), k.ps[:, 6:8, :].rearrange("p t n -> p (t n)"))

    def softplus_and_beta(act):
        act.wait_ge(k.vectors, MAGNITUDE)
        k.achain(softplus_scalar(k, s.t2))
        nc.scalar.activation(s.ea, k.rows_bc[:, 0:4], ACT.Exp)
        nc.scalar.activation(th(s.beta), k.small[:, :, 0:4], ACT.Sigmoid).then_inc(k.activations, 1)

    def rows(act):
        act.wait_ge(k.vectors, ROWS)
        k.achain(nc.scalar.activation(qkv, qkv, ACT.Silu))
        nc.scalar.activation(norms, flat, ACT.Square).then_inc(k.activations, 1)

    def scales(act):
        act.wait_ge(k.vectors, REST)
        nc.scalar.activation(s.eG, s.G, ACT.Exp)
        nc.scalar.activation(s.eGr, s.t2, ACT.Exp)
        act.wait_ge(k.products, NORM_SUMS)
        k.achain(nc.scalar.activation(norms, k.ps[:, 4:8, :].rearrange("p b n -> p (b n)"), ACT.Ln, bias=k.const("eps")))
        nc.scalar.activation(norms[:, 0:4 * S], norms[:, 0:4 * S], ACT.Exp, scale=-0.5, bias=k.const("log_scale"))
        nc.scalar.activation(norms[:, 4 * S:8 * S], norms[:, 4 * S:8 * S], ACT.Exp, scale=-0.5).then_inc(k.activations, 1)

    def running_sums(pe):
        pe.wait_ge(k.vectors, DECAYS)
        nc.tensor.matmul(k.ps[:, 4, 0:8], k.const("upper"), s.g, start=True, stop=True)
        nc.tensor.matmul(k.ps[:, 4, 8:16], k.const("ones"), s.g, start=True, stop=True).then_inc(k.products, 1)

    def norm_sums(pe):
        pe.wait_ge(k.activations, SQUARES)
        pe.wait_ge(k.vectors, REST)
        for b in range(4):
            last = nc.tensor.matmul(k.ps[:, 4 + b, :], k.const("ones"), norms[:, b * BANK:(b + 1) * BANK], start=True, stop=True)
        last.then_inc(k.products, 1)

    def turn_rows(pe):
        pe.wait_ge(k.vectors, NORMALISED)
        for t in range(TT):
            for h in range(4):
                nc.tensor.transpose(k.ps[:, 4 + t, h * P:(h + 1) * P], qkv[:, 4 + h, t * P:(t + 1) * P], k.const("ident"))
                last = nc.tensor.transpose(k.ps[:, 6 + t, h * P:(h + 1) * P], qkv[:, 8 + h, t * P:(t + 1) * P], k.const("ident"))
        last.then_inc(k.products, 1)
    between = {1: {"scalar": softplus_and_beta},
               5: {"tensor": running_sums, "scalar": rows},
               6: {"tensor": norm_sums, "scalar": scales},
               7: {"tensor": turn_rows}}
    return {"vector": vector, "between": between}, {"products": 3, "vectors": 5, "activations": 3}


def delta_rule(k, s, out):
    nc = k.nc
    qkv, k_tok, v_tok = s.qkv, s.k_tok, s.v_tok
    beta, g, g_neg, G, eG, eGr, t1, t2 = s.beta, s.g, s.g_neg, s.G, s.eG, s.eGr, s.t1, s.t2

    n8 = 8 * P
    A, A_t, U, X, Y, qk = [matrices(s.take(n8)) for _ in range(6)]
    decay, decay_t = U, X
    k.U = U
    p0, v0, a0 = k.starts()
    start = k.inverses
    with nc.Block() as block:
        @block.tensor
        def _(pe):
            def spread(a, n):
                return a[:, n:n + 1].broadcast_to([P, P])
            for t in range(TT):
                for h in range(4):
                    n = 4 * t + h
                    kT, qT = qkv[:, 4 + h, t * P:(t + 1) * P], qkv[:, h, t * P:(t + 1) * P]
                    c = slice(h * P, (h + 1) * P)
                    nc.tensor.matmul(k.ps[:, t, c], k.const("upper"), spread(g, n), start=True, stop=False)
                    nc.tensor.matmul(k.ps[:, t, c], spread(g_neg, n), k.const("upper"), start=False, stop=True)
                    nc.tensor.matmul(k.ps[:, 2 + t, c], spread(g, n), k.const("upper"), start=True, stop=False)
                    nc.tensor.matmul(k.ps[:, 2 + t, c], k.const("upper"), spread(g_neg, n), start=False, stop=True)
                    nc.tensor.matmul(k.ps[:, 4 + t, c], kT, kT, start=True, stop=True)
                    last = nc.tensor.matmul(k.ps[:, 6 + t, c], kT, qT, start=True, stop=True)
            last.then_inc(k.products, 1)
            pe.wait_ge(k.vectors, v0 + 2)
            for n in range(8):
                last = nc.tensor.transpose(k.ps[:, n // 4, (n % 4) * P:(n % 4 + 1) * P], A(n), k.const("ident"))
            last.then_inc(k.products, 1)
            pe.wait_ge(k.vectors, v0 + 3)
            invert_tensor(k, pe, 2, 2, 7, A_t, X, Y)

        @block.vector
        def _(dve):
            def bank(b):
                return k.ps[:, b:b + 2, :].rearrange("p b (m n) -> p (b m) n", m=4)
            dve.wait_ge(k.products, p0 + 1)
            nc.vector.tensor_tensor(decay(0, 8), bank(0), over(k.const("neg_not_lower"), 8), ALU.add)
            nc.vector.tensor_tensor(decay_t(0, 8), bank(2), over(k.const("neg_not_upper"), 8), ALU.add).then_inc(k.vectors, 1)
            dve.wait_ge(k.activations, a0 + 1)
            k.vchain(nc.vector.tensor_tensor(A(0, 8), bank(4), decay(0, 8), ALU.mult))
            nc.vector.tensor_tensor(qk(0, 8), bank(6), decay_t(0, 8), ALU.mult)
            k.vchain(nc.vector.tensor_tensor(A(0, 8), A(0, 8), over(k.const("lower_strict"), 8), ALU.mult))
            nc.vector.tensor_tensor(A(0, 8), A(0, 8), along(beta, P), ALU.mult).then_inc(k.vectors, 1)
            dve.wait_ge(k.products, p0 + 2)
            k.vchain(nc.vector.tensor_copy(A_t(0, 8), bank(0)))
            nc.vector.tensor_tensor(X(0, 8), A(0, 8), over(k.const("level0"), 8), ALU.mult)
            k.vchain(nc.vector.tensor_tensor(Y(0, 8), A_t(0, 8), over(k.const("level0_t"), 8), ALU.mult))
            nc.vector.tensor_tensor(X(0, 8), X(0, 8), over(k.const("ident"), 8), ALU.add)
            nc.vector.tensor_tensor(Y(0, 8), Y(0, 8), over(k.const("ident"), 8), ALU.add).then_inc(k.vectors, 1)
            invert_vector(k, dve, 2, 2, 7, A_t, X, Y)

        @block.scalar
        def _(act):
            act.wait_ge(k.vectors, v0 + 1)
            nc.scalar.activation(decay(0, 8), decay(0, 8), ACT.Exp)
            nc.scalar.activation(decay_t(0, 8), decay_t(0, 8), ACT.Exp).then_inc(k.activations, 1)
    k.inverses = start + 6 * 2 * 2
    k.advance(products=2, vectors=3, activations=1)

    kb = A(0, 8)
    vb = A_t(0, 8)
    kd = U(0, 4)
    w_t = X(0, 4)
    state = X(4, 4)
    q_state = U(4, 4)
    u_new = s.take(n8).rearrange("p (m n) -> p m n", m=8)
    eighth = "p (m n) -> p m n"
    p0, v0, a0 = k.starts()
    with nc.Block() as block:
        @block.vector
        def _(dve):
            k8 = k_tok.rearrange("p t (m n) -> p (t m) n", m=4)
            v8 = v_tok.rearrange("p t (m n) -> p (t m) n", m=4)
            nc.vector.tensor_tensor(vb, v8, along(beta, P), ALU.mult)
            nc.vector.tensor_tensor(kd, k8[:, 0:4, :], along(eGr[:, 0:4], P), ALU.mult)
            k.vchain(nc.vector.tensor_tensor(kb, k8, along(beta, P), ALU.mult))
            nc.vector.tensor_tensor(kb, kb, along(eG, P), ALU.mult).then_inc(k.vectors, 1)
            dve.wait_ge(k.products, p0 + 1)
            nc.vector.tensor_copy(u_new, k.ps[:, 0:2, :].rearrange("p b (m n) -> p (b m) n", m=4))
            nc.vector.tensor_copy(w_t, k.ps[:, 2, :].rearrange(eighth, m=4)).then_inc(k.vectors, 1)
            dve.wait_ge(k.products, p0 + 2)
            nc.vector.tensor_copy(state, k.ps[:, 3, :].rearrange(eighth, m=4)).then_inc(k.vectors, 1)
            dve.wait_ge(k.products, p0 + 3)
            nc.vector.tensor_tensor(u_new[:, 4:8, :], u_new[:, 4:8, :], k.ps[:, 4, :].rearrange(eighth, m=4), ALU.subtract).then_inc(k.vectors, 1)
            k.vchain(nc.vector.tensor_tensor(q_state, k.ps[:, 5, :].rearrange(eighth, m=4), along(eG[:, 4:8], P), ALU.mult))
            dve.wait_ge(k.products, p0 + 4)
            o = out[:, :, 0:512].rearrange("p t (m n) -> p t m n", m=4)
            nc.vector.tensor_copy(o[:, 0], k.ps[:, 6, :].rearrange(eighth, m=4))
            k.vchain(nc.vector.tensor_tensor(o[:, 1], k.ps[:, 7, :].rearrange(eighth, m=4), q_state, ALU.add))
            for t in range(TT):
                last = nc.vector.tensor_tensor(kb[:, 4 * t:4 * t + 4, :], o[:, t], o[:, t], ALU.mult)
            k.vchain(last)
            nc.vector.tensor_reduce(t1, kb, AX_X, ALU.add).then_inc(k.vectors, 1)
            dve.wait_ge(k.activations, a0 + 1)
            for t in range(TT):
                last = nc.vector.tensor_tensor(o[:, t], o[:, t], along(t1[:, 4 * t:4 * t + 4], P), ALU.mult)
            k.vchain(last)
            for t in range(TT):
                last = nc.vector.tensor_tensor(o[:, t], o[:, t], over(k_tok[:, 0, 0:P], 4), ALU.mult)
            k.vchain(last)
            for t in range(TT):
                last = nc.vector.tensor_tensor(out[:, t, 0:512], out[:, t, 0:512], k.tok[:, t, 0:512], ALU.mult)
            k.vchain(last)

        @block.sync
        def _(sp):
            sp.wait_ge(k.vectors, v0 + 1)
            sp.dma_start(k_tok[:, 0, 0:P], k.ins["dn_norm_g"].partition_broadcast(P).rearrange("p a n -> p (a n)")).then_inc(k.loads, 16)

        @block.scalar
        def _(act):
            act.wait_ge(k.vectors, v0 + 5)
            act.wait_ge(k.loads, 16 * (k.count["loads"] + 1))
            k.achain(nc.scalar.activation(t1, t1, ACT.Ln, bias=k.const("eps"), scale=1.0 / DN_D))
            nc.scalar.activation(t1, t1, ACT.Exp, scale=-0.5).then_inc(k.activations, 1)

        @block.tensor
        def _(pe):
            pe.wait_ge(k.vectors, v0 + 1)
            for n in range(8):
                nc.tensor.matmul(k.ps[:, n // 4, (n % 4) * P:(n % 4 + 1) * P], Y(n), vb[:, n, :], start=True, stop=True)
            for h in range(4):
                last = nc.tensor.matmul(k.ps[:, 2, h * P:(h + 1) * P], kb[:, 4 + h, :], Y(4 + h), start=True, stop=True)
            last.then_inc(k.products, 1)
            pe.wait_ge(k.vectors, v0 + 2)
            for h in range(4):
                last = nc.tensor.matmul(k.ps[:, 3, h * P:(h + 1) * P], kd[:, h, :], u_new[:, h, :], start=True, stop=True)
            last.then_inc(k.products, 1)
            pe.wait_ge(k.vectors, v0 + 3)
            for h in range(4):
                nc.tensor.matmul(k.ps[:, 4, h * P:(h + 1) * P], w_t[:, h, :], state[:, h, :], start=True, stop=True)
                last = nc.tensor.matmul(k.ps[:, 5, h * P:(h + 1) * P], qkv[:, h, P:S], state[:, h, :], start=True, stop=True)
            last.then_inc(k.products, 1)
            pe.wait_ge(k.vectors, v0 + 4)
            for n in range(8):
                last = nc.tensor.matmul(k.ps[:, 6 + n // 4, (n % 4) * P:(n % 4 + 1) * P], qk(n), u_new[:, n, :], start=True, stop=True)
            last.then_inc(k.products, 1)
    k.advance(products=4, vectors=5, activations=1, loads=1)


def first_layer(k):
    nc, w = k.nc, k.ins["w_in"]
    stream = Stream(k, [
        chan_part(k, w, 0, 512, 3, 0),
        chan_part(k, w, 2056, 512, 2, 12),
        tok_part(k, w, 1536, 512, 1, 0, ACT.Silu),
        tok_part(k, w, 3080, 512, 1, 512),
        tok_part(k, w, 3592, 512, 1, 1024, ACT.Silu),
        tok_part(k, w, 4104, 512, 2, 1536, ACT.Sigmoid),
        tok_part(k, w, 4104 + 2 * 512, 512, 1, 1536 + 2 * 512, ACT.Sigmoid),
        tok_part(k, w, 4104 + 3 * 512, 512, 1, 1536 + 3 * 512, ACT.Sigmoid),
    ])
    modulation(k, stream.ahead())
    turn(k, k.xn, DC, k.hT, scale=lambda c: k.mod[:, DC + c:DC + c + 1], shift=lambda c: k.mod[:, c:c + 1])
    s = FirstScratch(k)
    beside, counts = delta_inputs(k, s, stream.parts[0])
    project(k, k.hT, stream, narrow=(k.narrow_w[:, 0:64].rearrange("p (c n) -> p c n", n=8), k.small[:, :, 0:8], 8), **beside)
    k.advance(**counts)
    delta_rule(k, s, k.xn)
    turn(k, k.xn, 4, k.hT[:, 0:4, :])
    causal = k.const("causal").rearrange("p (t n) -> p t n", t=TT)
    attention(k, MB_H, lambda h: k.chan[64 * (h % 2):64 * (h % 2) + 64, 12 + h // 2, PAD:PAD + S],
              lambda h: k.chan[64 * (h % 2):64 * (h % 2) + 64, 16 + h // 2, PAD:PAD + S],
              lambda t, h: k.tok[:, t, 512 + h * 64:512 + h * 64 + 64], MB_D ** -0.5,
              lambda t: over(causal[:, t, 0:(t + 1) * P], MB_H), k.xn, causal=True, gate=k.tok[:, :, 1024:1536])
    stream = WideStream(k, [
        {"lhs": lambda c: k.hT[:, c, :], "w": k.ins["w_proj_dn"][0], "chunks": 4, "out": ("gate_set", k.xn, k.tok[:, :, 1536:2560])},
        {"lhs": lambda c: k.hT[:, 4 + c, :], "w": k.ins["w_proj_mb"][0], "chunks": 4, "out": ("gate_add", k.xn, k.tok[:, :, 2560:3584])},
    ])
    turn(k, k.xn, 4, k.hT[:, 4:8, :], ahead=stream.ahead())
    project_wide(k, stream)
    stream = WideStream(k, [{"lhs": lambda c: k.hT[:, c, :], "w": k.ins["w_out"][0], "chunks": DC, "out": ("set", k.xn)}])
    turn(k, k.xn, DC, k.hT, ahead=stream.ahead())
    project_wide(k, stream)

    s = Scratch(k)
    gate_diag = s.take(D)
    gain = s.take(D)
    squares = s.take(TT * D).rearrange("p (t n) -> p t n", t=TT)
    sums, rstd = k.stat[:, 0:2], k.stat[:, 2:4]
    p0, v0, a0 = k.starts()
    with nc.Block() as block:
        @block.sync
        def _(sp):
            sp.dma_start(gain, k.ins["g_post"].partition_broadcast(P).rearrange("p a n -> p (a n)")).then_inc(k.loads, 16)

        @block.vector
        def _(dve):
            for c in range(DC):
                last = nc.vector.tensor_scalar(gate_diag[:, c * P:(c + 1) * P], k.const("ident"), k.mod[:, 2 * DC + c:2 * DC + c + 1], None, ALU.mult)
            last.then_inc(k.vectors, 1)
            dve.wait_ge(k.products, p0 + 1)
            dve.wait_ge(k.loads, 16 * (k.count["loads"] + 1))
            k.vchain(nc.vector.tensor_tensor(gain, gain, k.ps[:, 0:2, :].rearrange("p b n -> p (b n)"), ALU.mult))
            dve.wait_ge(k.activations, a0 + 1)
            for t in range(TT):
                last = nc.vector.scalar_tensor_tensor(out=k.xn[:, t, :], in0=k.xn[:, t, :], scalar=rstd[:, t:t + 1], in1=gain, op0=ALU.mult, op1=ALU.mult)
            k.vchain(last)
            for t in range(TT):
                nc.vector.tensor_tensor(k.x[:, t, :], k.x[:, t, :], k.xn[:, t, :], ALU.add)

        @block.tensor
        def _(pe):
            pe.wait_ge(k.vectors, v0 + 1)
            for b in range(2):
                last = nc.tensor.matmul(k.ps[:, b, :], k.const("ones"), gate_diag[:, b * BANK:(b + 1) * BANK], start=True, stop=True)
            last.then_inc(k.products, 1)

        @block.scalar
        def _(act):
            for t in range(TT):
                last = nc.scalar.activation(squares[:, t, :], k.xn[:, t, :], ACT.Square, accum_out=sums[:, t:t + 1])
            k.achain(last)
            k.achain(nc.scalar.activation(rstd, sums, ACT.Ln, bias=k.const("eps"), scale=1.0 / D))
            nc.scalar.activation(rstd, rstd, ACT.Exp, scale=-0.5).then_inc(k.activations, 1)
    k.advance(products=1, vectors=1, activations=1, loads=1)



def softplus_vector(k, dve, z, magnitude):
    return k.nc.vector.scalar_tensor_tensor(out=magnitude, in0=z, scalar=-1.0, in1=z, op0=ALU.mult, op1=ALU.max)


def softplus_scalar(k, magnitude):
    k.achain(k.nc.scalar.activation(magnitude, magnitude, ACT.Exp, scale=-1.0))
    return k.nc.scalar.activation(magnitude, magnitude, ACT.Ln, bias=k.const("ones")[:, 0:1])


class SecondScratch(Scratch):

    def __init__(self, k):
        super().__init__(k)
        self.qk = self.take(4 * S).rearrange("p (c s) -> p c s", s=S)
        self.xa = self.take(2 * S).rearrange("p (c s) -> p c s", s=S)
        self.gates_w = self.take(2 * 2 * P).rearrange("p (w c n) -> p w c n", w=2, c=2)
        self.lru = [self.take(2 * S).rearrange("p (c s) -> p c s", s=S) for _ in range(5)]
        self.diag = self.take(8 * P).rearrange("p (m n) -> p m n", n=P)
        self.f, self.mag, self.i, self.b, self.rows = [k.stat[:, 8 * n:8 * n + 8] for n in range(5)]
        self.rate, self.lru_mag = k.stat[:, 64:66], k.stat[:, 66:68]


def lru_and_weights(k, s, part0, out):
    nc = k.nc
    r, i, a, th, h = s.lru
    g, row, n, _, _ = PARAM_ROWS["lru_lambda_2"]
    lam = k.cols[:, g, row:row + n]
    p0, v0, a0 = k.starts()
    p0 += 1
    q0, l0 = k.count["pools"], k.count["loads"]
    MAGNITUDES, ROWS_QK, ROWS_XA, FORGET, LOG_A, SQUARED, DIAG = [v0 + n for n in (2, 3, 4, 5, 6, 7, 8)]
    SOFTPLUS, GATES, DECAYS, ROOT, GELU = [a0 + n for n in (1, 2, 3, 4, 5)]
    GATE_SUMS, RUNNING = p0 + 1, p0 + 2

    def halves(x):
        return x.rearrange("p (t h) -> p t h", t=TT)

    def gpsimd(pool):
        nc.gpsimd.memset(s.gates_w, 0.0).then_inc(k.pools, 1)

    def sync(sp):
        sp.wait_ge(k.pools, q0 + 1)
        for n, name in enumerate(("lru_wa_2", "lru_wx_2")):
            for half in range(2):
                q = slice(64 * half, 64 * half + 64)
                src = k.ins[name][0].rearrange("(c r) i j -> r i c j", r=2)[half]
                sp.dma_start(s.gates_w[q, n, :, q], src).then_inc(k.loads, 16)

    def gate_products(pe):
        pe.wait_ge(k.loads, 16 * (l0 + 4))
        pe.wait_ge(k.vectors, ROWS_XA)
        for n in range(2):
            for c in range(2):
                last = nc.tensor.matmul(k.ps[:, 4 + n, c * S:(c + 1) * S], s.gates_w[:, n, c, :], s.xa[:, c, :], start=True, stop=True)
        last.then_inc(k.products, 1)

    def running_sums(pe):
        pe.wait_ge(k.vectors, FORGET)
        nc.tensor.matmul(k.ps[:, 6, 0:4], k.const("upper"), s.f[:, 0:4], start=True, stop=True)
        nc.tensor.matmul(k.ps[:, 6, 4:8], k.const("upper"), s.f[:, 4:8], start=True, stop=False)
        nc.tensor.matmul(k.ps[:, 6, 4:8], k.const("ones"), s.f[:, 0:4], start=False, stop=True).then_inc(k.products, 1)

    def log_weights(pe):
        pe.wait_ge(k.activations, GATES)
        pe.wait_ge(k.vectors, DIAG)
        for n in range(2):
            nc.tensor.matmul(k.ps[:, 4 + n, :], k.const("ones"), s.diag[:, 4 * n:4 * n + 4, :].rearrange("p m n -> p (m n)"), start=True, stop=True)

    def softplus(act):
        act.wait_ge(k.vectors, MAGNITUDES)
        softplus_scalar(k, s.lru_mag)
        softplus_scalar(k, s.mag).then_inc(k.activations, 1)

    def gates(act):
        act.wait_ge(k.products, GATE_SUMS)
        for c in range(2):
            nc.scalar.activation(r[:, c, :], k.ps[:, 4, c * S:(c + 1) * S], ACT.Sigmoid, bias=k.col("lru_ba_2", c))
            last = nc.scalar.activation(i[:, c, :], k.ps[:, 5, c * S:(c + 1) * S], ACT.Sigmoid, bias=k.col("lru_bx_2", c))
        last.then_inc(k.activations, 1)
        act.wait_ge(k.vectors, LOG_A)
        nc.scalar.activation(a, r, ACT.Exp)
        nc.scalar.activation(th, r, ACT.Tanh, scale=-1.0).then_inc(k.activations, 1)
        act.wait_ge(k.vectors, SQUARED)
        nc.scalar.activation(th, th, ACT.Sqrt).then_inc(k.activations, 1)

    def rows(act):
        act.wait_ge(k.vectors, ROWS_QK)
        nc.scalar.activation(s.qk, s.qk, ACT.Silu)
        act.wait_ge(k.activations, DECAYS)
        nc.scalar.activation(r, k.chan[:, 2:4, PAD:PAD + S], ACT.Gelu_apprx_tanh).then_inc(k.activations, 1)

    def vector(dve):
        wait_copied(k, dve, part0)
        nc.vector.tensor_tensor(halves(s.i), k.small[:, :, 0:4], over(k.rows_bc[:, 8:12], TT), ALU.add)
        k.vchain(nc.vector.tensor_tensor(halves(s.f), k.small[:, :, 4:8], over(k.rows_bc[:, 12:16], TT), ALU.add))
        softplus_vector(k, dve, s.f, s.mag).then_inc(k.vectors, 1)
        softplus_vector(k, dve, lam, s.lru_mag).then_inc(k.vectors, 1)
        convolve(k, dve, 4, 4, lambda tap, c: k.col("conv_mlstm_w_2", tap * 4 + c), s.qk)
        dve.sem_inc(k.vectors, 1)
        convolve(k, dve, 0, 2, lambda tap, c: k.col("conv_lru_w_2", tap * 2 + c), s.xa)
        dve.sem_inc(k.vectors, 1)
        dve.wait_ge(k.activations, SOFTPLUS)
        nc.vector.scalar_tensor_tensor(out=s.f, in0=s.f, scalar=0.0, in1=s.mag, op0=ALU.min, op1=ALU.subtract).then_inc(k.vectors, 1)
        k.vchain(nc.vector.tensor_scalar(s.rate, lam, -1.0, 0.0, ALU.mult, ALU.max))
        k.vchain(nc.vector.tensor_tensor(s.rate, s.rate, s.lru_mag, ALU.add))
        k.vchain(nc.vector.tensor_scalar(s.rate, s.rate, -8.0, None, ALU.mult))
        dve.wait_ge(k.activations, GATES)
        for c in range(2):
            last = nc.vector.tensor_scalar(r[:, c, :], r[:, c, :], s.rate[:, c:c + 1], None, ALU.mult)
        last.then_inc(k.vectors, 1)
        nc.vector.tensor_tensor(i, i, s.xa, ALU.mult)
        dve.wait_ge(k.activations, DECAYS)
        k.vchain(nc.vector.tensor_tensor(h, a, a, ALU.mult))
        nc.vector.scalar_tensor_tensor(out=th, in0=h, scalar=1.0, in1=th, op0=ALU.add, op1=ALU.mult).then_inc(k.vectors, 1)
        dve.wait_ge(k.activations, ROOT)
        k.vchain(nc.vector.tensor_tensor(i, i, th, ALU.mult))
        for c in range(2):
            last = nc.vector.tensor_tensor_scan(h[:, c, :], a[:, c, :], i[:, c, :], 0.0, ALU.mult, ALU.add)
        k.vchain(last)
        dve.wait_ge(k.products, RUNNING)
        k.vchain(nc.vector.tensor_copy(s.b, k.ps[:, 6, 0:8]))
        k.vchain(nc.vector.tensor_tensor(s.rows.rearrange("p (h t) -> p t h", t=TT), halves(s.i), halves(s.b), ALU.subtract))
        nc.vector.tensor_tensor(s.diag, over(k.const("ident"), 8), along(s.rows, P), ALU.mult).then_inc(k.vectors, 1)
        dve.wait_ge(k.activations, GELU)
        nc.vector.tensor_tensor(out, h, r, ALU.mult)
    between = {2: {"scalar": softplus},
               5: {"tensor": gate_products, "scalar": gates},
               6: {"tensor": running_sums, "scalar": rows},
               7: {"tensor": log_weights}}
    counts = {"products": 2, "vectors": 8, "activations": 5, "pools": 1, "loads": 4}
    return {"gpsimd": gpsimd, "sync": sync, "vector": vector, "between": between}, counts


def mlstm(k, s, out):
    nc = k.nc
    qk, b = s.qk, s.b
    w_s = s.take(4 * S).rearrange("p (h n) -> p h n", h=4)
    w_t = s.take(TT * 4 * P).rearrange("p (j h q) -> p j h q", j=TT, h=4)
    mu, den, low = [k.stat[:, 40 + 4 * n:44 + 4 * n] for n in range(3)]
    causal = k.const("causal").rearrange("p (t n) -> p t n", t=TT)
    SCORES, TURNED, MIXED = 1, 2, 3
    SHIFTED, WEIGHTS, DONE = 1, 2, 3
    EXPS, COPIED = 1, 2
    p0, v0, a0 = k.starts()
    with nc.Block() as block:
        @block.tensor
        def _(pe):
            for t in range(TT):
                keys = (t + 1) * P
                if t:
                    pe.wait_ge(k.vectors, v0 + 3 * (t - 1) + DONE)
                for h in range(4):
                    half = slice(64 * (h % 2), 64 * (h % 2) + 64)
                    last = nc.tensor.matmul(k.ps[:, 2 * (h % 2), h // 2 * S:h // 2 * S + keys], qk[half, h // 2, t * P:(t + 1) * P],
                                            qk[half, 2 + h // 2, 0:keys], start=True, stop=True)
                last.then_inc(k.products, 1)
                pe.wait_ge(k.vectors, v0 + 3 * t + WEIGHTS)
                for j in range(t + 1):
                    for h in range(4):
                        last = nc.tensor.transpose(k.ps[:, 6 + j, h * P:(h + 1) * P], w_s[:, h, j * P:(j + 1) * P], k.const("ident"))
                last.then_inc(k.products, 1)
                pe.wait_ge(k.activations, a0 + 2 * t + COPIED)
                for h in range(4):
                    for j in range(t + 1):
                        last = nc.tensor.matmul(k.ps[:, 1, h * 64:(h + 1) * 64], w_t[:, j, h, :], k.tok[:, j, h * 64:(h + 1) * 64],
                                                start=j == 0, stop=j == t)
                last.then_inc(k.products, 1)

        @block.vector
        def _(dve):
            for t in range(TT):
                keys = (t + 1) * P
                w = w_s[:, :, 0:keys]
                row = k.ps[:, 4:6, :].rearrange("p b (m n) -> p (b m) n", m=2)[:, :, 0:keys]
                k.vchain(nc.vector.tensor_tensor(w, row, over(causal[:, t, 0:keys], 4), ALU.add))
                k.vchain(nc.vector.tensor_reduce(mu, w, AX_X, ALU.max))
                k.vchain(nc.vector.tensor_scalar(mu, mu, 0.0, None, ALU.max))
                nc.vector.tensor_tensor(low, mu, b[:, 4 * t:4 * t + 4], ALU.add)
                nc.vector.tensor_tensor(w, w, along(mu, keys), ALU.subtract).then_inc(k.vectors, 1)
                dve.wait_ge(k.activations, a0 + 2 * t + EXPS)
                dve.wait_ge(k.products, p0 + 3 * t + SCORES)
                for r in range(2):
                    sums = k.ps[:, 2 * r, :].rearrange("p (h n) -> p h n", h=2)[:, :, 0:keys]
                    last = nc.vector.scalar_tensor_tensor(out=w[:, r::2, :], in0=sums, scalar=ML_D ** -0.5, in1=w[:, r::2, :],
                                                          op0=ALU.mult, op1=ALU.mult)
                last.then_inc(k.vectors, 1)
                dve.wait_ge(k.vectors, v0 + 3 * t + WEIGHTS)
                k.vchain(nc.vector.tensor_reduce(den, w, AX_X, ALU.add))
                k.vchain(nc.vector.scalar_tensor_tensor(out=den, in0=den, scalar=-1.0, in1=den, op0=ALU.mult, op1=ALU.max))
                k.vchain(nc.vector.tensor_tensor(den, den, low, ALU.max))
                k.vchain(nc.vector.reciprocal(den, den))
                dve.wait_ge(k.products, p0 + 3 * t + MIXED)
                o = out[:, t, 0:256]
                k.vchain(nc.vector.tensor_tensor(o.rearrange("p (h d) -> p h d", h=4), k.ps[:, 1, 0:256].rearrange("p (h d) -> p h d", h=4),
                                                 along(den, 64), ALU.mult))
                nc.vector.tensor_tensor(o, o, k.tok[:, t, 256:512], ALU.mult).then_inc(k.vectors, 1)

        @block.scalar
        def _(act):
            for t in range(TT):
                keys = (t + 1) * P
                act.wait_ge(k.vectors, v0 + 3 * t + SHIFTED)
                nc.scalar.activation(low, low, ACT.Exp, scale=-1.0)
                nc.scalar.activation(w_s[:, :, 0:keys], w_s[:, :, 0:keys], ACT.Exp).then_inc(k.activations, 1)
                act.wait_ge(k.products, p0 + 3 * t + TURNED)
                nc.scalar.copy(w_t[:, 0:t + 1, :, :].rearrange("p j h q -> p (j h q)"),
                               k.ps[:, 6:7 + t, :].rearrange("p b n -> p (b n)")).then_inc(k.activations, 1)
    k.advance(products=6, vectors=6, activations=4)


def stick_breaking(k, out):
    nc = k.nc
    s = Scratch(k)
    W = TT * P + P
    z, mag, sp_ = [s.take(4 * W).rearrange("p (h n) -> p h n", h=4) for _ in range(3)]
    p0, v0, a0 = k.starts()

    def q(h):
        return k.chan[64 * (h % 2):64 * (h % 2) + 64, 8 + h // 2, PAD:PAD + S]

    def key(h):
        return k.chan[64 * (h % 2):64 * (h % 2) + 64, 10 + h // 2, PAD:PAD + S]

    def v(t, h):
        return k.tok[:, t, 512 + h * 64:512 + (h + 1) * 64]
    pairs = [(g, slice(2 * g, 2 * g + 2)) for g in range(2)]
    with nc.Block() as block:
        @block.tensor
        def _(pe):
            for g, pair in pairs:
                for h in (2 * g, 2 * g + 1):
                    nc.tensor.matmul(k.ps[:, h, 0:S], key(h)[:, 0:P], q(h), start=True, stop=True)
                    last = nc.tensor.matmul(k.ps[:, h, S:W], key(h)[:, P:S], q(h)[:, P:S], start=True, stop=True)
                last.then_inc(k.products, 1)
            for g, pair in pairs:
                pe.wait_ge(k.vectors, v0 + 3 + g)
                for h in (2 * g, 2 * g + 1):
                    nc.tensor.matmul(k.ps[:, 4 + h, 0:P], k.const("lower"), sp_[:, h, 0:P], start=True, stop=True)
                    nc.tensor.matmul(k.ps[:, 4 + h, P:S], k.const("lower"), sp_[:, h, P:S], start=True, stop=False)
                    nc.tensor.matmul(k.ps[:, 4 + h, P:S], k.const("ones"), sp_[:, h, S:W], start=False, stop=True)
                    last = nc.tensor.matmul(k.ps[:, 4 + h, S:W], k.const("lower"), sp_[:, h, S:W], start=True, stop=True)
                last.then_inc(k.products, 1)
            for g, pair in pairs:
                pe.wait_ge(k.activations, a0 + 3 + g)
                for h in (2 * g, 2 * g + 1):
                    c = slice(h % 2 * 64, (h % 2 + 1) * 64)
                    nc.tensor.matmul(k.ps[:, 2 * g, c], z[:, h, 0:P], v(0, h), start=True, stop=True)
                    nc.tensor.matmul(k.ps[:, 2 * g + 1, c], z[:, h, P:S], v(0, h), start=True, stop=False)
                    last = nc.tensor.matmul(k.ps[:, 2 * g + 1, c], z[:, h, S:W], v(1, h), start=False, stop=True)
                last.then_inc(k.products, 1)

        @block.vector
        def _(dve):
            for g, pair in pairs:
                dve.wait_ge(k.products, p0 + 1 + g)
                k.vchain(nc.vector.tensor_scalar(z[:, pair], k.ps[:, pair, 0:W], SB_D ** -0.5, None, ALU.mult))
                softplus_vector(k, dve, z[:, pair], mag[:, pair]).then_inc(k.vectors, 1)
            for g, pair in pairs:
                dve.wait_ge(k.activations, a0 + 1 + g)
                k.vchain(nc.vector.scalar_tensor_tensor(out=sp_[:, pair], in0=z[:, pair], scalar=0.0, in1=mag[:, pair], op0=ALU.max, op1=ALU.add))
                nc.vector.tensor_tensor(sp_[:, pair, 0:P], sp_[:, pair, 0:P], over(k.const("upper_strict"), 2), ALU.mult)
                nc.vector.tensor_tensor(sp_[:, pair, S:W], sp_[:, pair, S:W], over(k.const("upper_strict"), 2), ALU.mult).then_inc(k.vectors, 1)
            for g, pair in pairs:
                dve.wait_ge(k.products, p0 + 3 + g)
                k.vchain(nc.vector.tensor_tensor(z[:, pair], z[:, pair], k.ps[:, 4 + 2 * g:6 + 2 * g, 0:W], ALU.subtract))
                nc.vector.tensor_tensor(z[:, pair, 0:P], z[:, pair, 0:P], over(k.const("neg_not_upper_strict"), 2), ALU.add)
                nc.vector.tensor_tensor(z[:, pair, S:W], z[:, pair, S:W], over(k.const("neg_not_upper_strict"), 2), ALU.add).then_inc(k.vectors, 1)
            for g, pair in pairs:
                dve.wait_ge(k.products, p0 + 5 + g)
                nc.vector.tensor_copy(out[:, :, g * P:(g + 1) * P], k.ps[:, pair, 0:P])

        @block.scalar
        def _(act):
            for g, pair in pairs:
                act.wait_ge(k.vectors, v0 + 1 + g)
                softplus_scalar(k, mag[:, pair]).then_inc(k.activations, 1)
            for g, pair in pairs:
                act.wait_ge(k.vectors, v0 + 5 + g)
                nc.scalar.activation(z[:, pair], z[:, pair], ACT.Exp).then_inc(k.activations, 1)
    k.advance(products=6, vectors=6, activations=4)


def ffn_slot(k, slot):
    return k.ring[:, slot * SLOT:(slot + 1) * SLOT].rearrange("p (g c n) -> p g c n", g=2, n=S)


def ffn_part(k):
    w = k.ins["w_ffn_in_2"][0].rearrange("(c p) (g n) -> p g c n", p=P, g=2)
    return {"w": lambda n: w[:, :, :, bass.ds(n * S, S)], "width": 2 * S, "tiles": FF // S}


class FfnStream(Stream):
    def tile(self, part, n, slot):
        return ffn_slot(self.k, slot), part["w"](n)


def gated_ffn(k, dst, stream, ahead):
    nc = k.nc
    part, = stream.parts
    n_tiles, first, start, free = part["tiles"], part["first_slot"], part["start"], part["copied"]
    s_at = FFC * S
    half = k.ring[:, 2 * SLOT + s_at:2 * SLOT + s_at + 2 * BANK].rearrange("p (u n) -> p u n", u=2)
    silu_done = [k.sem(f"silu_done{u}") for u in range(2)]
    with nc.Block() as block:
        @block.sync
        def _(sp):
            def load(i, u, slot):
                dst, src = stream.tile(part, 2 * i + u, slot)
                sp.wait_ge(k.tile_done[slot], i + (start[slot] + 1))
                sp.dma_start(dst, src).then_inc(k.w_landed[slot], 16)
            each_tile(sp, n_tiles, first, load, skip=stream.skip)
            issue(k, sp, ahead)

        @block.tensor
        def _(pe):
            def multiply(i, u, slot):
                w = ffn_slot(k, slot)
                pe.wait_ge(k.w_landed[slot], i * 16 + 16 * (start[slot] + 1))
                pe.wait_ge(k.psum_free[slot], i + (free[slot] + 1))
                for g in range(2):
                    for n in range(2):
                        for c in range(DC):
                            last = nc.tensor.matmul(k.ps[:, 2 * slot + g, n * S:(n + 1) * S], w[:, g, c, n * P:(n + 1) * P],
                                                    k.hT[:, c, :], start=c == 0, stop=c == DC - 1)
                last.then_inc(k.tile_done[slot], 1)
            each_tile(pe, n_tiles, first, multiply)

        @block.scalar
        def _(act):
            def gate(i, u, slot):
                act.wait_ge(k.tile_done[slot], i + (start[slot] + 2))
                act.wait_ge(k.psum_free[slot], i + (free[slot] + 1))
                nc.scalar.activation(half[:, slot, :], k.ps[:, 2 * slot, :], ACT.Silu).then_inc(silu_done[slot], 1)
            each_tile(act, n_tiles, first, gate)

        @block.vector
        def _(dve):
            def up(i, u, slot):
                dve.wait_ge(silu_done[slot], i + 1)
                nc.vector.tensor_tensor(dst[:, bass.ds(i * (4 * S) + 2 * S * u, 2 * S)], half[:, slot, :], k.ps[:, 2 * slot + 1, :], ALU.mult)\
                    .then_inc(k.psum_free[slot], 1)
            each_tile(dve, n_tiles, first, up)


def second_layer(k):
    nc, w = k.nc, k.ins["w_in_2"]
    stream = Stream(k, [
        chan_part(k, w, 0, 512, 2, 0),
        chan_part(k, w, 1544, 512, 1, 8),
        tok_part(k, w, 1024, 256, 1, 0),
        tok_part(k, w, 1280, 256, 1, 256, ACT.Sigmoid),
        tok_part(k, w, 2056, 256, 1, 512),
        tok_part(k, w, 2312, 512, 2, 768, ACT.Sigmoid),
        tok_part(k, w, 2312 + 2 * 512, 512, 2, 768 + 2 * 512, ACT.Sigmoid),
        tok_part(k, w, 2312 + 4 * 512, 512, 2, 768 + 4 * 512, ACT.Sigmoid),
    ])
    turn(k, k.xn, DC, k.hT, scale=lambda c: k.col("norm_mix_g_2", c), norm_of=k.x, ahead=stream.ahead())
    s = SecondScratch(k)
    beside, counts = lru_and_weights(k, s, stream.parts[0], k.chan[:, 0:2, PAD:PAD + S])
    project(k, k.hT, stream, narrow=(k.narrow_w[:, 64:128].rearrange("p (c n) -> p c n", n=8), k.small[:, :, 0:8], 8), **beside)
    k.advance(**counts)
    mlstm(k, s, k.xn)
    turn(k, k.xn, 2, k.hT[:, 2:4, :])
    stick_breaking(k, k.xn)
    names = ("w_out_lru_2", "w_out_mlstm_2", "w_out_sb_2")
    stream = WideStream(k, [{"lhs": lambda c, n=n: k.hT[:, 2 * n + c, :] if n else k.chan[:, c, PAD:PAD + S], "w": k.ins[name][0], "chunks": 2,
                             "out": ("gate_add" if n else "gate_set", k.xn, k.tok[:, :, 768 + n * D:768 + (n + 1) * D])}
                            for n, name in enumerate(names)])
    turn(k, k.xn, 2, k.hT[:, 4:6, :], ahead=stream.ahead())
    project_wide(k, stream)
    stream = WideStream(k, [{"lhs": lambda c: k.hT[:, c, :], "w": k.ins["w_o_2"][0], "chunks": DC, "out": ("add", k.x)}])
    turn(k, k.xn, DC, k.hT, ahead=stream.ahead())
    project_wide(k, stream)

    act = k.ring[:, 2 * SLOT:2 * SLOT + FFC * S]
    stream = FfnStream(k, [ffn_part(k)])
    wide = WideStream(k, [{"lhs": lambda c: act[:, c * S:(c + 1) * S], "w": k.ins["w_ffn_out_2"][0], "chunks": FFC, "out": ("add", k.x)}])
    turn(k, k.xn, DC, k.hT, scale=lambda c: k.col("norm_ffn_g_2", c), norm_of=k.x, ahead=stream.ahead())
    gated_ffn(k, act, stream, wide.ahead())
    project_wide(k, wide)
    norm_rows(k, k.ins["final_norm_g_2"])



def load_bias(k, sp, mirrored, landed):
    rpb = k.ins["na_rpb_3"]
    rows, cols = 2 * NA_ROWS - 1, 2 * NA_COLS - 1
    n_rows = S // GRID
    v = mirrored.rearrange("p (t h n) -> p t h n", t=TT, h=NA_H)
    for r in range(n_rows):
        at = GRID * (1 - r % 2)
        for i in range(n_rows):
            first = (NA_ROWS - 1 - r + i) * cols + NA_COLS - 1 - (GRID - 1)
            src = bass.AP(tensor=rpb.tensor, offset=rpb.offset + first, ap=[[1, GRID], [rows * cols, NA_H], [1, GRID]])
            sp.dma_start(v[at:at + GRID, r // 2, :, i * GRID:(i + 1) * GRID], src).then_inc(landed, 16)
    return n_rows ** 2


class RwkvScratch:

    def __init__(self, k):
        n6 = 6 * S
        first = 2 * SLOT

        def chans(n):
            return k.ring[:, first + n * n6:first + (n + 1) * n6].rearrange("p (d s) -> p d s", s=S)
        self.r, self.kt, self.v, self.b, self.a, self.w_log, self.L, self.prod = [chans(n) for n in range(8)]
        at = first + 8 * n6
        self.tmp = k.ring[:, at:at + 10 * S].rearrange("p (c s) -> p c s", s=S)
        at += 10 * S
        self.lora = k.ring[:, at:at + 2 * RW_W].rearrange("p (d n) -> p d n", d=2)
        at += 2 * RW_W
        self.lat = k.ring[:, at:at + 2 * S].rearrange("p (d s) -> p d s", d=2)
        at += 2 * S
        self.lat_g = k.ring[:, at:at + S]
        assert at + S <= RING * SLOT
        self.g_w = k.xn[:, 0, 0:RW_W]
        self.decay_c = k.stat[:, 0:24].rearrange("p (d j) -> p d j", j=4)
        self.rk = k.stat[:, 24:48]
        W = RW_M * 64

        def squares(ap):
            return ap.rearrange("p (m n) -> p m n", n=64)
        self.A_t, self.X, self.Y, self.U, self.ak = [squares(k.ring[:, n * W:(n + 1) * W]) for n in range(5)]
        at = first + 5 * n6
        self.rb = squares(k.ring[:, at:at + W])
        self.rkm = squares(k.chan[:, 6:16, :].rearrange("p c s -> p (c s)")[:, 0:W])
        at += W
        self.tokens = [k.ring[:, at + n * TT * 768:at + (n + 1) * TT * 768].rearrange("p (d n) -> p d n", n=P) for n in range(4)]
        assert 5 * W <= first and at + 4 * TT * 768 <= RING * SLOT
        self.XA = k.ring[:, first + n6:first + 2 * n6].rearrange("p (d n) -> p d n", n=P)
        self.XW, self.Z, self.W1 = [squares(k.ring[:, first + (2 + n) * n6:first + (3 + n) * n6]) for n in range(3)]
        self.y, self.bonus = self.X, self.U


def rwkv_inputs(k, s, shifted_parts):
    nc = k.nc
    r, kt, v, b, a, w_log, L, prod, tmp = s.r, s.kt, s.v, s.b, s.a, s.w_log, s.L, s.prod, s.tmp
    lora, lat, lat_g = s.lora, s.lat, s.lat_g
    kk, decay, tmp6 = a, w_log, tmp[:, 0:6, :]
    mu_w = PARAM_ROWS["rw_mu_w_3"]
    p0, v0, a0 = k.starts()
    l0 = k.count["loads"]
    MIXED, SQUARES, LOG_DECAY, BONUS, NORM_SQUARES, NORMALISED = [v0 + n for n in range(1, 7)]
    LATENT, DECAY_RATES, RATES, NORMS, DECAYS = [a0 + n for n in range(1, 6)]
    W_SUMS, A_SUMS, SUMS = [p0 + n for n in range(1, 4)]

    def sync(sp):
        for d in range(2):
            sp.dma_start(lora[0:64, d, :], k.ins["rw_w2_3"][0, d]).then_inc(k.loads, 16)
            sp.dma_start(lora[64:128, d, :], k.ins["rw_a2_3"][0, d]).then_inc(k.loads, 16)
        sp.dma_start(s.g_w, k.ins["rw_g2_3"][0]).then_inc(k.loads, 16)

    def vector(dve):
        for part in shifted_parts:
            wait_copied(k, dve, part)
        for d in range(2):
            here = k.chan[:, 6:16, PAD:PAD + S]
            there = k.chan[:, 6:16, PAD - 1 + 2 * d:PAD - 1 + 2 * d + S]
            k.vchain(nc.vector.tensor_tensor(tmp, there, here, ALU.subtract))
            for n in range(10):
                mu = k.col("rw_mu_rkv_3", d * 9 + n) if n < 9 else k.cols[:, 1, mu_w[1] + d:mu_w[1] + d + 1]
                dst = (r, kt, v)[n // 3][:, 3 * d + n % 3, :] if n < 9 else lat[:, d, :]
                last = nc.vector.scalar_tensor_tensor(out=dst[:, ::-1] if d else dst, in0=tmp[:, n, :], scalar=mu,
                                                      in1=k.chan[:, 6 + n, PAD:PAD + S], op0=ALU.mult, op1=ALU.add)
            k.vchain(last)
        dve.sem_inc(k.vectors, 1)
        for n in range(6):
            last = nc.vector.tensor_scalar(kk[:, n, :], kt[:, n, :], k.col("rw_k_k_3", n % 3), None, ALU.mult)
        k.vchain(last)
        nc.vector.tensor_tensor(tmp6, kk, kk, ALU.mult).then_inc(k.vectors, 1)
        dve.wait_ge(k.activations, DECAY_RATES)
        k.vchain(nc.vector.tensor_scalar(w_log, w_log, -float(np.exp(-0.5)), None, ALU.mult))
        for n in range(3):
            last = nc.vector.tensor_tensor_scan(L[:, 2 * n:2 * n + 2, :].rearrange("p d s -> p (d s)"), k.const("not_chunk_start"),
                                                w_log[:, 2 * n:2 * n + 2, :].rearrange("p d s -> p (d s)"), 0.0, ALU.mult, ALU.add)
        k.vchain(last)
        nc.vector.tensor_tensor(decay, L, w_log, ALU.subtract).then_inc(k.vectors, 1)
        dve.wait_ge(k.activations, RATES)
        for n in range(6):
            last = nc.vector.tensor_scalar(prod[:, n, :], b[:, n, :], -1.0, k.col("rw_k_a_3", n % 3), ALU.add, ALU.mult)
        k.vchain(last)
        k.vchain(nc.vector.scalar_tensor_tensor(out=kt, in0=prod, scalar=1.0, in1=kt, op0=ALU.add, op1=ALU.mult))
        for n in range(6):
            last = nc.vector.scalar_tensor_tensor(out=prod[:, n, :], in0=r[:, n, :], scalar=k.col("rw_r_k_3", n % 3),
                                                  in1=kt[:, n, :], op0=ALU.mult, op1=ALU.mult)
        k.vchain(last)
        dve.sem_inc(k.vectors, 1)
        dve.wait_ge(k.products, SUMS)
        nc.vector.tensor_scalar(tmp6, k.ps[:, 4:7, :].rearrange("p b (m s) -> p (b m) s", s=S), k.const("tiny"), None, ALU.max).then_inc(k.vectors, 1)
        nc.vector.tensor_copy(s.rk.rearrange("p (h t d) -> p t d h", h=2, t=TT), k.ps[:, 7, 0:24].rearrange("p (t d h) -> p t d h", t=TT, h=2))
        dve.wait_ge(k.activations, NORMS)
        k.vchain(nc.vector.tensor_tensor(kk, kk, tmp6, ALU.mult))
        dve.sem_inc(k.vectors, 1)
        k.vchain(nc.vector.tensor_tensor(b, b, kk, ALU.mult))
        dve.wait_ge(k.activations, DECAYS)
        nc.vector.scalar_tensor_tensor(out=a, in0=kk, scalar=-1.0, in1=decay, op0=ALU.mult, op1=ALU.mult)
        nc.vector.tensor_tensor(b, b, tmp6, ALU.mult)
        nc.vector.tensor_tensor(kt, kt, tmp6, ALU.mult)
        k.vchain(nc.vector.tensor_tensor(r, r, L, ALU.mult))
        nc.vector.tensor_copy(s.decay_c.rearrange("p d j -> p (d j)"), L.rearrange("p d (j s) -> p (d j) s", s=64)[:, :, 63])

    def latent(act):
        act.wait_ge(k.vectors, MIXED)
        nc.scalar.activation(lat_g, k.chan[:, 16, PAD:PAD + S], ACT.Sigmoid)
        k.achain(nc.scalar.activation(lat[0:64], lat[0:64], ACT.Tanh))
        act.sem_inc(k.activations, 1)

    def low_rank(rows, t):
        def products(pe):
            if t == 0:
                pe.wait_ge(k.loads, 16 * (l0 + 5))
                pe.wait_ge(k.activations, LATENT)
            else:
                pe.wait_ge(k.activations, DECAY_RATES)
            for n in range(6):
                nc.tensor.matmul(k.ps[:, 4 + n // 2, n % 2 * S:(n % 2 + 1) * S], lora[rows, n // 3, n % 3 * P:(n % 3 + 1) * P],
                                 lat[rows, n // 3, :], start=True, stop=True)
            nc.tensor.matmul(k.ps[:, 7, 0:RW_W], lat_g[:, t * P:(t + 1) * P], s.g_w, start=True, stop=True).then_inc(k.products, 1)
        return products

    def sigmoids(dst, bias, t):
        def read(act):
            act.wait_ge(k.products, (W_SUMS, A_SUMS)[t])
            for n in range(6):
                nc.scalar.activation(dst[:, n, :], k.ps[:, 4 + n // 2, n % 2 * S:(n % 2 + 1) * S], ACT.Sigmoid, bias=k.col(bias, n))
            nc.scalar.copy(k.tok[:, t, RW_W:2 * RW_W], k.ps[:, 7, 0:RW_W]).then_inc(k.activations, 1)
        return read

    def sums(pe):
        pe.wait_ge(k.vectors, SQUARES)
        pe.wait_ge(k.activations, RATES)
        for n in range(3):
            nc.tensor.matmul(k.ps[:, 4 + n, :], k.const("half_ones"), tmp[:, 2 * n:2 * n + 2, :].rearrange("p c s -> p (c s)"), start=True, stop=True)
        pe.wait_ge(k.vectors, BONUS)
        for t in range(TT):
            for n in range(6):
                last = nc.tensor.matmul(k.ps[:, 7, 12 * t + 2 * n:12 * t + 2 * n + 2], prod[:, n, t * P:(t + 1) * P], k.const("half_of"), start=True, stop=True)
        last.then_inc(k.products, 1)

    def decays(act):
        act.wait_ge(k.vectors, NORM_SQUARES)
        k.achain(nc.scalar.activation(tmp6, tmp6, ACT.Ln, scale=float(2.0 ** 17)))
        nc.scalar.activation(tmp6, tmp6, ACT.Exp, scale=-0.5, bias=k.const("ln_norm_scale")).then_inc(k.activations, 1)
        nc.scalar.activation(decay, decay, ACT.Exp)
        act.wait_ge(k.vectors, NORMALISED)
        nc.scalar.activation(tmp6, L, ACT.Exp, scale=-1.0)
        k.achain(nc.scalar.activation(L, L, ACT.Exp))
        act.sem_inc(k.activations, 1)
    between = {4: {"scalar": latent},
               5: {"tensor": low_rank(slice(0, 64), 0), "scalar": sigmoids(w_log, "rw_w0_3", 0)},
               6: {"tensor": low_rank(slice(64, 128), 1), "scalar": sigmoids(b, "rw_a0_3", 1)},
               7: {"tensor": sums, "scalar": decays}}
    return {"sync": sync, "vector": vector, "between": between}, {"products": 3, "vectors": 6, "activations": 5, "loads": 5}


def rwkv(k, s, out, mem, bias):
    nc = k.nc
    r, kt, v, b, a = s.r, s.kt, s.v, s.b, s.a
    decay_c, rk = s.decay_c, s.rk
    A_t, X, Y, U, ak, rb, rkm = s.A_t, s.X, s.Y, s.U, s.ak, s.rb, s.rkm
    a_tok, b_tok, k_tok, v_tok = s.tokens
    XA, XW, Z, W1, y, bonus = s.XA, s.XW, s.Z, s.W1, s.y, s.bonus
    M = RW_M
    xn = out.rearrange("p t n -> p (t n)")
    state = [xn[:, n * 384:(n + 1) * 384].rearrange("p (d n) -> p d n", n=64) for n in range(4)]

    def bank_units(first, m, n):
        return k.ps[:, first:first + (m * n + BANK - 1) // BANK, :].rearrange("p b n -> p (b n)")[:, 0:m * n].rearrange("p (m n) -> p m n", n=n)

    def rows64(j):
        return slice(64 * j, 64 * j + 64)

    kinds = [(a, b), (b, a), (kt, a), (b, r), (kt, r)]
    turned_at = (4, 0, 4, 0)
    p0, v0, a0 = k.starts()
    with nc.Block() as block:
        @block.tensor
        def _(pe):
            for n, (lhs, rhs) in enumerate(kinds):
                if n >= 2:
                    pe.wait_ge(k.vectors, v0 + n - 1)
                for half in range(2):
                    for j in range(2):
                        q = rows64(half)
                        for t in range(TT):
                            for dc in range(6):
                                at = 6 * t + dc
                                tk = slice(t * P + 64 * j, t * P + 64 * j + 64)
                                last = nc.tensor.matmul(k.ps[rows64(j), 4 * (n % 2) + 2 * half + at // 8, at % 8 * 64:(at % 8 + 1) * 64],
                                                        lhs[q, dc, tk], rhs[q, dc, tk], start=True, stop=True)
                last.then_inc(k.products, 1)
            for n, src in enumerate((a, b, kt, v)):
                if n < 2:
                    pe.wait_ge(k.vectors, v0 + 4 + n)
                else:
                    pe.wait_ge(k.activations, a0 + n - 1)
                for at in range(TT * 6):
                    last = nc.tensor.transpose(k.ps[:, turned_at[n] + at // 4, at % 4 * P:(at % 4 + 1) * P],
                                               src[:, at % 6, at // 6 * P:(at // 6 + 1) * P], k.const("ident"))
                last.then_inc(k.products, 1)

        @block.vector
        def _(dve):
            def masked(n, dst, scale, mask):
                dve.wait_ge(k.products, p0 + n + 1)
                for half in range(2):
                    last = nc.vector.scalar_tensor_tensor(out=dst[:, 12 * half:12 * half + 12, :], in0=bank_units(4 * (n % 2) + 2 * half, 12, 64),
                                                          scalar=scale, in1=over(mask, 12), op0=ALU.mult, op1=ALU.mult)
                last.then_inc(k.vectors, 1)
            masked(0, X, -1.0, k.const("chunk_level0"))
            masked(1, A_t, -1.0, k.const("chunk_half_upper_strict"))
            masked(2, ak, 1.0, k.const("chunk_half_upper_strict"))
            masked(3, rb, 1.0, k.const("chunk_half_upper"))
            masked(4, rkm, 1.0, k.const("chunk_half_upper"))
            nc.vector.memset(state[0], 0.0)
            dve.wait_ge(k.vectors, v0 + 2)
            k.vchain(nc.vector.tensor_tensor(Y, A_t, over(k.const("chunk_level0_t"), M), ALU.mult))
            nc.vector.tensor_tensor(X, X, over(k.const("chunk_ident"), M), ALU.add)
            nc.vector.tensor_tensor(Y, Y, over(k.const("chunk_ident"), M), ALU.add)

        @block.scalar
        def _(act):
            for n, dst in enumerate((a_tok, b_tok, k_tok, v_tok)):
                act.wait_ge(k.products, p0 + 6 + n)
                nc.scalar.copy(dst, bank_units(turned_at[n], TT * 6, P)).then_inc(k.activations, 1)
    k.advance(products=9, vectors=5, activations=4)

    GROUPS = M // 8
    low, high = slice(0, 32), slice(32, 64)
    p0, v0, a0 = k.starts()
    with nc.Block() as block:
        @block.tensor
        def _(pe):
            def products(bank, lhs, rhs, g):
                for j in range(2):
                    q = rows64(j)
                    for m in range(8):
                        last = nc.tensor.matmul(k.ps[q, bank, m * 64:(m + 1) * 64], lhs[q, 8 * g + m, :], rhs[q, 8 * g + m, :], start=True, stop=True)
                return last
            for n in range(4):
                before = v0 + 2 * GROUPS * n
                for g in range(GROUPS):
                    if n:
                        pe.wait_ge(k.vectors, before - GROUPS + g + 1)
                    products(g, A_t, X, g).then_inc(k.products, 1)
                for g in range(GROUPS):
                    pe.wait_ge(k.vectors, before + g + 1)
                    products(g, Y, U, g)
                    products(GROUPS + g, U, Y, g).then_inc(k.products, 1)

            def block_products(bank, lhs, rhs, g, lhs_cols, rhs_cols, rows, to):
                for j in range(2):
                    q, dst = slice(64 * j + rows, 64 * j + rows + 32), slice(64 * j + to, 64 * j + to + 32)
                    for m in range(8):
                        last = nc.tensor.matmul(k.ps[dst, bank, m * 32:(m + 1) * 32], lhs[q, 8 * g + m, lhs_cols], rhs[q, 8 * g + m, rhs_cols],
                                                start=True, stop=True)
                return last
            before = v0 + 2 * GROUPS * 4
            for g in range(GROUPS):
                pe.wait_ge(k.vectors, before - GROUPS + g + 1)
                block_products(g, A_t, X, g, high, low, 0, 32).then_inc(k.products, 1)
            for g in range(GROUPS):
                pe.wait_ge(k.vectors, before + g + 1)
                block_products(GROUPS + g, U, Y, g, low, high, 32, 0).then_inc(k.products, 1)

        @block.vector
        def _(dve):
            for n in range(4):
                before = p0 + 2 * GROUPS * n
                for g in range(GROUPS):
                    dve.wait_ge(k.products, before + g + 1)
                    nc.vector.tensor_tensor(U[:, 8 * g:8 * g + 8, :], bank_units(g, 8, 64), over(k.const(f"chunk_level{n + 1}"), 8), ALU.mult).then_inc(k.vectors, 1)
                for g in range(GROUPS):
                    dve.wait_ge(k.products, before + GROUPS + g + 1)
                    nc.vector.tensor_tensor(X[:, 8 * g:8 * g + 8, :], X[:, 8 * g:8 * g + 8, :], bank_units(g, 8, 64), ALU.add)
                    nc.vector.tensor_tensor(Y[:, 8 * g:8 * g + 8, :], Y[:, 8 * g:8 * g + 8, :], bank_units(GROUPS + g, 8, 64), ALU.add).then_inc(k.vectors, 1)
            before = p0 + 2 * GROUPS * 4
            for g in range(GROUPS):
                dve.wait_ge(k.products, before + g + 1)
                for j in range(2):
                    q = slice(64 * j + 32, 64 * j + 64)
                    last = nc.vector.tensor_scalar(U[q, 8 * g:8 * g + 8, low], bank_units(g, 8, 32)[q], -1.0, None, ALU.mult)
                last.then_inc(k.vectors, 1)
            for g in range(GROUPS):
                dve.wait_ge(k.products, before + GROUPS + g + 1)
                for j in range(2):
                    q = slice(64 * j, 64 * j + 32)
                    last = nc.vector.tensor_tensor(Y[q, 8 * g:8 * g + 8, high], Y[q, 8 * g:8 * g + 8, high], bank_units(GROUPS + g, 8, 32)[q], ALU.add)
                last.then_inc(k.vectors, 1)
    k.advance(products=2 * GROUPS * 5, vectors=2 * GROUPS * 5)

    p0, v0, a0 = k.starts()
    units = [(half, t, dc) for half in range(2) for t in range(TT) for dc in range(6)]
    STEPS = 2 * TT
    with nc.Block() as block:
        @block.tensor
        def _(pe):
            for j in range(2):
                q = rows64(j)
                for m, (half, t, dc) in enumerate(units):
                    last = nc.tensor.matmul(bank_units(0, M, 64)[q, m, :], ak[q, m, :], v_tok[q, 6 * t + dc, rows64(half)], start=True, stop=True)
            last.then_inc(k.products, 1)
            for j in range(2):
                q = rows64(j)
                for m, (half, t, dc) in enumerate(units):
                    at = 6 * t + dc
                    last = nc.tensor.matmul(k.ps[rows64(half), 4 + 2 * j + at // 8, at % 8 * 64:(at % 8 + 1) * 64],
                                            a_tok[q, at, rows64(half)], Y[q, m, :], start=True, stop=True)
            last.then_inc(k.products, 1)
            pe.wait_ge(k.vectors, v0 + 1)
            for j in range(2):
                q = rows64(j)
                for m in range(M):
                    last = nc.tensor.matmul(bank_units(0, M, 64)[q, m, :], Y[q, m, :], W1[q, m, :], start=True, stop=True)
            last.then_inc(k.products, 1)
            for step in range(STEPS):
                t, j = step // 2, step % 2
                tk = rows64(j)
                pe.wait_ge(k.vectors, v0 + 2 + 2 * step)
                pe.wait_ge(k.activations, a0 + 1 + step)
                for bank, lhs in ((4, XA), (6, r)):
                    for half in range(2):
                        q = rows64(half)
                        for dc in range(6):
                            rows = lhs[q, 6 * t + dc, tk] if bank == 4 else lhs[q, dc, t * P + 64 * j:t * P + 64 * j + 64]
                            last = nc.tensor.matmul(k.ps[tk, bank + half, dc * 64:(dc + 1) * 64], rows, state[step][q, dc, :], start=True, stop=True)
                    last.then_inc(k.products, 1)
                pe.wait_ge(k.vectors, v0 + 3 + 2 * step)
                if step < STEPS - 1:
                    for half in range(2):
                        q = rows64(half)
                        for dc in range(6):
                            nc.tensor.matmul(k.ps[q, 3, dc * 64:(dc + 1) * 64], b_tok[tk, 6 * t + dc, q], Z[tk, 12 * half + 6 * t + dc, :], start=True, stop=False)
                            last = nc.tensor.matmul(k.ps[q, 3, dc * 64:(dc + 1) * 64], k_tok[tk, 6 * t + dc, q], v_tok[tk, 6 * t + dc, q], start=False, stop=True)
                    last.then_inc(k.products, 1)
                for m, (half, t_m, dc) in enumerate(units):
                    if t_m == t:
                        nc.tensor.matmul(bank_units(0, M, 64)[tk, m, :], rb[tk, m, :], Z[tk, m, :], start=True, stop=False)
                        last = nc.tensor.matmul(bank_units(0, M, 64)[tk, m, :], rkm[tk, m, :], v_tok[tk, 6 * t + dc, rows64(half)], start=False, stop=True)
            last.then_inc(k.products, 1)

        @block.vector
        def _(dve):
            dve.wait_ge(k.products, p0 + 1)
            nc.vector.tensor_copy(W1, bank_units(0, M, 64)).then_inc(k.vectors, 1)
            dve.wait_ge(k.products, p0 + 3)
            nc.vector.tensor_copy(XW, bank_units(0, M, 64)).then_inc(k.vectors, 1)
            dve.wait_ge(k.vectors, v0 + 2)
            for step in range(STEPS):
                t, tk = step // 2, rows64(step % 2)
                dve.wait_ge(k.products, p0 + 4 + 3 * step)
                for half in range(2):
                    m = slice(12 * half + 6 * t, 12 * half + 6 * t + 6)
                    last = nc.vector.tensor_tensor(Z[tk, m, :], XW[tk, m, :], k.ps[tk, 4 + half, 0:384].rearrange("p (d n) -> p d n", n=64), ALU.add)
                last.then_inc(k.vectors, 1)
                if step < STEPS - 1:
                    dve.wait_ge(k.products, p0 + 6 + 3 * step)
                    new = state[step + 1]
                    k.vchain(nc.vector.tensor_tensor(new, state[step], k.ps[:, 3, 0:384].rearrange("p (d n) -> p d n", n=64), ALU.add))
                    nc.vector.tensor_tensor(new, new, along(decay_c[:, :, step], 64), ALU.mult).then_inc(k.vectors, 1)
            for half in range(2):
                m = slice(12 * half, 12 * half + 12)
                nc.vector.tensor_tensor(bonus[:, m, :], v_tok[:, :, rows64(half)], along(rk[:, m], 64), ALU.mult)
            dve.wait_ge(k.products, p0 + 3 * STEPS + 3)
            dve.wait_ge(k.activations, a0 + 1 + STEPS)
            nc.vector.tensor_tensor(y, y, bank_units(0, M, 64), ALU.add)

        @block.scalar
        def _(act):
            act.wait_ge(k.products, p0 + 2)
            for j in range(2):
                last = nc.scalar.copy(XA[:, :, rows64(j)], bank_units(4 + 2 * j, 12, 64))
            last.then_inc(k.activations, 1)
            for step in range(STEPS):
                t, tk = step // 2, rows64(step % 2)
                act.wait_ge(k.products, p0 + 5 + 3 * step)
                for half in range(2):
                    last = nc.scalar.copy(y[tk, 12 * half + 6 * t:12 * half + 6 * t + 6, :], k.ps[tk, 6 + half, 0:384].rearrange("p (d n) -> p d n", n=64))
                last.then_inc(k.activations, 1)
    k.advance(products=3 + 3 * STEPS, vectors=1 + 2 * STEPS, activations=1 + STEPS)

    rest = Scratch(k, first_slot=3)
    junk = rest.take(TT * D).rearrange("p (t n) -> p t n", t=TT)
    rest.take(SLOT - TT * D)
    gain, offset = rest.take(RW_W), rest.take(RW_W)
    sq, extra = [rest.take(TT * RW_W).rearrange("p (t n) -> p t n", t=TT) for _ in range(2)]
    mirrored = k.ring[:, 2 * SLOT:2 * SLOT + TT * NA_H * S]
    banks = TT * NA_H * S // BANK
    mean, rstd = k.stat[:, 48:60], k.stat[:, 60:72]
    mem_sums, mem_rstd = k.stat[:, 72:74], k.stat[:, 74:76]
    yo = out[:, :, 0:RW_W]
    mem_landed, bias_landed = k.sem("mem_landed"), k.sem("bias_landed")
    BIAS_LOADS = (S // GRID) ** 2
    p0, v0, a0 = k.starts()
    loads0 = k.count["loads"]
    with nc.Block() as block:
        @block.sync
        def _(sp):
            sp.dma_start(mem, k.ins["mem_3"].rearrange("b (t p) d -> p (b t) d", p=P)).then_inc(mem_landed, 16)
            sp.dma_start(gain, k.ins["rw_ln_g_3"].partition_broadcast(P).rearrange("p a n -> p (a n)")).then_inc(k.loads, 16)
            sp.dma_start(offset, k.ins["rw_ln_b_3"].partition_broadcast(P).rearrange("p a n -> p (a n)")).then_inc(k.loads, 16)
            load_bias(k, sp, mirrored, bias_landed)

        @block.tensor
        def _(pe):
            for n, src in enumerate((y, bonus)):
                both = src.rearrange("p (h t d c) n -> p t d c h n", h=2, t=TT, d=2)
                for t in range(TT):
                    nc.tensor.matmul(k.ps[:, 2 * n + t, 0:RW_W], k.const("ident"), both[:, t, 0], start=True, stop=False)
                    last = nc.tensor.matmul(k.ps[:, 2 * n + t, 0:RW_W], k.const("anti"), both[:, 1 - t, 1], start=False, stop=True)
            last.then_inc(k.products, 1)
            pe.wait_ge(bias_landed, 16 * BIAS_LOADS)
            pe.wait_ge(k.vectors, v0 + 1)
            for b in range(banks):
                last = nc.tensor.matmul(k.ps[:, b, :], k.const("anti"), mirrored[:, b * BANK:(b + 1) * BANK], start=True, stop=True)
            last.then_inc(k.products, 1)

        @block.vector
        def _(dve):
            def heads(ap):
                return ap.rearrange("p (h n) -> p h n", n=64)
            dve.wait_ge(k.products, p0 + 1)
            nc.vector.tensor_copy(extra, k.ps[:, 2:4, 0:RW_W])
            k.vchain(nc.vector.tensor_copy(yo, k.ps[:, 0:2, 0:RW_W]))
            for t in range(TT):
                last = nc.vector.tensor_reduce(mean[:, 6 * t:6 * t + 6], heads(yo[:, t]), AX_X, ALU.add)
            k.vchain(last)
            k.vchain(nc.vector.tensor_scalar(mean, mean, 1.0 / 64, None, ALU.mult))
            for t in range(TT):
                last = nc.vector.tensor_tensor(heads(yo[:, t]), heads(yo[:, t]), along(mean[:, 6 * t:6 * t + 6], 64), ALU.subtract)
            k.vchain(last)
            k.vchain(nc.vector.tensor_tensor(sq, yo, yo, ALU.mult))
            nc.vector.tensor_reduce(rstd, sq.rearrange("p t (h n) -> p (t h) n", n=64), AX_X, ALU.add).then_inc(k.vectors, 1)
            dve.wait_ge(k.activations, a0 + 1)
            for t in range(TT):
                nc.vector.tensor_scalar(mem[:, t, :], mem[:, t, :], mem_rstd[:, t:t + 1], None, ALU.mult)
            dve.wait_ge(k.activations, a0 + 2)
            dve.wait_ge(k.loads, 16 * (loads0 + 2))
            for t in range(TT):
                last = nc.vector.tensor_tensor(heads(yo[:, t]), heads(yo[:, t]), along(rstd[:, 6 * t:6 * t + 6], 64), ALU.mult)
            k.vchain(last)
            k.vchain(nc.vector.tensor_tensor(yo, yo, over(gain, TT), ALU.mult))
            k.vchain(nc.vector.tensor_tensor(yo, yo, over(offset, TT), ALU.add))
            k.vchain(nc.vector.tensor_tensor(yo, yo, extra, ALU.add))
            nc.vector.tensor_tensor(yo, yo, k.tok[:, :, RW_W:2 * RW_W], ALU.mult)
            dve.wait_ge(k.products, p0 + 2)
            nc.vector.tensor_tensor(bias.rearrange("p (m c) -> p m c", c=GRID), k.ps[:, 0:banks, :].rearrange("p b (m c) -> p (b m) c", c=GRID),
                                    over(k.const("window"), TT * NA_H * S // GRID), ALU.add)

        @block.scalar
        def _(act):
            act.wait_ge(mem_landed, 16)
            for t in range(TT):
                last = nc.scalar.activation(junk[:, t, :], mem[:, t, :], ACT.Square, accum_out=mem_sums[:, t:t + 1])
            k.achain(last)
            k.achain(nc.scalar.activation(mem_rstd, mem_sums, ACT.Ln, bias=k.const("eps"), scale=1.0 / D))
            nc.scalar.activation(mem_rstd, mem_rstd, ACT.Exp, scale=-0.5).then_inc(k.activations, 1)
            act.wait_ge(k.vectors, v0 + 1)
            k.achain(nc.scalar.activation(rstd, rstd, ACT.Ln, bias=k.const("gn_eps"), scale=1.0 / 64))
            nc.scalar.activation(rstd, rstd, ACT.Exp, scale=-0.5).then_inc(k.activations, 1)
    k.advance(products=2, vectors=1, activations=2, loads=2)


def expert_tiles(k):
    def w_in(name, n):
        return lambda e: k.ins[name][0, bass.ds(e, 1), :, n * TILE:(n + 1) * TILE].rearrange("a (c p) n -> p (a c) n", p=P)

    def w_down(n):
        return lambda e: k.ins["w_exp_down_3"][0, bass.ds(e, 1), n * TILE:(n + 1) * TILE, :].rearrange("a (c p) n -> p (a c) n", p=P)
    tiles = []
    for n in range(EFF // TILE):
        tiles += [(w_in("w_exp_gate_3", n), TILE), (w_in("w_exp_up_3", n), TILE)]
    return tiles + [(w_down(n), D) for n in range(EFF // TILE)]


def expert_choice(k):
    nc = k.nc
    turn(k, k.xn, DC, k.hT, scale=lambda c: k.col("norm_ffn_g_3", c), norm_of=k.x)
    tok = k.tok[:, :, :].rearrange("p t n -> p (t n)")
    xeT = tok[:, 0:4096].rearrange("p (c n) -> p c n", c=DC)
    one_hot = tok[:, 4096:5120].rearrange("p (t n) -> p t n", t=TT)
    weighted = tok[:, 5120:6144].rearrange("p (t n) -> p t n", t=TT)
    rows = tok[0:EXP, 6144:6144 + 5 * S].rearrange("p (n s) -> p n s", s=S)
    aff_t, work, chosen, number, ones = [rows[:, n, :] for n in range(5)]
    back = k.chan[:, :, :].rearrange("p c s -> p (c s)")[:, 0:EXP * S].rearrange("p (e s) -> p e s", e=EXP)
    aff = k.stat[:, 0:2 * EXP].rearrange("p (t e) -> p t e", t=TT)
    pos = k.stat[:, 32:32 + 2 * EXP].rearrange("p (t e) -> p t e", t=TT)
    top, total = k.stat[:, 64:66], k.stat[:, 66:68]
    best = k.stat[0:EXP, 72:80]
    router = k.narrow_w[:, 128:256].rearrange("p (c n) -> p c n", n=EXP)
    tiles = expert_tiles(k)
    n_tiles = len(tiles)
    base = list(k.tiles)
    first = n_tiles // RING

    refills = k.sem("refills")

    def load(sp, e, q, before):
        src, width = tiles[q]
        u = q % RING
        dst = k.ring[:, u * SLOT:(u + 1) * SLOT].rearrange("p (c n) -> p c n", n=width)
        sp.wait_ge(k.tile_done[u], before)
        sp.sem_inc(refills, 1)
        sp.dma_start(dst, src(e)).then_inc(k.w_landed[u], 16)

    p0, v0, a0 = k.starts()
    with nc.Block() as block:
        @block.sync
        def _(sp):
            for q in range(RING):
                load(sp, 0, q, base[q] + 1)

        @block.tensor
        def _(pe):
            for t in range(TT):
                for c in range(DC):
                    last = nc.tensor.matmul(k.ps[:, 0, t * EXP:(t + 1) * EXP], k.hT[:, c, t * P:(t + 1) * P], router[:, c, :],
                                            start=c == 0, stop=c == DC - 1)
            last.then_inc(k.products, 1)
            pe.wait_ge(k.vectors, v0 + 2)
            for t in range(TT):
                last = nc.tensor.transpose(k.ps[0:EXP, 1, t * P:(t + 1) * P], aff[:, t, :], k.const("ident"))
            last.then_inc(k.products, 1)
            pe.wait_ge(k.vectors, v0 + 3)
            for t in range(TT):
                last = nc.tensor.transpose(k.ps[:, 2, t * EXP:(t + 1) * EXP], number[:, t * P:(t + 1) * P], k.const("ident")[0:EXP, 0:EXP])
            last.then_inc(k.products, 1)

        @block.scalar
        def _(act):
            act.wait_ge(k.vectors, v0 + 1)
            nc.scalar.activation(aff, aff, ACT.Exp).then_inc(k.activations, 1)

        @block.vector
        def _(dve):
            nc.vector.memset(ones, 1.0)
            dve.wait_ge(k.products, p0 + 1)
            k.vchain(nc.vector.tensor_copy(aff, k.ps[:, 0, 0:2 * EXP].rearrange("p (t e) -> p t e", t=TT)))
            k.vchain(nc.vector.tensor_reduce(top, aff, AX_X, ALU.max))
            nc.vector.tensor_tensor(aff, aff, along(top, EXP), ALU.subtract).then_inc(k.vectors, 1)
            dve.wait_ge(k.activations, a0 + 1)
            k.vchain(nc.vector.tensor_reduce(total, aff, AX_X, ALU.add))
            k.vchain(nc.vector.reciprocal(total, total))
            nc.vector.tensor_tensor(aff, aff, along(total, EXP), ALU.mult).then_inc(k.vectors, 1)
            dve.wait_ge(k.products, p0 + 2)
            k.vchain(nc.vector.tensor_copy(aff_t, k.ps[0:EXP, 1, 0:S]))
            for n in range(CAP // 8):
                src = aff_t if n == 0 else work
                k.vchain(nc.vector.max(best, src))
                k.vchain(nc.vector.match_replace(work, best, src, -1.0))
            k.vchain(nc.vector.tensor_scalar(chosen, work, 0.0, None, ALU.is_lt))
            k.vchain(nc.vector.tensor_tensor_scan(number, ones, chosen, 0.0, ALU.mult, ALU.add))
            k.vchain(nc.vector.tensor_tensor(number, number, chosen, ALU.mult))
            nc.vector.tensor_scalar(number, number, -1.0, None, ALU.add).then_inc(k.vectors, 1)
            dve.wait_ge(k.products, p0 + 3)
            k.vchain(nc.vector.tensor_copy(pos, k.ps[:, 2, 0:2 * EXP].rearrange("p (t e) -> p t e", t=TT)))
            for t in range(TT):
                hot = one_hot[:, t, :].rearrange("p (e j) -> p e j", e=EXP)
                last = nc.vector.tensor_tensor(hot, over(k.const("slot_number"), EXP), along(pos[:, t, :], CAP), ALU.is_equal)
            k.vchain(last)
            for t in range(TT):
                hot = one_hot[:, t, :].rearrange("p (e j) -> p e j", e=EXP)
                nc.vector.tensor_tensor(weighted[:, t, :].rearrange("p (e j) -> p e j", e=EXP), hot, along(aff[:, t, :], CAP), ALU.mult)
    k.advance(products=3, vectors=3, activations=1)

    p0, v0, a0 = k.starts()
    order = [2, 3, 4, 5, 6, 7, 0, 1]
    even, odd = order[0::2], order[1::2]
    turned_w = k.hT[:, 0:4, :]
    with nc.Block() as block:
        @block.tensor
        def _(pe):
            for g in range(4):
                for t in range(TT):
                    last = nc.tensor.transpose(k.ps[:, g // 2, g % 2 * S + t * P:g % 2 * S + (t + 1) * P],
                                               weighted[:, t, g * P:(g + 1) * P], k.const("ident"))
            last.then_inc(k.products, 1)
            for c in order:
                if c == 0:
                    pe.wait_ge(k.vectors, v0 + 1)
                for t in range(TT):
                    last = nc.tensor.matmul(k.ps[:, c, :], k.xn[:, t, c * P:(c + 1) * P], one_hot[:, t, :], start=t == 0, stop=t == TT - 1)
                last.then_inc(k.products, 1)
            for n in order:
                if n % 2:
                    pe.wait_ge(k.activations, a0 + odd.index(n) + 1)
                else:
                    pe.wait_ge(k.vectors, v0 + even.index(n) + 2)
                for e in (2 * n, 2 * n + 1):
                    last = nc.tensor.matmul(k.ps[:, n, e % 2 * S:(e % 2 + 1) * S], k.const(f"four_times{e % 4}"), turned_w[:, e // 4, :], start=True, stop=True)
                last.then_inc(k.products, 1)

        @block.vector
        def _(dve):
            dve.wait_ge(k.products, p0 + 1)
            nc.vector.tensor_copy(turned_w.rearrange("p g s -> p (g s)"), k.ps[:, 0:2, :].rearrange("p b n -> p (b n)")).then_inc(k.vectors, 1)
            for c in even:
                dve.wait_ge(k.products, p0 + 2 + order.index(c))
                nc.vector.tensor_scalar(xeT[:, c, :], k.ps[:, c, :], k.col("norm_ffn_g_3", c), None, ALU.mult).then_inc(k.vectors, 1)
            for n in even:
                dve.wait_ge(k.products, p0 + 2 + DC + order.index(n))
                nc.vector.tensor_copy(back[:, 2 * n:2 * n + 2, :].rearrange("p e s -> p (e s)"), k.ps[:, n, :])

        @block.scalar
        def _(act):
            for c in odd:
                act.wait_ge(k.products, p0 + 2 + order.index(c))
                nc.scalar.activation(xeT[:, c, :], k.ps[:, c, :], ACT.Copy, scale=k.col("norm_ffn_g_3", c)).then_inc(k.activations, 1)
            for n in odd:
                act.wait_ge(k.products, p0 + 2 + DC + order.index(n))
                nc.scalar.copy(back[:, 2 * n:2 * n + 2, :].rearrange("p e s -> p (e s)"), k.ps[:, n, :])
    k.advance(products=2 * DC + 1, vectors=DC // 2 + 1, activations=DC // 2)

    hT = k.hT[:, :, :].rearrange("p c s -> p (c s)")
    xn = k.xn[:, :, :].rearrange("p t n -> p (t n)")
    part = [[hT[:, (2 * g + n) * TILE:(2 * g + n + 1) * TILE] for n in range(2)] for g in range(2)]
    y = xn[:, 0:D]
    xe = xn[:, D:D + DC * CAP].rearrange("p (c n) -> p c n", c=DC)
    act_t = xn[:, D + 256:D + 256 + EFF // P * CAP].rearrange("p (f n) -> p f n", n=CAP)
    gated = xn[:, D + 768:D + 768 + 4 * CAP]
    way = tok[:, 4096:4096 + S]
    zeros = tok[:, 4608:4608 + BANK]
    xe_ready = k.sem("expert_tokens_ready")
    last_up = (2 * (EFF // TILE) - 1) % RING
    way_ready, way_used = k.sem("way_back_ready"), k.sem("way_back_used")
    gate_copied, up_copied = k.sem("gate_copied"), k.sem("up_copied")
    turned, silu, hidden = k.sem("turned"), k.sem("silu"), k.sem("hidden")
    y_done, y_copied0, y_copied1 = k.sem("y_done"), k.sem("y_copied0"), k.sem("y_copied1")
    zeroed = k.sem("zeroed")
    NG = EFF // TILE
    with nc.Block() as block:
        @block.sync
        def _(sp):
            with sp.Fori(0, EXP - 1) as e:
                for q in range(RING, n_tiles + RING):
                    u, turn_of_ring = q % RING, q // RING
                    load(sp, e if q < n_tiles else e + 1, q % n_tiles, e * first + (base[u] + 1 + turn_of_ring))
            for q in range(RING, n_tiles):
                load(sp, EXP - 1, q, (EXP - 1) * first + base[q % RING] + 1 + q // RING)

        @block.gpsimd
        def _(pool):
            nc.gpsimd.memset(zeros, 0.0).then_inc(zeroed, 1)
            nc.gpsimd.tensor_copy(xe, xeT[:, :, 0:CAP]).then_inc(xe_ready, 1)
            nc.gpsimd.tensor_copy(way, back[:, 0, :]).then_inc(way_ready, 1)
            with pool.Fori(1, EXP) as e:
                pool.wait_ge(k.tile_done[last_up], e * first + (base[last_up] + 1))
                nc.gpsimd.tensor_copy(xe, xeT[:, :, bass.ds(e * CAP, CAP)]).then_inc(xe_ready, 1)
                pool.wait_ge(way_used, e)
                nc.gpsimd.tensor_copy(way, back[:, bass.ds(e, 1), :].rearrange("p e s -> p (e s)")).then_inc(way_ready, 1)

        @block.tensor
        def _(pe):
            pe.wait_ge(zeroed, 1)
            for b in range(4):
                nc.tensor.matmul(k.ps[:, b, :], zeros[:, 0:P], zeros, start=True, stop=True, skip_group_check=True)
            for sem in (gate_copied, up_copied, y_copied0, y_copied1):
                pe.sem_inc(sem, 1)

            def slot(q, width):
                u = q % RING
                return k.ring[:, u * SLOT:(u + 1) * SLOT].rearrange("p (c n) -> p c n", n=width)

            def landed(e, q):
                u = q % RING
                pe.wait_ge(k.w_landed[u], e * (16 * first) + 16 * (base[u] + 1 + q // RING))

            def gate_up(e, n):
                for g, copied in enumerate((gate_copied, up_copied)):
                    landed(e, 2 * n + g)
                    pe.wait_ge(copied, e * NG + (n + 1))
                    if n == 0:
                        pe.wait_ge((y_copied0, y_copied1)[g], e + 1)
                    for half in range(2):
                        for j in range(4):
                            c = 4 * half + j
                            last = nc.tensor.matmul(k.ps[32 * j:32 * j + 32, 4 + g, :], xe[:, c, :], slot(2 * n + g, TILE)[:, c, :],
                                                    start=half == 0, stop=half == 1)
                    last.then_inc(k.tile_done[(2 * n + g) % RING], 1)

            def turn_part(e, n):
                pe.wait_ge(gate_copied, e * NG + (n + 2))
                pe.wait_ge(up_copied, e * NG + (n + 2))
                if n >= 2:
                    pe.wait_ge(hidden, e * NG + (n - 1))
                for g in range(2):
                    for i in range(4):
                        last = nc.tensor.matmul(k.ps[:, 6 + n % 2, (4 * g + i) * CAP:(4 * g + i + 1) * CAP], part[g][n % 2][:, i * P:(i + 1) * P],
                                                k.const("four_idents"), start=True, stop=True)
                last.then_inc(turned, 1)

            with pe.Fori(0, EXP) as e:
                pe.wait_ge(xe_ready, e + 1)
                gate_up(e, 0)
                for n in range(1, NG):
                    gate_up(e, n)
                    turn_part(e, n - 1)
                turn_part(e, NG - 1)
                for n in range(NG):
                    pe.wait_ge(hidden, e * NG + (n + 1))
                    landed(e, 2 * NG + n)
                    for h in range(2):
                        for j in range(4):
                            last = nc.tensor.matmul(k.ps[32 * j:32 * j + 32, 4 + h, :], act_t[:, 4 * n + j, :],
                                                    slot(2 * NG + n, D)[:, j, h * BANK:(h + 1) * BANK], start=n == 0, stop=n == NG - 1)
                    last.then_inc(k.tile_done[(2 * NG + n) % RING], 1)
                pe.wait_ge(way_ready, e + 1)
                for h in range(2):
                    pe.wait_ge((y_copied0, y_copied1)[h], e + 2)
                    for t in range(TT):
                        last = nc.tensor.matmul(k.ps[:, 2 * t + h, :], way[:, t * P:(t + 1) * P], y[:, h * BANK:(h + 1) * BANK],
                                                start=False, stop=True, skip_group_check=True)
                last.then_inc(way_used, 1)

        @block.scalar
        def _(act):
            with act.Fori(0, EXP) as e:
                def copy(n):
                    u = (2 * n) % RING
                    act.wait_ge(k.tile_done[u], e * first + (base[u] + 2 + 2 * n // RING))
                    if n >= 2:
                        act.wait_ge(turned, e * NG + (n - 1))
                    nc.scalar.copy(part[0][n % 2], k.ps[:, 4, :]).then_inc(gate_copied, 1)

                def gate(n):
                    act.wait_ge(turned, e * NG + (n + 1))
                    if n:
                        act.wait_ge(hidden, e * NG + n)
                    nc.scalar.activation(gated, k.ps[:, 6 + n % 2, 0:4 * CAP], ACT.Silu).then_inc(silu, 1)
                copy(0)
                for n in range(1, NG):
                    copy(n)
                    gate(n - 1)
                gate(NG - 1)
                u = (3 * NG - 1) % RING
                act.wait_ge(k.tile_done[u], e * first + (base[u] + 2 + (3 * NG - 1) // RING))
                nc.scalar.copy(y[:, 0:BANK], k.ps[:, 4, :]).then_inc(y_copied0, 1)

        @block.vector
        def _(dve):
            with dve.Fori(0, EXP) as e:
                def copy(n):
                    u = (2 * n + 1) % RING
                    dve.wait_ge(k.tile_done[u], e * first + (base[u] + 2 + (2 * n + 1) // RING))
                    if n >= 2:
                        dve.wait_ge(turned, e * NG + (n - 1))
                    nc.vector.tensor_copy(part[1][n % 2], k.ps[:, 5, :]).then_inc(up_copied, 1)

                def gate(n):
                    dve.wait_ge(silu, e * NG + (n + 1))
                    nc.vector.tensor_tensor(act_t[:, 4 * n:4 * n + 4, :].rearrange("p f n -> p (f n)"), gated, k.ps[:, 6 + n % 2, 4 * CAP:8 * CAP], ALU.mult)\
                        .then_inc(hidden, 1)
                copy(0)
                for n in range(1, NG):
                    copy(n)
                    gate(n - 1)
                gate(NG - 1)
                u = (3 * NG - 1) % RING
                dve.wait_ge(k.tile_done[u], e * first + (base[u] + 2 + (3 * NG - 1) // RING))
                nc.vector.tensor_copy(y[:, BANK:D], k.ps[:, 5, :]).then_inc(y_copied1, 1)
            dve.wait_ge(way_used, EXP)
            for t in range(TT):
                nc.vector.tensor_tensor(k.x[:, t, :], k.x[:, t, :], k.ps[:, 2 * t:2 * t + 2, :].rearrange("p b n -> p (b n)"), ALU.add)
    for u in range(RING):
        k.tiles[u] += first * EXP


def third_layer(k):
    nc, w = k.nc, k.ins["w_in_3"]
    stream = Stream(k, [
        chan_part(k, w, 0, 384, 2, 0),
        chan_part(k, w, 1152, 384, 3, 6),
        chan_part(k, w, 2304, 512, 1, 15),
        tok_part(k, w, 768, 384, 1, 0),
        *[tok_part(k, w, 2816 + n * 512, 512, tiles, 768 + n * 512, ACT.Sigmoid) for n, tiles in enumerate((1, 1, 1, 1, 2))],
    ])
    turn(k, k.xn, DC, k.hT, scale=lambda c: k.col("norm_mix_g_3", c), norm_of=k.x, ahead=stream.ahead())
    s = RwkvScratch(k)
    beside, counts = rwkv_inputs(k, s, stream.parts[1:3])
    project(k, k.hT, stream, **beside)
    k.advance(**counts)
    n = TT * NA_H * S
    bias = k.ring[:, RING * SLOT - n:RING * SLOT]
    mem_at = RING * SLOT - n - TT * D
    mem = k.ring[:, mem_at:mem_at + TT * D].rearrange("p (t n) -> p t n", t=TT)
    rwkv(k, s, k.xn, mem, bias)
    turn(k, k.xn, 3, k.chan[:, 6:9, PAD:PAD + S])

    def heads(chunk):
        return lambda h: k.chan[64 * (h % 2):64 * (h % 2) + 64, chunk + h // 2, PAD:PAD + S]

    def values(at):
        return lambda t, h: k.tok[:, t, at + h * HD:at + (h + 1) * HD]
    by_tile = bias.rearrange("p (t h n) -> p t h n", t=TT, h=NA_H)
    attention(k, NA_H, heads(0), heads(3), values(0), HD ** -0.5, lambda t: by_tile[:, t], k.xn)
    turn(k, k.xn, 3, k.chan[:, 0:3, PAD:PAD + S])
    stream = Stream(k, [chan_part(k, k.ins["w_mem_kv_3"], 0, 256, 1, 3), tok_part(k, k.ins["w_mem_kv_3"], 256, 256, 1, 0)])
    turn(k, mem, DC, k.hT, scale=lambda c: k.col("norm_mem_g_3", c), ahead=stream.ahead())
    project(k, k.hT, stream)
    attention(k, MEM_H, heads(17), heads(3), values(0), HD ** -0.5, None, k.xn)
    stream = WideStream(k, [
        {"lhs": lambda c: k.chan[:, c, PAD:PAD + S], "w": k.ins["w_branch_na_3"][0], "chunks": 3, "out": ("gate_set", k.xn, k.tok[:, :, 768:1792])},
        {"lhs": lambda c: k.chan[:, 6 + c, PAD:PAD + S], "w": k.ins["w_branch_rw_3"][0], "chunks": 3, "out": ("gate_add", k.xn, k.tok[:, :, 1792:2816])},
        {"lhs": lambda c: k.hT[:, 6 + c, :], "w": k.ins["w_branch_mem_3"][0], "chunks": 2, "out": ("gate_add", k.xn, k.tok[:, :, 2816:3840])},
    ])
    turn(k, k.xn, 2, k.hT[:, 6:8, :], ahead=stream.ahead())
    project_wide(k, stream)
    stream = WideStream(k, [{"lhs": lambda c: k.hT[:, c, :], "w": k.ins["w_out_3"][0], "chunks": DC, "out": ("add", k.x)}])
    turn(k, k.xn, DC, k.hT, ahead=stream.ahead())
    project_wide(k, stream)
    expert_choice(k)
    norm_rows(k, k.ins["norm_final_g_3"])


def norm_rows(k, gain_row):
    nc = k.nc
    s = Scratch(k)
    gain = s.take(D)
    squares = s.take(TT * D).rearrange("p (t n) -> p t n", t=TT)
    sums, rstd = k.stat[:, 0:2], k.stat[:, 2:4]
    p0, v0, a0 = k.starts()
    with nc.Block() as block:
        @block.sync
        def _(sp):
            sp.dma_start(gain, gain_row.partition_broadcast(P)).then_inc(k.loads, 16)

        @block.scalar
        def _(act):
            for t in range(TT):
                last = nc.scalar.activation(squares[:, t, :], k.x[:, t, :], ACT.Square, accum_out=sums[:, t:t + 1])
            k.achain(last)
            k.achain(nc.scalar.activation(rstd, sums, ACT.Ln, bias=k.const("eps"), scale=1.0 / D))
            nc.scalar.activation(rstd, rstd, ACT.Exp, scale=-0.5).then_inc(k.activations, 1)

        @block.vector
        def _(dve):
            dve.wait_ge(k.activations, a0 + 1)
            dve.wait_ge(k.loads, 16 * (k.count["loads"] + 1))
            for t in range(TT):
                nc.vector.scalar_tensor_tensor(out=k.x[:, t, :], in0=k.x[:, t, :], scalar=rstd[:, t:t + 1], in1=gain, op0=ALU.mult, op1=ALU.mult)
    k.advance(activations=1, loads=1)


def store(k, out):
    nc = k.nc
    stored = k.sem("stored")
    with nc.Block() as block:
        @block.sync
        def _(sp):
            sp.dma_start(out.rearrange("b (t p) d -> p (b t) d", p=P), k.x[:, :, :]).then_inc(stored, 16)
            sp.wait_ge(stored, 16)


def program(nc, x, ins, out):
    with ExitStack() as ctx:
        k = Chip(nc, ctx, ins)
        load_parameters(k, x)
        first_layer(k)
        second_layer(k)
        third_layer(k)
        store(k, out)


def kernel(**inputs):
    import concourse.bacc as bacc
    from concourse.bass_utils import run_bass_kernel_spmd as run

    nc = bacc.Bacc("TRN2", target_bir_lowering=False, num_devices=1)
    arrays = {name: np.ascontiguousarray(a) for name, a in inputs.items()}
    arrays["constants"] = np.concatenate(list(constant_tables().values()), axis=1)
    aps = {name: nc.dram_tensor(f"in_{name}", a.shape, mybir.dt.from_np(a.dtype), kind="ExternalInput").ap()
           for name, a in arrays.items()}
    out = nc.dram_tensor("out", (1, S, D), F32, kind="ExternalOutput").ap()
    program(nc, aps["x"], aps, out)
    r = run(nc, [{f"in_{name}": a for name, a in arrays.items()}], core_ids=[0])
    return r.results[0]["out"]
```
